# Optimizing a Trainium2 kernel written in Bass

```python
import jax, jax.numpy as jnp
from jax import lax
import numpy as np
import math
import jax
import jax.numpy as jnp

D_MODEL = 1024
BATCH = 1
SEQ = 1024
DEPTH = 1

N_META = 16
HGRN_HEAD_V = 128
HGRN_WIDTH = D_MODEL // 2
HGRN_HEADS = HGRN_WIDTH // HGRN_HEAD_V
HGRN_EXPAND = 128
HGRN_KDIM = HGRN_HEADS * HGRN_EXPAND
CHUNK = 64
POOL_WINDOWS = (2, 4, 8, 16)
POOL_GROUPS = len(POOL_WINDOWS)
POOL_WIDTH = D_MODEL // 2
POOL_GROUP_DIM = POOL_WIDTH // POOL_GROUPS
D_FF = 2816
CONV_WIDTH = 3
EPS = 1e-6
LOG_FLOOR = 1e-30
SPLITS = (HGRN_KDIM, HGRN_KDIM, HGRN_WIDTH, HGRN_WIDTH, POOL_WIDTH, D_MODEL, D_MODEL)
IN_COLS = sum(SPLITS)


def rmsnorm(x, gain):
    xf = x.astype(jnp.float32)
    y = xf * lax.rsqrt(jnp.mean(xf * xf, axis=-1, keepdims=True) + EPS)
    return (y * gain.astype(jnp.float32)).astype(x.dtype)

def _hgrn2_chunk_step(state, xs):
    q, k, v, lf = xs
    c = q.shape[2]
    b = jnp.cumsum(lf, axis=2)
    o_inter = jnp.einsum('bhtk,bhkv->bhtv', q * jnp.exp(b), state)
    diff = b[:, :, :, None, :] - b[:, :, None, :, :]
    causal = (jnp.arange(c)[:, None] >= jnp.arange(c)[None, :])[None, None, :, :, None]
    decay = jnp.where(causal, jnp.exp(jnp.where(causal, diff, 0.0)), 0.0)
    scores = jnp.einsum('bhtk,bhtsk,bhsk->bhts', q, decay, k)
    o_intra = jnp.einsum('bhts,bhsv->bhtv', scores, v)
    b_last = b[:, :, -1, :]
    k_dec = k * jnp.exp(b_last[:, :, None, :] - b)
    new_state = jnp.exp(b_last)[..., None] * state + jnp.einsum('bhsk,bhsv->bhkv', k_dec, v)
    return new_state, o_inter + o_intra

def hgrn2(q, f_logit, i, g, lb, out_gain):
    bsz, L, _ = q.shape
    lb = lb.astype(jnp.float32)
    fl = f_logit.astype(jnp.float32)
    f = lb + (1.0 - lb) * jax.nn.sigmoid(fl)
    log_f = jnp.log(jnp.maximum(f, LOG_FLOOR))
    k = (1.0 - lb) * jax.nn.sigmoid(-fl)
    pad = CHUNK - N_META
    def prep(t, d):
        t = jnp.pad(t.astype(jnp.float32), ((0, 0), (pad, 0), (0, 0)))
        n = t.shape[1] // CHUNK
        return t.reshape(bsz, n, CHUNK, HGRN_HEADS, d).transpose(1, 0, 3, 2, 4)
    xs = (prep(q, HGRN_EXPAND), prep(k, HGRN_EXPAND), prep(i, HGRN_HEAD_V), prep(log_f, HGRN_EXPAND))
    state0 = jnp.zeros((bsz, HGRN_HEADS, HGRN_EXPAND, HGRN_HEAD_V), jnp.float32)
    _, o = lax.scan(_hgrn2_chunk_step, state0, xs)
    o = o.transpose(1, 0, 3, 2, 4).reshape(bsz, -1, HGRN_HEADS, HGRN_HEAD_V)[:, pad:]
    o = o * lax.rsqrt(jnp.mean(o * o, axis=-1, keepdims=True) + EPS)
    o = o.reshape(bsz, L, HGRN_WIDTH) * out_gain.astype(jnp.float32)
    return o * jax.nn.sigmoid(g.astype(jnp.float32))

def multiscale_pool(v, proj, scale):
    bsz, L, _ = v.shape
    vg = v.astype(jnp.float32).reshape(bsz, L, POOL_GROUPS, POOL_GROUP_DIM)
    cs0 = jnp.pad(jnp.cumsum(vg, axis=1), ((0, 0), (1, 0), (0, 0), (0, 0)))
    t1 = jnp.arange(1, L + 1)
    outs = []
    for gi, w in enumerate(POOL_WINDOWS):
        hi = cs0[:, 1:, gi]
        lo = jnp.pad(cs0[:, :L + 1 - w, gi], ((0, 0), (w - 1, 0), (0, 0)))
        cnt = jnp.minimum(t1, w).astype(jnp.float32)[None, :, None]
        outs.append((hi - lo) / cnt - vg[:, :, gi])
    pooled = jnp.stack(outs, axis=2)
    y = jnp.einsum('blgc,gcd->blgd', pooled, proj.astype(jnp.float32))
    return y.reshape(bsz, L, POOL_WIDTH) * scale.astype(jnp.float32)

def causal_dwconv(x, w, b):
    L = x.shape[1]
    xp = jnp.pad(x, ((0, 0), (CONV_WIDTH - 1, 0), (0, 0)))
    y = b
    for j in range(CONV_WIDTH):
        y = y + xp[:, j:j + L] * w[j]
    return y

def first_inputs(seed: int = 0) -> dict:
    key = jax.random.key(seed)
    ks = jax.random.split(key, 24)
    nrm = lambda k, shape, s: jax.random.normal(k, shape, jnp.float32) * s
    gain = lambda k, shape: 1.0 + nrm(k, shape, 0.05)
    return {
        "x": nrm(ks[0], (BATCH, SEQ, D_MODEL), 1.0),
        "meta_tokens": nrm(ks[1], (N_META, D_MODEL), 1.0),
        "mix_norm_pre": gain(ks[2], (DEPTH, D_MODEL)),
        "mix_norm_post": gain(ks[3], (DEPTH, D_MODEL)),
        "w_in": nrm(ks[4], (DEPTH, D_MODEL, IN_COLS), D_MODEL ** -0.5),
        "hgrn_lower_bounds": nrm(ks[5], (DEPTH, HGRN_KDIM), 0.5),
        "hgrn_out_norm": gain(ks[6], (DEPTH, HGRN_WIDTH)),
        "w_branch_hgrn": nrm(ks[7], (DEPTH, HGRN_WIDTH, D_MODEL), HGRN_WIDTH ** -0.5),
        "pool_proj": nrm(ks[8], (DEPTH, POOL_GROUPS, POOL_GROUP_DIM, POOL_GROUP_DIM), POOL_GROUP_DIM ** -0.5),
        "pool_scale": gain(ks[9], (DEPTH, POOL_WIDTH)),
        "w_branch_pool": nrm(ks[10], (DEPTH, POOL_WIDTH, D_MODEL), POOL_WIDTH ** -0.5),
        "w_out": nrm(ks[11], (DEPTH, D_MODEL, D_MODEL), D_MODEL ** -0.5),
        "ffn_norm_pre": gain(ks[12], (DEPTH, D_MODEL)),
        "ffn_norm_post": gain(ks[13], (DEPTH, D_MODEL)),
        "ffn_w_gate": nrm(ks[14], (DEPTH, D_MODEL, D_FF), D_MODEL ** -0.5),
        "ffn_w_up": nrm(ks[15], (DEPTH, D_MODEL, D_FF), D_MODEL ** -0.5),
        "ffn_conv_w": nrm(ks[16], (DEPTH, CONV_WIDTH, D_FF), CONV_WIDTH ** -0.5),
        "ffn_conv_b": nrm(ks[17], (DEPTH, D_FF), 0.02),
        "ffn_w_down": nrm(ks[18], (DEPTH, D_FF, D_MODEL), D_FF ** -0.5),
    }

def first_block(x, meta_tokens, mix_norm_pre, mix_norm_post, w_in, hgrn_lower_bounds, hgrn_out_norm,
              w_branch_hgrn, pool_proj, pool_scale, w_branch_pool, w_out, ffn_norm_pre, ffn_norm_post,
              ffn_w_gate, ffn_w_up, ffn_conv_w, ffn_conv_b, ffn_w_down):
    bsz = x.shape[0]
    meta = jnp.broadcast_to(meta_tokens[None].astype(x.dtype), (bsz, N_META, D_MODEL))
    h = jnp.concatenate([meta, x], axis=1)
    gam = jax.nn.softmax(hgrn_lower_bounds.astype(jnp.float32), axis=0)
    lbs = jnp.clip(jnp.cumsum(gam, axis=0) - gam[0], 0.0, 1.0)
    cuts = list(np.cumsum(SPLITS)[:-1])
    for l in range(DEPTH):
        u = rmsnorm(h, mix_norm_pre[l])
        proj = u @ w_in[l]
        q, f_logit, i_in, g_out, v_pool, gate_a, gate_b = jnp.split(proj, cuts, axis=-1)
        a = hgrn2(q, f_logit, i_in, g_out, lbs[l], hgrn_out_norm[l])
        p = multiscale_pool(v_pool, pool_proj[l], pool_scale[l])
        z = (jax.nn.sigmoid(gate_a.astype(jnp.float32)) * (a @ w_branch_hgrn[l])
             + jax.nn.sigmoid(gate_b.astype(jnp.float32)) * (p @ w_branch_pool[l]))
        h = h + rmsnorm(z @ w_out[l], mix_norm_post[l])
        u = rmsnorm(h, ffn_norm_pre[l])
        gt = causal_dwconv(u @ ffn_w_gate[l], ffn_conv_w[l], ffn_conv_b[l])
        y = (jax.nn.gelu(gt, approximate=True) * (u @ ffn_w_up[l])) @ ffn_w_down[l]
        h = h + rmsnorm(y, ffn_norm_post[l])
    return h[:, N_META:]


Q_BLOCK = 128
HEAD_DIM = 64
N_MIX_HEADS = D_MODEL // HEAD_DIM
MLA_HEADS = N_MIX_HEADS // 4
RWKV_HEADS = (N_MIX_HEADS - MLA_HEADS) // 2
GDN_HEADS = N_MIX_HEADS - MLA_HEADS - RWKV_HEADS
RWKV_WIDTH = RWKV_HEADS * HEAD_DIM
MLA_WIDTH = MLA_HEADS * HEAD_DIM
GDN_WIDTH = GDN_HEADS * HEAD_DIM
MIX_WIDTH = RWKV_WIDTH + MLA_WIDTH + GDN_WIDTH

RWKV_DECAY_LORA = 64
RWKV_ICLR_LORA = 64
RWKV_GATE_LORA = 128
RWKV_GN_EPS = 64e-5

MLA_NOPE_DIM = 64
MLA_ROPE_DIM = 32
MLA_QK_DIM = MLA_NOPE_DIM + MLA_ROPE_DIM
MLA_V_DIM = HEAD_DIM
MLA_Q_LORA = 256
MLA_KV_LORA = 128
ROPE_BASE = 10000.0

GDN_CONV = 4

D_FF_2 = 4 * D_MODEL
NORM_EPS = 1e-6

RWKV_SPLITS = (RWKV_WIDTH, RWKV_WIDTH, RWKV_WIDTH, RWKV_DECAY_LORA, RWKV_ICLR_LORA, RWKV_GATE_LORA)
MLA_SPLITS = (MLA_Q_LORA, MLA_KV_LORA, MLA_ROPE_DIM)
GDN_SPLITS = (GDN_WIDTH, GDN_WIDTH, GDN_WIDTH, GDN_WIDTH, GDN_HEADS, GDN_HEADS)
RWKV_IN = 3 * RWKV_WIDTH + RWKV_DECAY_LORA + RWKV_ICLR_LORA + RWKV_GATE_LORA
MLA_IN = MLA_Q_LORA + MLA_KV_LORA + MLA_ROPE_DIM
GDN_IN = 4 * GDN_WIDTH + 2 * GDN_HEADS
P_IN = RWKV_IN + MLA_IN + GDN_IN


def _split(t, sizes):
    idx = np.cumsum(np.array(sizes))[:-1].tolist()
    return jnp.split(t, idx, axis=-1)

def _rms(x, g, eps=NORM_EPS):
    xf = x.astype(jnp.float32)
    y = xf * lax.rsqrt(jnp.mean(xf * xf, axis=-1, keepdims=True) + eps)
    return (y * g.astype(jnp.float32)).astype(x.dtype)

def _l2norm(x, eps=1e-6):
    xf = x.astype(jnp.float32)
    return xf * lax.rsqrt(jnp.sum(xf * xf, axis=-1, keepdims=True) + eps)

def _rope(t, cos, sin):
    t1, t2 = jnp.split(t, 2, axis=-1)
    return jnp.concatenate([t1 * cos - t2 * sin, t1 * sin + t2 * cos], axis=-1)

def rwkv7_time_mix(p, mu, w0, w2, a0, a2, g2, k_k, k_a, r_k, gn_g, gn_b):
    f32 = jnp.float32
    B, S, _ = p.shape
    p_prev = jnp.pad(p, ((0, 0), (1, 0), (0, 0)))[:, :-1]
    z = p + (p_prev - p) * mu
    r, k, v, zw, za, zg = _split(z, RWKV_SPLITS)
    w_logit = (w0 + jnp.tanh(zw) @ w2).astype(f32)
    decay = jnp.exp(-jnp.exp(-jax.nn.softplus(-w_logit) - 0.5))
    a = jax.nn.sigmoid((a0 + za @ a2).astype(f32))
    g = jax.nn.sigmoid(zg) @ g2
    hs = lambda t: t.reshape(B, S, RWKV_HEADS, HEAD_DIM).astype(f32)
    hp = lambda t: t.reshape(RWKV_HEADS, HEAD_DIM).astype(f32)
    r, k, v, a, decay = hs(r), hs(k), hs(v), hs(a), hs(decay)
    kk = _l2norm(k * hp(k_k))
    k = k * (1.0 + (a - 1.0) * hp(k_a))

    def step(state, inp):
        r_t, w_t, k_t, v_t, kk_t, b_t = inp
        sa = jnp.einsum('bhvk,bhk->bhv', state, -kk_t)
        state = (state * w_t[:, :, None, :] + sa[..., None] * b_t[:, :, None, :]
                 + v_t[..., None] * k_t[:, :, None, :])
        return state, jnp.einsum('bhvk,bhk->bhv', state, r_t)

    tm = lambda t: jnp.moveaxis(t, 1, 0)
    s0 = jnp.zeros((B, RWKV_HEADS, HEAD_DIM, HEAD_DIM), f32)
    _, y = lax.scan(step, s0, (tm(r), tm(decay), tm(k), tm(v), tm(kk), tm(kk * a)))
    y = jnp.moveaxis(y, 0, 1)
    mean = jnp.mean(y, axis=-1, keepdims=True)
    var = jnp.mean(jnp.square(y - mean), axis=-1, keepdims=True)
    y = ((y - mean) * lax.rsqrt(var + RWKV_GN_EPS)).reshape(B, S, RWKV_WIDTH)
    y = y * gn_g.astype(f32) + gn_b.astype(f32)
    bonus = jnp.sum(r * k * r_k.astype(f32), axis=-1, keepdims=True) * v
    y = y + bonus.reshape(B, S, RWKV_WIDTH)
    return (y * g.astype(f32)).astype(p.dtype)

def mla_attention(p, positions, q_norm_g, w_uq, kv_norm_g, w_ukv, q_qk_g, k_qk_g):
    f32 = jnp.float32
    B, S, _ = p.shape
    c_q, c_kv, k_rope = _split(p, MLA_SPLITS)
    q = (_rms(c_q, q_norm_g) @ w_uq).reshape(B, S, MLA_HEADS, MLA_QK_DIM)
    kv = (_rms(c_kv, kv_norm_g) @ w_ukv).reshape(B, S, MLA_HEADS, MLA_NOPE_DIM + MLA_V_DIM)
    k_nope, v = jnp.split(kv, [MLA_NOPE_DIM], axis=-1)
    k_rope = jnp.broadcast_to(k_rope[:, :, None, :], (B, S, MLA_HEADS, MLA_ROPE_DIM))
    k = jnp.concatenate([k_nope, k_rope], axis=-1)
    q = _rms(q, q_qk_g)
    k = _rms(k, k_qk_g)
    inv_freq = ROPE_BASE ** (-jnp.arange(0, MLA_ROPE_DIM, 2, dtype=f32) / MLA_ROPE_DIM)
    ang = positions.astype(f32)[..., None] * inv_freq
    cos = jnp.cos(ang)[:, :, None, :].astype(q.dtype)
    sin = jnp.sin(ang)[:, :, None, :].astype(q.dtype)
    q = jnp.concatenate([q[..., :MLA_NOPE_DIM], _rope(q[..., MLA_NOPE_DIM:], cos, sin)], axis=-1)
    k = jnp.concatenate([k[..., :MLA_NOPE_DIM], _rope(k[..., MLA_NOPE_DIM:], cos, sin)], axis=-1)
    scale = MLA_QK_DIM ** -0.5
    nb = S // Q_BLOCK
    qb = jnp.moveaxis(q.reshape(B, nb, Q_BLOCK, MLA_HEADS, MLA_QK_DIM), 1, 0)
    k_chunk = jnp.arange(S) // CHUNK

    def block(args):
        q_blk, i = args
        s = jnp.einsum('bqhd,bkhd->bhqk', q_blk, k).astype(f32) * scale
        q_chunk = (i * Q_BLOCK + jnp.arange(Q_BLOCK)) // CHUNK
        s = jnp.where(k_chunk[None, :] <= q_chunk[:, None], s, -jnp.inf)
        prob = jax.nn.softmax(s, axis=-1).astype(v.dtype)
        return jnp.einsum('bhqk,bkhd->bqhd', prob, v)

    o = lax.map(block, (qb, jnp.arange(nb)))
    return jnp.moveaxis(o, 0, 1).reshape(B, S, MLA_WIDTH)

def _chunk_gated_delta_rule(q, k, v, beta, g):
    B, S, H, Dk = q.shape
    Dv = v.shape[-1]
    NC, L = S // CHUNK, CHUNK
    ch = lambda t: jnp.moveaxis(t.reshape(B, NC, L, H, -1), 3, 1)
    q, k, v = ch(q), ch(k), ch(v)
    beta, g = ch(beta[..., None])[..., 0], ch(g[..., None])[..., 0]
    gc = jnp.cumsum(g, axis=-1)
    idx = jnp.arange(L)
    incl = idx[:, None] >= idx[None, :]
    strict = idx[:, None] > idx[None, :]
    decay = jnp.exp(jnp.where(incl, gc[..., :, None] - gc[..., None, :], -jnp.inf))
    A = jnp.where(strict, jnp.einsum('bhnld,bhnmd->bhnlm', k, k) * decay * beta[..., :, None], 0.0)
    rhs = jnp.concatenate([v * beta[..., None], k * (beta * jnp.exp(gc))[..., None]], axis=-1)
    sol = lax.linalg.triangular_solve(A + jnp.eye(L, dtype=A.dtype), rhs,
                                      left_side=True, lower=True, unit_diagonal=True)
    u, w = sol[..., :Dv], sol[..., Dv:]
    attn = jnp.einsum('bhnld,bhnmd->bhnlm', q, k) * decay
    q_dec = q * jnp.exp(gc)[..., None]
    k_dec = k * jnp.exp(gc[..., -1:] - gc)[..., None]
    chunk_decay = jnp.exp(gc[..., -1])

    def step(state, inp):
        u_c, w_c, attn_c, q_c, k_c, d_c = inp
        delta = u_c - jnp.einsum('bhlk,bhkv->bhlv', w_c, state)
        o_c = jnp.einsum('bhlk,bhkv->bhlv', q_c, state) + jnp.einsum('bhlm,bhmv->bhlv', attn_c, delta)
        state = d_c[..., None, None] * state + jnp.einsum('bhlk,bhlv->bhkv', k_c, delta)
        return state, o_c

    cm = lambda t: jnp.moveaxis(t, 2, 0)
    s0 = jnp.zeros((B, H, Dk, Dv), jnp.float32)
    _, o = lax.scan(step, s0, (cm(u), cm(w), cm(attn), cm(q_dec), cm(k_dec), cm(chunk_decay)))
    return jnp.transpose(o, (1, 0, 3, 2, 4)).reshape(B, S, H, Dv)

def gated_deltanet(p, conv_w, a_log, dt_bias, o_norm_g):
    f32 = jnp.float32
    B, S, _ = p.shape
    q, k, v, gate, b, a = _split(p, GDN_SPLITS)
    qkv = jnp.concatenate([q, k, v], axis=-1)
    qkv = lax.conv_general_dilated(qkv, conv_w[:, None, :].astype(qkv.dtype), window_strides=(1,),
                                   padding=[(GDN_CONV - 1, 0)], dimension_numbers=('NWC', 'WIO', 'NWC'),
                                   feature_group_count=3 * GDN_WIDTH)
    q, k, v = jnp.split(jax.nn.silu(qkv), 3, axis=-1)
    hd = lambda t: t.reshape(B, S, GDN_HEADS, HEAD_DIM)
    q = _l2norm(hd(q)) * (HEAD_DIM ** -0.5)
    k = _l2norm(hd(k))
    v = hd(v).astype(f32)
    beta = jax.nn.sigmoid(b.astype(f32))
    g = -jnp.exp(a_log.astype(f32)) * jax.nn.softplus(a.astype(f32) + dt_bias.astype(f32))
    o = _chunk_gated_delta_rule(q, k, v, beta, g)
    o = _rms(o, o_norm_g) * jax.nn.silu(hd(gate).astype(f32))
    return o.reshape(B, S, GDN_WIDTH).astype(p.dtype)

def second_inputs(seed: int = 0) -> dict:
    key = jax.random.key(seed)
    keys = list(jax.random.split(key, 40))
    f32 = jnp.float32
    L = DEPTH

    def nrm(shape, scale):
        return jax.random.normal(keys.pop(), shape, f32) * scale

    def gain(shape):
        return 1.0 + 0.05 * jax.random.normal(keys.pop(), shape, f32)

    inp = {}
    inp['x'] = nrm((BATCH, SEQ, D_MODEL), 1.0)
    inp['positions'] = jnp.tile(jnp.arange(SEQ, dtype=jnp.int32)[None, :], (BATCH, 1))
    inp['ln_mix_g'] = gain((L, D_MODEL))
    inp['w_in'] = nrm((L, D_MODEL, P_IN), D_MODEL ** -0.5)
    inp['w_out'] = nrm((L, MIX_WIDTH, D_MODEL), MIX_WIDTH ** -0.5)
    inp['ln_ffn_g'] = gain((L, D_MODEL))
    inp['w_ff1'] = nrm((L, D_MODEL, D_FF_2), D_MODEL ** -0.5)
    inp['w_ff2'] = nrm((L, D_FF_2, D_MODEL), D_FF_2 ** -0.5)
    inp['rwkv_mu'] = jax.random.uniform(keys.pop(), (L, RWKV_IN), f32, 0.0, 1.0)
    inp['rwkv_w0'] = jax.random.uniform(keys.pop(), (L, RWKV_WIDTH), f32, -6.0, 1.0)
    inp['rwkv_w2'] = nrm((L, RWKV_DECAY_LORA, RWKV_WIDTH), 0.5 * RWKV_DECAY_LORA ** -0.5)
    inp['rwkv_a0'] = nrm((L, RWKV_WIDTH), 0.1)
    inp['rwkv_a2'] = nrm((L, RWKV_ICLR_LORA, RWKV_WIDTH), 0.5 * RWKV_ICLR_LORA ** -0.5)
    inp['rwkv_g2'] = nrm((L, RWKV_GATE_LORA, RWKV_WIDTH), RWKV_GATE_LORA ** -0.5)
    inp['rwkv_k_k'] = 0.85 + nrm((L, RWKV_WIDTH), 0.05)
    inp['rwkv_k_a'] = 1.0 + nrm((L, RWKV_WIDTH), 0.05)
    inp['rwkv_r_k'] = nrm((L, RWKV_HEADS, HEAD_DIM), 0.1)
    inp['rwkv_gn_g'] = gain((L, RWKV_WIDTH))
    inp['rwkv_gn_b'] = nrm((L, RWKV_WIDTH), 0.02)
    inp['mla_q_norm_g'] = gain((L, MLA_Q_LORA))
    inp['mla_w_uq'] = nrm((L, MLA_Q_LORA, MLA_HEADS * MLA_QK_DIM), MLA_Q_LORA ** -0.5)
    inp['mla_kv_norm_g'] = gain((L, MLA_KV_LORA))
    inp['mla_w_ukv'] = nrm((L, MLA_KV_LORA, MLA_HEADS * (MLA_NOPE_DIM + MLA_V_DIM)), MLA_KV_LORA ** -0.5)
    inp['mla_q_qk_g'] = gain((L, MLA_QK_DIM))
    inp['mla_k_qk_g'] = gain((L, MLA_QK_DIM))
    inp['gdn_conv_w'] = nrm((L, GDN_CONV, 3 * GDN_WIDTH), GDN_CONV ** -0.5)
    inp['gdn_a_log'] = jnp.log(jax.random.uniform(keys.pop(), (L, GDN_HEADS), f32, 1.0, 16.0))
    dt = jnp.exp(jax.random.uniform(keys.pop(), (L, GDN_HEADS), f32, math.log(1e-3), math.log(1e-1)))
    inp['gdn_dt_bias'] = dt + jnp.log(-jnp.expm1(-dt))
    inp['gdn_o_norm_g'] = gain((L, HEAD_DIM))
    return inp

def second_block(x, positions, ln_mix_g, w_in, w_out, ln_ffn_g, w_ff1, w_ff2,
              rwkv_mu, rwkv_w0, rwkv_w2, rwkv_a0, rwkv_a2, rwkv_g2, rwkv_k_k, rwkv_k_a,
              rwkv_r_k, rwkv_gn_g, rwkv_gn_b,
              mla_q_norm_g, mla_w_uq, mla_kv_norm_g, mla_w_ukv, mla_q_qk_g, mla_k_qk_g,
              gdn_conv_w, gdn_a_log, gdn_dt_bias, gdn_o_norm_g):
    h = x
    for l in range(DEPTH):
        u = _rms(h, ln_mix_g[l])
        p = u @ w_in[l]
        p_rwkv, p_mla, p_gdn = _split(p, (RWKV_IN, MLA_IN, GDN_IN))
        y_rwkv = rwkv7_time_mix(p_rwkv, rwkv_mu[l], rwkv_w0[l], rwkv_w2[l], rwkv_a0[l], rwkv_a2[l],
                                rwkv_g2[l], rwkv_k_k[l], rwkv_k_a[l], rwkv_r_k[l],
                                rwkv_gn_g[l], rwkv_gn_b[l])
        y_mla = mla_attention(p_mla, positions, mla_q_norm_g[l], mla_w_uq[l], mla_kv_norm_g[l],
                              mla_w_ukv[l], mla_q_qk_g[l], mla_k_qk_g[l])
        y_gdn = gated_deltanet(p_gdn, gdn_conv_w[l], gdn_a_log[l], gdn_dt_bias[l], gdn_o_norm_g[l])
        y = jnp.concatenate([y_rwkv, y_mla, y_gdn], axis=-1)
        h = h + y @ w_out[l]
        u = _rms(h, ln_ffn_g[l])
        h = h + jnp.square(jax.nn.relu(u @ w_ff1[l])) @ w_ff2[l]
    return h


def setup_inputs(seed=0):
    out = dict(first_inputs(seed))
    for name, value in second_inputs(seed + 1).items():
        if name != "x":
            out[name + "_2"] = value
    return out


def reference(
    x, meta_tokens, mix_norm_pre, mix_norm_post, w_in, hgrn_lower_bounds, hgrn_out_norm,
    w_branch_hgrn, pool_proj, pool_scale, w_branch_pool, w_out, ffn_norm_pre, ffn_norm_post,
    ffn_w_gate, ffn_w_up, ffn_conv_w, ffn_conv_b, ffn_w_down, positions_2, ln_mix_g_2, w_in_2,
    w_out_2, ln_ffn_g_2, w_ff1_2, w_ff2_2, rwkv_mu_2, rwkv_w0_2, rwkv_w2_2, rwkv_a0_2,
    rwkv_a2_2, rwkv_g2_2, rwkv_k_k_2, rwkv_k_a_2, rwkv_r_k_2, rwkv_gn_g_2, rwkv_gn_b_2,
    mla_q_norm_g_2, mla_w_uq_2, mla_kv_norm_g_2, mla_w_ukv_2, mla_q_qk_g_2, mla_k_qk_g_2,
    gdn_conv_w_2, gdn_a_log_2, gdn_dt_bias_2, gdn_o_norm_g_2,
):
    x = first_block(
        x, meta_tokens, mix_norm_pre, mix_norm_post, w_in, hgrn_lower_bounds, hgrn_out_norm,
        w_branch_hgrn, pool_proj, pool_scale, w_branch_pool, w_out, ffn_norm_pre, ffn_norm_post,
        ffn_w_gate, ffn_w_up, ffn_conv_w, ffn_conv_b, ffn_w_down,
    )
    return second_block(
        x, positions_2, ln_mix_g_2, w_in_2, w_out_2, ln_ffn_g_2, w_ff1_2, w_ff2_2, rwkv_mu_2,
        rwkv_w0_2, rwkv_w2_2, rwkv_a0_2, rwkv_a2_2, rwkv_g2_2, rwkv_k_k_2, rwkv_k_a_2,
        rwkv_r_k_2, rwkv_gn_g_2, rwkv_gn_b_2, mla_q_norm_g_2, mla_w_uq_2, mla_kv_norm_g_2,
        mla_w_ukv_2, mla_q_qk_g_2, mla_k_qk_g_2, gdn_conv_w_2, gdn_a_log_2, gdn_dt_bias_2,
        gdn_o_norm_g_2,
    )


_drawn_inputs = setup_inputs


def setup_inputs(seed=0):
    import zlib

    import numpy as np

    out = dict(_drawn_inputs(seed))
    spreads = {}
    factors = {'ffn_conv_b': 4.266,
     'rwkv_w2_2': 8.0,
     'rwkv_a0_2': 7.327,
     'rwkv_k_k_2': 38.97,
     'rwkv_k_a_2': 5.463,
     'rwkv_gn_g_2': 18.122,
     'rwkv_gn_b_2': 46.718,
     'mla_q_norm_g_2': 8.0,
     'mla_kv_norm_g_2': 8.0,
     'mla_q_qk_g_2': 8.0,
     'mla_k_qk_g_2': 8.0,
     'gdn_o_norm_g_2': 15.426,
     'ln_ffn_g_2': 4.098}
    for name, (base, spread) in spreads.items():
        noise = np.random.default_rng([zlib.crc32(name.encode()), seed]).standard_normal(out[name].shape)
        drawn = base * np.exp(spread * noise) if base else spread * noise
        out[name] = jnp.asarray(drawn.astype(out[name].dtype))
    for name, factor in factors.items():
        out[name] = (out[name] * factor).astype(out[name].dtype)
    return out
```

```python
from contextlib import ExitStack

import numpy as np
import concourse.bass as bass
from concourse import mybir

F32 = mybir.dt.float32
F32R = mybir.dt.float32r
I32 = mybir.dt.int32
ALU = mybir.AluOpType
ACT = mybir.ActivationFunctionType
AX_X = mybir.AxisListType.X
P = 128
ds = bass.ds

D = 1024
KD = D // P
SEQ = 1024
META = 16
PAD = P - META
T1 = PAD + META + SEQ
NC1 = T1 // P
TAIL = 2
EPS = 1e-6


RETIRED = []


def signal(nc, ctx, name):
    sem = nc.alloc_semaphore(name)
    ctx.callback(RETIRED.append, sem)
    return sem


def clear_retired(nc):
    nc.clear_and_free_semaphores(list(RETIRED))
    nc.all_engine_barrier()
    RETIRED.clear()


class Products:

    RAW = 2
    PRIME = 64
    UNIT = 1024

    def __init__(self, nc, ctx, slots, banks):
        self.nc, self.slots, self.banks = nc, slots, banks
        sem = lambda name: signal(nc, ctx, name)
        self.landed = [sem(f"weights_landed{r}") for r in range(self.RAW)]
        self.hi_done = sem("weights_hi_done")
        self.ready = sem("weights_ready")
        self.full = sem("psum_full")
        self.carried = sem("waits_carried")
        self.free = [sem(f"psum_free{b}") for b in range(banks)]
        self.units = 0
        self.chunks = 0
        self.ends = []
        self.uses = [0] * banks

    def carry(self, eng):
        eng.sem_inc(self.carried, 1)

    def memory(self, raw, hi, lo, zero, psum):
        self.raw, self.hi, self.lo, self.zero, self.psum = raw, hi, lo, zero, psum

    def stage(self, n, sources, chunks):
        return Stage(self, n, sources, chunks)


class Stage:

    def __init__(self, pr, n, sources, chunks, rows=P):
        self.pr, self.n, self.sources, self.body, self.rows = pr, n, sources, chunks, rows
        U, C = len(sources), len(chunks)
        assert n == 1 or (U % pr.slots == 0 and U % pr.RAW == 0 and C % pr.banks == 0)
        self.U, self.C, self.u0, self.c0 = U, C, pr.units, pr.chunks
        last = [max(c for c in range(C) if any(k[0] == j for k in chunks[c][1])) + 1 for j in range(U)]
        for i in range(n):
            pr.ends += [self.c0 + i * C + e for e in last]
        self.bank = [(self.c0 + c) % pr.banks for c in range(C)]
        self.used, uses = [], list(pr.uses)
        for b in self.bank:
            self.used.append(uses[b])
            uses[b] += 1
        per = [b - a for a, b in zip(pr.uses, uses)]
        self.per = per
        pr.uses = [a + n * k for a, k in zip(pr.uses, per)]
        pr.units += n * U
        pr.chunks += n * C

    def _slot_free(self, j):
        e = lambda u: self.pr.ends[u] if u >= 0 else 0
        at = self.u0 + j - self.pr.slots
        v = e(at)
        if self.n > 1:
            v = max(v, e(at + self.U) - self.C)
        return v

    def load(self, sp, i, j):
        pr, u = self.pr, self.u0 + j
        dst = pr.raw[0:self.rows, u % pr.RAW]
        src = self.sources[j](i)
        sp.wait_ge(pr.ready, u + 1 + i * self.U)
        pr.carry(sp)
        if len(src.shape) == 3:
            dst = dst[:, 0:src.shape[1] * src.shape[2]].rearrange("p (a b) -> p a b", a=src.shape[1])
        else:
            dst = dst[:, 0:src.shape[1]]
        sp.dma_start(dst, src).then_inc(pr.landed[u % pr.RAW], 16)

    def split(self, pool, i, j):
        pr, u = self.pr, self.u0 + j
        r, s, rows = u % pr.RAW, u % pr.slots, self.rows
        width = int(np.prod(self.sources[j](0).shape[1:]))
        pool.wait_ge(pr.full, pr.PRIME + self._slot_free(j) + i * self.C)
        pool.wait_ge(pr.landed[r], 16 * (u // pr.RAW + 1) + i * (16 * self.U // pr.RAW))
        pr.nc.gpsimd.tensor_tensor(pr.hi[0:rows, s, 0:width], pr.raw[0:rows, r, 0:width],
                                   pr.zero[0:rows, 0:1].to_broadcast([rows, width]), ALU.add).then_inc(pr.hi_done, 1)
        pool.wait_ge(pr.hi_done, u + 1 + i * self.U)
        pr.nc.gpsimd.tensor_tensor(pr.lo[0:rows, s, 0:width], pr.raw[0:rows, r, 0:width],
                                   pr.hi[0:rows, s, 0:width].bitcast(F32), ALU.subtract).then_inc(pr.ready, 1)

    def bank_of(self, c, rows=P):
        return self.pr.psum[0:rows, self.bank[c], 0:self.body[c][0]]

    def multiply(self, pe, i, c):
        pr = self.pr
        width, terms = self.body[c]
        b = self.bank[c]
        need = max(t[0] for t in terms)
        pe.wait_ge(pr.ready, pr.RAW + self.u0 + need + 1 + i * self.U)
        pe.wait_ge(pr.free[b], 1 + self.used[c] + i * self.per[b])
        last = None
        for t, (j, pick, xh, xl) in enumerate(terms):
            s = (self.u0 + j) % pr.slots
            wh, wl = pick(pr.hi[:, s]), pick(pr.lo[:, s])
            out = pr.psum[0:wh.shape[-1], b, 0:width]
            end = t == len(terms) - 1
            pr.nc.tensor.matmul(out, wh, xh, start=t == 0, stop=False)
            pr.nc.tensor.matmul(out, wh, xl, start=False, stop=False)
            last = pr.nc.tensor.matmul(out, wl, xh, start=False, stop=end)
        last.then_inc(pr.full, 1)

    def wait_full(self, eng, i, c):
        eng.wait_ge(self.pr.full, self.pr.PRIME + self.c0 + c + 1 + i * self.C)

    def freed(self, c):
        return self.pr.free[self.bank[c]]


class Steps:

    def __init__(self, nc, ctx, name, names, n=1):
        self.sem = signal(nc, ctx, name)
        self.names, self.next = list(names), 0
        assert len(set(names)) == len(names)

    def prime(self, eng):
        eng.sem_inc(self.sem, len(self.names))

    def did(self, name):
        assert self.names[self.next] == name, (self.names[self.next], name)
        self.next = (self.next + 1) % len(self.names)
        return self.sem, 1

    def at(self, name, i=0):
        return self.sem, (i + 1) * len(self.names) + self.names.index(name) + 1


def chunks_of(start, total, parts):
    w = total // parts // 2 * 2
    out = [(start + n * w, w) for n in range(parts)]
    out[-1] = (out[-1][0], total - (parts - 1) * w)
    return out


def chunk_terms(unit, xh, xl, kd, off, width, piece=P):
    return (width, [(unit, (lambda t, k=k: t[:, k * piece:k * piece + P]),
                     xh[:, k, off:off + width], xl[:, k, off:off + width]) for k in range(kd)])


def columns(w, at):
    return w.rearrange("(k p) m -> p k m", p=P)[:, :, ds(at, P)]


class Params:

    def __init__(self):
        self.at, self.n = {}, 0

    def add(self, name, n):
        self.at[name] = (self.n, n)
        self.n += n


def param_layout():
    pl = Params()
    for name, n in PARAM_TILES:
        pl.add(name, n)
    return pl


PARAM_TILES = [
    ("mix_norm_pre", 8), ("mix_norm_post", 8), ("hgrn_lower_bounds", 4), ("hgrn_out_norm", 4),
    ("pool_scale", 4), ("ffn_norm_pre", 8), ("ffn_norm_post", 8), ("ffn_conv_w", 66), ("ffn_conv_b", 22),
    ("ln_mix_g_2", 8), ("ln_ffn_g_2", 8), ("rwkv_mu_2", 11), ("rwkv_w0_2", 3), ("rwkv_a0_2", 3),
    ("rwkv_k_k_2", 3), ("rwkv_k_a_2", 3), ("rwkv_r_k_2", 3), ("rwkv_gn_g_2", 3), ("rwkv_gn_b_2", 3),
    ("gdn_conv_w_2", 36), ("gdn_o_norm_g_2", 1), ("mla_q_norm_g_2", 2), ("mla_kv_norm_g_2", 1),
]


class Core:

    def __init__(self, nc, ctx, dram):
        self.nc, self.ctx, self.dram = nc, ctx, dram
        sb = lambda name, shape, dt=F32: ctx.enter_context(nc.sbuf_tensor(name, shape, dt))
        self.pl = param_layout()
        self.ident = sb("ident", [P, P])
        self.ones = sb("ones", [P, P])
        self.zero = sb("zero", [P, 1])
        self.eps = sb("eps", [P, 1])
        self.gn_eps = sb("gn_eps", [P, 1])
        self.prm = sb("prm", [P, self.pl.n])
        self.pr = Products(nc, ctx, 4, 2)
        self.psum = ctx.enter_context(nc.psum_tensor("psum", [P, 8, 512], F32))

    def weights(self, ctx, slots=4):
        sb = lambda name, shape, dt=F32: ctx.enter_context(self.nc.sbuf_tensor(f"{name}_{self.pr.units}", shape, dt))
        self.pr.slots = slots
        self.pr.memory(sb("w_raw", [P, 2, 1024]), sb("w_hi", [P, slots, 1024], F32R), sb("w_lo", [P, slots, 1024], F32R),
                       self.zero, self.psum[:, 0:2])

    def par(self, name, k=0):
        at = self.pl.at[name][0]
        if isinstance(k, int):
            return self.prm[:, at + k:at + k + 1]
        return self.prm[:, ds(k + at, 1)]


def start_up(co):
    nc, pr = co.nc, co.pr
    with ExitStack() as ctx:
        loaded = signal(nc, ctx, "vectors_loaded")
        made = signal(nc, ctx, "constants_made")
        block = ctx.enter_context(nc.Block())

        @block.sync
        def _(sp):
            sp.dma_start(co.prm[:], co.dram["vectors"]).then_inc(loaded, 16)
            sp.wait_ge(loaded, 16)

        @block.gpsimd
        def _(pool):
            pool.sem_inc(pr.ready, pr.RAW)
            nc.gpsimd.memset(co.zero[:], 0.0).then_inc(made, 1)
            nc.gpsimd.memset(co.ones[:], 1.0).then_inc(made, 1)
            nc.gpsimd.memset(co.ident[:], 0.0).then_inc(made, 1)
            nc.gpsimd.memset(co.eps[:], EPS).then_inc(made, 1)
            nc.gpsimd.memset(co.gn_eps[:], 64e-5).then_inc(made, 1)
            pool.wait_ge(made, 5)
            nc.gpsimd.affine_select(out=co.ident[:], in_=co.ident[:], compare_op=ALU.not_equal, fill=1.0,
                                    base=0, pattern=[[-1, P]], channel_multiplier=1).then_inc(made, 1)
            pool.wait_ge(made, 6)

        @block.vector
        def _(dve):
            for b in range(pr.banks):
                dve.sem_inc(pr.free[b], 1)

        @block.tensor
        def _(pe):
            pe.sem_inc(pr.full, pr.PRIME)


def norm_split(co, tag, source, pad, total, gain, u_hi, u_lo, keep=None, h_given=None):
    nc = co.nc
    width = pad + total
    cut = chunks_of(pad, total, -(-total // 512))
    with ExitStack() as ctx:
        sb = lambda name, shape, dt=F32: ctx.enter_context(nc.sbuf_tensor(tag + name, shape, dt))
        h = h_given if h_given is not None else sb("h", [P, KD, total])
        sq = sb("sq", [P, 2, total])
        rstd = sb("rstd", [P, total])
        u = sb("u", [P, 2, total])
        landed = [signal(nc, ctx, f"{tag}h_landed{k}") for k in range(KD)]
        pool_s = Steps(nc, ctx, tag + "pool_steps", [f"pad{k}" for k in range(2 * KD)])
        pe_s = Steps(nc, ctx, tag + "pe_steps", [f"sum{k}" for k in range(KD)])
        act_s = Steps(nc, ctx, tag + "act_steps", [f"square{k}" for k in range(KD)]
                      + [f"ln{n}" for n in range(len(cut))] + ["root"] + [f"hi{k}" for k in range(KD)])
        dve_s = Steps(nc, ctx, tag + "dve_steps", [x for k in range(KD) for x in ([f"u{k}"] + ([f"lo{k - 1}"] if k else []))] + [f"lo{KD - 1}"])
        sums = co.psum[:, 2:2 + len(cut)]
        block = ctx.enter_context(nc.Block())

        if h_given is None:
            @block.sync
            def _(sp):
                for k in range(KD):
                    sp.dma_start(h[:, k], source[k * P:(k + 1) * P, :]).then_inc(landed[k], 16)
                for k in range(KD):
                    sp.wait_ge(landed[k], 16)

        if pad:
            @block.vector
            def _(dve):
                for k in range(KD):
                    nc.vector.memset(u_hi[:, k, 0:pad].bitcast(I32), 0).then_inc(*pool_s.did(f"pad{2 * k}"))
                    nc.vector.memset(u_lo[:, k, 0:pad].bitcast(I32), 0).then_inc(*pool_s.did(f"pad{2 * k + 1}"))

        @block.scalar
        def _(act):
            act_s.prime(act)
            for k in range(KD):
                if h_given is None:
                    act.wait_ge(landed[k], 16)
                if k >= 2:
                    act.wait_ge(*pe_s.at(f"sum{k - 2}"))
                nc.scalar.activation(sq[:, k % 2], h[:, k], ACT.Square).then_inc(*act_s.did(f"square{k}"))
            act.wait_ge(*pe_s.at(f"sum{KD - 1}"))
            for n, (off, w) in enumerate(cut):
                nc.scalar.activation(rstd[:, off - pad:off - pad + w], sums[:, n, 0:w], ACT.Ln, scale=1.0 / D,
                                     bias=co.eps[:]).then_inc(*act_s.did(f"ln{n}"))
            act.wait_ge(*act_s.at(f"ln{len(cut) - 1}"))
            nc.scalar.activation(rstd[:], rstd[:], ACT.Exp, scale=-0.5).then_inc(*act_s.did("root"))
            for k in range(KD):
                act.wait_ge(*dve_s.at(f"u{k}"))
                nc.scalar.copy(u_hi[:, k, pad:width], u[:, k % 2]).then_inc(*act_s.did(f"hi{k}"))

        @block.tensor
        def _(pe):
            pe_s.prime(pe)
            for k in range(KD):
                pe.wait_ge(*act_s.at(f"square{k}"))
                for n, (off, w) in enumerate(cut):
                    last = nc.tensor.matmul(sums[:, n, 0:w], co.ones[:], sq[:, k % 2, off - pad:off - pad + w],
                                            start=k == 0, stop=k == KD - 1)
                last.then_inc(*pe_s.did(f"sum{k}"))

        @block.vector
        def _(dve):
            dve_s.prime(dve)
            dve.wait_ge(*act_s.at("root"))

            def lo(k):
                dve.wait_ge(*act_s.at(f"hi{k}"))
                nc.vector.tensor_tensor(u_lo[:, k, pad:width], u[:, k % 2], u_hi[:, k, pad:width].bitcast(F32),
                                        ALU.subtract).then_inc(*dve_s.did(f"lo{k}"))

            for k in range(KD):
                if k >= 2:
                    dve.wait_ge(*dve_s.at(f"lo{k - 2}"))
                nc.vector.scalar_tensor_tensor(u[:, k % 2], h[:, k], co.par(gain, k), rstd[:], ALU.mult,
                                               ALU.mult).then_inc(*dve_s.did(f"u{k}"))
                if k:
                    lo(k - 1)
            lo(KD - 1)


LEVELS = [64, 32, 16, 8, 4, 2, 1]


def hgrn_heads(co, u_hi, u_lo):
    nc, pr = co.nc, co.pr
    HEADS = 4
    w_in = co.dram["w_in"]
    sub = HEADS * P
    cut = chunks_of(PAD, META + SEQ, 3)
    C = slice(PAD, T1)
    tail0 = T1 - SEQ - TAIL
    tcut = chunks_of(tail0, SEQ + TAIL, 3)
    sources = [(lambda i, j=j: columns(w_in, i * P + j * sub)) for j in range(4)]
    body = [chunk_terms(j, u_hi, u_lo, KD, off, w) for j in range(4) for off, w in cut]
    st = pr.stage(HEADS, sources, body)
    with ExitStack() as ctx:
        sb = lambda name, shape, dt=F32: ctx.enter_context(nc.sbuf_tensor(name, shape, dt))
        q, f, k, vT, g, b = (sb("hg_" + n, [P, T1]) for n in ("q", "f", "k", "vT", "g", "b"))
        E = sb("hg_E", [P, T1])
        ah = sb("hg_ah", [P, SEQ + TAIL])
        G = sb("hg_G", [P, 2, T1])
        qE, kd = sb("hg_qE", [P, T1]), sb("hg_kd", [P, T1])
        V, kdT = sb("hg_V", [P, NC1, P]), sb("hg_kdT", [P, NC1, P])
        pT = sb("hg_pT", [P, NC1, P])
        states = sb("hg_states", [P, NC1, P])
        decay = sb("hg_decay", [P, NC1])
        lb, oml, lbt = sb("hg_lb", [P, HEADS]), sb("hg_oml", [P, HEADS]), sb("hg_lbt", [P, HEADS])
        mask = sb("hg_mask", [P, len(LEVELS), 64], I32)
        maskd = sb("hg_maskd", [P, P], I32)
        big = co.psum[:, 2:5]
        bigf = big.rearrange("p a b -> p (a b)")
        big3 = bigf[:, 0:T1].rearrange("p (c t) -> p c t", t=P)
        gram = co.psum[:, 5:7].rearrange("p a b -> p (a b)")[:, 0:NC1 * 64]
        gram2 = co.psum[:, 7:8]
        bc = b[:].rearrange("p (c t) -> p c t", t=P)

        pool_c = signal(nc, ctx, "hg_masks")
        act_n = ["f0", "f1", "f2", "sqrt", "ln", "e_last", "e_kd", "e_q", "V", "kdT"] + \
            [f"{x}{l}" for l in range(7) for x in ("e1_", "e2_")] + ["o", "square", "ln_ms", "root"]
        dve_n = ["floor", "max"] + [f"scan{c}" for c in range(NC1)] + ["d_kd", "kmul", "m_kd", "m_qE"]
        for l in range(7):
            dve_n += [f"d{l}", f"gk{l}", f"gq{l}"]
            if l == 0:
                dve_n += [f"st{c}" for c in range(NC1 - 1)]
            if l >= 1:
                dve_n += [f"p{l - 1}"]
        dve_n += ["p6", "pd", "a", "ag"]
        pe_n = ["vT", "kT", "U"] + [f"gram{l}" for l in range(7)] + ["diag", "o", "sum"]
        act_s = Steps(nc, ctx, "hg_act", act_n)
        dve_s = Steps(nc, ctx, "hg_dve", dve_n)
        pe_s = Steps(nc, ctx, "hg_pe", pe_n)
        lbs = signal(nc, ctx, "hg_bounds")
        stored = signal(nc, ctx, "hg_stored")
        block = ctx.enter_context(nc.Block())

        @block.sync
        def _(sp):
            with sp.Fori(0, HEADS) as i:
                for j in range(4):
                    st.load(sp, i, j)
                sp.wait_ge(*dve_s.at("ag", i))
                sp.dma_start(co.dram["aT"][ds(i * P, P), :], ah[:]).then_inc(stored, 16)
            sp.wait_ge(stored, 16 + 16 * HEADS)

        @block.gpsimd
        def _(pool):
            nc.gpsimd.memset(mask[:], 1).then_inc(pool_c, 1)
            nc.gpsimd.memset(maskd[:], 0).then_inc(pool_c, 1)
            pool.wait_ge(pool_c, 2)
            n = 2
            for l, m in enumerate(LEVELS):
                view = mask[:, l].rearrange("p (b m) -> p b m", m=m)
                nb = 64 // m
                nc.gpsimd.affine_select(out=view, in_=view, compare_op=ALU.is_ge, fill=0.0, base=0,
                                        pattern=[[-2 * m, nb], [0, m]], channel_multiplier=1).then_inc(pool_c, 1)
                n += 1
                pool.wait_ge(pool_c, n)
                nc.gpsimd.affine_select(out=view, in_=view, compare_op=ALU.is_ge, fill=0.0, base=m - 1,
                                        pattern=[[2 * m, nb], [0, m]], channel_multiplier=-1).then_inc(pool_c, 1)
                n += 1
            nc.gpsimd.affine_select(out=maskd[:], in_=maskd[:], compare_op=ALU.not_equal, fill=1.0, base=0,
                                    pattern=[[-1, P]], channel_multiplier=1).then_inc(pool_c, 1)
            n += 1
            for x in (f, k, q, vT):
                nc.gpsimd.memset(x[:, 0:PAD], 0.0).then_inc(pool_c, 1)
                n += 1
            nc.gpsimd.memset(pT[:], 0.0).then_inc(pool_c, 1)
            nc.gpsimd.memset(states[:, 0], 0.0).then_inc(pool_c, 1)
            n += 2
            assert n == 2 + 14 + 1 + 4 + 2
            with pool.Fori(0, HEADS) as i:
                for j in range(4):
                    st.split(pool, i, j)

        CONSTS = 23

        @block.scalar
        def _(act):
            act_s.prime(act)
            act.wait_ge(lbs, 1)
            nc.scalar.activation(lbt[:], lbt[:], ACT.Exp).then_inc(lbs, 1)
            act.wait_ge(pool_c, CONSTS)
            with act.Fori(0, HEADS) as i:
                for n, (off, w) in enumerate(cut):
                    st.wait_full(act, i, n)
                    if n == 0:
                        act.wait_ge(*dve_s.at("ag", i - 1))
                    nc.scalar.copy(q[:, off:off + w], st.bank_of(n)).then_inc(st.freed(n), 1)
                for n, (off, w) in enumerate(cut):
                    st.wait_full(act, i, 3 + n)
                    nc.scalar.activation(f[:, off:off + w], st.bank_of(3 + n), ACT.Sigmoid).then_inc(*act_s.did(f"f{n}"))
                    nc.scalar.activation(k[:, off:off + w], st.bank_of(3 + n), ACT.Sigmoid,
                                         scale=-1.0).then_inc(st.freed(3 + n), 1)
                for n, (off, w) in enumerate(cut):
                    st.wait_full(act, i, 6 + n)
                    nc.scalar.copy(vT[:, off:off + w], st.bank_of(6 + n)).then_inc(st.freed(6 + n), 1)
                for n, (off, w) in enumerate(cut):
                    st.wait_full(act, i, 9 + n)
                    nc.scalar.activation(g[:, off:off + w], st.bank_of(9 + n), ACT.Sigmoid).then_inc(st.freed(9 + n), 1)
                act.wait_ge(*dve_s.at("max", i))
                nc.scalar.activation(f[:, C], f[:, C], ACT.Sqrt).then_inc(*act_s.did("sqrt"))
                act.wait_ge(*act_s.at("sqrt", i))
                nc.scalar.activation(f[:, C], f[:, C], ACT.Ln).then_inc(*act_s.did("ln"))
                act.wait_ge(*dve_s.at("d_kd", i))
                nc.scalar.activation(decay[:], bc[:, :, P - 1], ACT.Exp, scale=2.0).then_inc(*act_s.did("e_last"))
                nc.scalar.activation(kd[:], kd[:], ACT.Exp, scale=2.0).then_inc(*act_s.did("e_kd"))
                nc.scalar.activation(qE[:], b[:], ACT.Exp, scale=2.0).then_inc(*act_s.did("e_q"))
                act.wait_ge(*pe_s.at("vT", i))
                nc.scalar.copy(V[:], big3).then_inc(*act_s.did("V"))
                act.wait_ge(*pe_s.at("kT", i))
                nc.scalar.copy(kdT[:], big3).then_inc(*act_s.did("kdT"))
                for l, m in enumerate(LEVELS):
                    act.wait_ge(*dve_s.at(f"d{l}", i))
                    Ev = E[:].rearrange("p (b two m) -> p b two m", two=2, m=m)
                    nc.scalar.activation(Ev[:, :, 0], Ev[:, :, 0], ACT.Exp, scale=-2.0).then_inc(*act_s.did(f"e1_{l}"))
                    nc.scalar.activation(Ev[:, :, 1], Ev[:, :, 1], ACT.Exp, scale=2.0).then_inc(*act_s.did(f"e2_{l}"))
                act.wait_ge(*pe_s.at("o", i))
                nc.scalar.copy(kd[:, tail0:T1], bigf[:, tail0:T1]).then_inc(*act_s.did("o"))
                act.wait_ge(*act_s.at("o", i))
                nc.scalar.activation(E[:, tail0:T1], kd[:, tail0:T1], ACT.Square).then_inc(*act_s.did("square"))
                act.wait_ge(*pe_s.at("sum", i))
                nc.scalar.activation(b[:, tail0:T1].rearrange("p (n t) -> p n t", n=3), big[:, :, 0:(SEQ + TAIL) // 3], ACT.Ln,
                                     scale=1.0 / P, bias=co.eps[:]).then_inc(*act_s.did("ln_ms"))
                act.wait_ge(*act_s.at("ln_ms", i))
                nc.scalar.activation(b[:, tail0:T1], b[:, tail0:T1], ACT.Exp, scale=-0.5).then_inc(*act_s.did("root"))

        @block.tensor
        def _(pe):
            pe_s.prime(pe)
            pe.wait_ge(pool_c, CONSTS)
            with pe.Fori(0, HEADS) as i:
                for c in range(12):
                    st.multiply(pe, i, c)
                pe.wait_ge(*act_s.at("sqrt", i))
                pe.wait_ge(*act_s.at("root", i - 1))
                for c in range(NC1):
                    last = nc.tensor.transpose(big3[:, c], vT[:, c * P:(c + 1) * P], co.ident[:])
                last.then_inc(*pe_s.did("vT"))
                pe.wait_ge(*dve_s.at("m_kd", i))
                pe.wait_ge(*act_s.at("V", i))
                for c in range(NC1):
                    last = nc.tensor.transpose(big3[:, c], kd[:, c * P:(c + 1) * P], co.ident[:])
                last.then_inc(*pe_s.did("kT"))
                pe.wait_ge(*act_s.at("kdT", i))
                for c in range(NC1):
                    last = nc.tensor.matmul(big3[:, c], kdT[:, c], V[:, c], start=True, stop=True)
                last.then_inc(*pe_s.did("U"))
                for l, m in enumerate(LEVELS):
                    pe.wait_ge(*dve_s.at(f"gq{l}", i))
                    if l:
                        pe.wait_ge(*dve_s.at(f"p{l - 1}", i))
                    for c in range(NC1):
                        cols = G[:, l % 2, c * P:(c + 1) * P]
                        rhs = cols.rearrange("p (b two m) -> p b two m", two=2, m=m)[:, :, 1]
                        last = nc.tensor.matmul(gram[:, c * 64:(c + 1) * 64], cols, rhs, start=True, stop=True)
                    last.then_inc(*pe_s.did(f"gram{l}"))
                pe.wait_ge(*dve_s.at(f"st{NC1 - 2}", i))
                for c in range(NC1):
                    last = nc.tensor.matmul(big3[:, c], k[:, c * P:(c + 1) * P], q[:, c * P:(c + 1) * P],
                                            start=True, stop=True)
                last.then_inc(*pe_s.did("diag"))
                pe.wait_ge(*dve_s.at("pd", i))
                for c in range(NC1):
                    nc.tensor.matmul(big3[:, c], V[:, c], pT[:, c], start=True, stop=False)
                    last = nc.tensor.matmul(big3[:, c], states[:, c], qE[:, c * P:(c + 1) * P], start=False, stop=True)
                last.then_inc(*pe_s.did("o"))
                pe.wait_ge(*act_s.at("square", i))
                for n, (off, w) in enumerate(tcut):
                    last = nc.tensor.matmul(big[:, n, 0:w], co.ones[:], E[:, off:off + w], start=True, stop=True)
                last.then_inc(*pe_s.did("sum"))

        @block.vector
        def _(dve):
            dve_s.prime(dve)
            dve.sem_inc(stored, 16)
            raw = co.prm[:, co.pl.at["hgrn_lower_bounds"][0]:co.pl.at["hgrn_lower_bounds"][0] + HEADS]
            n = [0]

            def step(ins, add=1):
                ins.then_inc(lbs, 1)
                n[0] += 1
                dve.wait_ge(lbs, n[0] + add)
            nc.vector.tensor_tensor(lbt[:], raw, raw, ALU.subtract).then_inc(lbs, 1)
            n[0] = 1
            dve.wait_ge(lbs, 2)
            step(nc.vector.reciprocal(lb[:], lbt[:]))
            step(nc.vector.tensor_tensor(lb[:], lb[:], lbt[:], ALU.mult))
            step(nc.vector.tensor_tensor(lb[:], lb[:], lb[:], ALU.subtract))
            step(nc.vector.tensor_scalar(lb[:], lb[:], 0.0, 1.0, ALU.max, ALU.min))
            step(nc.vector.tensor_scalar(oml[:], lb[:], -1.0, 1.0, ALU.mult, ALU.add))
            dve.wait_ge(pool_c, CONSTS)
            with dve.Fori(0, HEADS) as i:
                lb_h, oml_h = lb[:, ds(i, 1)], oml[:, ds(i, 1)]
                dve.wait_ge(*act_s.at("f2", i))
                nc.vector.tensor_scalar(f[:, C], f[:, C], oml_h, lb_h, ALU.mult, ALU.add).then_inc(*dve_s.did("floor"))
                dve.wait_ge(*dve_s.at("floor", i))
                nc.vector.tensor_scalar(f[:, C], f[:, C], 1e-30, None, ALU.max).then_inc(*dve_s.did("max"))
                dve.wait_ge(*act_s.at("ln", i))
                for c in range(NC1):
                    nc.vector.tensor_tensor_scan(b[:, c * P:(c + 1) * P], co.ones[:], f[:, c * P:(c + 1) * P], 0.0,
                                                 ALU.mult, ALU.add).then_inc(*dve_s.did(f"scan{c}"))
                dve.wait_ge(*dve_s.at(f"scan{NC1 - 1}", i))
                nc.vector.tensor_tensor(kd[:].rearrange("p (c t) -> p c t", t=P),
                                        bc[:, :, P - 1:P].to_broadcast([P, NC1, P]), bc,
                                        ALU.subtract).then_inc(*dve_s.did("d_kd"))
                nc.vector.tensor_scalar(k[:, C], k[:, C], oml_h, None, ALU.mult).then_inc(*dve_s.did("kmul"))
                dve.wait_ge(*dve_s.at("kmul", i))
                dve.wait_ge(*act_s.at("e_q", i))
                nc.vector.tensor_tensor(kd[:], kd[:], k[:], ALU.mult).then_inc(*dve_s.did("m_kd"))
                nc.vector.tensor_tensor(qE[:], qE[:], q[:], ALU.mult).then_inc(*dve_s.did("m_qE"))

                def score(l):
                    m = LEVELS[l]
                    if l:
                        dve.wait_ge(*dve_s.at(f"p{l - 1}", i))
                    dve.wait_ge(*pe_s.at(f"gram{l}", i))
                    pr.carry(dve)
                    nb = 64 // m
                    out = pT[:].rearrange("p c (b two m) -> p c b two m", two=2, m=m)[:, :, :, 1]
                    src = gram.rearrange("p (c b m) -> p c b m", b=nb, m=m)
                    mk = mask[:, l].rearrange("p (b m) -> p b m", m=m).unsqueeze(1).to_broadcast([P, NC1, nb, m])
                    nc.vector.copy_predicated(out, mk, src).then_inc(*dve_s.did(f"p{l}"))

                for l, m in enumerate(LEVELS):
                    if l:
                        dve.wait_ge(*dve_s.at(f"gq{l - 1}", i))
                    bv = b[:].rearrange("p (n t) -> p n t", t=2 * m)
                    nc.vector.tensor_tensor(E[:].rearrange("p (n t) -> p n t", t=2 * m), bv,
                                            bv[:, :, m - 1:m].to_broadcast([P, T1 // (2 * m), 2 * m]),
                                            ALU.subtract).then_inc(*dve_s.did(f"d{l}"))
                    Ev, kv, qv, Gv = (x.rearrange("p (b two m) -> p b two m", two=2, m=m)
                                      for x in (E[:], k[:], q[:], G[:, l % 2]))
                    if l >= 2:
                        dve.wait_ge(*pe_s.at(f"gram{l - 2}", i))
                    dve.wait_ge(*act_s.at(f"e2_{l}", i))
                    nc.vector.tensor_tensor(Gv[:, :, 0], Ev[:, :, 0], kv[:, :, 0], ALU.mult).then_inc(*dve_s.did(f"gk{l}"))
                    nc.vector.tensor_tensor(Gv[:, :, 1], Ev[:, :, 1], qv[:, :, 1], ALU.mult).then_inc(*dve_s.did(f"gq{l}"))
                    if l == 0:
                        dve.wait_ge(*pe_s.at("U", i))
                        for c in range(NC1 - 1):
                            if c:
                                dve.wait_ge(*dve_s.at(f"st{c - 1}", i))
                            nc.vector.scalar_tensor_tensor(states[:, c + 1], states[:, c], decay[:, c:c + 1],
                                                           big3[:, c], ALU.mult, ALU.add).then_inc(*dve_s.did(f"st{c}"))
                    if l >= 1:
                        score(l - 1)
                score(6)
                dve.wait_ge(*dve_s.at("p6", i))
                dve.wait_ge(*pe_s.at("diag", i))
                pr.carry(dve)
                nc.vector.copy_predicated(pT[:], maskd[:].unsqueeze(1).to_broadcast([P, NC1, P]),
                                          big3).then_inc(*dve_s.did("pd"))
                dve.wait_ge(*act_s.at("root", i))
                nc.vector.scalar_tensor_tensor(kd[:, tail0:T1], kd[:, tail0:T1], co.par("hgrn_out_norm", i),
                                               b[:, tail0:T1], ALU.mult, ALU.mult).then_inc(*dve_s.did("a"))
                dve.wait_ge(*dve_s.at("a", i))
                dve.wait_ge(stored, 16 * i + 16)
                nc.vector.tensor_tensor(ah[:], kd[:, tail0:T1], g[:, tail0:T1], ALU.mult).then_inc(*dve_s.did("ag"))


def pool_branch(co, u_hi, u_lo, p_hi, p_lo):
    nc, pr = co.nc, co.pr
    W = SEQ + TAIL
    t0 = T1 - W
    cut = chunks_of(PAD, META + SEQ, 3)
    tcut = chunks_of(t0, W, 3)
    at = 4 * 512
    st = pr.stage(1, [(lambda i, j=j: columns(co.dram["w_in"], at + j * P)) for j in range(4)],
                  [chunk_terms(j, u_hi, u_lo, KD, off, w) for j in range(4) for off, w in cut])
    with ExitStack() as ctx:
        sb = lambda name, shape, dt=F32: ctx.enter_context(nc.sbuf_tensor(name, shape, dt))
        v = sb("pl_v", [P, 2, T1])
        s = sb("pl_s", [P, 2, T1])
        m = sb("pl_m", [P, W])
        y = sb("pl_y", [P, W])
        proj = sb("pl_proj", [P, 4, P])
        loaded = signal(nc, ctx, "pl_proj_loaded")
        pads = signal(nc, ctx, "pl_pads")
        act_n, dve_n = [], []
        for j in range(4):
            act_n += [f"y{j}", f"hi{j}"]
            dve_n += [f"s{j}_{r}" for r in range(j + 1)] + ([f"mean{j}"] if j < 3 else ["mean3", "mean3b"]) + \
                [f"m{j}", f"lo{j}"]
        act_s = Steps(nc, ctx, "pl_act", act_n)
        dve_s = Steps(nc, ctx, "pl_dve", dve_n)
        pe_s = Steps(nc, ctx, "pl_pe", [f"y{j}" for j in range(4)])
        out = co.psum[:, 2:5]
        block = ctx.enter_context(nc.Block())

        @block.sync
        def _(sp):
            for j in range(4):
                st.load(sp, 0, j)
            sp.dma_start(proj[:], co.dram["pool_proj"].rearrange("g c d -> c g d")).then_inc(loaded, 16)

        @block.gpsimd
        def _(pool):
            for r in range(2):
                nc.gpsimd.memset(v[:, r, 0:PAD], 0.0).then_inc(pads, 1)
            for j in range(4):
                st.split(pool, 0, j)

        @block.scalar
        def _(act):
            act_s.prime(act)

            def take(j):
                if j >= 2:
                    act.wait_ge(*dve_s.at(f"m{j - 2}"))
                for n, (off, w) in enumerate(cut):
                    st.wait_full(act, 0, 3 * j + n)
                    nc.scalar.copy(v[:, j % 2, off:off + w], st.bank_of(3 * j + n)).then_inc(st.freed(3 * j + n), 1)

            take(0)
            for j in range(4):
                if j < 3:
                    take(j + 1)
                act.wait_ge(*pe_s.at(f"y{j}"))
                if j:
                    act.wait_ge(*dve_s.at(f"lo{j - 1}"))
                nc.scalar.mul(y[:].rearrange("p (a b) -> p a b", a=3), out[:, :, 0:W // 3],
                              co.par("pool_scale", j)).then_inc(*act_s.did(f"y{j}"))
                act.wait_ge(*act_s.at(f"y{j}"))
                nc.scalar.copy(p_hi[:, j], y[:]).then_inc(*act_s.did(f"hi{j}"))

        def project(pe, j):
            pe.wait_ge(loaded, 16)
            pe.wait_ge(*dve_s.at(f"m{j}"))
            if j:
                pe.wait_ge(*act_s.at(f"y{j - 1}"))
            for n in range(3):
                last = nc.tensor.matmul(out[:, n, 0:W // 3], proj[:, j], m[:, n * (W // 3):(n + 1) * (W // 3)],
                                        start=True, stop=True)
            last.then_inc(*pe_s.did(f"y{j}"))

        @block.tensor
        def _(pe):
            pe_s.prime(pe)
            for j in range(4):
                for c in range(3):
                    st.multiply(pe, 0, 3 * j + c)
                if j >= 1:
                    project(pe, j - 1)
            project(pe, 3)

        @block.vector
        def _(dve):
            dve_s.prime(dve)
            dve.wait_ge(pads, 2)
            for j in range(4):
                st_wait_taken(dve, st, j)
                src = v[:, j % 2]
                for r in range(j + 1):
                    if r:
                        dve.wait_ge(*dve_s.at(f"s{j}_{r - 1}"))
                    step = 1 << r
                    lo = 2 * step - 1
                    nc.vector.tensor_tensor(s[:, r % 2, lo:T1], src[:, lo:T1], src[:, lo - step:T1 - step],
                                            ALU.add).then_inc(*dve_s.did(f"s{j}_{r}"))
                    src = s[:, r % 2]
                window = 2 << j
                dve.wait_ge(*dve_s.at(f"s{j}_{j}"))
                if j:
                    dve.wait_ge(*pe_s.at(f"y{j - 1}"))
                if j < 3:
                    nc.vector.tensor_scalar(m[:], src[:, t0:T1], 1.0 / window, None, ALU.mult).then_inc(*dve_s.did(f"mean{j}"))
                    dve.wait_ge(*dve_s.at(f"mean{j}"))
                else:
                    short = META - TAIL + 1
                    nc.vector.tensor_scalar(m[:, 0:1], src[:, t0:t0 + 1], 1.0 / short, None, ALU.mult).then_inc(*dve_s.did("mean3"))
                    nc.vector.tensor_scalar(m[:, 1:W], src[:, t0 + 1:T1], 1.0 / window, None, ALU.mult).then_inc(*dve_s.did("mean3b"))
                    dve.wait_ge(*dve_s.at("mean3b"))
                nc.vector.tensor_tensor(m[:], m[:], v[:, j % 2, t0:T1], ALU.subtract).then_inc(*dve_s.did(f"m{j}"))
                dve.wait_ge(*act_s.at(f"hi{j}"))
                nc.vector.tensor_tensor(p_lo[:, j], y[:], p_hi[:, j].bitcast(F32),
                                        ALU.subtract).then_inc(*dve_s.did(f"lo{j}"))


def st_wait_taken(eng, st, j):
    for c in range(3 * j, 3 * j + 3):
        eng.wait_ge(st.freed(c), 2 + st.used[c])


def gated_sum(co, u_hi, u_lo, a_hi, a_lo, p_hi, p_lo):
    nc, pr = co.nc, co.pr
    W = SEQ + TAIL
    N = W // 3
    t0 = T1 - W
    at = 5 * 512
    half = lambda w: (lambda i: columns(co.dram[w], i * P))
    sources = [lambda i: columns(co.dram["w_in"], at + i * P), lambda i: columns(co.dram["w_in"], at + D + i * P),
               half("w_branch_hgrn"), half("w_branch_pool")]
    body = []
    for n in range(3):
        body.append(chunk_terms(0, u_hi, u_lo, KD, t0 + n * N, N))
    for n in range(3):
        body.append(chunk_terms(1, u_hi, u_lo, KD, t0 + n * N, N))
    for n in range(3):
        body.append(chunk_terms(2, a_hi, a_lo, 4, n * N, N))
    for n in range(3):
        body.append(chunk_terms(3, p_hi, p_lo, 4, n * N, N))
    st = pr.stage(KD, sources, body)
    with ExitStack() as ctx:
        sb = lambda name, shape, dt=F32: ctx.enter_context(nc.sbuf_tensor(name, shape, dt))
        sa, sg, z = sb("gs_a", [P, W]), sb("gs_b", [P, W]), sb("gs_z", [P, W])
        stored = signal(nc, ctx, "gs_stored")
        act_s = Steps(nc, ctx, "gs_act", [f"a{n}" for n in range(3)] + [f"b{n}" for n in range(3)])
        dve_s = Steps(nc, ctx, "gs_dve", [f"za{n}" for n in range(3)] + [x for n in range(3) for x in (f"zb{n}", f"z{n}")])
        block = ctx.enter_context(nc.Block())

        @block.sync
        def _(sp):
            with sp.Fori(0, KD) as i:
                for j in range(4):
                    st.load(sp, i, j)
                sp.wait_ge(*dve_s.at("z2", i))
                sp.dma_start(co.dram["zT"][ds(i * P, P), :], z[:]).then_inc(stored, 16)
            sp.wait_ge(stored, 16 + 16 * KD)

        @block.gpsimd
        def _(pool):
            with pool.Fori(0, KD) as i:
                for j in range(4):
                    st.split(pool, i, j)

        @block.scalar
        def _(act):
            act_s.prime(act)
            with act.Fori(0, KD) as i:
                for g, buf in ((0, sa), (1, sg)):
                    for n in range(3):
                        c = 3 * g + n
                        st.wait_full(act, i, c)
                        act.wait_ge(*dve_s.at("z2", i - 1))
                        nc.scalar.activation(buf[:, n * N:(n + 1) * N], st.bank_of(c), ACT.Sigmoid).then_inc(st.freed(c), 1)

        @block.tensor
        def _(pe):
            with pe.Fori(0, KD) as i:
                for c in range(12):
                    st.multiply(pe, i, c)

        @block.vector
        def _(dve):
            dve_s.prime(dve)
            dve.sem_inc(stored, 16)
            with dve.Fori(0, KD) as i:
                for b in range(pr.banks):
                    c = max(c for c in range(6) if st.bank[c] == b)
                    dve.wait_ge(st.freed(c), 2 + st.used[c] + i * st.per[b])
                dve.wait_ge(stored, 16 * i + 16)
                for n in range(3):
                    cols = slice(n * N, (n + 1) * N)
                    st.wait_full(dve, i, 6 + n)
                    nc.vector.tensor_tensor(z[:, cols], sa[:, cols], st.bank_of(6 + n), ALU.mult).then_inc(*dve_s.did(f"za{n}"))
                    dve.wait_ge(*dve_s.at(f"za{n}", i))
                    dve.sem_inc(st.freed(6 + n), 1)
                for n in range(3):
                    cols = slice(n * N, (n + 1) * N)
                    st.wait_full(dve, i, 9 + n)
                    nc.vector.tensor_tensor(sg[:, cols], sg[:, cols], st.bank_of(9 + n), ALU.mult).then_inc(*dve_s.did(f"zb{n}"))
                    dve.wait_ge(*dve_s.at(f"zb{n}", i))
                    dve.sem_inc(st.freed(9 + n), 1)
                    nc.vector.tensor_tensor(z[:, cols], z[:, cols], sg[:, cols], ALU.add).then_inc(*dve_s.did(f"z{n}"))


def split_from_dram(co, tag, source, tiles, width, hi, lo):
    nc = co.nc
    with ExitStack() as ctx:
        x = ctx.enter_context(nc.sbuf_tensor(tag + "x", [P, 2, width], F32))
        landed = [signal(nc, ctx, f"{tag}in{r}") for r in range(2)]
        act_s = Steps(nc, ctx, tag + "act", [f"hi{k}" for k in range(tiles)])
        dve_s = Steps(nc, ctx, tag + "dve", [f"lo{k}" for k in range(tiles)])
        block = ctx.enter_context(nc.Block())

        @block.sync
        def _(sp):
            for k in range(tiles):
                if k >= 2:
                    sp.wait_ge(*dve_s.at(f"lo{k - 2}"))
                sp.dma_start(x[:, k % 2], source[k * P:(k + 1) * P, :]).then_inc(landed[k % 2], 16)

        @block.scalar
        def _(act):
            act_s.prime(act)
            for k in range(tiles):
                act.wait_ge(landed[k % 2], 16 * (k // 2 + 1))
                nc.scalar.copy(hi[:, k], x[:, k % 2]).then_inc(*act_s.did(f"hi{k}"))

        @block.vector
        def _(dve):
            dve_s.prime(dve)
            for k in range(tiles):
                dve.wait_ge(*act_s.at(f"hi{k}"))
                nc.vector.tensor_tensor(lo[:, k], x[:, k % 2], hi[:, k].bitcast(F32),
                                        ALU.subtract).then_inc(*dve_s.did(f"lo{k}"))


def square_product(co, tag, w, x_hi, x_lo, y, width, parts):
    nc, pr = co.nc, co.pr
    N = width // parts
    st = pr.stage(2, [(lambda i, j=j: columns(w, (4 * i + j) * P)) for j in range(4)],
                  [chunk_terms(j, x_hi, x_lo, KD, n * N, N) for j in range(4) for n in range(parts)])
    with ExitStack() as ctx:
        block = ctx.enter_context(nc.Block())

        @block.sync
        def _(sp):
            with sp.Fori(0, 2) as i:
                for j in range(4):
                    st.load(sp, i, j)

        @block.gpsimd
        def _(pool):
            with pool.Fori(0, 2) as i:
                for j in range(4):
                    st.split(pool, i, j)

        @block.tensor
        def _(pe):
            with pe.Fori(0, 2) as i:
                for c in range(4 * parts):
                    st.multiply(pe, i, c)

        @block.scalar
        def _(act):
            with act.Fori(0, 2) as i:
                for c in range(4 * parts):
                    j, n = divmod(c, parts)
                    st.wait_full(act, i, c)
                    nc.scalar.copy(y[:, ds(4 * i + j, 1), n * N:(n + 1) * N].rearrange("p o t -> p (o t)"),
                                   st.bank_of(c)).then_inc(st.freed(c), 1)


def residual_norm(co, tag, res, y, width, gain, dest, skip=0, gained=True):
    nc = co.nc
    parts = -(-width // 512)
    N = width // parts
    with ExitStack() as ctx:
        sb = lambda name, shape, dt=F32: ctx.enter_context(nc.sbuf_tensor(tag + name, shape, dt))
        x = sb("x", [P, 4, width])
        sq = sb("sq", [P, 2, width])
        rstd = sb("rstd", [P, width])
        o = sb("o", [P, 4, width])
        landed = [signal(nc, ctx, f"{tag}in{r}") for r in range(4)]
        stored = [signal(nc, ctx, f"{tag}out{r}") for r in range(4)]
        norm = gain is not None
        pe_s = Steps(nc, ctx, tag + "pe", [f"sum{k}" for k in range(KD)])
        act_s = Steps(nc, ctx, tag + "act", [f"square{k}" for k in range(KD)] + ["ln", "root"])
        dve_s = Steps(nc, ctx, tag + "dve", [f"{x}{k}" for k in range(KD) for x in (("t", "o") if norm else ("o",))])
        sums = co.psum[:, 2:2 + parts]
        block = ctx.enter_context(nc.Block())

        @block.sync
        def _(sp):
            for k in range(KD):
                if k >= 4:
                    sp.wait_ge(*dve_s.at(f"o{k - 4}"))
                sp.dma_start(x[:, k % 4], res[k * P:(k + 1) * P, :]).then_inc(landed[k % 4], 16)
            for k in range(KD):
                sp.wait_ge(*dve_s.at(f"o{k}"))
                sp.dma_start(dest[k * P:(k + 1) * P, :], o[:, k % 4, skip:]).then_inc(stored[k % 4], 16)
            for r in range(4):
                sp.wait_ge(stored[r], 16 * KD // 4)

        if norm:
            @block.scalar
            def _(act):
                act_s.prime(act)
                for k in range(KD):
                    if k >= 2:
                        act.wait_ge(*pe_s.at(f"sum{k - 2}"))
                    nc.scalar.activation(sq[:, k % 2], y[:, k], ACT.Square).then_inc(*act_s.did(f"square{k}"))
                act.wait_ge(*pe_s.at(f"sum{KD - 1}"))
                nc.scalar.activation(rstd[:].rearrange("p (a b) -> p a b", a=parts), sums[:, :, 0:N], ACT.Ln, scale=1.0 / D,
                                     bias=co.eps[:]).then_inc(*act_s.did("ln"))
                act.wait_ge(*act_s.at("ln"))
                nc.scalar.activation(rstd[:], rstd[:], ACT.Exp, scale=-0.5).then_inc(*act_s.did("root"))

            @block.tensor
            def _(pe):
                pe_s.prime(pe)
                for k in range(KD):
                    pe.wait_ge(*act_s.at(f"square{k}"))
                    for n in range(parts):
                        last = nc.tensor.matmul(sums[:, n, 0:N], co.ones[:], sq[:, k % 2, n * N:(n + 1) * N],
                                                start=k == 0, stop=k == KD - 1)
                    last.then_inc(*pe_s.did(f"sum{k}"))

        @block.vector
        def _(dve):
            dve_s.prime(dve)
            if norm:
                dve.wait_ge(*act_s.at("root"))
            for k in range(KD):
                if k >= 4:
                    dve.wait_ge(stored[k % 4], 16 * (k // 4))
                part = y[:, k]
                if norm:
                    nc.vector.scalar_tensor_tensor(o[:, k % 4], y[:, k], co.par(gain, k), rstd[:], ALU.mult,
                                                   ALU.mult).then_inc(*dve_s.did(f"t{k}"))
                    dve.wait_ge(*dve_s.at(f"t{k}"))
                    part = o[:, k % 4]
                dve.wait_ge(landed[k % 4], 16 * (k // 4 + 1))
                nc.vector.tensor_tensor(o[:, k % 4], part, x[:, k % 4], ALU.add).then_inc(*dve_s.did(f"o{k}"))


def feed_forward(co, tag, u_hi, u_lo, w_up, w_down, acc, w_gate=None):
    nc, pr = co.nc, co.pr
    gated = w_gate is not None
    tail = TAIL if gated else 0
    W = SEQ + tail
    G = W // 3
    H = SEQ // 2
    pairs = w_up.shape[1] // (2 * P)
    up_src = [(lambda i, j=j: columns(w_up, (2 * i + j) * P)) for j in range(2)]
    gate_src = [(lambda i, j=j: columns(w_gate, (2 * i + j) * P)) for j in range(2)] if gated else []
    down_src = [(lambda i, j=j: w_down[ds((2 * i + j) * P, P), :] if not isinstance(i, int)
                 else w_down[(2 * i + j) * P:(2 * i + j + 1) * P, :]) for j in range(2)]
    with ExitStack() as ctx:
        sb = lambda name, shape, dt=F32: ctx.enter_context(nc.sbuf_tensor(tag + name, shape, dt))
        hid = sb("hid", [P, 2, SEQ])
        h_hi, h_lo = sb("h_hi", [P, 2, SEQ], F32R), sb("h_lo", [P, 2, SEQ], F32R)
        if gated:
            gt, cv = sb("gt", [P, 2, W]), sb("cv", [P, 2, SEQ])
        gate = [chunk_terms(j, u_hi, u_lo, KD, n * G, G) for j in range(2) for n in range(3)] if gated else []

        def up(first):
            return [chunk_terms(first + j, u_hi, u_lo, KD, tail + n * H, H) for j in range(2) for n in range(2)]

        def down(first):
            return [(H, [(first + j, (lambda t, m=m: t[:, m * P:(m + 1) * P]), h_hi[:, j, n * H:(n + 1) * H],
                          h_lo[:, j, n * H:(n + 1) * H]) for j in range(2)]) for m in range(KD) for n in range(2)]

        ng = len(gate)
        g2 = len(gate_src)
        later = lambda src: (lambda i: src(i + 1))
        first = pr.stage(1, gate_src + up_src, gate + up(g2))
        main = pr.stage(pairs - 1, [later(s) for s in gate_src] + down_src + [later(s) for s in up_src],
                        gate + down(g2) + up(g2 + 2))
        last = pr.stage(1, [(lambda i, s=s: s(pairs - 1)) for s in down_src], down(0))

        act_n = [f"gelu{j}" for j in range(2)] + [f"hi{j}" for j in range(2)] if gated else \
            [f"{x}{j}" for j in range(2) for x in ("square", "hi")]
        dve_n = ([x for j in range(2) for x in (f"c0{j}", f"c1{j}", f"c2{j}")] if gated else []) + \
            [f"acc{n}" for n in range(16)] + [f"h{j}{n}" for j in range(2) for n in range(2)] + [f"lo{j}" for j in range(2)]
        act_s = Steps(nc, ctx, tag + "act", act_n)
        dve_s = Steps(nc, ctx, tag + "dve", dve_n)
        block = ctx.enter_context(nc.Block())

        def each(eng, body):
            body(first, 0, 0, False)
            with eng.Fori(0, pairs - 1) as i:
                body(main, i, i + 1, True)

        @block.sync
        def _(sp):
            each(sp, lambda st, i, it, steady: [st.load(sp, i, j) for j in range(st.U)])
            for j in range(2):
                last.load(sp, 0, j)

        @block.gpsimd
        def _(pool):
            each(pool, lambda st, i, it, steady: [st.split(pool, i, j) for j in range(st.U)])
            for j in range(2):
                last.split(pool, 0, j)

        @block.tensor
        def _(pe):
            def body(st, i, it, steady):
                for c in range(ng):
                    st.multiply(pe, i, c)
                at = ng
                if steady:
                    pe.wait_ge(*dve_s.at("lo1", it - 1))
                    for c in range(at, at + 16):
                        st.multiply(pe, i, c)
                    at += 16
                for c in range(at, at + 4):
                    st.multiply(pe, i, c)

            each(pe, body)
            pe.wait_ge(*dve_s.at("lo1", pairs - 1))
            for c in range(16):
                last.multiply(pe, 0, c)

        @block.scalar
        def _(act):
            act_s.prime(act)

            def body(st, i, it, steady):
                for c in range(ng):
                    j, n = divmod(c, 3)
                    st.wait_full(act, i, c)
                    act.wait_ge(*dve_s.at(f"c2{j}", it - 1))
                    nc.scalar.copy(gt[:, j, n * G:(n + 1) * G], st.bank_of(c)).then_inc(st.freed(c), 1)
                if gated:
                    for j in range(2):
                        act.wait_ge(*dve_s.at(f"c2{j}", it))
                        nc.scalar.activation(cv[:, j], cv[:, j], ACT.Gelu_apprx_tanh).then_inc(*act_s.did(f"gelu{j}"))
                for j in range(2):
                    act.wait_ge(*dve_s.at(f"h{j}1", it))
                    if not gated:
                        nc.scalar.activation(hid[:, j], hid[:, j], ACT.Square).then_inc(*act_s.did(f"square{j}"))
                        act.wait_ge(*act_s.at(f"square{j}", it))
                    nc.scalar.copy(h_hi[:, j], hid[:, j]).then_inc(*act_s.did(f"hi{j}"))

            each(act, body)

        @block.vector
        def _(dve):
            dve_s.prime(dve)
            def add(st, i, it, c0):
                for c in range(16):
                    m, n = divmod(c, 2)
                    st.wait_full(dve, i, c0 + c)
                    part = acc[:, m, n * H:(n + 1) * H]
                    dve.wait_ge(*dve_s.at(f"acc{c}", it - 1))
                    nc.vector.tensor_tensor(part, part, st.bank_of(c0 + c), ALU.add).then_inc(*dve_s.did(f"acc{c}"))
                    free(st, c0 + c, f"acc{c}", it)

            def free(st, c, step, it):
                dve.wait_ge(*dve_s.at(step, it))
                dve.sem_inc(st.freed(c), 1)

            def body(st, i, it, steady):
                if gated:
                    for j in range(2):
                        for b in range(2):
                            c = max(c for c in range(3 * j, 3 * j + 3) if st.bank[c] == (st.bank[0] + b) % 2)
                            dve.wait_ge(st.freed(c), 2 + st.used[c] + i * st.per[st.bank[c]])
                        dve.wait_ge(*dve_s.at(f"h{j}1", it - 1))
                        tile = 2 * it + j
                        nc.vector.tensor_scalar(cv[:, j], gt[:, j, 0:SEQ], co.par("ffn_conv_w", tile),
                                                co.par("ffn_conv_b", tile), ALU.mult, ALU.add).then_inc(*dve_s.did(f"c0{j}"))
                        for r in (1, 2):
                            dve.wait_ge(*dve_s.at(f"c{r - 1}{j}", it))
                            nc.vector.scalar_tensor_tensor(cv[:, j], gt[:, j, r:SEQ + r], co.par("ffn_conv_w", tile + 2 * pairs * r),
                                                           cv[:, j], ALU.mult, ALU.add).then_inc(*dve_s.did(f"c{r}{j}"))
                at = ng
                if steady:
                    add(st, i, it, at)
                    at += 16
                else:
                    for c in range(16):
                        m, n = divmod(c, 2)
                        nc.vector.memset(acc[:, m, n * H:(n + 1) * H], 0.0).then_inc(*dve_s.did(f"acc{c}"))
                for j in range(2):
                    dve.wait_ge(*act_s.at(f"hi{j}", it - 1))
                    dve.wait_ge(*dve_s.at(f"lo{j}", it - 1))
                    if gated:
                        dve.wait_ge(*act_s.at(f"gelu{j}", it))
                    for n in range(2):
                        c = at + 2 * j + n
                        st.wait_full(dve, i, c)
                        cols = slice(n * H, (n + 1) * H)
                        if gated:
                            ins = nc.vector.tensor_tensor(hid[:, j, cols], cv[:, j, cols], st.bank_of(c), ALU.mult)
                        else:
                            ins = nc.vector.tensor_scalar(hid[:, j, cols], st.bank_of(c), 0.0, None, ALU.max)
                        ins.then_inc(*dve_s.did(f"h{j}{n}"))
                        free(st, c, f"h{j}{n}", it)
                for j in range(2):
                    dve.wait_ge(*act_s.at(f"hi{j}", it))
                    nc.vector.tensor_tensor(h_lo[:, j], hid[:, j], h_hi[:, j].bitcast(F32),
                                            ALU.subtract).then_inc(*dve_s.did(f"lo{j}"))

            each(dve, body)
            for c in range(16):
                m, n = divmod(c, 2)
                last.wait_full(dve, 0, c)
                part = acc[:, m, n * H:(n + 1) * H]
                nc.vector.tensor_tensor(part, part, last.bank_of(c), ALU.add).then_inc(last.freed(c), 1)


HD = 64
NC2 = SEQ // P
PAIRS = 3
RW = PAIRS * P
RWKV_IN = 3 * RW + 2 * P
MLA_IN = 256 + 128 + 32
GDN_AT = RWKV_IN + MLA_IN
P_IN = GDN_AT + 4 * RW + 12
DECAY = float(np.exp(-0.5))
STAGE_TILES = P_IN // P // 4 * 4


def input_projection(co, u_hi, u_lo):
    nc, pr = co.nc, co.pr
    H = SEQ // 2
    w = co.dram["w_in_2"]
    n = STAGE_TILES // 4
    st = pr.stage(n, [(lambda i, j=j: columns(w, (4 * i + j) * P)) for j in range(4)],
                  [chunk_terms(j, u_hi, u_lo, KD, h * H, H) for j in range(4) for h in range(2)])
    rest = [(t * P, min(P, P_IN - t * P)) for t in range(STAGE_TILES, -(-P_IN // P))]

    def rest_terms(j, m, h):
        return (H, [(j, (lambda t, k=k: t[:, k * m:(k + 1) * m]), u_hi[:, k, h * H:(h + 1) * H],
                     u_lo[:, k, h * H:(h + 1) * H]) for k in range(KD)])

    end = pr.stage(1, [(lambda i, at=at, m=m: w.rearrange("(k p) m -> p k m", p=P)[:, :, at:at + m]) for at, m in rest],
                   [rest_terms(j, m, h) for j, (at, m) in enumerate(rest) for h in range(2)])
    with ExitStack() as ctx:
        o = ctx.enter_context(nc.sbuf_tensor("ip_o", [P, 4, SEQ], F32))
        act_s = Steps(nc, ctx, "ip_act", [f"o{j}" for j in range(4)])
        stored = [signal(nc, ctx, f"ip_stored{j}") for j in range(4)]
        block = ctx.enter_context(nc.Block())

        @block.sync
        def _(sp):
            def store(i, j, at, m):
                dest = co.dram["ppT"][ds(at, m), :] if not isinstance(at, int) else co.dram["ppT"][at:at + m, :]
                sp.wait_ge(*act_s.at(f"o{j}", i))
                sp.dma_start(dest, o[0:m, j]).then_inc(stored[j], 16)

            with sp.Fori(0, n) as i:
                for j in range(4):
                    st.load(sp, i, j)
                for j in range(4):
                    store(i, j, (4 * i + j) * P, P)
            for j in range(len(rest)):
                end.load(sp, 0, j)
            for j, (at, m) in enumerate(rest):
                store(n, j, at, m)
            for j in range(4):
                sp.wait_ge(stored[j], 16 + 16 * n + (16 if j < len(rest) else 0))

        @block.gpsimd
        def _(pool):
            with pool.Fori(0, n) as i:
                for j in range(4):
                    st.split(pool, i, j)
            for j in range(len(rest)):
                end.split(pool, 0, j)

        @block.tensor
        def _(pe):
            with pe.Fori(0, n) as i:
                for c in range(8):
                    st.multiply(pe, i, c)
            for c in range(2 * len(rest)):
                end.multiply(pe, 0, c)

        @block.scalar
        def _(act):
            act_s.prime(act)
            for j in range(4):
                act.sem_inc(stored[j], 16)

            def take(s, i, it, j, m):
                act.wait_ge(stored[j], 16 + 16 * it)
                for h in range(2):
                    c = 2 * j + h
                    s.wait_full(act, i, c)
                    ins = nc.scalar.copy(o[0:m, j, h * H:(h + 1) * H], s.bank_of(c, m))
                    if h == 0:
                        ins.then_inc(s.freed(c), 1)
                    else:
                        ins.then_inc(*act_s.did(f"o{j}"))
                        act.wait_ge(*act_s.at(f"o{j}", it))
                        act.sem_inc(s.freed(c), 1)

            with act.Fori(0, n) as i:
                for j in range(4):
                    take(st, i, i, j, P)
            for j, (at, m) in enumerate(rest):
                take(end, 0, n, j, m)


class Masks:

    COUNT = 23

    def __init__(self, co, ctx):
        nc = co.nc
        sb = lambda name, shape, dt=F32: ctx.enter_context(nc.sbuf_tensor(name, shape, dt))
        self.high = sb("mk_high", [P, len(LEVELS), 64], I32)
        self.strict = sb("mk_strict", [P, P], I32)
        self.incl = sb("mk_incl", [P, P], I32)
        self.inclf = sb("mk_inclf", [P, P])
        self.block = sb("mk_block", [P, P])
        self.half = sb("mk_half", [P, P])
        with ExitStack() as c2:
            made = signal(nc, c2, "mk_made")
            block = c2.enter_context(nc.Block())

            @block.gpsimd
            def _(pool):
                n = [0]

                def did(ins):
                    ins.then_inc(made, 1)
                    n[0] += 1
                    pool.wait_ge(made, n[0])

                for m_ in (self.high, self.strict, self.incl):
                    did(nc.gpsimd.memset(m_[:], 1))
                for m_ in (self.inclf, self.block):
                    did(nc.gpsimd.memset(m_[:], 1.0))

                def keep(view, base, pattern, mult):
                    did(nc.gpsimd.affine_select(out=view, in_=view, compare_op=ALU.is_ge, fill=0.0, base=base,
                                                pattern=pattern, channel_multiplier=mult))

                for l, m in enumerate(LEVELS):
                    nb = 64 // m
                    view = self.high[:, l].rearrange("p (b m) -> p b m", m=m)
                    keep(view, 0, [[-2 * m, nb], [0, m]], 1)
                    keep(view, m - 1, [[2 * m, nb], [0, m]], -1)
                keep(self.strict[:], -1, [[1, P]], -1)
                keep(self.incl[:], 0, [[1, P]], -1)
                keep(self.inclf[:], 0, [[1, P]], -1)
                keep(self.block[:, 64:P], -64, [[0, 64]], 1)
                keep(self.block[:, 0:64], 63, [[0, 64]], -1)
                did(nc.gpsimd.tensor_scalar(self.half[:], self.block[:], 1.0 / HD, None, ALU.mult))


def inverse_names():
    last = len(LEVELS) - 1
    pe, act, dve = [], [], ["xt_eye"] + [f"inv_t0{e}" for e in range(2)]
    for l in range(last + 1):
        if l:
            for x in ("y", "z"):
                pe += [f"inv_{x}{l}{e}" for e in range(2)]
            act += [f"inv_y{l}{e}" for e in range(2)]
            dve += [f"inv_t{l}{e}" for e in range(2)]
        if l < last:
            pe += [f"inv_x{l}{e}" for e in range(2)]
            act += [f"inv_x{l}{e}" for e in range(2)]
    return pe, act, dve


class Inverse:

    def __init__(self, co, mk, gT, X, XT, Y, steps):
        self.co, self.mk, self.gT, self.X, self.XT, self.Y = co, mk, gT, X, XT, Y
        self.pe_s, self.act_s, self.dve_s = steps
        self.last = len(LEVELS) - 1

    def bank(self, b):
        return self.co.psum[:, b:b + 2].rearrange("p a (c t) -> p (a c) t", t=P)

    def pe(self, pe, i):
        nc, co = self.co.nc, self.co
        for l in range(self.last + 1):
            if l:
                for e in range(2):
                    pe.wait_ge(*self.act_s.at(f"inv_x{l - 1}{e}", i))
                    for c in range(NC2):
                        q = e * NC2 + c
                        last = nc.tensor.matmul(self.bank(4 * e)[:, c], self.gT[:, q], self.X[:, q], start=True, stop=True)
                    last.then_inc(*self.pe_s.did(f"inv_y{l}{e}"))
                for e in range(2):
                    pe.wait_ge(*self.act_s.at(f"inv_y{l}{e}", i))
                    for c in range(NC2):
                        q = e * NC2 + c
                        last = nc.tensor.matmul(self.bank(4 * e + 2)[:, c], self.Y[:, q], self.XT[:, q], start=True, stop=True)
                    last.then_inc(*self.pe_s.did(f"inv_z{l}{e}"))
            if l < self.last:
                for e in range(2):
                    pe.wait_ge(*self.dve_s.at(f"inv_t{l}{e}", i))
                    for c in range(NC2):
                        last = nc.tensor.transpose(self.bank(4 * e)[:, c], self.XT[:, e * NC2 + c], co.ident[:])
                    last.then_inc(*self.pe_s.did(f"inv_x{l}{e}"))

    def act(self, act, i, other):
        nc = self.co.nc
        for l in range(self.last + 1):
            for x, dst, there in (("y", self.Y, l > 0), ("x", self.X, l < self.last)):
                for e in range(2 if there else 0):
                    act.wait_ge(*self.pe_s.at(f"inv_{x}{l}{e}", i))
                    nc.scalar.copy(dst[:, e * NC2:(e + 1) * NC2], self.bank(4 * e)).then_inc(*self.act_s.did(f"inv_{x}{l}{e}"))
            next(other, None)

    def eye(self, dve, i):
        nc, co = self.co.nc, self.co
        eye = co.ident[:].unsqueeze(1).to_broadcast([P, 2 * NC2, P])
        nc.vector.tensor_copy(self.XT[:], eye).then_inc(*self.dve_s.did("xt_eye"))

    def dve(self, dve, i, other):
        nc, co = self.co.nc, self.co
        for l, m in enumerate(reversed(LEVELS)):
            half = lambda x: x.rearrange("p c (b two m) -> p c b two m", two=2, m=m)[:, :, :, 1]
            mask = self.mk.high[:, self.last - l].rearrange("p (b m) -> p b m", m=m).unsqueeze(1).to_broadcast([P, NC2, 64 // m, m])
            for e in range(2):
                mine = slice(e * NC2, (e + 1) * NC2)
                if l:
                    dve.wait_ge(*self.pe_s.at(f"inv_z{l}{e}", i))
                    dve.wait_ge(*self.dve_s.at(f"inv_t{l - 1}{e}", i))
                    source = self.bank(4 * e + 2)
                else:
                    source = self.gT[:, mine]
                co.pr.carry(dve)
                nc.vector.copy_predicated(half(self.XT[:, mine]), mask, half(source)).then_inc(*self.dve_s.did(f"inv_t{l}{e}"))
            next(other, None)


def rows(x, at, i):
    return x[ds(at + i * P, P), :] if not isinstance(i, int) else x[at + i * P:at + i * P + P, :]


def each_pair(eng, first, body):
    for _ in first(0):
        pass
    with eng.Fori(0, PAIRS - 1) as i:
        body(i, first(i + 1))
    body(PAIRS - 1, iter(()))


def rwkv(co, mk):
    nc = co.nc
    N = SEQ
    ppT = co.dram["ppT"]
    with ExitStack() as ctx:
        sb = lambda name, shape, dt=F32: ctx.enter_context(nc.sbuf_tensor("rw_" + name, shape, dt))
        buf = sb("buf", [P, 3, N + 1])
        z = sb("z", [P, 3, N])
        lora, sg = sb("lora", [P, N]), sb("sg", [P, N])
        lw = sb("lw", [P, 3, P])
        oma = sb("oma", [P, PAIRS])
        w, a, g = sb("w", [P, N]), sb("a", [P, N]), sb("g", [P, N])
        s, kk, bv, bo = sb("s", [P, N]), sb("kk", [P, N]), sb("bv", [P, N]), sb("bo", [P, N])
        d1, ep, em, ex = sb("d1", [P, N]), sb("ep", [P, N]), sb("em", [P, N]), sb("ex", [P, N])
        ar = sb("ar", [P, NC2, 2, P])
        bf, kf = sb("bf", [P, N]), sb("kf", [P, N])
        bp, kp = sb("bp", [P, 2, N]), sb("kp", [P, 2, N])
        vt, bt, kt = sb("vt", [P, NC2, P]), sb("bt", [P, NC2, P]), sb("kt", [P, NC2, P])
        gT, ak, rb, rk = (sb(n, [P, 2 * NC2, P]) for n in ("gT", "ak", "rb", "rk"))
        X, XT, Y = (sb(n, [P, 2 * NC2, P]) for n in ("X", "XT", "Y"))
        H = sb("H", [P, NC2, P])
        rh, sa, ht = sb("rh", [P, P]), sb("sa", [P, NC2, P]), sb("ht", [P, P])
        ratio = sb("ratio", [P, NC2])
        zr, zk, zv = z[:, 0], z[:, 1], z[:, 2]
        ch = lambda x: x.rearrange("p (c t) -> p c t", t=P)
        ps = co.psum
        two = lambda b: ps[:, b:b + 2].rearrange("p a b -> p (a b)")
        par = co.par

        ipe, iact, idve = inverse_names()
        chunkwise = [x for c in range(NC2) for x in ([f"r{c}", f"sa{c}", f"h{c}", f"y{c}"] if c < NC2 - 1 else [f"r{c}", f"sa{c}", f"y{c}"])]
        pe_s = Steps(nc, ctx, "rw_pe", ["lora", "ss", "bonus", "vt", "bt", "kt"] + [f"g{x}{e}" for e in range(2) for x in "bk"]
                     + ipe + chunkwise + ["mean", "var"])
        act_a = Steps(nc, ctx, "rw_act_a", ["sq"])
        act_s = Steps(nc, ctx, "rw_act", ["w", "a", "g", "ln", "root", "ep", "em", "ratio", "ex", "vt", "bt", "kt"] + iact
                      + [x for c in range(NC2) for x in (f"r{c}", f"sa{c}")] + ["y", "ysq", "yln", "yroot"])
        dve_a = Steps(nc, ctx, "rw_dve_a", [f"{x}{n}" for n in range(3) for x in ("sh", "z")] + ["kk"])
        dve_n = [f"s{c}" for c in range(NC2)] + \
            ["ta", "k2", "kkn", "d1", "d2", "rt0", "rt1", "rkr", "bonus", "bv", "bf", "kf", "A", "R", "bo"] + ["xt_eye"] + \
            [f"{x}{e}" for e in range(2) for x in ("gT", "rb", "ak", "rk")] + idve[1:] + \
            [x for c in range(NC2 - 1) for x in (f"ht{c}", f"H{c}")] + ["yc", "yn", "yb", "yo"]
        dve_s = Steps(nc, ctx, "rw_dve", dve_n)
        pool_s = Steps(nc, ctx, "rw_pool", ["bp0", "bp1", "kp0", "kp1"])
        inv = Inverse(co, mk, gT, X, XT, Y, (pe_s, act_s, dve_s))
        in_s = signal(nc, ctx, "rw_in")
        lw_s = signal(nc, ctx, "rw_lw")
        out_s = signal(nc, ctx, "rw_out")
        pre_in = signal(nc, ctx, "rw_pre_in")
        pre_v = signal(nc, ctx, "rw_pre_dve")
        pre_a = signal(nc, ctx, "rw_pre_act")
        zeros = signal(nc, ctx, "rw_zeros")
        ZEROS = 9
        block = ctx.enter_context(nc.Block())

        @block.sync
        def _(sp):
            sp.wait_ge(zeros, 2)
            sp.dma_start(buf[:, 0, 1:N + 1], ppT[3 * RW:3 * RW + P, :]).then_inc(pre_in, 16)
            sp.dma_start(buf[:, 1, 1:N + 1], ppT[3 * RW + P:3 * RW + 2 * P, :]).then_inc(pre_in, 16)
            sp.wait_ge(pre_v, 5)
            def first(i):
                src = [rows(ppT, n * RW, i) for n in range(3)]
                sp.wait_ge(*dve_a.at("z2", i - 1))
                for n in range(3):
                    sp.dma_start(buf[:, n, 1:N + 1], src[n]).then_inc(in_s, 16)
                yield

            def body(i, following):
                cols = ds(i * P, P) if not isinstance(i, int) else slice(i * P, (i + 1) * P)
                w2 = co.dram["rwkv_w2_2"][:, cols]
                sp.wait_ge(*pe_s.at("lora", i - 1))
                co.pr.carry(sp)
                sp.dma_start(lw[0:HD, 0], w2).then_inc(lw_s, 16)
                sp.dma_start(lw[HD:P, 1], co.dram["rwkv_a2_2"][:, cols]).then_inc(lw_s, 16)
                sp.dma_start(lw[:, 2], co.dram["rwkv_g2_2"][:, cols]).then_inc(lw_s, 16)
                for _ in following:
                    pass
                dest = rows(co.dram["yT"], 0, i)
                sp.wait_ge(*dve_s.at("yo", i))
                sp.dma_start(dest, bo[:]).then_inc(out_s, 16)

            each_pair(sp, first, body)
            sp.wait_ge(out_s, 16 + 16 * PAIRS)

        @block.gpsimd
        def _(pool):
            pool_s.prime(pool)
            nc.gpsimd.memset(lw[:], 0.0).then_inc(zeros, 1)
            nc.gpsimd.memset(buf[:, :, 0:1], 0.0).then_inc(zeros, 1)
            for x in (bp, kp, gT, ak, rb, rk):
                nc.gpsimd.memset(x[:], 0.0).then_inc(zeros, 1)
            nc.gpsimd.memset(H[:, 0], 0.0).then_inc(zeros, 1)
            pool.wait_ge(zeros, ZEROS)
            with pool.Fori(0, PAIRS) as i:
                for n, (dst, src, name) in enumerate(((bp, bf, "b"), (kp, kf, "k"))):
                    pool.wait_ge(*dve_s.at(f"{name}f", i))
                    pool.wait_ge(*pe_s.at("gk1", i - 1))
                    for e in range(2):
                        rows = slice(e * HD, (e + 1) * HD)
                        nc.gpsimd.tensor_tensor(dst[rows, e], src[rows], co.zero[rows].to_broadcast([HD, N]),
                                                ALU.add).then_inc(*pool_s.did(f"{name}p{e}"))

        @block.scalar
        def _(act):
            act_a.prime(act)
            act_s.prime(act)
            act.sem_inc(out_s, 16)
            act.wait_ge(pre_v, 2)
            nc.scalar.activation(lora[0:HD], lora[0:HD], ACT.Tanh).then_inc(pre_a, 1)
            act.wait_ge(pre_v, 4)
            nc.scalar.activation(sg[:], sg[:], ACT.Sigmoid).then_inc(pre_a, 1)

            def first(i):
                for _ in range(4):
                    yield
                act.wait_ge(*dve_a.at("kk", i))
                nc.scalar.activation(bf[:], kk[:], ACT.Square).then_inc(*act_a.did("sq"))

            def body(i, following):
                act.wait_ge(*pe_s.at("lora", i))
                act.wait_ge(*dve_s.at("yo", i - 1))
                nc.scalar.activation(w[:], two(0), ACT.Sigmoid, bias=par("rwkv_w0_2", i)).then_inc(*act_s.did("w"))
                nc.scalar.activation(a[:], two(2), ACT.Sigmoid, bias=par("rwkv_a0_2", i)).then_inc(*act_s.did("a"))
                nc.scalar.copy(g[:], two(4)).then_inc(*act_s.did("g"))
                act.wait_ge(*pe_s.at("ss", i))
                nc.scalar.activation(ex[:], two(0), ACT.Ln, bias=co.eps[:]).then_inc(*act_s.did("ln"))
                act.wait_ge(*act_s.at("ln", i))
                nc.scalar.activation(bv[:], ex[:], ACT.Exp, scale=-0.5).then_inc(*act_s.did("root"))
                act.wait_ge(*dve_s.at("rt1", i))
                nc.scalar.activation(ep[:], d1[:], ACT.Exp, scale=DECAY).then_inc(*act_s.did("ep"))
                nc.scalar.activation(em[:], d1[:], ACT.Exp, scale=-DECAY).then_inc(*act_s.did("em"))
                nc.scalar.activation(ratio[:], ratio[:], ACT.Exp, scale=-DECAY).then_inc(*act_s.did("ratio"))
                nc.scalar.activation(ex[:], w[:], ACT.Exp, scale=-DECAY).then_inc(*act_s.did("ex"))
                act.wait_ge(*pe_s.at("vt", i))
                nc.scalar.copy(vt[:], ch(two(0))).then_inc(*act_s.did("vt"))
                act.wait_ge(*pe_s.at("bt", i))
                nc.scalar.copy(bt[:], ch(two(4))).then_inc(*act_s.did("bt"))
                act.wait_ge(*pe_s.at("kt", i))
                nc.scalar.copy(kt[:], ch(two(6))).then_inc(*act_s.did("kt"))
                inv.act(act, i, following)
                for c in range(NC2):
                    act.wait_ge(*pe_s.at(f"r{c}", i))
                    nc.scalar.copy(rh[:], ps[:, 0, 0:P]).then_inc(*act_s.did(f"r{c}"))
                    act.wait_ge(*pe_s.at(f"sa{c}", i))
                    nc.scalar.copy(sa[:, c], ps[:, 1, 0:P]).then_inc(*act_s.did(f"sa{c}"))
                act.wait_ge(*pe_s.at(f"y{NC2 - 1}", i))
                nc.scalar.copy(d1[:], two(4)).then_inc(*act_s.did("y"))
                act.wait_ge(*dve_s.at("yc", i))
                nc.scalar.activation(em[:], d1[:], ACT.Square).then_inc(*act_s.did("ysq"))
                act.wait_ge(*pe_s.at("var", i))
                nc.scalar.activation(ex[:], two(2), ACT.Ln, bias=co.gn_eps[:]).then_inc(*act_s.did("yln"))
                act.wait_ge(*act_s.at("yln", i))
                nc.scalar.activation(ex[:], ex[:], ACT.Exp, scale=-0.5).then_inc(*act_s.did("yroot"))

            each_pair(act, first, body)

        @block.tensor
        def _(pe):
            pe_s.prime(pe)
            pe.wait_ge(pre_a, 2)
            pe.wait_ge(pre_v, 5)
            pe.wait_ge(zeros, ZEROS)
            halves = [slice(0, 512), slice(512, 1024)]

            def wide(bank, lhsT, rhs):
                for h, cols in enumerate(halves):
                    last = nc.tensor.matmul(ps[:, bank + h], lhsT, rhs[:, cols], start=True, stop=True)
                return last

            with pe.Fori(0, PAIRS) as i:
                pe.wait_ge(lw_s, 48 * i + 48)
                pe.wait_ge(*act_s.at("yln", i - 1))
                wide(0, lw[:, 0], lora)
                wide(2, lw[:, 1], lora)
                wide(4, lw[:, 2], sg).then_inc(*pe_s.did("lora"))
                pe.wait_ge(*act_a.at("sq", i))
                pe.wait_ge(*act_s.at("w", i))
                wide(0, mk.block[:], bf).then_inc(*pe_s.did("ss"))
                pe.wait_ge(*dve_s.at("bonus", i))
                wide(2, mk.block[:], bo).then_inc(*pe_s.did("bonus"))
                pe.wait_ge(*dve_a.at("z2", i))
                pe.wait_ge(*act_s.at("ln", i))
                for c in range(NC2):
                    last = nc.tensor.transpose(ch(two(0))[:, c], zv[:, c * P:(c + 1) * P], co.ident[:])
                last.then_inc(*pe_s.did("vt"))
                pe.wait_ge(*dve_s.at("bf", i))
                pe.wait_ge(*act_s.at("g", i))
                for c in range(NC2):
                    last = nc.tensor.transpose(ch(two(4))[:, c], bf[:, c * P:(c + 1) * P], co.ident[:])
                last.then_inc(*pe_s.did("bt"))
                pe.wait_ge(*dve_s.at("kf", i))
                for c in range(NC2):
                    last = nc.tensor.transpose(ch(two(6))[:, c], kf[:, c * P:(c + 1) * P], co.ident[:])
                last.then_inc(*pe_s.did("kt"))
                pe.wait_ge(*dve_s.at("bo", i))
                pe.wait_ge(*act_s.at("kt", i))
                pe.wait_ge(*pool_s.at("kp1", i))
                for e in range(2):
                    for n, (src, x, last_read) in enumerate(((bp, "b", "rb"), (kp, "k", "rk"))):
                        if e:
                            pe.wait_ge(*dve_s.at(f"{last_read}0", i))
                        for c in range(NC2):
                            last = nc.tensor.matmul(ps[:, 4 * n + c // 2, (c % 2) * 256:(c % 2) * 256 + 256],
                                                    src[:, e, c * P:(c + 1) * P],
                                                    ar[:, c].rearrange("p a t -> p (a t)"), start=True, stop=True)
                        last.then_inc(*pe_s.did(f"g{x}{e}"))
                pe.wait_ge(*dve_s.at("rk1", i))
                inv.pe(pe, i)
                for c in range(NC2):
                    if c == 0:
                        pe.wait_ge(*dve_s.at("inv_t61", i))
                    else:
                        pe.wait_ge(*dve_s.at(f"H{c - 1}", i))
                    nc.tensor.matmul(ps[:, 0, 0:P], ar[:, c, 0], H[:, c], start=True, stop=False)
                    for e in range(2):
                        cols = slice(e * HD, (e + 1) * HD)
                        last = nc.tensor.matmul(ps[:, 0, cols], ak[:, e * NC2 + c], vt[:, c, cols], start=False, stop=e == 1)
                    last.then_inc(*pe_s.did(f"r{c}"))
                    pe.wait_ge(*act_s.at(f"r{c}", i))
                    for e in range(2):
                        cols = slice(e * HD, (e + 1) * HD)
                        last = nc.tensor.matmul(ps[:, 1, cols], XT[:, e * NC2 + c], rh[:, cols], start=True, stop=True)
                    last.then_inc(*pe_s.did(f"sa{c}"))
                    pe.wait_ge(*act_s.at(f"sa{c}", i))
                    if c < NC2 - 1:
                        nc.tensor.matmul(ps[:, 2, 0:P], kt[:, c], vt[:, c], start=True, stop=False)
                        nc.tensor.matmul(ps[:, 2, 0:P], bt[:, c], sa[:, c], start=False, stop=True)\
                          .then_inc(*pe_s.did(f"h{c}"))
                    for e in range(2):
                        cols = slice(e * HD, (e + 1) * HD)
                        out = ch(two(4))[cols, c]
                        nc.tensor.matmul(out, sa[:, c, cols], rb[:, e * NC2 + c], start=True, stop=False)
                        nc.tensor.matmul(out, vt[:, c, cols], rk[:, e * NC2 + c], start=False, stop=False)
                        last = nc.tensor.matmul(out, H[:, c, cols], ar[:, c, 1], start=False, stop=True)
                    last.then_inc(*pe_s.did(f"y{c}"))
                pe.wait_ge(*act_s.at("y", i))
                wide(0, mk.half[:], d1).then_inc(*pe_s.did("mean"))
                pe.wait_ge(*act_s.at("ysq", i))
                wide(2, mk.half[:], em).then_inc(*pe_s.did("var"))

        @block.vector
        def _(dve):
            dve_a.prime(dve)
            dve_s.prime(dve)
            V = nc.vector
            dve.wait_ge(zeros, ZEROS)
            dve.wait_ge(pre_in, 32)
            for n, dst in ((0, lora), (1, sg)):
                V.tensor_tensor(dst[:], buf[:, n, 0:N], buf[:, n, 1:N + 1], ALU.subtract).then_inc(pre_v, 1)
                dve.wait_ge(pre_v, 2 * n + 1)
                V.scalar_tensor_tensor(dst[:], dst[:], par("rwkv_mu_2", 9 + n), buf[:, n, 1:N + 1], ALU.mult,
                                       ALU.add).then_inc(pre_v, 1)
            at = co.pl.at["rwkv_k_a_2"][0]
            V.tensor_scalar(oma[:], co.prm[:, at:at + PAIRS], -1.0, 1.0, ALU.mult, ALU.add).then_inc(pre_v, 1)
            dve.wait_ge(pre_v, 5)

            def first(i):
                def did(name, ins, wait=False):
                    ins.then_inc(*dve_a.did(name))
                    if wait:
                        dve.wait_ge(*dve_a.at(name, i))

                dve.wait_ge(in_s, 48 * i + 48)
                for n in range(3):
                    did(f"sh{n}", V.tensor_tensor(z[:, n], buf[:, n, 0:N], buf[:, n, 1:N + 1], ALU.subtract), True)
                    did(f"z{n}", V.scalar_tensor_tensor(z[:, n], z[:, n], par("rwkv_mu_2", i + 3 * n), buf[:, n, 1:N + 1],
                                                        ALU.mult, ALU.add), n == 1)
                    yield
                did("kk", V.tensor_scalar(kk[:], zk, par("rwkv_k_k_2", i), None, ALU.mult))

            def body(i, following):
                def did(name, ins, wait=False):
                    ins.then_inc(*dve_s.did(name))
                    if wait:
                        dve.wait_ge(*dve_s.at(name, i))

                dve.wait_ge(*act_s.at("w", i))
                for c in range(NC2):
                    did(f"s{c}", V.tensor_tensor_scan(s[:, c * P:(c + 1) * P], co.ones[:], w[:, c * P:(c + 1) * P], 0.0,
                                                      ALU.mult, ALU.add))
                dve.wait_ge(*act_s.at("a", i))
                did("ta", V.tensor_scalar(d1[:], a[:], par("rwkv_k_a_2", i), oma[:, ds(i, 1)] if not isinstance(i, int) else oma[:, i:i + 1],
                                          ALU.mult, ALU.add), True)
                did("k2", V.tensor_tensor(zk, zk, d1[:], ALU.mult), True)
                dve.wait_ge(*act_s.at("root", i))
                did("kkn", V.tensor_tensor(kk[:], kk[:], bv[:], ALU.mult), True)
                sc = ch(s[:])
                did("d1", V.tensor_tensor(ch(d1[:]), sc, sc[:, :, HD - 1:HD].to_broadcast([P, NC2, P]), ALU.subtract), True)
                did("d2", V.tensor_tensor(w[:], d1[:], w[:], ALU.subtract))
                did("rt0", V.tensor_copy(ratio[:], ch(d1[:])[:, :, P - 1]), True)
                did("rt1", V.tensor_tensor(ratio[:, 0:NC2 - 1], ratio[:, 0:NC2 - 1], sc[:, 1:NC2, HD - 1], ALU.add))
                dve.wait_ge(out_s, 16 * i + 16)
                did("rkr", V.tensor_tensor(bo[:], zr, zk, ALU.mult), True)
                did("bonus", V.tensor_scalar(bo[:], bo[:], par("rwkv_r_k_2", i), None, ALU.mult))
                did("bv", V.scalar_tensor_tensor(bv[:], kk[:], -1.0, a[:], ALU.mult, ALU.mult), True)
                dve.wait_ge(*act_s.at("ep", i))
                did("bf", V.tensor_tensor(bf[:], bv[:], ep[:], ALU.mult))
                did("kf", V.tensor_tensor(kf[:], zk, ep[:], ALU.mult))
                dve.wait_ge(*act_s.at("ex", i))
                did("A", V.tensor_tensor(ar[:, :, 0], ch(kk[:]), ch(ex[:]), ALU.mult))
                did("R", V.tensor_tensor(ar[:, :, 1], ch(zr), ch(em[:]), ALU.mult))
                dve.wait_ge(*pe_s.at("bonus", i))
                did("bo", V.tensor_tensor(bo[:], two(2), zv, ALU.mult))
                inv.eye(dve, i)
                for e in range(2):
                    for x, n, half, mask, src in (("gT", 0, 0, mk.strict, gT), ("rb", 0, 1, mk.incl, rb),
                                                  ("ak", 1, 0, mk.strict, ak), ("rk", 1, 1, mk.incl, rk)):
                        if half == 0:
                            dve.wait_ge(*pe_s.at(f"g{'bk'[n]}{e}", i))
                            co.pr.carry(dve)
                        grams = ps[:, 4 * n:4 * n + 4].rearrange("p a b -> p (a b)").rearrange("p (c h t) -> p c h t", h=2, t=P)
                        did(f"{x}{e}", V.copy_predicated(src[:, e * NC2:(e + 1) * NC2],
                                                         mask[:].unsqueeze(1).to_broadcast([P, NC2, P]), grams[:, :, half]))
                dve.wait_ge(*dve_s.at("rk1", i))
                inv.dve(dve, i, following)
                for c in range(NC2 - 1):
                    dve.wait_ge(*pe_s.at(f"h{c}", i))
                    did(f"ht{c}", V.tensor_tensor(ht[:], ps[:, 2, 0:P], H[:, c], ALU.add), True)
                    did(f"H{c}", V.scalar_tensor_tensor(H[:, c + 1], ht[:], ratio[:, c:c + 1], mk.block[:], ALU.mult, ALU.mult), True)
                dve.wait_ge(*pe_s.at("mean", i))
                did("yc", V.tensor_tensor(d1[:], d1[:], two(0), ALU.subtract))
                dve.wait_ge(*act_s.at("yroot", i))
                did("yn", V.scalar_tensor_tensor(d1[:], d1[:], par("rwkv_gn_g_2", i), ex[:], ALU.mult, ALU.mult), True)
                did("yb", V.scalar_tensor_tensor(bo[:], d1[:], par("rwkv_gn_b_2", i), bo[:], ALU.add, ALU.add), True)
                did("yo", V.tensor_tensor(bo[:], bo[:], g[:], ALU.mult))

            each_pair(dve, first, body)


HEADS2 = 2 * PAIRS


def deltanet(co, mk):
    nc = co.nc
    N = SEQ
    ppT = co.dram["ppT"]
    par = co.par
    ps = co.psum
    ch = lambda x: x.rearrange("p (c t) -> p c t", t=P)
    two = lambda b: ps[:, b:b + 2].rearrange("p a b -> p (a b)")
    halves = [slice(0, 512), slice(512, 1024)]
    with ExitStack() as ctx:
        sb = lambda name, shape, dt=F32: ctx.enter_context(nc.sbuf_tensor("gd_" + name, shape, dt))
        gB, bB = sb("gB", [P, PAIRS, N]), sb("bB", [P, PAIRS, N])
        rowsel = sb("rowsel", [P, 2, P])
        delta_gates(co, gB, bB, rowsel)
        buf = sb("buf", [P, 3, N + 3])
        z, sg = sb("z", [P, 3, N]), sb("sg", [P, 3, N])
        gi, ga, y, o = sb("gi", [P, N]), sb("ga", [P, N]), sb("y", [P, N]), sb("o", [P, N])
        gc, eg, kd = sb("gc", [P, N]), sb("eg", [P, N]), sb("kd", [P, N])
        gct, decay = sb("gct", [P, NC2, 2]), sb("decay", [P, NC2])
        ar = sb("ar", [P, NC2, 2, P])
        At, qe, kp = sb("At", [P, N]), sb("qe", [P, N]), sb("kp", [P, 2, N])
        Dm = sb("Dm", [P, 2, N])
        gq = sb("gq", [P, 2 * NC2, 2, P])
        vt, kt = sb("vt", [P, NC2, P]), sb("kt", [P, NC2, P])
        X, XT, Y = (sb(n, [P, 2 * NC2, P]) for n in ("X", "XT", "Y"))
        H, sa = sb("H", [P, NC2, P]), sb("sa", [P, NC2, P])
        rh, ht = sb("rh", [P, P]), sb("ht", [P, P])
        rs, sq = Dm, sg[:, 0:2]
        q, k, v = z[:, 0], z[:, 1], z[:, 2]

        ipe, iact, idve = inverse_names()
        pe_s = Steps(nc, ctx, "gd_pe", ["ss", "row", "gct", "vt", "kt", "g0", "g1"] + ipe
                     + [x for c in range(NC2) for x in ([f"r{c}", f"sa{c}"] + ([f"h{c}"] if c < NC2 - 1 else []) + [f"y{c}"])]
                     + ["mean"])
        act_a = Steps(nc, ctx, "gd_act_a", ["sg", "sq"])
        act_s = Steps(nc, ctx, "gd_act", ["ln", "root", "eg", "kd", "decay", "gct", "D", "vt", "kt"] + iact + ["so"]
                      + [f"sa{c}" for c in range(NC2)] + ["y", "ysq", "yln", "yroot"])
        dve_a = Steps(nc, ctx, "gd_dve_a", [f"c{r}{n}" for n in range(3) for r in range(4)]
                      + [f"s{c}" for c in range(NC2)] + ["dkd", "silu"])
        dve_s = Steps(nc, ctx, "gd_dve", ["last", "q", "k", "bk", "v", "kdk", "At", "qe"]
                      + [f"D{e}{c}" for e in range(2) for c in range(NC2)] + ["xt_eye", "gq0", "gq1"] + idve[1:] + ["gate"]
                      + [x for c in range(NC2) for x in ([f"r{c}"] + ([f"ht{c}", f"H{c}"] if c < NC2 - 1 else []))]
                      + ["yn", "yo"])
        pool_s = Steps(nc, ctx, "gd_pool", ["kp0", "kp1", "D"])
        inv = Inverse(co, mk, gq[:, :, 0], X, XT, Y, (pe_s, act_s, dve_s))
        in_s, gate_s, out_s, zeros = (signal(nc, ctx, n) for n in ("gd_in", "gd_gate_in", "gd_out", "gd_zeros"))
        ZEROS = 3
        block = ctx.enter_context(nc.Block())

        @block.sync
        def _(sp):
            def first(i):
                src = [rows(ppT, GDN_AT + n * RW, i) for n in range(3)]
                sp.wait_ge(*dve_a.at("c32", i - 1))
                for n in range(3):
                    sp.dma_start(buf[:, n, 3:N + 3], src[n]).then_inc(in_s, 16)
                yield

            def body(i, following):
                gate = rows(ppT, GDN_AT + 3 * RW, i)
                dest = rows(co.dram["yT"], RW + 4 * HD, i)
                sp.wait_ge(*dve_s.at("gate", i - 1))
                sp.dma_start(gi[:], gate).then_inc(gate_s, 16)
                for _ in following:
                    pass
                sp.wait_ge(*dve_s.at("yo", i))
                sp.dma_start(dest, o[:]).then_inc(out_s, 16)

            each_pair(sp, first, body)
            sp.wait_ge(out_s, 16 + 16 * PAIRS)

        @block.gpsimd
        def _(pool):
            pool_s.prime(pool)
            nc.gpsimd.memset(buf[:, :, 0:3], 0.0).then_inc(zeros, 1)
            nc.gpsimd.memset(kp[:], 0.0).then_inc(zeros, 1)
            nc.gpsimd.memset(H[:, 0], 0.0).then_inc(zeros, 1)
            pool.wait_ge(zeros, ZEROS)
            with pool.Fori(0, PAIRS) as i:
                pool.wait_ge(*pool_s.at("D", i - 1))
                pool.wait_ge(*dve_s.at("k", i))
                pool.wait_ge(*pe_s.at("g1", i - 1))
                for e in range(2):
                    rows = slice(e * HD, (e + 1) * HD)
                    nc.gpsimd.tensor_tensor(kp[rows, e], k[rows], co.zero[rows].to_broadcast([HD, N]),
                                            ALU.add).then_inc(*pool_s.did(f"kp{e}"))
                pool.wait_ge(*pool_s.at("kp1", i))
                pool.wait_ge(*act_s.at("D", i))
                dmv = Dm[:].rearrange("p e (c t) -> p (e c) t", t=P)
                nc.gpsimd.tensor_tensor(dmv, dmv, mk.inclf[:].unsqueeze(1).to_broadcast([P, 2 * NC2, P]),
                                        ALU.mult).then_inc(*pool_s.did("D"))

        @block.scalar
        def _(act):
            act_a.prime(act)
            act_s.prime(act)
            act.sem_inc(out_s, 16)

            def first(i):
                for _ in range(4):
                    yield
                act.wait_ge(*dve_a.at("c32", i))
                nc.scalar.activation(sg[:], z[:], ACT.Sigmoid).then_inc(*act_a.did("sg"))
                yield
                act.wait_ge(*dve_a.at("silu", i))
                nc.scalar.activation(sq, z[:, 0:2], ACT.Square).then_inc(*act_a.did("sq"))

            def body(i, following):
                act.wait_ge(*pe_s.at("ss", i))
                nc.scalar.activation(rs[:].rearrange("p a (b t) -> p (a b) t", b=2), ps[:, 0:4], ACT.Ln,
                                     bias=co.eps[:]).then_inc(*act_s.did("ln"))
                act.wait_ge(*act_s.at("ln", i))
                nc.scalar.activation(rs[:], rs[:], ACT.Exp, scale=-0.5).then_inc(*act_s.did("root"))
                act.wait_ge(*dve_a.at("dkd", i))
                nc.scalar.activation(eg[:], gc[:], ACT.Exp).then_inc(*act_s.did("eg"))
                nc.scalar.activation(kd[:], kd[:], ACT.Exp).then_inc(*act_s.did("kd"))
                act.wait_ge(*dve_s.at("last", i))
                nc.scalar.activation(decay[:], decay[:], ACT.Exp).then_inc(*act_s.did("decay"))
                act.wait_ge(*pe_s.at("gct", i))
                nc.scalar.copy(gct[:], ch(two(4)).rearrange("p c (e k) -> p c e k", e=2)[:, :, :, 0]).then_inc(*act_s.did("gct"))
                act.wait_ge(*dve_s.at(f"D1{NC2 - 1}", i))
                nc.scalar.activation(Dm[:], Dm[:], ACT.Exp).then_inc(*act_s.did("D"))
                act.wait_ge(*pe_s.at("vt", i))
                nc.scalar.copy(vt[:], ch(two(6))).then_inc(*act_s.did("vt"))
                act.wait_ge(*pe_s.at("kt", i))
                nc.scalar.copy(kt[:], ch(two(4))).then_inc(*act_s.did("kt"))
                inv.act(act, i, following)
                act.wait_ge(gate_s, 16 * i + 16)
                act.wait_ge(*dve_s.at("yo", i - 1))
                nc.scalar.activation(ga[:], gi[:], ACT.Sigmoid).then_inc(*act_s.did("so"))
                for c in range(NC2):
                    act.wait_ge(*pe_s.at(f"sa{c}", i))
                    nc.scalar.copy(sa[:, c], ps[:, 1, 0:P]).then_inc(*act_s.did(f"sa{c}"))
                act.wait_ge(*pe_s.at(f"y{NC2 - 1}", i))
                nc.scalar.copy(y[:], two(4)).then_inc(*act_s.did("y"))
                act.wait_ge(*act_s.at("y", i))
                nc.scalar.activation(At[:], y[:], ACT.Square).then_inc(*act_s.did("ysq"))
                act.wait_ge(*pe_s.at("mean", i))
                nc.scalar.activation(At[:], two(0), ACT.Ln, bias=co.eps[:]).then_inc(*act_s.did("yln"))
                act.wait_ge(*act_s.at("yln", i))
                nc.scalar.activation(At[:], At[:], ACT.Exp, scale=-0.5).then_inc(*act_s.did("yroot"))

            each_pair(act, first, body)

        @block.tensor
        def _(pe):
            pe_s.prime(pe)
            pe.wait_ge(zeros, ZEROS)

            def wide(bank, lhsT, rhs):
                for h, cols in enumerate(halves):
                    last = nc.tensor.matmul(ps[:, bank + h], lhsT, rhs[:, cols], start=True, stop=True)
                return last

            with pe.Fori(0, PAIRS) as i:
                pe.wait_ge(*act_s.at("yln", i - 1))
                pe.wait_ge(*act_a.at("sq", i))
                wide(0, mk.block[:], sq[:, 0])
                wide(2, mk.block[:], sq[:, 1]).then_inc(*pe_s.did("ss"))
                pe.wait_ge(*act_s.at("ln", i))
                wide(0, rowsel[:, 0], gc)
                wide(2, rowsel[:, 1], gc).then_inc(*pe_s.did("row"))
                for c in range(NC2):
                    last = nc.tensor.transpose(ch(two(4))[:, c], gc[:, c * P:(c + 1) * P], co.ident[:])
                last.then_inc(*pe_s.did("gct"))
                pe.wait_ge(*dve_s.at("kdk", i))
                for c in range(NC2):
                    last = nc.tensor.transpose(ch(two(6))[:, c], v[:, c * P:(c + 1) * P], co.ident[:])
                last.then_inc(*pe_s.did("vt"))
                pe.wait_ge(*act_s.at("gct", i))
                for c in range(NC2):
                    last = nc.tensor.transpose(ch(two(4))[:, c], kd[:, c * P:(c + 1) * P], co.ident[:])
                last.then_inc(*pe_s.did("kt"))
                pe.wait_ge(*pool_s.at("kp1", i))
                for e in range(2):
                    if e == 0:
                        pe.wait_ge(*dve_s.at(f"D1{NC2 - 1}", i))
                    else:
                        pe.wait_ge(*act_s.at("kt", i))
                    for c in range(NC2):
                        last = nc.tensor.matmul(ps[:, 4 * e + c // 2, (c % 2) * 256:(c % 2) * 256 + 256],
                                                kp[:, e, c * P:(c + 1) * P],
                                                ar[:, c].rearrange("p a t -> p (a t)"), start=True, stop=True)
                    last.then_inc(*pe_s.did(f"g{e}"))
                pe.wait_ge(*dve_s.at("gq1", i))
                inv.pe(pe, i)
                for c in range(NC2):
                    if c == 0:
                        pe.wait_ge(*dve_s.at("inv_t61", i))
                    else:
                        pe.wait_ge(*dve_s.at(f"H{c - 1}", i))
                    nc.tensor.matmul(ps[:, 0, 0:P], At[:, c * P:(c + 1) * P], H[:, c], start=True, stop=True)\
                      .then_inc(*pe_s.did(f"r{c}"))
                    pe.wait_ge(*dve_s.at(f"r{c}", i))
                    for e in range(2):
                        cols = slice(e * HD, (e + 1) * HD)
                        last = nc.tensor.matmul(ps[:, 1, cols], XT[:, e * NC2 + c], rh[:, cols], start=True, stop=True)
                    last.then_inc(*pe_s.did(f"sa{c}"))
                    pe.wait_ge(*act_s.at(f"sa{c}", i))
                    if c < NC2 - 1:
                        nc.tensor.matmul(ps[:, 2, 0:P], kt[:, c], sa[:, c], start=True, stop=True).then_inc(*pe_s.did(f"h{c}"))
                    for e in range(2):
                        cols = slice(e * HD, (e + 1) * HD)
                        out = ch(two(4))[cols, c]
                        nc.tensor.matmul(out, sa[:, c, cols], gq[:, e * NC2 + c, 1], start=True, stop=False)
                        last = nc.tensor.matmul(out, H[:, c, cols], qe[:, c * P:(c + 1) * P], start=False, stop=True)
                    last.then_inc(*pe_s.did(f"y{c}"))
                pe.wait_ge(*act_s.at("ysq", i))
                wide(0, mk.half[:], At).then_inc(*pe_s.did("mean"))

        @block.vector
        def _(dve):
            dve_a.prime(dve)
            dve_s.prime(dve)
            dve.wait_ge(zeros, ZEROS)
            V = nc.vector

            def first(i):
                def did(name, ins, wait=False):
                    ins.then_inc(*dve_a.did(name))
                    if wait:
                        dve.wait_ge(*dve_a.at(name, i))

                dve.wait_ge(in_s, 48 * i + 48)
                for n in range(3):
                    tap = lambda r: par("gdn_conv_w_2", i + (9 * r + 3 * n))
                    did(f"c0{n}", V.tensor_scalar(z[:, n], buf[:, n, 0:N], tap(0), None, ALU.mult), True)
                    for r in range(1, 4):
                        did(f"c{r}{n}", V.scalar_tensor_tensor(z[:, n], buf[:, n, r:N + r], tap(r), z[:, n], ALU.mult, ALU.add),
                            r < 3)
                    yield
                for c in range(NC2):
                    decays = gB[:, ds(i, 1), c * P:(c + 1) * P].rearrange("p o t -> p (o t)") if not isinstance(i, int) \
                        else gB[:, i, c * P:(c + 1) * P]
                    did(f"s{c}", V.tensor_tensor_scan(gc[:, c * P:(c + 1) * P], co.ones[:], decays, 0.0, ALU.mult, ALU.add),
                        c == NC2 - 1)
                did("dkd", V.tensor_tensor(ch(kd[:]), ch(gc[:])[:, :, P - 1:P].to_broadcast([P, NC2, P]), ch(gc[:]), ALU.subtract))
                yield
                dve.wait_ge(*act_a.at("sg", i))
                dve.wait_ge(*dve_a.at("c32", i))
                did("silu", V.tensor_tensor(z[:], z[:], sg[:], ALU.mult))

            def body(i, following):
                def did(name, ins, wait=False):
                    ins.then_inc(*dve_s.did(name))
                    if wait:
                        dve.wait_ge(*dve_s.at(name, i))

                beta = bB[:, ds(i, 1)].rearrange("p o t -> p (o t)") if not isinstance(i, int) else bB[:, i]
                did("last", V.tensor_copy(decay[:], ch(gc[:])[:, :, P - 1]))
                dve.wait_ge(*act_s.at("root", i))
                did("q", V.scalar_tensor_tensor(ar[:, :, 1], ch(q), HD ** -0.5, ch(rs[:, 0]), ALU.mult, ALU.mult))
                did("k", V.tensor_tensor(k, k, rs[:, 1], ALU.mult), True)
                did("bk", V.scalar_tensor_tensor(ar[:, :, 0], ch(k), -1.0, ch(beta), ALU.mult, ALU.mult))
                did("v", V.tensor_tensor(v, v, beta, ALU.mult))
                dve.wait_ge(*act_s.at("kd", i))
                did("kdk", V.tensor_tensor(kd[:], kd[:], k, ALU.mult), True)
                did("At", V.tensor_tensor(ch(At[:]), ar[:, :, 0], ch(eg[:]), ALU.mult))
                did("qe", V.tensor_tensor(ch(qe[:]), ar[:, :, 1], ch(eg[:]), ALU.mult))
                dve.wait_ge(*pe_s.at("row", i))
                dve.wait_ge(*act_s.at("gct", i))
                for e in range(2):
                    for c in range(NC2):
                        did(f"D{e}{c}", V.tensor_scalar(Dm[:, e, c * P:(c + 1) * P], ch(two(2 * e))[:, c], gct[:, c, e:e + 1], 0.0,
                                                        ALU.subtract, ALU.min))
                inv.eye(dve, i)
                dve.wait_ge(*pool_s.at("D", i))
                for e in range(2):
                    dve.wait_ge(*pe_s.at(f"g{e}", i))
                    grams = ps[:, 4 * e:4 * e + 4].rearrange("p a b -> p (a b)").rearrange("p (c h t) -> p c h t", h=2, t=P)
                    did(f"gq{e}", V.tensor_tensor(gq[:, e * NC2:(e + 1) * NC2], grams,
                                                  ch(Dm[:, e]).unsqueeze(2).to_broadcast([P, NC2, 2, P]), ALU.mult))
                dve.wait_ge(*dve_s.at("gq1", i))
                inv.dve(dve, i, following)
                dve.wait_ge(*act_s.at("so", i))
                did("gate", V.tensor_tensor(ga[:], ga[:], gi[:], ALU.mult))
                dve.wait_ge(*act_s.at("vt", i))
                for c in range(NC2):
                    dve.wait_ge(*pe_s.at(f"r{c}", i))
                    did(f"r{c}", V.tensor_tensor(rh[:], ps[:, 0, 0:P], vt[:, c], ALU.add))
                    if c < NC2 - 1:
                        dve.wait_ge(*pe_s.at(f"h{c}", i))
                        did(f"ht{c}", V.scalar_tensor_tensor(ht[:], H[:, c], decay[:, c:c + 1], ps[:, 2, 0:P], ALU.mult, ALU.add), True)
                        did(f"H{c}", V.tensor_tensor(H[:, c + 1], ht[:], mk.block[:], ALU.mult), True)
                dve.wait_ge(*act_s.at("yroot", i))
                did("yn", V.scalar_tensor_tensor(y[:], y[:], par("gdn_o_norm_g_2"), At[:], ALU.mult, ALU.mult), True)
                dve.wait_ge(out_s, 16 * i + 16)
                did("yo", V.tensor_tensor(o[:], y[:], ga[:], ALU.mult))

            each_pair(dve, first, body)


def delta_gates(co, gB, bB, rowsel):
    nc = co.nc
    N = SEQ
    H6 = HEADS2
    ps = co.psum
    with ExitStack() as ctx:
        sb = lambda name, shape, dt=F32: ctx.enter_context(nc.sbuf_tensor("dg_" + name, shape, dt))
        b, a, al, e, u, t, lu = (sb(n, [H6, N]) for n in ("b", "a", "al", "e", "u", "t", "lu"))
        cols = sb("cols", [H6, 2])
        sel = sb("sel", [H6, PAIRS, 2, HD])
        sem = lambda n: signal(nc, ctx, "dg_" + n)
        loaded, sels, act_d, dve_d, pe_d = (sem(n) for n in ("loaded", "sels", "act", "dve", "pe"))
        block = ctx.enter_context(nc.Block())

        @block.sync
        def _(sp):
            at = GDN_AT + 4 * RW
            sp.dma_start(b[:], co.dram["ppT"][at:at + H6, :]).then_inc(loaded, 16)
            sp.dma_start(a[:], co.dram["ppT"][at + H6:at + 2 * H6, :]).then_inc(loaded, 16)
            sp.dma_start(cols[:, 0:1], co.dram["gdn_a_log_2"]).then_inc(loaded, 16)
            sp.dma_start(cols[:, 1:2], co.dram["gdn_dt_bias_2"]).then_inc(loaded, 16)

        @block.gpsimd
        def _(pool):
            nc.gpsimd.memset(sel[:], 0.0).then_inc(sels, 1)
            nc.gpsimd.memset(rowsel[:], 0.0).then_inc(sels, 1)
            pool.wait_ge(sels, 2)
            nc.gpsimd.affine_select(out=sel[:], in_=sel[:], compare_op=ALU.not_equal, fill=1.0, base=0,
                                    pattern=[[-2, PAIRS], [-1, 2], [0, HD]], channel_multiplier=1).then_inc(sels, 1)
            nc.gpsimd.affine_select(out=rowsel[:], in_=rowsel[:], compare_op=ALU.not_equal, fill=1.0, base=0,
                                    pattern=[[-HD, 2], [0, P]], channel_multiplier=1).then_inc(sels, 1)
            pool.wait_ge(sels, 4)

        @block.scalar
        def _(act):
            act.wait_ge(loaded, 64)
            nc.scalar.activation(b[:], b[:], ACT.Sigmoid).then_inc(act_d, 1)
            nc.scalar.activation(cols[:, 0:1], cols[:, 0:1], ACT.Exp).then_inc(act_d, 1)
            act.wait_ge(dve_d, 2)
            nc.scalar.activation(e[:], al[:], ACT.Exp, scale=-1.0).then_inc(act_d, 1)
            act.wait_ge(dve_d, 3)
            nc.scalar.activation(lu[:], u[:], ACT.Ln).then_inc(act_d, 1)
            act.wait_ge(pe_d, 1)
            nc.scalar.copy(gB[:].rearrange("p i (h t) -> p (i h) t", h=2), ps[:, 0:6]).then_inc(act_d, 1)
            act.wait_ge(pe_d, 2)
            nc.scalar.copy(bB[:].rearrange("p i (h t) -> p (i h) t", h=2), ps[:, 0:6]).then_inc(act_d, 1)

        @block.tensor
        def _(pe):
            pe.wait_ge(sels, 4)
            for n, x in enumerate((t, b)):
                if n == 0:
                    pe.wait_ge(dve_d, 9)
                else:
                    pe.wait_ge(act_d, 5)
                for i in range(PAIRS):
                    for h in range(2):
                        last = nc.tensor.matmul(ps[:, 2 * i + h], sel[:, i].rearrange("p e k -> p (e k)"),
                                                x[:, h * 512:(h + 1) * 512], start=True, stop=True)
                last.then_inc(pe_d, 1)

        @block.vector
        def _(dve):
            V = nc.vector
            n = [0]

            def did(ins):
                ins.then_inc(dve_d, 1)
                n[0] += 1
                dve.wait_ge(dve_d, n[0])

            dve.wait_ge(loaded, 64)
            did(V.tensor_scalar(a[:], a[:], cols[:, 1:2], None, ALU.add))
            did(V.scalar_tensor_tensor(al[:], a[:], -1.0, a[:], ALU.mult, ALU.max))
            dve.wait_ge(act_d, 3)
            did(V.tensor_scalar(u[:], e[:], 1.0, None, ALU.add))
            did(V.scalar_tensor_tensor(t[:], u[:], -1.0, e[:], ALU.add, ALU.subtract))
            did(V.reciprocal(al[:], u[:]))
            did(V.tensor_tensor(t[:], t[:], al[:], ALU.mult))
            dve.wait_ge(act_d, 4)
            did(V.tensor_tensor(lu[:], lu[:], t[:], ALU.subtract))
            did(V.scalar_tensor_tensor(t[:], a[:], 0.0, lu[:], ALU.max, ALU.add))
            did(V.tensor_scalar(t[:], t[:], cols[:, 0:1], -1.0, ALU.mult, ALU.mult))


HEADS_A = 4
QK = 96
ROT = 32
HALF_TURN = 3.1415925


def attention(co):
    nc = co.nc
    N = SEQ
    ppT, par, ps = co.dram["ppT"], co.par, co.psum
    ch = lambda x: x.rearrange("p (c t) -> p c t", t=P)
    two = lambda b: ps[:, b:b + 2].rearrange("p a b -> p (a b)")
    halves = [slice(0, 512), slice(512, 1024)]
    SCALE = QK ** -0.5
    with ExitStack() as ctx:
        sb = lambda name, shape, dt=F32: ctx.enter_context(nc.sbuf_tensor("at_" + name, shape, dt))
        cq, ckv = sb("cq", [P, 2, N]), sb("ckv", [P, N])
        cs = sb("cs", [P, 2, N])
        rot = sb("rot", [P, P])
        gain = sb("gain", [P, 2])
        vals = sb("vals", [P, NC2, HEADS_A * HD])
        latent(co, cq, ckv, cs, rot, gain, vals)
        wq, wk = sb("wq", [P, 2, P]), sb("wk", [P, P])
        raw = sb("raw", [P, 2, N])
        sq, rs = sb("sq", [P, 2, N]), sb("rs", [P, 2, N])
        qk, t = sb("qk", [P, 2, N]), sb("t", [P, 2, N])
        vh = sb("vh", [P, NC2, HD])
        Pm, PT = sb("Pm", [P, 2, N]), sb("PT", [P, NC2, P])
        mx, nm, sm, ri = (sb(n, [P, NC2]) for n in ("mx", "nm", "sm", "ri"))
        dg = sb("dg", [P, 2, P])
        o = sb("o", [HD, N])
        B = range(NC2)
        pe_s = Steps(nc, ctx, "at_pe", ["q", "k", "ss", "rot", "s0"] + [x for c in B for x in ([f"s{c + 1}"] if c < NC2 - 1 else []) + [f"t{c}", f"o{c}"]])
        act_s = Steps(nc, ctx, "at_act", ["q", "k", "sq", "ln", "root"] + [x for c in B for x in (f"e{c}", f"t{c}")] + ["o"])
        order = ["mask0", "mx0", "nm0"]
        for c in B:
            if c < NC2 - 1:
                order += [f"mask{c + 1}", f"mx{c + 1}", f"nm{c + 1}"]
            order += [f"ri{c}", f"dg{c}"]
        dve_s = Steps(nc, ctx, "at_dve", ["vh", "q", "k", "sin", "cos", "qk"] + order)
        w_s, out_s, zeros = (signal(nc, ctx, "at_" + n) for n in ("w", "out", "zeros"))
        rope_s = signal(nc, ctx, "at_rope")
        ZEROS = 3
        block = ctx.enter_context(nc.Block())

        @block.sync
        def _(sp):
            at = RWKV_IN + 2 * P + P
            sp.wait_ge(zeros, ZEROS)
            sp.dma_start(raw[HD:QK, 1], ppT[at:at + ROT, :]).then_inc(rope_s, 16)
            with sp.Fori(0, HEADS_A) as i:
                src_q = co.dram["mla_w_uq_2"].rearrange("(k p) m -> p k m", p=P)[:, :, ds(i * QK, QK)]
                src_k = co.dram["mla_w_ukv_2"][:, ds(i * 2 * HD, HD)]
                dest = co.dram["yT"][ds(RW + i * HD, HD), :]
                sp.wait_ge(*pe_s.at("k", i - 1))
                sp.dma_start(wq[:, :, 0:QK], src_q).then_inc(w_s, 16)
                sp.dma_start(wk[:, 0:HD], src_k).then_inc(w_s, 16)
                sp.wait_ge(*act_s.at("o", i))
                sp.dma_start(dest, o[:]).then_inc(out_s, 16)
            sp.wait_ge(out_s, 16 + 16 * HEADS_A)

        @block.gpsimd
        def _(pool):
            for x in (wq, wk, raw):
                nc.gpsimd.memset(x[:], 0.0).then_inc(zeros, 1)

        @block.scalar
        def _(act):
            act_s.prime(act)
            act.sem_inc(out_s, 16)
            act.wait_ge(zeros, ZEROS)
            act.wait_ge(rope_s, 16)
            with act.Fori(0, HEADS_A) as i:
                act.wait_ge(*pe_s.at("q", i))
                nc.scalar.copy(raw[:, 0], two(0)).then_inc(*act_s.did("q"))
                act.wait_ge(*pe_s.at("k", i))
                nc.scalar.copy(raw[0:HD, 1], two(2)[0:HD]).then_inc(*act_s.did("k"))
                act.wait_ge(*act_s.at("k", i))
                nc.scalar.activation(sq[:], raw[:], ACT.Square).then_inc(*act_s.did("sq"))
                act.wait_ge(*pe_s.at("ss", i))
                nc.scalar.activation(rs[:].rearrange("p a (b t) -> p (a b) t", b=2), ps[:, 4:8], ACT.Ln, scale=1.0 / QK,
                                     bias=co.eps[:]).then_inc(*act_s.did("ln"))
                act.wait_ge(*act_s.at("ln", i))
                nc.scalar.activation(rs[:], rs[:], ACT.Exp, scale=-0.5).then_inc(*act_s.did("root"))
                for c in B:
                    L = (c + 1) * P
                    act.wait_ge(*dve_s.at(f"nm{c}", i))
                    if c >= 2:
                        act.wait_ge(*pe_s.at(f"t{c - 2}", i))
                    nc.scalar.activation(Pm[:, c % 2, 0:L], two(2 * (c % 2))[:, 0:L], ACT.Exp, bias=nm[:, c:c + 1],
                                         scale=SCALE, accum_out=sm[:, c:c + 1]).then_inc(*act_s.did(f"e{c}"))
                    act.wait_ge(*pe_s.at(f"t{c}", i))
                    nc.scalar.copy(PT[:, 0:c + 1], ch(two(4))[:, 0:c + 1]).then_inc(*act_s.did(f"t{c}"))
                act.wait_ge(out_s, 16 * i + 16)
                act.wait_ge(*pe_s.at(f"o{NC2 - 1}", i))
                nc.scalar.copy(o[:], two(6)[0:HD]).then_inc(*act_s.did("o"))

        @block.tensor
        def _(pe):
            pe_s.prime(pe)
            with pe.Fori(0, HEADS_A) as i:
                pe.wait_ge(w_s, 32 * i + 32)
                pe.wait_ge(*act_s.at(f"e{NC2 - 1}", i - 1))
                for k in range(2):
                    for h, cols in enumerate(halves):
                        last = nc.tensor.matmul(ps[:, h], wq[:, k], cq[:, k, cols], start=k == 0, stop=k == 1)
                last.then_inc(*pe_s.did("q"))
                for h, cols in enumerate(halves):
                    last = nc.tensor.matmul(ps[:, 2 + h], wk[:], ckv[:, cols], start=True, stop=True)
                last.then_inc(*pe_s.did("k"))
                pe.wait_ge(*act_s.at("sq", i))
                pe.wait_ge(*act_s.at("o", i - 1))
                for x in range(2):
                    for h, cols in enumerate(halves):
                        last = nc.tensor.matmul(ps[:, 4 + 2 * x + h], co.ones[:], sq[:, x, cols], start=True, stop=True)
                last.then_inc(*pe_s.did("ss"))
                pe.wait_ge(*dve_s.at("k", i))
                for x in range(2):
                    for h, cols in enumerate(halves):
                        last = nc.tensor.matmul(ps[:, 2 * x + h], rot[:], qk[:, x, cols], start=True, stop=True)
                last.then_inc(*pe_s.did("rot"))

                def scores(c):
                    L = (c + 1) * P
                    if c >= 2:
                        pe.wait_ge(*act_s.at(f"e{c - 2}", i))
                    for h in range(-(-L // 512)):
                        cols = slice(h * 512, min(L, (h + 1) * 512))
                        last = nc.tensor.matmul(two(2 * (c % 2))[:, cols], qk[:, 0, c * P:L], qk[:, 1, cols], start=True, stop=True)
                    last.then_inc(*pe_s.did(f"s{c}"))

                pe.wait_ge(*dve_s.at("qk", i))
                scores(0)
                for c in B:
                    if c < NC2 - 1:
                        scores(c + 1)
                    pe.wait_ge(*dve_s.at(f"dg{c}", i))
                    if c:
                        pe.wait_ge(*act_s.at(f"t{c - 1}", i))
                    for k in range(c + 1):
                        last = nc.tensor.matmul(ch(two(4))[:, k], Pm[:, c % 2, k * P:(k + 1) * P], dg[:, c % 2], start=True, stop=True)
                    last.then_inc(*pe_s.did(f"t{c}"))
                    pe.wait_ge(*act_s.at(f"t{c}", i))
                    for k in range(c + 1):
                        last = nc.tensor.matmul(ch(two(6))[0:HD, c], vh[:, k], PT[:, k], start=k == 0, stop=k == c)
                    last.then_inc(*pe_s.did(f"o{c}"))

        @block.vector
        def _(dve):
            dve_s.prime(dve)
            V = nc.vector
            with dve.Fori(0, HEADS_A) as i:
                def did(name, ins, wait=False):
                    ins.then_inc(*dve_s.did(name))
                    if wait:
                        dve.wait_ge(*dve_s.at(name, i))

                dve.wait_ge(*pe_s.at(f"o{NC2 - 1}", i - 1))
                did("vh", V.tensor_copy(vh[:], vals[:, :, ds(i * HD, HD)]))
                dve.wait_ge(*act_s.at("root", i))
                for x, name in enumerate("qk"):
                    did(name, V.scalar_tensor_tensor(qk[:, x], raw[:, x], gain[:, x:x + 1], rs[:, x], ALU.mult, ALU.mult))
                dve.wait_ge(*pe_s.at("rot", i))
                flat = lambda n: cs[:, n].unsqueeze(1).to_broadcast([P, 2, N])
                did("sin", V.tensor_tensor(t[:], ps[:, 0:4].rearrange("p (a b) t -> p a (b t)", a=2), flat(1), ALU.mult))
                did("cos", V.tensor_tensor(qk[:], qk[:], flat(0), ALU.mult), True)
                did("qk", V.tensor_tensor(qk[:], qk[:], t[:], ALU.add))

                def maximum(c):
                    L = (c + 1) * P
                    bank = two(2 * (c % 2))
                    dve.wait_ge(*pe_s.at(f"s{c}", i))
                    did(f"mask{c}", V.memset(bank[0:HD, L - HD:L], -1e30), True)
                    did(f"mx{c}", V.tensor_reduce(mx[:, c:c + 1], bank[:, 0:L], AX_X, ALU.max), True)
                    did(f"nm{c}", V.tensor_scalar(nm[:, c:c + 1], mx[:, c:c + 1], -SCALE, None, ALU.mult))

                maximum(0)
                for c in B:
                    if c < NC2 - 1:
                        maximum(c + 1)
                    dve.wait_ge(*act_s.at(f"e{c}", i))
                    did(f"ri{c}", V.reciprocal(ri[:, c:c + 1], sm[:, c:c + 1]), True)
                    if c >= 2:
                        dve.wait_ge(*pe_s.at(f"t{c - 2}", i))
                    did(f"dg{c}", V.tensor_scalar(dg[:, c % 2], co.ident[:], ri[:, c:c + 1], None, ALU.mult))


def latent(co, cq, ckv, cs, rot, gain, vals):
    nc = co.nc
    N = SEQ
    ps, par = co.psum, co.par
    TURN = 2 * np.pi
    C1 = 6.28125
    C2 = 507 / 2.0 ** 18
    C3 = TURN - C1 - C2
    MAGIC = 1.5 * 2.0 ** 23
    with ExitStack() as ctx:
        sb = lambda name, shape, dt=F32: ctx.enter_context(nc.sbuf_tensor("la_" + name, shape, dt))
        sq, rs = sb("sq", [P, 3, N]), sb("rs", [P, 2, N])
        wv = sb("wv", [P, HEADS_A, HD])
        pos, freq = sb("pos", [P, N], I32), sb("freq", [P, 1])
        ang, turns = sb("ang", [P, N]), sb("turns", [P, 2, N])
        sem = lambda n: signal(nc, ctx, "la_" + n)
        in_s, freq_s, pos_s, zero_s, made = (sem(n) for n in ("in", "freq_in", "pos_in", "zero", "made"))
        act_d, dve_d, pe_d = (sem(n) for n in ("act", "dve", "pe"))
        block = ctx.enter_context(nc.Block())

        @block.sync
        def _(sp):
            at = RWKV_IN
            sp.dma_start(cq[:], co.dram["ppT"][at:at + 2 * P, :].rearrange("(k p) t -> p k t", p=P)).then_inc(in_s, 16)
            sp.dma_start(ckv[:], co.dram["ppT"][at + 2 * P:at + 3 * P, :]).then_inc(in_s, 16)
            sp.dma_start(wv[:], co.dram["mla_w_ukv_2"].rearrange("p (h k) -> p h k", k=2 * HD)[:, :, HD:2 * HD]).then_inc(in_s, 16)
            sp.dma_start(pos[:], co.dram["positions"].to_broadcast([P, N])).then_inc(pos_s, 16)
            sp.wait_ge(zero_s, 2)
            sp.dma_start(freq[HD:QK], co.dram["inverse_frequency"]).then_inc(freq_s, 16)
            sp.dma_start(gain[0:QK, 0:1], co.dram["mla_q_qk_g_2"]).then_inc(freq_s, 16)
            sp.dma_start(gain[0:QK, 1:2], co.dram["mla_k_qk_g_2"]).then_inc(freq_s, 16)

        @block.gpsimd
        def _(pool):
            nc.gpsimd.memset(freq[:], 0.0).then_inc(zero_s, 1)
            nc.gpsimd.memset(gain[:], 0.0).then_inc(zero_s, 1)
            nc.gpsimd.memset(rot[:], 0.0).then_inc(made, 1)
            pool.wait_ge(made, 1)
            for at, base, fill in ((HD, -HD - ROT // 2, -1.0), (HD + ROT // 2, -HD, 1.0)):
                view = rot[:, at:at + ROT // 2]
                nc.gpsimd.affine_select(out=view, in_=view, compare_op=ALU.not_equal, fill=fill, base=base,
                                        pattern=[[-1, ROT // 2]], channel_multiplier=1).then_inc(made, 1)
            pool.wait_ge(made, 3)

        @block.scalar
        def _(act):
            act.wait_ge(in_s, 48)
            nc.scalar.activation(sq[:, 0:2], cq[:], ACT.Square).then_inc(act_d, 1)
            nc.scalar.activation(sq[:, 2], ckv[:], ACT.Square).then_inc(act_d, 1)
            act.wait_ge(dve_d, 3)
            nc.scalar.activation(rs[:], rs[:], ACT.Sqrt).then_inc(act_d, 1)
            act.wait_ge(dve_d, 16)
            nc.scalar.activation(cs[:], cs[:], ACT.Sin).then_inc(act_d, 1)
            act.wait_ge(pe_d, 2)
            nc.scalar.copy(vals[:].rearrange("p (b c) m -> p b (c m)", b=4), ps[:, 4:8]).then_inc(act_d, 1)

        @block.tensor
        def _(pe):
            pe.wait_ge(act_d, 2)
            for h in range(2):
                cols = slice(h * 512, (h + 1) * 512)
                nc.tensor.matmul(ps[:, h], co.ones[:], sq[:, 0, cols], start=True, stop=False)
                nc.tensor.matmul(ps[:, h], co.ones[:], sq[:, 1, cols], start=False, stop=True)
                last = nc.tensor.matmul(ps[:, 2 + h], co.ones[:], sq[:, 2, cols], start=True, stop=True)
            last.then_inc(pe_d, 1)
            pe.wait_ge(dve_d, 6)
            for c in range(NC2):
                last = nc.tensor.matmul(ps[:, 4 + c // 2, (c % 2) * 256:(c % 2) * 256 + 256], ckv[:, c * P:(c + 1) * P],
                                        wv[:].rearrange("p h k -> p (h k)"), start=True, stop=True)
            last.then_inc(pe_d, 1)

        @block.vector
        def _(dve):
            V = nc.vector
            n = [0]

            def did(ins):
                ins.then_inc(dve_d, 1)
                n[0] += 1
                dve.wait_ge(dve_d, n[0])

            dve.wait_ge(pe_d, 1)
            did(V.tensor_scalar(rs[:, 0].rearrange("p (b t) -> p b t", b=2), ps[:, 0:2], 0.5 / P, EPS, ALU.mult, ALU.add))
            did(V.tensor_scalar(rs[:, 1].rearrange("p (b t) -> p b t", b=2), ps[:, 2:4], 1.0 / P, EPS, ALU.mult, ALU.add))
            did(V.reciprocal(rs[:], rs[:]))
            dve.wait_ge(act_d, 3)
            for k in range(2):
                did(V.scalar_tensor_tensor(cq[:, k], cq[:, k], par("mla_q_norm_g_2", k), rs[:, 0], ALU.mult, ALU.mult))
            did(V.scalar_tensor_tensor(ckv[:], ckv[:], par("mla_kv_norm_g_2"), rs[:, 1], ALU.mult, ALU.mult))
            dve.wait_ge(pos_s, 16)
            dve.wait_ge(freq_s, 48)
            did(V.tensor_copy(ang[:], pos[:]))
            did(V.tensor_scalar(ang[:], ang[:], freq[:], None, ALU.mult))
            for x in range(2):
                did(V.tensor_scalar(turns[:, x], ang[:], 1 / TURN, (0.25, 0.0)[x], ALU.mult, ALU.add))
            did(V.tensor_scalar(turns[:], turns[:], MAGIC, MAGIC, ALU.add, ALU.subtract))
            src = ang[:].unsqueeze(1).to_broadcast([P, 2, N])
            for part in (C1, C2, C3):
                did(V.scalar_tensor_tensor(cs[:], turns[:], -part, src, ALU.mult, ALU.add))
                src = cs[:]
            did(V.tensor_scalar(cs[:, 0], cs[:, 0], np.pi / 2, None, ALU.add))
            did(V.tensor_scalar(cs[:], cs[:], HALF_TURN, -HALF_TURN, ALU.min, ALU.max))


def build(nc, dram, stop=None, second_only=False):
    RETIRED.clear()
    with ExitStack() as ctx:
        co = Core(nc, ctx, dram)
        start_up(co)
        if second_only:
            return block_two(co, dram, stop)
        W = SEQ + TAIL
        with ExitStack() as mix:
            co.weights(mix)
            u_hi = mix.enter_context(nc.sbuf_tensor("u_hi", [P, KD, T1], F32R))
            u_lo = mix.enter_context(nc.sbuf_tensor("u_lo", [P, KD, T1], F32R))
            norm_split(co, "n1_", dram["h0T"], PAD, META + SEQ, "mix_norm_pre", u_hi, u_lo)
            if stop == "norm": return
            hgrn_heads(co, u_hi, u_lo)
            if stop == "hgrn": return
            a_hi, a_lo, p_hi, p_lo = (mix.enter_context(nc.sbuf_tensor(n, [P, 4, W], F32R))
                                      for n in ("a_hi", "a_lo", "p_hi", "p_lo"))
            split_from_dram(co, "as_", dram["aT"], 4, W, a_hi, a_lo)
            pool_branch(co, u_hi, u_lo, p_hi, p_lo)
            if stop == "pool": return
            gated_sum(co, u_hi, u_lo, a_hi, a_lo, p_hi, p_lo)
            if stop == "z": return
        with ExitStack() as out:
            y = out.enter_context(nc.sbuf_tensor("mix_y", [P, KD, W], F32))
            with ExitStack() as sq:
                co.weights(sq)
                z_hi, z_lo = (sq.enter_context(nc.sbuf_tensor(n, [P, KD, W], F32R)) for n in ("z_hi", "z_lo"))
                split_from_dram(co, "zs_", dram["zT"], KD, W, z_hi, z_lo)
                square_product(co, "wo_", dram["w_out"], z_hi, z_lo, y, W, 3)
            residual_norm(co, "r1_", dram["h0T"][:, META - TAIL:], y, W, "mix_norm_post", dram["h1T"])
            if stop == "h1": return
        with ExitStack() as ffn:
            acc = ffn.enter_context(nc.sbuf_tensor("ffn_acc", [P, KD, SEQ], F32))
            with ExitStack() as w:
                v_hi, v_lo = (w.enter_context(nc.sbuf_tensor(n, [P, KD, W], F32R)) for n in ("v_hi", "v_lo"))
                norm_split(co, "n2_", dram["h1T"], 0, W, "ffn_norm_pre", v_hi, v_lo)
                co.weights(w, 6)
                feed_forward(co, "f1_", v_hi, v_lo, dram["ffn_w_up"], dram["ffn_w_down"], acc, dram["ffn_w_gate"])
            residual_norm(co, "r2_", dram["h1T"][:, TAIL:], acc, SEQ, "ffn_norm_post", dram["h2T"])
            if stop == "h2": return
        clear_retired(nc)
        block_two(co, dram, stop)


def block_two(co, dram, stop=None):
    nc = co.nc
    with ExitStack() as ctx:
        u_hi, u_lo = (ctx.enter_context(nc.sbuf_tensor(n, [P, KD, SEQ], F32R)) for n in ("s_hi", "s_lo"))
        norm_split(co, "n3_", dram["h2T"], 0, SEQ, "ln_mix_g_2", u_hi, u_lo)
        co.weights(ctx)
        input_projection(co, u_hi, u_lo)
    if stop == "pp": return
    with ExitStack() as ctx:
        mk = Masks(co, ctx)
        rwkv(co, mk)
        if stop == "rwkv": return
        deltanet(co, mk)
    attention(co)
    with ExitStack() as out:
        y = out.enter_context(nc.sbuf_tensor("mix2_y", [P, KD, SEQ], F32))
        with ExitStack() as sq:
            co.weights(sq)
            y_hi, y_lo = (sq.enter_context(nc.sbuf_tensor(n, [P, KD, SEQ], F32R)) for n in ("y_hi", "y_lo"))
            split_from_dram(co, "ys_", dram["yT"], KD, SEQ, y_hi, y_lo)
            square_product(co, "wo2_", dram["w_out_2"], y_hi, y_lo, y, SEQ, 2)
        residual_norm(co, "r3_", dram["h2T"], y, SEQ, None, dram["h3T"])
        if stop == "h3": return
    with ExitStack() as ffn:
        acc = ffn.enter_context(nc.sbuf_tensor("ffn2_acc", [P, KD, SEQ], F32))
        with ExitStack() as w:
            v_hi, v_lo = (w.enter_context(nc.sbuf_tensor(n, [P, KD, SEQ], F32R)) for n in ("t_hi", "t_lo"))
            norm_split(co, "n4_", dram["h3T"], 0, SEQ, "ln_ffn_g_2", v_hi, v_lo)
            co.weights(w)
            feed_forward(co, "f2_", v_hi, v_lo, dram["w_ff1_2"], dram["w_ff2_2"], acc)
        residual_norm(co, "r4_", dram["h3T"], acc, SEQ, None, dram["outT"])


SCRATCH = [("aT", (D // 2, SEQ + TAIL)), ("zT", (D, SEQ + TAIL)), ("ppT", (P_IN, SEQ)), ("yT", (D, SEQ)), ("h1T", (D, SEQ + TAIL)), ("h2T", (D, SEQ)), ("h3T", (D, SEQ))]


def layout(x):
    out = {}
    for name in ("w_in", "w_branch_hgrn", "w_branch_pool", "w_out", "ffn_w_gate", "ffn_w_up", "ffn_w_down",
                 "w_in_2", "w_out_2", "w_ff1_2", "w_ff2_2", "rwkv_w2_2", "rwkv_a2_2", "rwkv_g2_2",
                 "mla_w_uq_2", "mla_w_ukv_2", "pool_proj"):
        out[name] = np.ascontiguousarray(x[name][0])
    out["h0T"] = np.ascontiguousarray(np.concatenate([x["meta_tokens"], x["x"][0]], axis=0).T)
    vectors = dict(x)
    vectors["gdn_o_norm_g_2"] = np.tile(x["gdn_o_norm_g_2"], (1, 2))
    out["vectors"] = np.ascontiguousarray(np.concatenate(
        [np.reshape(vectors[name], (n, P)) for name, n in PARAM_TILES], axis=0).T)
    for name in ("gdn_a_log_2", "gdn_dt_bias_2", "mla_q_qk_g_2", "mla_k_qk_g_2"):
        out[name] = np.reshape(x[name], (-1, 1))
    half = np.arange(0, ROT, 2) / ROT
    out["inverse_frequency"] = np.tile(10000.0 ** -half, 2).astype(np.float32).reshape(ROT, 1)
    out["positions"] = np.reshape(x["positions_2"], (1, SEQ))
    return out


def kernel(**inputs):
    import concourse.bacc as bacc
    from concourse.bass_utils import run_bass_kernel_spmd

    nc = bacc.Bacc("TRN2", target_bir_lowering=False, num_devices=1)
    arrays = layout({name: np.asarray(value) for name, value in inputs.items()})
    dram = {}
    for name, value in arrays.items():
        dram[name] = nc.dram_tensor(name, value.shape, mybir.dt.from_np(value.dtype), kind="ExternalInput").ap()
    for name, shape in SCRATCH:
        dram[name] = nc.dram_tensor(name, shape, F32, kind="Internal").ap()
    dram["outT"] = nc.dram_tensor("outT", (D, SEQ), F32, kind="ExternalOutput").ap()
    build(nc, dram)
    result = run_bass_kernel_spmd(nc, [arrays], core_ids=[0])
    return np.ascontiguousarray(result.results[0]["outT"].T).reshape(1, SEQ, D)
```

```python
from contextlib import ExitStack

import numpy as np
import concourse.bass as bass
from concourse import mybir

F32 = mybir.dt.float32
F32R = mybir.dt.float32r
I32 = mybir.dt.int32
ALU = mybir.AluOpType
ACT = mybir.ActivationFunctionType
AX_X = mybir.AxisListType.X
P = 128
ds = bass.ds

D = 1024
KD = D // P
SEQ = 1024
META = 16
PAD = P - META
T1 = PAD + META + SEQ
NC1 = T1 // P
TAIL = 2
EPS = 1e-6


RETIRED = []


def signal(nc, ctx, name):
    sem = nc.alloc_semaphore(name)
    ctx.callback(RETIRED.append, sem)
    return sem


def clear_retired(nc):
    nc.clear_and_free_semaphores(list(RETIRED))
    nc.all_engine_barrier()
    RETIRED.clear()


class Products:

    RAW = 2
    PRIME = 64
    UNIT = 1024

    def __init__(self, nc, ctx, slots, banks):
        self.nc, self.slots, self.banks = nc, slots, banks
        sem = lambda name: signal(nc, ctx, name)
        self.landed = [sem(f"weights_landed{r}") for r in range(self.RAW)]
        self.hi_done = sem("weights_hi_done")
        self.ready = sem("weights_ready")
        self.full = sem("psum_full")
        self.carried = sem("waits_carried")
        self.free = [sem(f"psum_free{b}") for b in range(banks)]
        self.units = 0
        self.chunks = 0
        self.ends = []
        self.uses = [0] * banks

    def carry(self, eng):
        eng.sem_inc(self.carried, 1)

    def memory(self, raw, hi, lo, zero, psum):
        self.raw, self.hi, self.lo, self.zero, self.psum = raw, hi, lo, zero, psum

    def stage(self, n, sources, chunks):
        return Stage(self, n, sources, chunks)


class Stage:

    def __init__(self, pr, n, sources, chunks, rows=P):
        self.pr, self.n, self.sources, self.body, self.rows = pr, n, sources, chunks, rows
        U, C = len(sources), len(chunks)
        assert n == 1 or (U % pr.slots == 0 and U % pr.RAW == 0 and C % pr.banks == 0)
        self.U, self.C, self.u0, self.c0 = U, C, pr.units, pr.chunks
        last = [max(c for c in range(C) if any(k[0] == j for k in chunks[c][1])) + 1 for j in range(U)]
        for i in range(n):
            pr.ends += [self.c0 + i * C + e for e in last]
        self.bank = [(self.c0 + c) % pr.banks for c in range(C)]
        self.used, uses = [], list(pr.uses)
        for b in self.bank:
            self.used.append(uses[b])
            uses[b] += 1
        per = [b - a for a, b in zip(pr.uses, uses)]
        self.per = per
        pr.uses = [a + n * k for a, k in zip(pr.uses, per)]
        pr.units += n * U
        pr.chunks += n * C

    def _slot_free(self, j):
        e = lambda u: self.pr.ends[u] if u >= 0 else 0
        at = self.u0 + j - self.pr.slots
        v = e(at)
        if self.n > 1:
            v = max(v, e(at + self.U) - self.C)
        return v

    def load(self, sp, i, j):
        pr, u = self.pr, self.u0 + j
        dst = pr.raw[0:self.rows, u % pr.RAW]
        src = self.sources[j](i)
        sp.wait_ge(pr.ready, u + 1 + i * self.U)
        pr.carry(sp)
        if len(src.shape) == 3:
            dst = dst[:, 0:src.shape[1] * src.shape[2]].rearrange("p (a b) -> p a b", a=src.shape[1])
        else:
            dst = dst[:, 0:src.shape[1]]
        sp.dma_start(dst, src).then_inc(pr.landed[u % pr.RAW], 16)

    def split(self, pool, i, j):
        pr, u = self.pr, self.u0 + j
        r, s, rows = u % pr.RAW, u % pr.slots, self.rows
        width = int(np.prod(self.sources[j](0).shape[1:]))
        pool.wait_ge(pr.full, pr.PRIME + self._slot_free(j) + i * self.C)
        pool.wait_ge(pr.landed[r], 16 * (u // pr.RAW + 1) + i * (16 * self.U // pr.RAW))
        pr.nc.gpsimd.tensor_tensor(pr.hi[0:rows, s, 0:width], pr.raw[0:rows, r, 0:width],
                                   pr.zero[0:rows, 0:1].to_broadcast([rows, width]), ALU.add).then_inc(pr.hi_done, 1)
        pool.wait_ge(pr.hi_done, u + 1 + i * self.U)
        pr.nc.gpsimd.tensor_tensor(pr.lo[0:rows, s, 0:width], pr.raw[0:rows, r, 0:width],
                                   pr.hi[0:rows, s, 0:width].bitcast(F32), ALU.subtract).then_inc(pr.ready, 1)

    def bank_of(self, c, rows=P):
        return self.pr.psum[0:rows, self.bank[c], 0:self.body[c][0]]

    def multiply(self, pe, i, c):
        pr = self.pr
        width, terms = self.body[c]
        b = self.bank[c]
        need = max(t[0] for t in terms)
        pe.wait_ge(pr.ready, pr.RAW + self.u0 + need + 1 + i * self.U)
        pe.wait_ge(pr.free[b], 1 + self.used[c] + i * self.per[b])
        last = None
        for t, (j, pick, xh, xl) in enumerate(terms):
            s = (self.u0 + j) % pr.slots
            wh, wl = pick(pr.hi[:, s]), pick(pr.lo[:, s])
            out = pr.psum[0:wh.shape[-1], b, 0:width]
            end = t == len(terms) - 1
            pr.nc.tensor.matmul(out, wh, xh, start=t == 0, stop=False)
            pr.nc.tensor.matmul(out, wh, xl, start=False, stop=False)
            last = pr.nc.tensor.matmul(out, wl, xh, start=False, stop=end)
        last.then_inc(pr.full, 1)

    def wait_full(self, eng, i, c):
        eng.wait_ge(self.pr.full, self.pr.PRIME + self.c0 + c + 1 + i * self.C)

    def freed(self, c):
        return self.pr.free[self.bank[c]]


class Steps:

    def __init__(self, nc, ctx, name, names, n=1):
        self.sem = signal(nc, ctx, name)
        self.names, self.next = list(names), 0
        assert len(set(names)) == len(names)

    def prime(self, eng):
        eng.sem_inc(self.sem, len(self.names))

    def did(self, name):
        assert self.names[self.next] == name, (self.names[self.next], name)
        self.next = (self.next + 1) % len(self.names)
        return self.sem, 1

    def at(self, name, i=0):
        return self.sem, (i + 1) * len(self.names) + self.names.index(name) + 1


def chunks_of(start, total, parts):
    w = total // parts // 2 * 2
    out = [(start + n * w, w) for n in range(parts)]
    out[-1] = (out[-1][0], total - (parts - 1) * w)
    return out


def chunk_terms(unit, xh, xl, kd, off, width, piece=P):
    return (width, [(unit, (lambda t, k=k: t[:, k * piece:k * piece + P]),
                     xh[:, k, off:off + width], xl[:, k, off:off + width]) for k in range(kd)])


def columns(w, at):
    return w.rearrange("(k p) m -> p k m", p=P)[:, :, ds(at, P)]


class Params:

    def __init__(self):
        self.at, self.n = {}, 0

    def add(self, name, n):
        self.at[name] = (self.n, n)
        self.n += n


def param_layout():
    pl = Params()
    for name, n in PARAM_TILES:
        pl.add(name, n)
    return pl


PARAM_TILES = [
    ("mix_norm_pre", 8), ("mix_norm_post", 8), ("hgrn_lower_bounds", 4), ("hgrn_out_norm", 4),
    ("pool_scale", 4), ("ffn_norm_pre", 8), ("ffn_norm_post", 8), ("ffn_conv_w", 66), ("ffn_conv_b", 22),
    ("ln_mix_g_2", 8), ("ln_ffn_g_2", 8), ("rwkv_mu_2", 11), ("rwkv_w0_2", 3), ("rwkv_a0_2", 3),
    ("rwkv_k_k_2", 3), ("rwkv_k_a_2", 3), ("rwkv_r_k_2", 3), ("rwkv_gn_g_2", 3), ("rwkv_gn_b_2", 3),
    ("gdn_conv_w_2", 36), ("gdn_o_norm_g_2", 1), ("mla_q_norm_g_2", 2), ("mla_kv_norm_g_2", 1),
]


class Core:

    def __init__(self, nc, ctx, dram):
        self.nc, self.ctx, self.dram = nc, ctx, dram
        sb = lambda name, shape, dt=F32: ctx.enter_context(nc.sbuf_tensor(name, shape, dt))
        self.pl = param_layout()
        self.ident = sb("ident", [P, P])
        self.ones = sb("ones", [P, P])
        self.zero = sb("zero", [P, 1])
        self.eps = sb("eps", [P, 1])
        self.gn_eps = sb("gn_eps", [P, 1])
        self.prm = sb("prm", [P, self.pl.n])
        self.pr = Products(nc, ctx, 4, 2)
        self.psum = ctx.enter_context(nc.psum_tensor("psum", [P, 8, 512], F32))

    def weights(self, ctx, slots=4):
        sb = lambda name, shape, dt=F32: ctx.enter_context(self.nc.sbuf_tensor(f"{name}_{self.pr.units}", shape, dt))
        self.pr.slots = slots
        self.pr.memory(sb("w_raw", [P, 2, 1024]), sb("w_hi", [P, slots, 1024], F32R), sb("w_lo", [P, slots, 1024], F32R),
                       self.zero, self.psum[:, 0:2])

    def par(self, name, k=0):
        at = self.pl.at[name][0]
        if isinstance(k, int):
            return self.prm[:, at + k:at + k + 1]
        return self.prm[:, ds(k + at, 1)]


def start_up(co):
    nc, pr = co.nc, co.pr
    with ExitStack() as ctx:
        loaded = signal(nc, ctx, "vectors_loaded")
        made = signal(nc, ctx, "constants_made")
        block = ctx.enter_context(nc.Block())

        @block.sync
        def _(sp):
            sp.dma_start(co.prm[:], co.dram["vectors"]).then_inc(loaded, 16)
            sp.wait_ge(loaded, 16)

        @block.gpsimd
        def _(pool):
            pool.sem_inc(pr.ready, pr.RAW)
            nc.gpsimd.memset(co.zero[:], 0.0).then_inc(made, 1)
            nc.gpsimd.memset(co.ones[:], 1.0).then_inc(made, 1)
            nc.gpsimd.memset(co.ident[:], 0.0).then_inc(made, 1)
            nc.gpsimd.memset(co.eps[:], EPS).then_inc(made, 1)
            nc.gpsimd.memset(co.gn_eps[:], 64e-5).then_inc(made, 1)
            pool.wait_ge(made, 5)
            nc.gpsimd.affine_select(out=co.ident[:], in_=co.ident[:], compare_op=ALU.not_equal, fill=1.0,
                                    base=0, pattern=[[-1, P]], channel_multiplier=1).then_inc(made, 1)
            pool.wait_ge(made, 6)

        @block.vector
        def _(dve):
            for b in range(pr.banks):
                dve.sem_inc(pr.free[b], 1)

        @block.tensor
        def _(pe):
            pe.sem_inc(pr.full, pr.PRIME)


def norm_split(co, tag, source, pad, total, gain, u_hi, u_lo, keep=None, h_given=None):
    nc = co.nc
    width = pad + total
    cut = chunks_of(pad, total, -(-total // 512))
    with ExitStack() as ctx:
        sb = lambda name, shape, dt=F32: ctx.enter_context(nc.sbuf_tensor(tag + name, shape, dt))
        h = h_given if h_given is not None else sb("h", [P, KD, total])
        sq = sb("sq", [P, 2, total])
        rstd = sb("rstd", [P, total])
        u = sb("u", [P, 2, total])
        landed = [signal(nc, ctx, f"{tag}h_landed{k}") for k in range(KD)]
        pool_s = Steps(nc, ctx, tag + "pool_steps", [f"pad{k}" for k in range(2 * KD)])
        pe_s = Steps(nc, ctx, tag + "pe_steps", [f"sum{k}" for k in range(KD)])
        act_s = Steps(nc, ctx, tag + "act_steps", [f"square{k}" for k in range(KD)]
                      + [f"ln{n}" for n in range(len(cut))] + ["root"] + [f"hi{k}" for k in range(KD)])
        dve_s = Steps(nc, ctx, tag + "dve_steps", [x for k in range(KD) for x in ([f"u{k}"] + ([f"lo{k - 1}"] if k else []))] + [f"lo{KD - 1}"])
        sums = co.psum[:, 2:2 + len(cut)]
        block = ctx.enter_context(nc.Block())

        if h_given is None:
            @block.sync
            def _(sp):
                for k in range(KD):
                    sp.dma_start(h[:, k], source[k * P:(k + 1) * P, :]).then_inc(landed[k], 16)
                for k in range(KD):
                    sp.wait_ge(landed[k], 16)

        if pad:
            @block.vector
            def _(dve):
                for k in range(KD):
                    nc.vector.memset(u_hi[:, k, 0:pad].bitcast(I32), 0).then_inc(*pool_s.did(f"pad{2 * k}"))
                    nc.vector.memset(u_lo[:, k, 0:pad].bitcast(I32), 0).then_inc(*pool_s.did(f"pad{2 * k + 1}"))

        @block.scalar
        def _(act):
            act_s.prime(act)
            for k in range(KD):
                if h_given is None:
                    act.wait_ge(landed[k], 16)
                if k >= 2:
                    act.wait_ge(*pe_s.at(f"sum{k - 2}"))
                nc.scalar.activation(sq[:, k % 2], h[:, k], ACT.Square).then_inc(*act_s.did(f"square{k}"))
            act.wait_ge(*pe_s.at(f"sum{KD - 1}"))
            for n, (off, w) in enumerate(cut):
                nc.scalar.activation(rstd[:, off - pad:off - pad + w], sums[:, n, 0:w], ACT.Ln, scale=1.0 / D,
                                     bias=co.eps[:]).then_inc(*act_s.did(f"ln{n}"))
            act.wait_ge(*act_s.at(f"ln{len(cut) - 1}"))
            nc.scalar.activation(rstd[:], rstd[:], ACT.Exp, scale=-0.5).then_inc(*act_s.did("root"))
            for k in range(KD):
                act.wait_ge(*dve_s.at(f"u{k}"))
                nc.scalar.copy(u_hi[:, k, pad:width], u[:, k % 2]).then_inc(*act_s.did(f"hi{k}"))

        @block.tensor
        def _(pe):
            pe_s.prime(pe)
            for k in range(KD):
                pe.wait_ge(*act_s.at(f"square{k}"))
                for n, (off, w) in enumerate(cut):
                    last = nc.tensor.matmul(sums[:, n, 0:w], co.ones[:], sq[:, k % 2, off - pad:off - pad + w],
                                            start=k == 0, stop=k == KD - 1)
                last.then_inc(*pe_s.did(f"sum{k}"))

        @block.vector
        def _(dve):
            dve_s.prime(dve)
            dve.wait_ge(*act_s.at("root"))

            def lo(k):
                dve.wait_ge(*act_s.at(f"hi{k}"))
                nc.vector.tensor_tensor(u_lo[:, k, pad:width], u[:, k % 2], u_hi[:, k, pad:width].bitcast(F32),
                                        ALU.subtract).then_inc(*dve_s.did(f"lo{k}"))

            for k in range(KD):
                if k >= 2:
                    dve.wait_ge(*dve_s.at(f"lo{k - 2}"))
                nc.vector.scalar_tensor_tensor(u[:, k % 2], h[:, k], co.par(gain, k), rstd[:], ALU.mult,
                                               ALU.mult).then_inc(*dve_s.did(f"u{k}"))
                if k:
                    lo(k - 1)
            lo(KD - 1)


LEVELS = [64, 32, 16, 8, 4, 2, 1]


def hgrn_heads(co, u_hi, u_lo):
    nc, pr = co.nc, co.pr
    HEADS = 4
    w_in = co.dram["w_in"]
    sub = HEADS * P
    cut = chunks_of(PAD, META + SEQ, 3)
    C = slice(PAD, T1)
    tail0 = T1 - SEQ - TAIL
    tcut = chunks_of(tail0, SEQ + TAIL, 3)
    sources = [(lambda i, j=j: columns(w_in, i * P + j * sub)) for j in (1, 0, 2, 3)] + \
        [(lambda i, j=j: columns(w_in, 5 * sub + (4 * i + j) * P)) for j in range(4)]
    body = [chunk_terms(j, u_hi, u_lo, KD, off, w) for j in range(4) for off, w in cut] + \
        [chunk_terms(4 + j, u_hi, u_lo, KD, off, w) for j in range(4) for off, w in tcut]
    st = pr.stage(HEADS, sources, body)
    with ExitStack() as ctx:
        sb = lambda name, shape, dt=F32: ctx.enter_context(nc.sbuf_tensor(name, shape, dt))
        q, f, k, vT, g, b = (sb("hg_" + n, [P, T1]) for n in ("q", "f", "k", "vT", "g", "b"))
        E = sb("hg_E", [P, T1])
        ah = sb("hg_ah", [P, SEQ + TAIL])
        logits = sb("hg_logits", [P, SEQ + TAIL])
        G = sb("hg_G", [P, 2, T1])
        qE, kd = sb("hg_qE", [P, T1]), sb("hg_kd", [P, T1])
        V, kdT = sb("hg_V", [P, NC1, P]), sb("hg_kdT", [P, NC1, P])
        pT = sb("hg_pT", [P, NC1, P])
        states = sb("hg_states", [P, NC1, P])
        decay = sb("hg_decay", [P, NC1])
        lb, oml, lbt = sb("hg_lb", [P, HEADS]), sb("hg_oml", [P, HEADS]), sb("hg_lbt", [P, HEADS])
        mask = sb("hg_mask", [P, len(LEVELS), 64], I32)
        maskd = sb("hg_maskd", [P, P], I32)
        big = co.psum[:, 2:5]
        bigf = big.rearrange("p a b -> p (a b)")
        big3 = bigf[:, 0:T1].rearrange("p (c t) -> p c t", t=P)
        gram = co.psum[:, 5:7].rearrange("p a b -> p (a b)")[:, 0:NC1 * 64]
        gram2 = co.psum[:, 7:8]
        bc = b[:].rearrange("p (c t) -> p c t", t=P)

        pool_c = signal(nc, ctx, "hg_masks")
        act_n = ["f0", "f1", "f2", "sqrt", "ln", "e_last", "e_kd", "e_q", "V", "kdT", "e1_0", "e2_0", "gate0", "gate1"] + \
            [x for l in range(1, 7) for x in (f"e1_{l}", f"e2_{l}", f"gate{l + 1}")] + \
            ["gate8", "gate9", "o", "square", "gate10", "ln_ms", "root", "gate11"]
        dve_n = ["floor", "max"] + [f"scan{c}" for c in range(NC1)] + ["d_kd", "kmul", "m_kd", "m_qE"]
        for l in range(7):
            dve_n += [f"d{l}", f"gk{l}", f"gq{l}"]
            if l == 0:
                dve_n += [f"st{c}" for c in range(NC1 - 1)]
            if l >= 1:
                dve_n += [f"p{l - 1}"]
        dve_n += ["p6", "pd", "a", "ag"]
        pe_n = ["vT", "kT", "U"] + [f"gram{l}" for l in range(7)] + ["diag", "o", "sum"]
        act_s = Steps(nc, ctx, "hg_act", act_n)
        dve_s = Steps(nc, ctx, "hg_dve", dve_n)
        pe_s = Steps(nc, ctx, "hg_pe", pe_n)
        lbs = signal(nc, ctx, "hg_bounds")
        stored = signal(nc, ctx, "hg_stored")
        gates_out = signal(nc, ctx, "hg_gates_stored")
        block = ctx.enter_context(nc.Block())

        @block.sync
        def _(sp):
            with sp.Fori(0, HEADS) as i:
                for j in range(8):
                    st.load(sp, i, j)
            sp.wait_ge(stored, 16 + 16 * HEADS)
            sp.wait_ge(gates_out, 16 + 16 * 4 * HEADS)

        @block.gpsimd
        def _(pool):
            nc.gpsimd.memset(mask[:], 1).then_inc(pool_c, 1)
            nc.gpsimd.memset(maskd[:], 0).then_inc(pool_c, 1)
            pool.wait_ge(pool_c, 2)
            n = 2
            for l, m in enumerate(LEVELS):
                view = mask[:, l].rearrange("p (b m) -> p b m", m=m)
                nb = 64 // m
                nc.gpsimd.affine_select(out=view, in_=view, compare_op=ALU.is_ge, fill=0.0, base=0,
                                        pattern=[[-2 * m, nb], [0, m]], channel_multiplier=1).then_inc(pool_c, 1)
                n += 1
                pool.wait_ge(pool_c, n)
                nc.gpsimd.affine_select(out=view, in_=view, compare_op=ALU.is_ge, fill=0.0, base=m - 1,
                                        pattern=[[2 * m, nb], [0, m]], channel_multiplier=-1).then_inc(pool_c, 1)
                n += 1
            nc.gpsimd.affine_select(out=maskd[:], in_=maskd[:], compare_op=ALU.not_equal, fill=1.0, base=0,
                                    pattern=[[-1, P]], channel_multiplier=1).then_inc(pool_c, 1)
            n += 1
            for x in (f, k, q, vT):
                nc.gpsimd.memset(x[:, 0:PAD], 0.0).then_inc(pool_c, 1)
                n += 1
            nc.gpsimd.memset(pT[:], 0.0).then_inc(pool_c, 1)
            nc.gpsimd.memset(states[:, 0], 0.0).then_inc(pool_c, 1)
            n += 2
            assert n == 2 + 14 + 1 + 4 + 2
            with pool.Fori(0, HEADS) as i:
                for j in range(8):
                    st.split(pool, i, j)

        CONSTS = 23

        @block.scalar
        def _(act):
            act_s.prime(act)
            act.wait_ge(lbs, 1)
            nc.scalar.activation(lbt[:], lbt[:], ACT.Exp).then_inc(lbs, 1)
            act.wait_ge(pool_c, CONSTS)
            act.sem_inc(gates_out, 16)

            def gate(i, n):
                j, part = divmod(n, 3)
                c = 12 + n
                W3 = (SEQ + TAIL) // 3
                if part == 0:
                    act.wait_ge(gates_out, 16 + 64 * i + 16 * j)
                st.wait_full(act, i, c)
                nc.scalar.copy(logits[:, part * W3:(part + 1) * W3], st.bank_of(c)).then_inc(*act_s.did(f"gate{n}"))
                act.wait_ge(*act_s.at(f"gate{n}", i))
                act.sem_inc(st.freed(c), 1)
                if part == 2:
                    act.dma_start(co.dram["gateT"][ds((4 * i + j) * P, P), :], logits[:]).then_inc(gates_out, 16)

            with act.Fori(0, HEADS) as i:
                for n, (off, w) in enumerate(cut):
                    st.wait_full(act, i, n)
                    nc.scalar.activation(f[:, off:off + w], st.bank_of(n), ACT.Sigmoid).then_inc(*act_s.did(f"f{n}"))
                    nc.scalar.activation(k[:, off:off + w], st.bank_of(n), ACT.Sigmoid,
                                         scale=-1.0).then_inc(st.freed(n), 1)
                for n, (off, w) in enumerate(cut):
                    st.wait_full(act, i, 3 + n)
                    nc.scalar.copy(q[:, off:off + w], st.bank_of(3 + n)).then_inc(st.freed(3 + n), 1)
                act.wait_ge(*dve_s.at("max", i))
                nc.scalar.activation(f[:, C], f[:, C], ACT.Sqrt).then_inc(*act_s.did("sqrt"))
                act.wait_ge(*act_s.at("sqrt", i))
                nc.scalar.activation(f[:, C], f[:, C], ACT.Ln).then_inc(*act_s.did("ln"))
                for n, (off, w) in enumerate(cut):
                    st.wait_full(act, i, 6 + n)
                    nc.scalar.copy(vT[:, off:off + w], st.bank_of(6 + n)).then_inc(st.freed(6 + n), 1)
                act.wait_ge(*dve_s.at("d_kd", i))
                nc.scalar.activation(decay[:], bc[:, :, P - 1], ACT.Exp, scale=2.0).then_inc(*act_s.did("e_last"))
                nc.scalar.activation(kd[:], kd[:], ACT.Exp, scale=2.0).then_inc(*act_s.did("e_kd"))
                nc.scalar.activation(qE[:], b[:], ACT.Exp, scale=2.0).then_inc(*act_s.did("e_q"))
                for n, (off, w) in enumerate(cut):
                    st.wait_full(act, i, 9 + n)
                    nc.scalar.activation(g[:, off:off + w], st.bank_of(9 + n), ACT.Sigmoid).then_inc(st.freed(9 + n), 1)
                act.wait_ge(*pe_s.at("vT", i))
                nc.scalar.copy(V[:], big3).then_inc(*act_s.did("V"))
                act.wait_ge(*pe_s.at("kT", i))
                nc.scalar.copy(kdT[:], big3).then_inc(*act_s.did("kdT"))
                for l, m in enumerate(LEVELS):
                    act.wait_ge(*dve_s.at(f"d{l}", i))
                    Ev = E[:].rearrange("p (b two m) -> p b two m", two=2, m=m)
                    nc.scalar.activation(Ev[:, :, 0], Ev[:, :, 0], ACT.Exp, scale=-2.0).then_inc(*act_s.did(f"e1_{l}"))
                    nc.scalar.activation(Ev[:, :, 1], Ev[:, :, 1], ACT.Exp, scale=2.0).then_inc(*act_s.did(f"e2_{l}"))
                    if l == 0:
                        gate(i, 0)
                    gate(i, l + 1)
                gate(i, 8)
                gate(i, 9)
                act.wait_ge(*pe_s.at("o", i))
                nc.scalar.copy(kd[:, tail0:T1], bigf[:, tail0:T1]).then_inc(*act_s.did("o"))
                act.wait_ge(*act_s.at("o", i))
                nc.scalar.activation(E[:, tail0:T1], kd[:, tail0:T1], ACT.Square).then_inc(*act_s.did("square"))
                gate(i, 10)
                act.wait_ge(*pe_s.at("sum", i))
                nc.scalar.activation(b[:, tail0:T1].rearrange("p (n t) -> p n t", n=3), big[:, :, 0:(SEQ + TAIL) // 3], ACT.Ln,
                                     scale=1.0 / P, bias=co.eps[:]).then_inc(*act_s.did("ln_ms"))
                act.wait_ge(*act_s.at("ln_ms", i))
                nc.scalar.activation(b[:, tail0:T1], b[:, tail0:T1], ACT.Exp, scale=-0.5).then_inc(*act_s.did("root"))
                gate(i, 11)
                act.wait_ge(*dve_s.at("ag", i))
                act.dma_start(co.dram["aT"][ds(i * P, P), :], ah[:]).then_inc(stored, 16)

        @block.tensor
        def _(pe):
            pe_s.prime(pe)
            pe.wait_ge(pool_c, CONSTS)
            with pe.Fori(0, HEADS) as i:
                for c in range(10):
                    st.multiply(pe, i, c)
                for b_ in range(2):
                    c = max(c for c in range(6, 9) if st.bank[c] == b_)
                    pe.wait_ge(st.freed(c), 2 + st.used[c] + i * st.per[b_])
                pe.wait_ge(*act_s.at("root", i - 1))
                for c in range(NC1):
                    last = nc.tensor.transpose(big3[:, c], vT[:, c * P:(c + 1) * P], co.ident[:])
                last.then_inc(*pe_s.did("vT"))
                for c in (10, 11):
                    st.multiply(pe, i, c)
                pe.wait_ge(*dve_s.at("m_kd", i))
                pe.wait_ge(*act_s.at("V", i))
                for c in range(NC1):
                    last = nc.tensor.transpose(big3[:, c], kd[:, c * P:(c + 1) * P], co.ident[:])
                last.then_inc(*pe_s.did("kT"))
                st.multiply(pe, i, 12)
                pe.wait_ge(*act_s.at("kdT", i))
                for c in range(NC1):
                    last = nc.tensor.matmul(big3[:, c], kdT[:, c], V[:, c], start=True, stop=True)
                last.then_inc(*pe_s.did("U"))
                st.multiply(pe, i, 13)
                for l, m in enumerate(LEVELS):
                    pe.wait_ge(*dve_s.at(f"gq{l}", i))
                    if l:
                        pe.wait_ge(*dve_s.at(f"p{l - 1}", i))
                    for c in range(NC1):
                        cols = G[:, l % 2, c * P:(c + 1) * P]
                        rhs = cols.rearrange("p (b two m) -> p b two m", two=2, m=m)[:, :, 1]
                        last = nc.tensor.matmul(gram[:, c * 64:(c + 1) * 64], cols, rhs, start=True, stop=True)
                    last.then_inc(*pe_s.did(f"gram{l}"))
                    st.multiply(pe, i, 14 + l)
                pe.wait_ge(*dve_s.at(f"st{NC1 - 2}", i))
                for c in range(NC1):
                    last = nc.tensor.matmul(big3[:, c], k[:, c * P:(c + 1) * P], q[:, c * P:(c + 1) * P],
                                            start=True, stop=True)
                last.then_inc(*pe_s.did("diag"))
                st.multiply(pe, i, 21)
                pe.wait_ge(*dve_s.at("pd", i))
                for c in range(NC1):
                    nc.tensor.matmul(big3[:, c], V[:, c], pT[:, c], start=True, stop=False)
                    last = nc.tensor.matmul(big3[:, c], states[:, c], qE[:, c * P:(c + 1) * P], start=False, stop=True)
                last.then_inc(*pe_s.did("o"))
                st.multiply(pe, i, 22)
                pe.wait_ge(*act_s.at("square", i))
                for n, (off, w) in enumerate(tcut):
                    last = nc.tensor.matmul(big[:, n, 0:w], co.ones[:], E[:, off:off + w], start=True, stop=True)
                last.then_inc(*pe_s.did("sum"))
                st.multiply(pe, i, 23)

        @block.vector
        def _(dve):
            dve_s.prime(dve)
            dve.sem_inc(stored, 16)
            raw = co.prm[:, co.pl.at["hgrn_lower_bounds"][0]:co.pl.at["hgrn_lower_bounds"][0] + HEADS]
            n = [0]

            def step(ins, add=1):
                ins.then_inc(lbs, 1)
                n[0] += 1
                dve.wait_ge(lbs, n[0] + add)
            nc.vector.tensor_tensor(lbt[:], raw, raw, ALU.subtract).then_inc(lbs, 1)
            n[0] = 1
            dve.wait_ge(lbs, 2)
            step(nc.vector.reciprocal(lb[:], lbt[:]))
            step(nc.vector.tensor_tensor(lb[:], lb[:], lbt[:], ALU.mult))
            step(nc.vector.tensor_tensor(lb[:], lb[:], lb[:], ALU.subtract))
            step(nc.vector.tensor_scalar(lb[:], lb[:], 0.0, 1.0, ALU.max, ALU.min))
            step(nc.vector.tensor_scalar(oml[:], lb[:], -1.0, 1.0, ALU.mult, ALU.add))
            dve.wait_ge(pool_c, CONSTS)
            with dve.Fori(0, HEADS) as i:
                lb_h, oml_h = lb[:, ds(i, 1)], oml[:, ds(i, 1)]
                dve.wait_ge(*act_s.at("f2", i))
                nc.vector.tensor_scalar(f[:, C], f[:, C], oml_h, lb_h, ALU.mult, ALU.add).then_inc(*dve_s.did("floor"))
                dve.wait_ge(*dve_s.at("floor", i))
                nc.vector.tensor_scalar(f[:, C], f[:, C], 1e-30, None, ALU.max).then_inc(*dve_s.did("max"))
                dve.wait_ge(*act_s.at("ln", i))
                for c in range(NC1):
                    nc.vector.tensor_tensor_scan(b[:, c * P:(c + 1) * P], co.ones[:], f[:, c * P:(c + 1) * P], 0.0,
                                                 ALU.mult, ALU.add).then_inc(*dve_s.did(f"scan{c}"))
                dve.wait_ge(*dve_s.at(f"scan{NC1 - 1}", i))
                nc.vector.tensor_tensor(kd[:].rearrange("p (c t) -> p c t", t=P),
                                        bc[:, :, P - 1:P].to_broadcast([P, NC1, P]), bc,
                                        ALU.subtract).then_inc(*dve_s.did("d_kd"))
                nc.vector.tensor_scalar(k[:, C], k[:, C], oml_h, None, ALU.mult).then_inc(*dve_s.did("kmul"))
                dve.wait_ge(*dve_s.at("kmul", i))
                dve.wait_ge(*act_s.at("e_q", i))
                nc.vector.tensor_tensor(kd[:], kd[:], k[:], ALU.mult).then_inc(*dve_s.did("m_kd"))
                nc.vector.tensor_tensor(qE[:], qE[:], q[:], ALU.mult).then_inc(*dve_s.did("m_qE"))

                def score(l):
                    m = LEVELS[l]
                    if l:
                        dve.wait_ge(*dve_s.at(f"p{l - 1}", i))
                    dve.wait_ge(*pe_s.at(f"gram{l}", i))
                    pr.carry(dve)
                    nb = 64 // m
                    out = pT[:].rearrange("p c (b two m) -> p c b two m", two=2, m=m)[:, :, :, 1]
                    src = gram.rearrange("p (c b m) -> p c b m", b=nb, m=m)
                    mk = mask[:, l].rearrange("p (b m) -> p b m", m=m).unsqueeze(1).to_broadcast([P, NC1, nb, m])
                    nc.vector.copy_predicated(out, mk, src).then_inc(*dve_s.did(f"p{l}"))

                for l, m in enumerate(LEVELS):
                    if l:
                        dve.wait_ge(*dve_s.at(f"gq{l - 1}", i))
                    bv = b[:].rearrange("p (n t) -> p n t", t=2 * m)
                    nc.vector.tensor_tensor(E[:].rearrange("p (n t) -> p n t", t=2 * m), bv,
                                            bv[:, :, m - 1:m].to_broadcast([P, T1 // (2 * m), 2 * m]),
                                            ALU.subtract).then_inc(*dve_s.did(f"d{l}"))
                    Ev, kv, qv, Gv = (x.rearrange("p (b two m) -> p b two m", two=2, m=m)
                                      for x in (E[:], k[:], q[:], G[:, l % 2]))
                    if l >= 2:
                        dve.wait_ge(*pe_s.at(f"gram{l - 2}", i))
                    dve.wait_ge(*act_s.at(f"e2_{l}", i))
                    nc.vector.tensor_tensor(Gv[:, :, 0], Ev[:, :, 0], kv[:, :, 0], ALU.mult).then_inc(*dve_s.did(f"gk{l}"))
                    nc.vector.tensor_tensor(Gv[:, :, 1], Ev[:, :, 1], qv[:, :, 1], ALU.mult).then_inc(*dve_s.did(f"gq{l}"))
                    if l == 0:
                        dve.wait_ge(*pe_s.at("U", i))
                        for c in range(NC1 - 1):
                            if c:
                                dve.wait_ge(*dve_s.at(f"st{c - 1}", i))
                            nc.vector.scalar_tensor_tensor(states[:, c + 1], states[:, c], decay[:, c:c + 1],
                                                           big3[:, c], ALU.mult, ALU.add).then_inc(*dve_s.did(f"st{c}"))
                    if l >= 1:
                        score(l - 1)
                score(6)
                dve.wait_ge(*dve_s.at("p6", i))
                dve.wait_ge(*pe_s.at("diag", i))
                pr.carry(dve)
                nc.vector.copy_predicated(pT[:], maskd[:].unsqueeze(1).to_broadcast([P, NC1, P]),
                                          big3).then_inc(*dve_s.did("pd"))
                dve.wait_ge(*act_s.at("root", i))
                nc.vector.scalar_tensor_tensor(kd[:, tail0:T1], kd[:, tail0:T1], co.par("hgrn_out_norm", i),
                                               b[:, tail0:T1], ALU.mult, ALU.mult).then_inc(*dve_s.did("a"))
                dve.wait_ge(*dve_s.at("a", i))
                dve.wait_ge(stored, 16 * i + 16)
                nc.vector.tensor_tensor(ah[:], kd[:, tail0:T1], g[:, tail0:T1], ALU.mult).then_inc(*dve_s.did("ag"))


def pool_branch(co, u_hi, u_lo, p_hi, p_lo, a_hi, a_lo):
    nc, pr = co.nc, co.pr
    W = SEQ + TAIL
    t0 = T1 - W
    cut = chunks_of(PAD, META + SEQ, 3)
    tcut = chunks_of(t0, W, 3)
    at = 4 * 512
    st = pr.stage(1, [(lambda i, j=j: columns(co.dram["w_in"], at + j * P)) for j in range(4)],
                  [chunk_terms(j, u_hi, u_lo, KD, off, w) for j in range(4) for off, w in cut])
    with ExitStack() as ctx:
        sb = lambda name, shape, dt=F32: ctx.enter_context(nc.sbuf_tensor(name, shape, dt))
        v = sb("pl_v", [P, 2, T1])
        s = sb("pl_s", [P, 2, T1])
        m = sb("pl_m", [P, W])
        y = sb("pl_y", [P, W])
        a = s[:, :, 0:W]
        a_in = [signal(nc, ctx, f"pl_a_in{r}") for r in range(2)]
        proj = sb("pl_proj", [P, 4, P])
        loaded = signal(nc, ctx, "pl_proj_loaded")
        pads = signal(nc, ctx, "pl_pads")
        act_n, dve_n = [f"ahi{k}" for k in range(4)], [f"alo{k}" for k in range(4)]
        for j in range(4):
            act_n += [f"y{j}", f"hi{j}"]
            dve_n += [f"s{j}_{r}" for r in range(j + 1)] + ([f"mean{j}"] if j < 3 else ["mean3", "mean3b"]) + \
                [f"m{j}", f"lo{j}"]
        act_s = Steps(nc, ctx, "pl_act", act_n)
        dve_s = Steps(nc, ctx, "pl_dve", dve_n)
        pe_s = Steps(nc, ctx, "pl_pe", [f"y{j}" for j in range(4)])
        out = co.psum[:, 2:5]
        block = ctx.enter_context(nc.Block())

        @block.sync
        def _(sp):
            for j in range(4):
                st.load(sp, 0, j)
            sp.dma_start(proj[:], co.dram["pool_proj"].rearrange("g c d -> c g d")).then_inc(loaded, 16)

        def load_a(pe, k):
            if k >= 2:
                pe.wait_ge(*dve_s.at(f"alo{k - 2}"))
            pe.dma_start(a[:, k % 2], co.dram["aT"][k * P:(k + 1) * P, :]).then_inc(a_in[k % 2], 16)

        @block.gpsimd
        def _(pool):
            for r in range(2):
                nc.gpsimd.memset(v[:, r, 0:PAD], 0.0).then_inc(pads, 1)
            for j in range(4):
                st.split(pool, 0, j)

        @block.scalar
        def _(act):
            act_s.prime(act)

            for k in range(4):
                load_a(act, k)
                act.wait_ge(a_in[k % 2], 16 * (k // 2 + 1))
                nc.scalar.copy(a_hi[:, k], a[:, k % 2]).then_inc(*act_s.did(f"ahi{k}"))

            def take(j):
                if j >= 2:
                    act.wait_ge(*dve_s.at(f"m{j - 2}"))
                for n, (off, w) in enumerate(cut):
                    st.wait_full(act, 0, 3 * j + n)
                    nc.scalar.copy(v[:, j % 2, off:off + w], st.bank_of(3 * j + n)).then_inc(st.freed(3 * j + n), 1)

            take(0)
            for j in range(4):
                if j < 3:
                    take(j + 1)
                act.wait_ge(*pe_s.at(f"y{j}"))
                if j:
                    act.wait_ge(*dve_s.at(f"lo{j - 1}"))
                nc.scalar.mul(y[:].rearrange("p (a b) -> p a b", a=3), out[:, :, 0:W // 3],
                              co.par("pool_scale", j)).then_inc(*act_s.did(f"y{j}"))
                act.wait_ge(*act_s.at(f"y{j}"))
                nc.scalar.copy(p_hi[:, j], y[:]).then_inc(*act_s.did(f"hi{j}"))

        def project(pe, j):
            pe.wait_ge(loaded, 16)
            pe.wait_ge(*dve_s.at(f"m{j}"))
            if j:
                pe.wait_ge(*act_s.at(f"y{j - 1}"))
            for n in range(3):
                last = nc.tensor.matmul(out[:, n, 0:W // 3], proj[:, j], m[:, n * (W // 3):(n + 1) * (W // 3)],
                                        start=True, stop=True)
            last.then_inc(*pe_s.did(f"y{j}"))

        @block.tensor
        def _(pe):
            pe_s.prime(pe)
            for j in range(4):
                for c in range(3):
                    st.multiply(pe, 0, 3 * j + c)
                if j >= 1:
                    project(pe, j - 1)
            project(pe, 3)

        @block.vector
        def _(dve):
            dve_s.prime(dve)
            for k in range(4):
                dve.wait_ge(*act_s.at(f"ahi{k}"))
                nc.vector.tensor_tensor(a_lo[:, k], a[:, k % 2], a_hi[:, k].bitcast(F32), ALU.subtract).then_inc(*dve_s.did(f"alo{k}"))
            dve.wait_ge(*dve_s.at("alo3"))
            dve.wait_ge(pads, 2)
            for j in range(4):
                st_wait_taken(dve, st, j)
                src = v[:, j % 2]
                for r in range(j + 1):
                    if r:
                        dve.wait_ge(*dve_s.at(f"s{j}_{r - 1}"))
                    step = 1 << r
                    lo = 2 * step - 1
                    nc.vector.tensor_tensor(s[:, r % 2, lo:T1], src[:, lo:T1], src[:, lo - step:T1 - step],
                                            ALU.add).then_inc(*dve_s.did(f"s{j}_{r}"))
                    src = s[:, r % 2]
                window = 2 << j
                dve.wait_ge(*dve_s.at(f"s{j}_{j}"))
                if j:
                    dve.wait_ge(*pe_s.at(f"y{j - 1}"))
                if j < 3:
                    nc.vector.tensor_scalar(m[:], src[:, t0:T1], 1.0 / window, None, ALU.mult).then_inc(*dve_s.did(f"mean{j}"))
                    dve.wait_ge(*dve_s.at(f"mean{j}"))
                else:
                    short = META - TAIL + 1
                    nc.vector.tensor_scalar(m[:, 0:1], src[:, t0:t0 + 1], 1.0 / short, None, ALU.mult).then_inc(*dve_s.did("mean3"))
                    nc.vector.tensor_scalar(m[:, 1:W], src[:, t0 + 1:T1], 1.0 / window, None, ALU.mult).then_inc(*dve_s.did("mean3b"))
                    dve.wait_ge(*dve_s.at("mean3b"))
                nc.vector.tensor_tensor(m[:], m[:], v[:, j % 2, t0:T1], ALU.subtract).then_inc(*dve_s.did(f"m{j}"))
                dve.wait_ge(*act_s.at(f"hi{j}"))
                nc.vector.tensor_tensor(p_lo[:, j], y[:], p_hi[:, j].bitcast(F32),
                                        ALU.subtract).then_inc(*dve_s.did(f"lo{j}"))


def st_wait_taken(eng, st, j):
    for c in range(3 * j, 3 * j + 3):
        eng.wait_ge(st.freed(c), 2 + st.used[c])


def gated_sum(co, a_hi, a_lo, p_hi, p_lo, z_hi, z_lo):
    nc, pr = co.nc, co.pr
    W = SEQ + TAIL
    N = W // 3
    sources = [(lambda i, w=w, h=h: columns(co.dram[w], (2 * i + h) * P)) for h in range(2) for w in ("w_branch_hgrn", "w_branch_pool")]
    body = [chunk_terms(2 * h + x, hi, lo, 4, n * N, N) for h in range(2) for x, (hi, lo) in enumerate(((a_hi, a_lo), (p_hi, p_lo)))
            for n in range(3)]
    st = pr.stage(KD // 2, sources, body)
    with ExitStack() as ctx:
        sb = lambda name, shape, dt=F32: ctx.enter_context(nc.sbuf_tensor(name, shape, dt))
        gate = [sb("gs_a", [P, W]), sb("gs_b", [P, W])]
        z = sb("gs_z", [P, 2, W])
        landed = [signal(nc, ctx, "gs_a_in"), signal(nc, ctx, "gs_b_in")]
        act_s = Steps(nc, ctx, "gs_act", ["a0", "b0", "a1", "b1", "hi0", "hi1"])
        dve_s = Steps(nc, ctx, "gs_dve", [x for h in range(2) for x in [f"za{n}{h}" for n in range(3)]
                                          + [f"zb{n}{h}" for n in range(3)] + [f"z{h}"]] + ["lo0", "lo1"])
        block = ctx.enter_context(nc.Block())

        def tile(x, k):
            return x[:, ds(k, 1), 0:W].rearrange("p o t -> p (o t)")

        def before(name, i, h):
            return dve_s.at(f"{name}0", i) if h else dve_s.at(f"{name}1", i - 1)

        @block.sync
        def _(sp):
            with sp.Fori(0, KD // 2) as i:
                for j in range(4):
                    st.load(sp, i, j)

        @block.gpsimd
        def _(pool):
            with pool.Fori(0, KD // 2) as i:
                for j in range(4):
                    st.split(pool, i, j)

        @block.scalar
        def _(act):
            act_s.prime(act)
            with act.Fori(0, KD // 2) as i:
                for h in range(2):
                    for x, name in enumerate("ab"):
                        src = co.dram["gateT"][ds((2 * i + h) * P + x * D, P), :]
                        act.wait_ge(*before(("za2", "z")[x], i, h))
                        act.dma_start(gate[x][:], src).then_inc(landed[x], 16)
                    for x, name in enumerate("ab"):
                        act.wait_ge(landed[x], 32 * i + 16 * h + 16)
                        nc.scalar.activation(gate[x][:], gate[x][:], ACT.Sigmoid).then_inc(*act_s.did(f"{name}{h}"))
                for h in range(2):
                    act.wait_ge(*dve_s.at(f"z{h}", i))
                    nc.scalar.copy(tile(z_hi, 2 * i + h), z[:, h]).then_inc(*act_s.did(f"hi{h}"))

        @block.tensor
        def _(pe):
            with pe.Fori(0, KD // 2) as i:
                for c in range(12):
                    st.multiply(pe, i, c)

        @block.vector
        def _(dve):
            dve_s.prime(dve)

            def lo(i, h):
                dve.wait_ge(*act_s.at(f"hi{h}", i))
                nc.vector.tensor_tensor(tile(z_lo, 2 * i + h), z[:, h], tile(z_hi, 2 * i + h).bitcast(F32),
                                        ALU.subtract).then_inc(*dve_s.did(f"lo{h}"))

            with dve.Fori(0, KD // 2) as i:
                for h in range(2):
                    dve.wait_ge(*dve_s.at(f"lo{h}", i - 1))
                    for x, name in enumerate("ab"):
                        dve.wait_ge(*act_s.at(f"{name}{h}", i))
                        for n in range(3):
                            cols = slice(n * N, (n + 1) * N)
                            c = 6 * h + 3 * x + n
                            st.wait_full(dve, i, c)
                            out = (z[:, h] if x == 0 else gate[1])[:, cols]
                            nc.vector.tensor_tensor(out, gate[x][:, cols], st.bank_of(c), ALU.mult)\
                              .then_inc(*dve_s.did(f"z{name}{n}{h}"))
                            dve.wait_ge(*dve_s.at(f"z{name}{n}{h}", i))
                            dve.sem_inc(st.freed(c), 1)
                    nc.vector.tensor_tensor(z[:, h], z[:, h], gate[1][:], ALU.add).then_inc(*dve_s.did(f"z{h}"))
                for h in range(2):
                    lo(i, h)


def split_from_dram(co, tag, source, tiles, width, hi, lo):
    nc = co.nc
    with ExitStack() as ctx:
        x = ctx.enter_context(nc.sbuf_tensor(tag + "x", [P, 2, width], F32))
        landed = [signal(nc, ctx, f"{tag}in{r}") for r in range(2)]
        act_s = Steps(nc, ctx, tag + "act", [f"hi{k}" for k in range(tiles)])
        dve_s = Steps(nc, ctx, tag + "dve", [f"lo{k}" for k in range(tiles)])
        block = ctx.enter_context(nc.Block())

        @block.sync
        def _(sp):
            for k in range(tiles):
                if k >= 2:
                    sp.wait_ge(*dve_s.at(f"lo{k - 2}"))
                sp.dma_start(x[:, k % 2], source[k * P:(k + 1) * P, :]).then_inc(landed[k % 2], 16)

        @block.scalar
        def _(act):
            act_s.prime(act)
            for k in range(tiles):
                act.wait_ge(landed[k % 2], 16 * (k // 2 + 1))
                nc.scalar.copy(hi[:, k], x[:, k % 2]).then_inc(*act_s.did(f"hi{k}"))

        @block.vector
        def _(dve):
            dve_s.prime(dve)
            for k in range(tiles):
                dve.wait_ge(*act_s.at(f"hi{k}"))
                nc.vector.tensor_tensor(lo[:, k], x[:, k % 2], hi[:, k].bitcast(F32),
                                        ALU.subtract).then_inc(*dve_s.did(f"lo{k}"))


def square_product(co, tag, w, x_hi, x_lo, y, width, parts):
    nc, pr = co.nc, co.pr
    N = width // parts
    st = pr.stage(2, [(lambda i, j=j: columns(w, (4 * i + j) * P)) for j in range(4)],
                  [chunk_terms(j, x_hi, x_lo, KD, n * N, N) for j in range(4) for n in range(parts)])
    with ExitStack() as ctx:
        block = ctx.enter_context(nc.Block())

        @block.sync
        def _(sp):
            with sp.Fori(0, 2) as i:
                for j in range(4):
                    st.load(sp, i, j)

        @block.gpsimd
        def _(pool):
            with pool.Fori(0, 2) as i:
                for j in range(4):
                    st.split(pool, i, j)

        @block.tensor
        def _(pe):
            with pe.Fori(0, 2) as i:
                for c in range(4 * parts):
                    st.multiply(pe, i, c)

        @block.scalar
        def _(act):
            with act.Fori(0, 2) as i:
                for c in range(4 * parts):
                    j, n = divmod(c, parts)
                    st.wait_full(act, i, c)
                    nc.scalar.copy(y[:, ds(4 * i + j, 1), n * N:(n + 1) * N].rearrange("p o t -> p (o t)"),
                                   st.bank_of(c)).then_inc(st.freed(c), 1)


def residual_norm(co, tag, res, y, width, gain, dest, skip=0, gained=True):
    nc = co.nc
    parts = -(-width // 512)
    N = width // parts
    with ExitStack() as ctx:
        sb = lambda name, shape, dt=F32: ctx.enter_context(nc.sbuf_tensor(tag + name, shape, dt))
        x = sb("x", [P, 4, width])
        sq = sb("sq", [P, 2, width])
        rstd = sb("rstd", [P, width])
        o = sb("o", [P, 4, width])
        landed = [signal(nc, ctx, f"{tag}in{r}") for r in range(4)]
        stored = [signal(nc, ctx, f"{tag}out{r}") for r in range(4)]
        norm = gain is not None
        pe_s = Steps(nc, ctx, tag + "pe", [f"sum{k}" for k in range(KD)])
        act_s = Steps(nc, ctx, tag + "act", [f"square{k}" for k in range(KD)] + ["ln", "root"])
        dve_s = Steps(nc, ctx, tag + "dve", [f"{x}{k}" for k in range(KD) for x in (("t", "o") if norm else ("o",))])
        sums = co.psum[:, 2:2 + parts]
        block = ctx.enter_context(nc.Block())

        @block.sync
        def _(sp):
            for k in range(KD):
                if k >= 4:
                    sp.wait_ge(*dve_s.at(f"o{k - 4}"))
                sp.dma_start(x[:, k % 4], res[k * P:(k + 1) * P, :]).then_inc(landed[k % 4], 16)
            for k in range(KD):
                sp.wait_ge(*dve_s.at(f"o{k}"))
                sp.dma_start(dest[k * P:(k + 1) * P, :], o[:, k % 4, skip:]).then_inc(stored[k % 4], 16)
            for r in range(4):
                sp.wait_ge(stored[r], 16 * KD // 4)

        if norm:
            @block.scalar
            def _(act):
                act_s.prime(act)
                for k in range(KD):
                    if k >= 2:
                        act.wait_ge(*pe_s.at(f"sum{k - 2}"))
                    nc.scalar.activation(sq[:, k % 2], y[:, k], ACT.Square).then_inc(*act_s.did(f"square{k}"))
                act.wait_ge(*pe_s.at(f"sum{KD - 1}"))
                nc.scalar.activation(rstd[:].rearrange("p (a b) -> p a b", a=parts), sums[:, :, 0:N], ACT.Ln, scale=1.0 / D,
                                     bias=co.eps[:]).then_inc(*act_s.did("ln"))
                act.wait_ge(*act_s.at("ln"))
                nc.scalar.activation(rstd[:], rstd[:], ACT.Exp, scale=-0.5).then_inc(*act_s.did("root"))

            @block.tensor
            def _(pe):
                pe_s.prime(pe)
                for k in range(KD):
                    pe.wait_ge(*act_s.at(f"square{k}"))
                    for n in range(parts):
                        last = nc.tensor.matmul(sums[:, n, 0:N], co.ones[:], sq[:, k % 2, n * N:(n + 1) * N],
                                                start=k == 0, stop=k == KD - 1)
                    last.then_inc(*pe_s.did(f"sum{k}"))

        @block.vector
        def _(dve):
            dve_s.prime(dve)
            if norm:
                dve.wait_ge(*act_s.at("root"))
            for k in range(KD):
                if k >= 4:
                    dve.wait_ge(stored[k % 4], 16 * (k // 4))
                part = y[:, k]
                if norm:
                    nc.vector.scalar_tensor_tensor(o[:, k % 4], y[:, k], co.par(gain, k), rstd[:], ALU.mult,
                                                   ALU.mult).then_inc(*dve_s.did(f"t{k}"))
                    dve.wait_ge(*dve_s.at(f"t{k}"))
                    part = o[:, k % 4]
                dve.wait_ge(landed[k % 4], 16 * (k // 4 + 1))
                nc.vector.tensor_tensor(o[:, k % 4], part, x[:, k % 4], ALU.add).then_inc(*dve_s.did(f"o{k}"))


def feed_forward(co, tag, u_hi, u_lo, w_up, w_down, acc, w_gate=None):
    nc, pr = co.nc, co.pr
    gated = w_gate is not None
    tail = TAIL if gated else 0
    W = SEQ + tail
    G = W // 3
    H = SEQ // 2
    pairs = w_up.shape[1] // (2 * P)
    up_src = [(lambda i, j=j: columns(w_up, (2 * i + j) * P)) for j in range(2)]
    gate_src = [(lambda i, j=j: columns(w_gate, (2 * i + j) * P)) for j in range(2)] if gated else []
    down_src = [(lambda i, j=j: w_down[ds((2 * i + j) * P, P), :] if not isinstance(i, int)
                 else w_down[(2 * i + j) * P:(2 * i + j + 1) * P, :]) for j in range(2)]
    with ExitStack() as ctx:
        sb = lambda name, shape, dt=F32: ctx.enter_context(nc.sbuf_tensor(tag + name, shape, dt))
        hid = sb("hid", [P, 2, SEQ])
        h_hi, h_lo = sb("h_hi", [P, 2, SEQ], F32R), sb("h_lo", [P, 2, SEQ], F32R)
        if gated:
            gt, cv = sb("gt", [P, 2, W]), sb("cv", [P, 2, SEQ])
        gate = [chunk_terms(j, u_hi, u_lo, KD, n * G, G) for j in range(2) for n in range(3)] if gated else []

        def up(first):
            return [chunk_terms(first + j, u_hi, u_lo, KD, tail + n * H, H) for j in range(2) for n in range(2)]

        def down(first):
            return [(H, [(first + j, (lambda t, m=m: t[:, m * P:(m + 1) * P]), h_hi[:, j, n * H:(n + 1) * H],
                          h_lo[:, j, n * H:(n + 1) * H]) for j in range(2)]) for m in range(KD) for n in range(2)]

        ng = len(gate)
        g2 = len(gate_src)
        later = lambda src: (lambda i: src(i + 1))
        first = pr.stage(1, gate_src + up_src, gate + up(g2))
        main = pr.stage(pairs - 1, [later(s) for s in gate_src] + down_src + [later(s) for s in up_src],
                        gate + down(g2) + up(g2 + 2))
        last = pr.stage(1, [(lambda i, s=s: s(pairs - 1)) for s in down_src], down(0))

        act_n = [f"gelu{j}" for j in range(2)] + [f"hi{j}" for j in range(2)] if gated else \
            [f"{x}{j}" for j in range(2) for x in ("square", "hi")]
        dve_n = ([x for j in range(2) for x in (f"c0{j}", f"c1{j}", f"c2{j}")] if gated else []) + \
            [f"acc{n}" for n in range(16)] + [f"h{j}{n}" for j in range(2) for n in range(2)] + [f"lo{j}" for j in range(2)]
        act_s = Steps(nc, ctx, tag + "act", act_n)
        dve_s = Steps(nc, ctx, tag + "dve", dve_n)
        block = ctx.enter_context(nc.Block())

        def each(eng, body):
            body(first, 0, 0, False)
            with eng.Fori(0, pairs - 1) as i:
                body(main, i, i + 1, True)

        @block.sync
        def _(sp):
            each(sp, lambda st, i, it, steady: [st.load(sp, i, j) for j in range(st.U)])
            for j in range(2):
                last.load(sp, 0, j)

        @block.gpsimd
        def _(pool):
            each(pool, lambda st, i, it, steady: [st.split(pool, i, j) for j in range(st.U)])
            for j in range(2):
                last.split(pool, 0, j)

        @block.tensor
        def _(pe):
            def body(st, i, it, steady):
                for c in range(ng):
                    st.multiply(pe, i, c)
                at = ng
                if steady:
                    pe.wait_ge(*dve_s.at("lo1", it - 1))
                    for c in range(at, at + 16):
                        st.multiply(pe, i, c)
                    at += 16
                for c in range(at, at + 4):
                    st.multiply(pe, i, c)

            each(pe, body)
            pe.wait_ge(*dve_s.at("lo1", pairs - 1))
            for c in range(16):
                last.multiply(pe, 0, c)

        @block.scalar
        def _(act):
            act_s.prime(act)

            def body(st, i, it, steady):
                for c in range(ng):
                    j, n = divmod(c, 3)
                    st.wait_full(act, i, c)
                    act.wait_ge(*dve_s.at(f"c2{j}", it - 1))
                    nc.scalar.copy(gt[:, j, n * G:(n + 1) * G], st.bank_of(c)).then_inc(st.freed(c), 1)
                if gated:
                    for j in range(2):
                        act.wait_ge(*dve_s.at(f"c2{j}", it))
                        nc.scalar.activation(cv[:, j], cv[:, j], ACT.Gelu_apprx_tanh).then_inc(*act_s.did(f"gelu{j}"))
                for j in range(2):
                    act.wait_ge(*dve_s.at(f"h{j}1", it))
                    if not gated:
                        nc.scalar.activation(hid[:, j], hid[:, j], ACT.Square).then_inc(*act_s.did(f"square{j}"))
                        act.wait_ge(*act_s.at(f"square{j}", it))
                    nc.scalar.copy(h_hi[:, j], hid[:, j]).then_inc(*act_s.did(f"hi{j}"))

            each(act, body)

        @block.vector
        def _(dve):
            dve_s.prime(dve)
            def add(st, i, it, c0):
                for c in range(16):
                    m, n = divmod(c, 2)
                    st.wait_full(dve, i, c0 + c)
                    part = acc[:, m, n * H:(n + 1) * H]
                    dve.wait_ge(*dve_s.at(f"acc{c}", it - 1))
                    nc.vector.tensor_tensor(part, part, st.bank_of(c0 + c), ALU.add).then_inc(*dve_s.did(f"acc{c}"))
                    free(st, c0 + c, f"acc{c}", it)

            def free(st, c, step, it):
                dve.wait_ge(*dve_s.at(step, it))
                dve.sem_inc(st.freed(c), 1)

            def body(st, i, it, steady):
                if gated:
                    for j in range(2):
                        for b in range(2):
                            c = max(c for c in range(3 * j, 3 * j + 3) if st.bank[c] == (st.bank[0] + b) % 2)
                            dve.wait_ge(st.freed(c), 2 + st.used[c] + i * st.per[st.bank[c]])
                        dve.wait_ge(*dve_s.at(f"h{j}1", it - 1))
                        tile = 2 * it + j
                        nc.vector.tensor_scalar(cv[:, j], gt[:, j, 0:SEQ], co.par("ffn_conv_w", tile),
                                                co.par("ffn_conv_b", tile), ALU.mult, ALU.add).then_inc(*dve_s.did(f"c0{j}"))
                        for r in (1, 2):
                            dve.wait_ge(*dve_s.at(f"c{r - 1}{j}", it))
                            nc.vector.scalar_tensor_tensor(cv[:, j], gt[:, j, r:SEQ + r], co.par("ffn_conv_w", tile + 2 * pairs * r),
                                                           cv[:, j], ALU.mult, ALU.add).then_inc(*dve_s.did(f"c{r}{j}"))
                at = ng
                if steady:
                    add(st, i, it, at)
                    at += 16
                else:
                    for c in range(16):
                        m, n = divmod(c, 2)
                        nc.vector.memset(acc[:, m, n * H:(n + 1) * H], 0.0).then_inc(*dve_s.did(f"acc{c}"))
                for j in range(2):
                    dve.wait_ge(*act_s.at(f"hi{j}", it - 1))
                    dve.wait_ge(*dve_s.at(f"lo{j}", it - 1))
                    if gated:
                        dve.wait_ge(*act_s.at(f"gelu{j}", it))
                    for n in range(2):
                        c = at + 2 * j + n
                        st.wait_full(dve, i, c)
                        cols = slice(n * H, (n + 1) * H)
                        if gated:
                            ins = nc.vector.tensor_tensor(hid[:, j, cols], cv[:, j, cols], st.bank_of(c), ALU.mult)
                        else:
                            ins = nc.vector.tensor_scalar(hid[:, j, cols], st.bank_of(c), 0.0, None, ALU.max)
                        ins.then_inc(*dve_s.did(f"h{j}{n}"))
                        free(st, c, f"h{j}{n}", it)
                for j in range(2):
                    dve.wait_ge(*act_s.at(f"hi{j}", it))
                    nc.vector.tensor_tensor(h_lo[:, j], hid[:, j], h_hi[:, j].bitcast(F32),
                                            ALU.subtract).then_inc(*dve_s.did(f"lo{j}"))

            each(dve, body)
            for c in range(16):
                m, n = divmod(c, 2)
                last.wait_full(dve, 0, c)
                part = acc[:, m, n * H:(n + 1) * H]
                nc.vector.tensor_tensor(part, part, last.bank_of(c), ALU.add).then_inc(last.freed(c), 1)


def residual_norm_split(co, tag, res, y, width, gain, dest, next_gain, x_hi, x_lo):
    nc = co.nc
    parts = -(-width // 512)
    N = width // parts
    norm = gain is not None
    with ExitStack() as ctx:
        sb = lambda name, shape, dt=F32: ctx.enter_context(nc.sbuf_tensor(tag + name, shape, dt))
        r = sb("r", [P, 4, width])
        sq = sb("sq", [P, 2, width])
        rstd = sb("rstd", [P, 2, width])
        u = sb("u", [P, 4, width])
        landed = [signal(nc, ctx, f"{tag}in{k}") for k in range(4)]
        stored = signal(nc, ctx, f"{tag}out")
        first = [f"{x}{k}" for k in range(KD) for x in (("t", "h") if norm else ("h",))]
        pe_s = Steps(nc, ctx, tag + "pe", ([f"sum{k}" for k in range(KD)] if norm else []) + [f"next{k}" for k in range(KD)])
        act_s = Steps(nc, ctx, tag + "act", ([f"square{k}" for k in range(KD)] + ["ln", "root"] if norm else [])
                      + [f"next{k}" for k in range(KD)] + ["next_ln", "next_root"] + [f"hi{k}" for k in range(KD)])
        dve_s = Steps(nc, ctx, tag + "dve", first + [x for k in range(KD) for x in ([f"u{k}", f"lo{k - 1}"] if k % 2 == 0 and k else [f"u{k}"])]
                      + [f"lo{KD - 1}"])
        pool_s = Steps(nc, ctx, tag + "pool", [f"lo{k}" for k in range(0, KD, 2)])
        sums = [co.psum[:, 2 + 3 * n:2 + 3 * n + parts] for n in range(2)]
        by_part = lambda x: x.rearrange("p (a b) -> p a b", a=parts)
        block = ctx.enter_context(nc.Block())

        def lo_done(eng, k):
            eng.wait_ge(*(dve_s if k % 2 else pool_s).at(f"lo{k}"))

        @block.sync
        def _(sp):
            for k in range(KD):
                if k >= 4:
                    sp.wait_ge(*dve_s.at(f"h{k - 4}"))
                sp.dma_start(r[:, k % 4], res[k * P:(k + 1) * P, :]).then_inc(landed[k % 4], 16)
            for k in range(KD):
                sp.wait_ge(*dve_s.at(f"h{k}"))
                sp.dma_start(dest[k * P:(k + 1) * P, :], y[:, k]).then_inc(stored, 16)
            sp.wait_ge(stored, 16 * KD)

        @block.scalar
        def _(act):
            act_s.prime(act)

            def mean_square(n, names):
                nc.scalar.activation(by_part(rstd[:, n]), sums[n][:, :, 0:N], ACT.Ln, scale=1.0 / D,
                                     bias=co.eps[:]).then_inc(*act_s.did(names[0]))
                act.wait_ge(*act_s.at(names[0]))
                nc.scalar.activation(rstd[:, n], rstd[:, n], ACT.Exp, scale=-0.5).then_inc(*act_s.did(names[1]))

            if norm:
                for k in range(KD):
                    if k >= 2:
                        act.wait_ge(*pe_s.at(f"sum{k - 2}"))
                    nc.scalar.activation(sq[:, k % 2], y[:, k], ACT.Square).then_inc(*act_s.did(f"square{k}"))
                act.wait_ge(*pe_s.at(f"sum{KD - 1}"))
                mean_square(0, ("ln", "root"))
            for k in range(KD):
                act.wait_ge(*dve_s.at(f"h{k}"))
                if k >= 2:
                    act.wait_ge(*pe_s.at(f"next{k - 2}"))
                nc.scalar.activation(sq[:, k % 2], y[:, k], ACT.Square).then_inc(*act_s.did(f"next{k}"))
            act.wait_ge(*pe_s.at(f"next{KD - 1}"))
            mean_square(1, ("next_ln", "next_root"))
            for k in range(KD):
                act.wait_ge(*dve_s.at(f"u{k}"))
                nc.scalar.copy(x_hi[:, k], u[:, k % 4]).then_inc(*act_s.did(f"hi{k}"))

        @block.tensor
        def _(pe):
            pe_s.prime(pe)
            for n, (act_name, pe_name) in enumerate((("square", "sum"), ("next", "next"))):
                if n or norm:
                    for k in range(KD):
                        pe.wait_ge(*act_s.at(f"{act_name}{k}"))
                        for part in range(parts):
                            last = nc.tensor.matmul(sums[n][:, part, 0:N], co.ones[:], sq[:, k % 2, part * N:(part + 1) * N],
                                                    start=k == 0, stop=k == KD - 1)
                        last.then_inc(*pe_s.did(f"{pe_name}{k}"))

        @block.gpsimd
        def _(pool):
            pool_s.prime(pool)
            for k in range(0, KD, 2):
                pool.wait_ge(*act_s.at(f"hi{k}"))
                nc.gpsimd.tensor_tensor(x_lo[:, k], u[:, k % 4], x_hi[:, k].bitcast(F32), ALU.subtract)\
                  .then_inc(*pool_s.did(f"lo{k}"))

        @block.vector
        def _(dve):
            dve_s.prime(dve)
            V = nc.vector
            if norm:
                dve.wait_ge(*act_s.at("root"))
            for k in range(KD):
                if norm:
                    V.scalar_tensor_tensor(y[:, k], y[:, k], co.par(gain, k), rstd[:, 0], ALU.mult,
                                           ALU.mult).then_inc(*dve_s.did(f"t{k}"))
                    dve.wait_ge(*dve_s.at(f"t{k}"))
                dve.wait_ge(landed[k % 4], 16 * (k // 4 + 1))
                V.tensor_tensor(y[:, k], y[:, k], r[:, k % 4], ALU.add).then_inc(*dve_s.did(f"h{k}"))
            dve.wait_ge(*act_s.at("next_root"))

            def lo(k):
                dve.wait_ge(*act_s.at(f"hi{k}"))
                V.tensor_tensor(x_lo[:, k], u[:, k % 4], x_hi[:, k].bitcast(F32), ALU.subtract).then_inc(*dve_s.did(f"lo{k}"))

            for k in range(KD):
                if k >= 4:
                    lo_done(dve, k - 4)
                V.scalar_tensor_tensor(u[:, k % 4], y[:, k], co.par(next_gain, k), rstd[:, 1], ALU.mult,
                                       ALU.mult).then_inc(*dve_s.did(f"u{k}"))
                if k % 2 == 0 and k:
                    lo(k - 1)
            lo(KD - 1)


HD = 64
NC2 = SEQ // P
PAIRS = 3
RW = PAIRS * P
RWKV_IN = 3 * RW + 2 * P
MLA_IN = 256 + 128 + 32
GDN_AT = RWKV_IN + MLA_IN
P_IN = GDN_AT + 4 * RW + 12
DECAY = float(np.exp(-0.5))
STAGE_TILES = P_IN // P // 4 * 4


def input_projection(co, u_hi, u_lo):
    nc, pr = co.nc, co.pr
    H = SEQ // 2
    w = co.dram["w_in_2"]
    n = STAGE_TILES // 4
    st = pr.stage(n, [(lambda i, j=j: columns(w, (4 * i + j) * P)) for j in range(4)],
                  [chunk_terms(j, u_hi, u_lo, KD, h * H, H) for j in range(4) for h in range(2)])
    rest = [(t * P, min(P, P_IN - t * P)) for t in range(STAGE_TILES, -(-P_IN // P))]

    def rest_terms(j, m, h):
        return (H, [(j, (lambda t, k=k: t[:, k * m:(k + 1) * m]), u_hi[:, k, h * H:(h + 1) * H],
                     u_lo[:, k, h * H:(h + 1) * H]) for k in range(KD)])

    end = pr.stage(1, [(lambda i, at=at, m=m: w.rearrange("(k p) m -> p k m", p=P)[:, :, at:at + m]) for at, m in rest],
                   [rest_terms(j, m, h) for j, (at, m) in enumerate(rest) for h in range(2)])
    with ExitStack() as ctx:
        o = ctx.enter_context(nc.sbuf_tensor("ip_o", [P, 4, SEQ], F32))
        act_s = Steps(nc, ctx, "ip_act", [f"o{j}" for j in range(4)])
        stored = [signal(nc, ctx, f"ip_stored{j}") for j in range(4)]
        block = ctx.enter_context(nc.Block())

        @block.sync
        def _(sp):
            def store(i, j, at, m):
                dest = co.dram["ppT"][ds(at, m), :] if not isinstance(at, int) else co.dram["ppT"][at:at + m, :]
                sp.wait_ge(*act_s.at(f"o{j}", i))
                sp.dma_start(dest, o[0:m, j]).then_inc(stored[j], 16)

            with sp.Fori(0, n) as i:
                for j in range(4):
                    st.load(sp, i, j)
                for j in range(4):
                    store(i, j, (4 * i + j) * P, P)
            for j in range(len(rest)):
                end.load(sp, 0, j)
            for j, (at, m) in enumerate(rest):
                store(n, j, at, m)
            for j in range(4):
                sp.wait_ge(stored[j], 16 + 16 * n + (16 if j < len(rest) else 0))

        @block.gpsimd
        def _(pool):
            with pool.Fori(0, n) as i:
                for j in range(4):
                    st.split(pool, i, j)
            for j in range(len(rest)):
                end.split(pool, 0, j)

        @block.tensor
        def _(pe):
            with pe.Fori(0, n) as i:
                for c in range(8):
                    st.multiply(pe, i, c)
            for c in range(2 * len(rest)):
                end.multiply(pe, 0, c)

        @block.scalar
        def _(act):
            act_s.prime(act)
            for j in range(4):
                act.sem_inc(stored[j], 16)

            def take(s, i, it, j, m):
                act.wait_ge(stored[j], 16 + 16 * it)
                for h in range(2):
                    c = 2 * j + h
                    s.wait_full(act, i, c)
                    ins = nc.scalar.copy(o[0:m, j, h * H:(h + 1) * H], s.bank_of(c, m))
                    if h == 0:
                        ins.then_inc(s.freed(c), 1)
                    else:
                        ins.then_inc(*act_s.did(f"o{j}"))
                        act.wait_ge(*act_s.at(f"o{j}", it))
                        act.sem_inc(s.freed(c), 1)

            with act.Fori(0, n) as i:
                for j in range(4):
                    take(st, i, i, j, P)
            for j, (at, m) in enumerate(rest):
                take(end, 0, n, j, m)


class Masks:

    COUNT = 23

    def __init__(self, co, ctx):
        nc = co.nc
        sb = lambda name, shape, dt=F32: ctx.enter_context(nc.sbuf_tensor(name, shape, dt))
        self.high = sb("mk_high", [P, len(LEVELS), 64], I32)
        self.strict = sb("mk_strict", [P, P], I32)
        self.incl = sb("mk_incl", [P, P], I32)
        self.inclf = sb("mk_inclf", [P, P])
        self.block = sb("mk_block", [P, P])
        self.half = sb("mk_half", [P, P])
        with ExitStack() as c2:
            made = signal(nc, c2, "mk_made")
            block = c2.enter_context(nc.Block())

            @block.gpsimd
            def _(pool):
                n = [0]

                def did(ins):
                    ins.then_inc(made, 1)
                    n[0] += 1
                    pool.wait_ge(made, n[0])

                for m_ in (self.high, self.strict, self.incl):
                    did(nc.gpsimd.memset(m_[:], 1))
                for m_ in (self.inclf, self.block):
                    did(nc.gpsimd.memset(m_[:], 1.0))

                def keep(view, base, pattern, mult):
                    did(nc.gpsimd.affine_select(out=view, in_=view, compare_op=ALU.is_ge, fill=0.0, base=base,
                                                pattern=pattern, channel_multiplier=mult))

                for l, m in enumerate(LEVELS):
                    nb = 64 // m
                    view = self.high[:, l].rearrange("p (b m) -> p b m", m=m)
                    keep(view, 0, [[-2 * m, nb], [0, m]], 1)
                    keep(view, m - 1, [[2 * m, nb], [0, m]], -1)
                keep(self.strict[:], -1, [[1, P]], -1)
                keep(self.incl[:], 0, [[1, P]], -1)
                keep(self.inclf[:], 0, [[1, P]], -1)
                keep(self.block[:, 64:P], -64, [[0, 64]], 1)
                keep(self.block[:, 0:64], 63, [[0, 64]], -1)
                did(nc.gpsimd.tensor_scalar(self.half[:], self.block[:], 1.0 / HD, None, ALU.mult))


def inverse_names():
    last = len(LEVELS) - 1
    pe, act, dve = [], [], ["xt_eye"] + [f"inv_t0{e}" for e in range(2)]
    for l in range(last + 1):
        if l:
            for x in ("y", "z"):
                pe += [f"inv_{x}{l}{e}" for e in range(2)]
            act += [f"inv_y{l}{e}" for e in range(2)]
            dve += [f"inv_t{l}{e}" for e in range(2)]
        if l < last:
            pe += [f"inv_x{l}{e}" for e in range(2)]
            act += [f"inv_x{l}{e}" for e in range(2)]
    return pe, act, dve


class Inverse:

    def __init__(self, co, mk, gT, X, XT, Y, steps):
        self.co, self.mk, self.gT, self.X, self.XT, self.Y = co, mk, gT, X, XT, Y
        self.pe_s, self.act_s, self.dve_s = steps
        self.last = len(LEVELS) - 1

    def bank(self, b):
        return self.co.psum[:, b:b + 2].rearrange("p a (c t) -> p (a c) t", t=P)

    def pe(self, pe, i):
        nc, co = self.co.nc, self.co
        for l in range(self.last + 1):
            if l:
                for e in range(2):
                    pe.wait_ge(*self.act_s.at(f"inv_x{l - 1}{e}", i))
                    for c in range(NC2):
                        q = e * NC2 + c
                        last = nc.tensor.matmul(self.bank(4 * e)[:, c], self.gT[:, q], self.X[:, q], start=True, stop=True)
                    last.then_inc(*self.pe_s.did(f"inv_y{l}{e}"))
                for e in range(2):
                    pe.wait_ge(*self.act_s.at(f"inv_y{l}{e}", i))
                    for c in range(NC2):
                        q = e * NC2 + c
                        last = nc.tensor.matmul(self.bank(4 * e + 2)[:, c], self.Y[:, q], self.XT[:, q], start=True, stop=True)
                    last.then_inc(*self.pe_s.did(f"inv_z{l}{e}"))
            if l < self.last:
                for e in range(2):
                    pe.wait_ge(*self.dve_s.at(f"inv_t{l}{e}", i))
                    for c in range(NC2):
                        last = nc.tensor.transpose(self.bank(4 * e)[:, c], self.XT[:, e * NC2 + c], co.ident[:])
                    last.then_inc(*self.pe_s.did(f"inv_x{l}{e}"))

    def act(self, act, i, other):
        nc = self.co.nc
        for l in range(self.last + 1):
            for x, dst, there in (("y", self.Y, l > 0), ("x", self.X, l < self.last)):
                for e in range(2 if there else 0):
                    act.wait_ge(*self.pe_s.at(f"inv_{x}{l}{e}", i))
                    nc.scalar.copy(dst[:, e * NC2:(e + 1) * NC2], self.bank(4 * e)).then_inc(*self.act_s.did(f"inv_{x}{l}{e}"))
            next(other, None)

    def eye(self, dve, i):
        nc, co = self.co.nc, self.co
        eye = co.ident[:].unsqueeze(1).to_broadcast([P, 2 * NC2, P])
        nc.vector.tensor_copy(self.XT[:], eye).then_inc(*self.dve_s.did("xt_eye"))

    def dve(self, dve, i, other):
        nc, co = self.co.nc, self.co
        for l, m in enumerate(reversed(LEVELS)):
            half = lambda x: x.rearrange("p c (b two m) -> p c b two m", two=2, m=m)[:, :, :, 1]
            mask = self.mk.high[:, self.last - l].rearrange("p (b m) -> p b m", m=m).unsqueeze(1).to_broadcast([P, NC2, 64 // m, m])
            for e in range(2):
                mine = slice(e * NC2, (e + 1) * NC2)
                if l:
                    dve.wait_ge(*self.pe_s.at(f"inv_z{l}{e}", i))
                    dve.wait_ge(*self.dve_s.at(f"inv_t{l - 1}{e}", i))
                    source = self.bank(4 * e + 2)
                else:
                    source = self.gT[:, mine]
                co.pr.carry(dve)
                nc.vector.copy_predicated(half(self.XT[:, mine]), mask, half(source)).then_inc(*self.dve_s.did(f"inv_t{l}{e}"))
            next(other, None)


def rows(x, at, i):
    return x[ds(at + i * P, P), :] if not isinstance(i, int) else x[at + i * P:at + i * P + P, :]


def each_pair(eng, first, body):
    for _ in first(0):
        pass
    with eng.Fori(0, PAIRS - 1) as i:
        body(i, first(i + 1))
    body(PAIRS - 1, iter(()))


def rwkv(co, mk):
    nc = co.nc
    N = SEQ
    ppT = co.dram["ppT"]
    with ExitStack() as ctx:
        sb = lambda name, shape, dt=F32: ctx.enter_context(nc.sbuf_tensor("rw_" + name, shape, dt))
        buf = sb("buf", [P, 3, N + 1])
        z = sb("z", [P, 3, N])
        lora, sg = sb("lora", [P, N]), sb("sg", [P, N])
        lw = sb("lw", [P, 3, P])
        oma = sb("oma", [P, PAIRS])
        w, a, g = sb("w", [P, N]), sb("a", [P, N]), sb("g", [P, N])
        s, kk, bv, bo = sb("s", [P, N]), sb("kk", [P, N]), sb("bv", [P, N]), sb("bo", [P, N])
        d1, ep, em, ex = sb("d1", [P, N]), sb("ep", [P, N]), sb("em", [P, N]), sb("ex", [P, N])
        ar = sb("ar", [P, NC2, 2, P])
        bf, kf = sb("bf", [P, N]), sb("kf", [P, N])
        bp, kp = sb("bp", [P, 2, N]), sb("kp", [P, 2, N])
        vt, bt, kt = sb("vt", [P, NC2, P]), sb("bt", [P, NC2, P]), sb("kt", [P, NC2, P])
        gT, ak, rb, rk = (sb(n, [P, 2 * NC2, P]) for n in ("gT", "ak", "rb", "rk"))
        X, XT, Y = (sb(n, [P, 2 * NC2, P]) for n in ("X", "XT", "Y"))
        H = sb("H", [P, NC2, P])
        rh, sa, ht = sb("rh", [P, P]), sb("sa", [P, NC2, P]), sb("ht", [P, P])
        ratio = sb("ratio", [P, NC2])
        zr, zk, zv = z[:, 0], z[:, 1], z[:, 2]
        ch = lambda x: x.rearrange("p (c t) -> p c t", t=P)
        ps = co.psum
        two = lambda b: ps[:, b:b + 2].rearrange("p a b -> p (a b)")
        par = co.par

        ipe, iact, idve = inverse_names()
        chunkwise = [x for c in range(NC2) for x in ([f"r{c}", f"sa{c}", f"h{c}", f"y{c}"] if c < NC2 - 1 else [f"r{c}", f"sa{c}", f"y{c}"])]
        pe_s = Steps(nc, ctx, "rw_pe", ["lora", "ss", "bonus", "vt", "bt", "kt"] + [f"g{x}{e}" for e in range(2) for x in "bk"]
                     + ipe + chunkwise + ["mean", "var"])
        act_a = Steps(nc, ctx, "rw_act_a", ["sq"])
        act_s = Steps(nc, ctx, "rw_act", ["w", "a", "g", "ln", "root", "ep", "em", "ratio", "ex", "vt", "bt", "kt"] + iact
                      + [x for c in range(NC2) for x in (f"r{c}", f"sa{c}")] + ["y", "ysq", "yln", "yroot"])
        dve_a = Steps(nc, ctx, "rw_dve_a", [f"{x}{n}" for n in range(3) for x in ("sh", "z")] + ["kk"])
        dve_n = [f"s{c}" for c in range(NC2)] + \
            ["ta", "k2", "kkn", "d1", "d2", "rt0", "rt1", "rkr", "bonus", "bv", "bf", "kf", "A", "R", "bo"] + ["xt_eye"] + \
            [f"{x}{e}" for e in range(2) for x in ("gT", "rb", "ak", "rk")] + idve[1:] + \
            [x for c in range(NC2 - 1) for x in (f"ht{c}", f"H{c}")] + ["yc", "yn", "yb", "yo"]
        dve_s = Steps(nc, ctx, "rw_dve", dve_n)
        pool_s = Steps(nc, ctx, "rw_pool", ["bp0", "bp1", "kp0", "kp1"])
        inv = Inverse(co, mk, gT, X, XT, Y, (pe_s, act_s, dve_s))
        in_s = signal(nc, ctx, "rw_in")
        lw_s = signal(nc, ctx, "rw_lw")
        out_s = signal(nc, ctx, "rw_out")
        pre_in = signal(nc, ctx, "rw_pre_in")
        pre_v = signal(nc, ctx, "rw_pre_dve")
        pre_a = signal(nc, ctx, "rw_pre_act")
        zeros = signal(nc, ctx, "rw_zeros")
        ZEROS = 9
        block = ctx.enter_context(nc.Block())

        @block.sync
        def _(sp):
            sp.wait_ge(zeros, 2)
            sp.dma_start(buf[:, 0, 1:N + 1], ppT[3 * RW:3 * RW + P, :]).then_inc(pre_in, 16)
            sp.dma_start(buf[:, 1, 1:N + 1], ppT[3 * RW + P:3 * RW + 2 * P, :]).then_inc(pre_in, 16)
            sp.wait_ge(pre_v, 5)
            def first(i):
                src = [rows(ppT, n * RW, i) for n in range(3)]
                sp.wait_ge(*dve_a.at("z2", i - 1))
                for n in range(3):
                    sp.dma_start(buf[:, n, 1:N + 1], src[n]).then_inc(in_s, 16)
                yield

            def body(i, following):
                cols = ds(i * P, P) if not isinstance(i, int) else slice(i * P, (i + 1) * P)
                w2 = co.dram["rwkv_w2_2"][:, cols]
                sp.wait_ge(*pe_s.at("lora", i - 1))
                co.pr.carry(sp)
                sp.dma_start(lw[0:HD, 0], w2).then_inc(lw_s, 16)
                sp.dma_start(lw[HD:P, 1], co.dram["rwkv_a2_2"][:, cols]).then_inc(lw_s, 16)
                sp.dma_start(lw[:, 2], co.dram["rwkv_g2_2"][:, cols]).then_inc(lw_s, 16)
                for _ in following:
                    pass
                dest = rows(co.dram["yT"], 0, i)
                sp.wait_ge(*dve_s.at("yo", i))
                sp.dma_start(dest, bo[:]).then_inc(out_s, 16)

            each_pair(sp, first, body)
            sp.wait_ge(out_s, 16 + 16 * PAIRS)

        @block.gpsimd
        def _(pool):
            pool_s.prime(pool)
            nc.gpsimd.memset(lw[:], 0.0).then_inc(zeros, 1)
            nc.gpsimd.memset(buf[:, :, 0:1], 0.0).then_inc(zeros, 1)
            for x in (bp, kp, gT, ak, rb, rk):
                nc.gpsimd.memset(x[:], 0.0).then_inc(zeros, 1)
            nc.gpsimd.memset(H[:, 0], 0.0).then_inc(zeros, 1)
            pool.wait_ge(zeros, ZEROS)
            with pool.Fori(0, PAIRS) as i:
                for n, (dst, src, name) in enumerate(((bp, bf, "b"), (kp, kf, "k"))):
                    pool.wait_ge(*dve_s.at(f"{name}f", i))
                    pool.wait_ge(*pe_s.at("gk1", i - 1))
                    for e in range(2):
                        rows = slice(e * HD, (e + 1) * HD)
                        nc.gpsimd.tensor_tensor(dst[rows, e], src[rows], co.zero[rows].to_broadcast([HD, N]),
                                                ALU.add).then_inc(*pool_s.did(f"{name}p{e}"))

        @block.scalar
        def _(act):
            act_a.prime(act)
            act_s.prime(act)
            act.sem_inc(out_s, 16)
            act.wait_ge(pre_v, 2)
            nc.scalar.activation(lora[0:HD], lora[0:HD], ACT.Tanh).then_inc(pre_a, 1)
            act.wait_ge(pre_v, 4)
            nc.scalar.activation(sg[:], sg[:], ACT.Sigmoid).then_inc(pre_a, 1)

            def first(i):
                for _ in range(4):
                    yield
                act.wait_ge(*dve_a.at("kk", i))
                nc.scalar.activation(bf[:], kk[:], ACT.Square).then_inc(*act_a.did("sq"))

            def body(i, following):
                act.wait_ge(*pe_s.at("lora", i))
                act.wait_ge(*dve_s.at("yo", i - 1))
                nc.scalar.activation(w[:], two(0), ACT.Sigmoid, bias=par("rwkv_w0_2", i)).then_inc(*act_s.did("w"))
                nc.scalar.activation(a[:], two(2), ACT.Sigmoid, bias=par("rwkv_a0_2", i)).then_inc(*act_s.did("a"))
                nc.scalar.copy(g[:], two(4)).then_inc(*act_s.did("g"))
                act.wait_ge(*pe_s.at("ss", i))
                nc.scalar.activation(ex[:], two(0), ACT.Ln, bias=co.eps[:]).then_inc(*act_s.did("ln"))
                act.wait_ge(*act_s.at("ln", i))
                nc.scalar.activation(bv[:], ex[:], ACT.Exp, scale=-0.5).then_inc(*act_s.did("root"))
                act.wait_ge(*dve_s.at("rt1", i))
                nc.scalar.activation(ep[:], d1[:], ACT.Exp, scale=DECAY).then_inc(*act_s.did("ep"))
                nc.scalar.activation(em[:], d1[:], ACT.Exp, scale=-DECAY).then_inc(*act_s.did("em"))
                nc.scalar.activation(ratio[:], ratio[:], ACT.Exp, scale=-DECAY).then_inc(*act_s.did("ratio"))
                nc.scalar.activation(ex[:], w[:], ACT.Exp, scale=-DECAY).then_inc(*act_s.did("ex"))
                act.wait_ge(*pe_s.at("vt", i))
                nc.scalar.copy(vt[:], ch(two(0))).then_inc(*act_s.did("vt"))
                act.wait_ge(*pe_s.at("bt", i))
                nc.scalar.copy(bt[:], ch(two(4))).then_inc(*act_s.did("bt"))
                act.wait_ge(*pe_s.at("kt", i))
                nc.scalar.copy(kt[:], ch(two(6))).then_inc(*act_s.did("kt"))
                inv.act(act, i, following)
                for c in range(NC2):
                    act.wait_ge(*pe_s.at(f"r{c}", i))
                    nc.scalar.copy(rh[:], ps[:, 0, 0:P]).then_inc(*act_s.did(f"r{c}"))
                    act.wait_ge(*pe_s.at(f"sa{c}", i))
                    nc.scalar.copy(sa[:, c], ps[:, 1, 0:P]).then_inc(*act_s.did(f"sa{c}"))
                act.wait_ge(*pe_s.at(f"y{NC2 - 1}", i))
                nc.scalar.copy(d1[:], two(4)).then_inc(*act_s.did("y"))
                act.wait_ge(*dve_s.at("yc", i))
                nc.scalar.activation(em[:], d1[:], ACT.Square).then_inc(*act_s.did("ysq"))
                act.wait_ge(*pe_s.at("var", i))
                nc.scalar.activation(ex[:], two(2), ACT.Ln, bias=co.gn_eps[:]).then_inc(*act_s.did("yln"))
                act.wait_ge(*act_s.at("yln", i))
                nc.scalar.activation(ex[:], ex[:], ACT.Exp, scale=-0.5).then_inc(*act_s.did("yroot"))

            each_pair(act, first, body)

        @block.tensor
        def _(pe):
            pe_s.prime(pe)
            pe.wait_ge(pre_a, 2)
            pe.wait_ge(pre_v, 5)
            pe.wait_ge(zeros, ZEROS)
            halves = [slice(0, 512), slice(512, 1024)]

            def wide(bank, lhsT, rhs):
                for h, cols in enumerate(halves):
                    last = nc.tensor.matmul(ps[:, bank + h], lhsT, rhs[:, cols], start=True, stop=True)
                return last

            with pe.Fori(0, PAIRS) as i:
                pe.wait_ge(lw_s, 48 * i + 48)
                pe.wait_ge(*act_s.at("yln", i - 1))
                wide(0, lw[:, 0], lora)
                wide(2, lw[:, 1], lora)
                wide(4, lw[:, 2], sg).then_inc(*pe_s.did("lora"))
                pe.wait_ge(*act_a.at("sq", i))
                pe.wait_ge(*act_s.at("w", i))
                wide(0, mk.block[:], bf).then_inc(*pe_s.did("ss"))
                pe.wait_ge(*dve_s.at("bonus", i))
                wide(2, mk.block[:], bo).then_inc(*pe_s.did("bonus"))
                pe.wait_ge(*dve_a.at("z2", i))
                pe.wait_ge(*act_s.at("ln", i))
                for c in range(NC2):
                    last = nc.tensor.transpose(ch(two(0))[:, c], zv[:, c * P:(c + 1) * P], co.ident[:])
                last.then_inc(*pe_s.did("vt"))
                pe.wait_ge(*dve_s.at("bf", i))
                pe.wait_ge(*act_s.at("g", i))
                for c in range(NC2):
                    last = nc.tensor.transpose(ch(two(4))[:, c], bf[:, c * P:(c + 1) * P], co.ident[:])
                last.then_inc(*pe_s.did("bt"))
                pe.wait_ge(*dve_s.at("kf", i))
                for c in range(NC2):
                    last = nc.tensor.transpose(ch(two(6))[:, c], kf[:, c * P:(c + 1) * P], co.ident[:])
                last.then_inc(*pe_s.did("kt"))
                pe.wait_ge(*dve_s.at("bo", i))
                pe.wait_ge(*act_s.at("kt", i))
                pe.wait_ge(*pool_s.at("kp1", i))
                for e in range(2):
                    for n, (src, x, last_read) in enumerate(((bp, "b", "rb"), (kp, "k", "rk"))):
                        if e:
                            pe.wait_ge(*dve_s.at(f"{last_read}0", i))
                        for c in range(NC2):
                            last = nc.tensor.matmul(ps[:, 4 * n + c // 2, (c % 2) * 256:(c % 2) * 256 + 256],
                                                    src[:, e, c * P:(c + 1) * P],
                                                    ar[:, c].rearrange("p a t -> p (a t)"), start=True, stop=True)
                        last.then_inc(*pe_s.did(f"g{x}{e}"))
                pe.wait_ge(*dve_s.at("rk1", i))
                inv.pe(pe, i)
                for c in range(NC2):
                    if c == 0:
                        pe.wait_ge(*dve_s.at("inv_t61", i))
                    else:
                        pe.wait_ge(*dve_s.at(f"H{c - 1}", i))
                    nc.tensor.matmul(ps[:, 0, 0:P], ar[:, c, 0], H[:, c], start=True, stop=False)
                    for e in range(2):
                        cols = slice(e * HD, (e + 1) * HD)
                        last = nc.tensor.matmul(ps[:, 0, cols], ak[:, e * NC2 + c], vt[:, c, cols], start=False, stop=e == 1)
                    last.then_inc(*pe_s.did(f"r{c}"))
                    pe.wait_ge(*act_s.at(f"r{c}", i))
                    for e in range(2):
                        cols = slice(e * HD, (e + 1) * HD)
                        last = nc.tensor.matmul(ps[:, 1, cols], XT[:, e * NC2 + c], rh[:, cols], start=True, stop=True)
                    last.then_inc(*pe_s.did(f"sa{c}"))
                    pe.wait_ge(*act_s.at(f"sa{c}", i))
                    if c < NC2 - 1:
                        nc.tensor.matmul(ps[:, 2, 0:P], kt[:, c], vt[:, c], start=True, stop=False)
                        nc.tensor.matmul(ps[:, 2, 0:P], bt[:, c], sa[:, c], start=False, stop=True)\
                          .then_inc(*pe_s.did(f"h{c}"))
                    for e in range(2):
                        cols = slice(e * HD, (e + 1) * HD)
                        out = ch(two(4))[cols, c]
                        nc.tensor.matmul(out, sa[:, c, cols], rb[:, e * NC2 + c], start=True, stop=False)
                        nc.tensor.matmul(out, vt[:, c, cols], rk[:, e * NC2 + c], start=False, stop=False)
                        last = nc.tensor.matmul(out, H[:, c, cols], ar[:, c, 1], start=False, stop=True)
                    last.then_inc(*pe_s.did(f"y{c}"))
                pe.wait_ge(*act_s.at("y", i))
                wide(0, mk.half[:], d1).then_inc(*pe_s.did("mean"))
                pe.wait_ge(*act_s.at("ysq", i))
                wide(2, mk.half[:], em).then_inc(*pe_s.did("var"))

        @block.vector
        def _(dve):
            dve_a.prime(dve)
            dve_s.prime(dve)
            V = nc.vector
            dve.wait_ge(zeros, ZEROS)
            dve.wait_ge(pre_in, 32)
            for n, dst in ((0, lora), (1, sg)):
                V.tensor_tensor(dst[:], buf[:, n, 0:N], buf[:, n, 1:N + 1], ALU.subtract).then_inc(pre_v, 1)
                dve.wait_ge(pre_v, 2 * n + 1)
                V.scalar_tensor_tensor(dst[:], dst[:], par("rwkv_mu_2", 9 + n), buf[:, n, 1:N + 1], ALU.mult,
                                       ALU.add).then_inc(pre_v, 1)
            at = co.pl.at["rwkv_k_a_2"][0]
            V.tensor_scalar(oma[:], co.prm[:, at:at + PAIRS], -1.0, 1.0, ALU.mult, ALU.add).then_inc(pre_v, 1)
            dve.wait_ge(pre_v, 5)

            def first(i):
                def did(name, ins, wait=False):
                    ins.then_inc(*dve_a.did(name))
                    if wait:
                        dve.wait_ge(*dve_a.at(name, i))

                dve.wait_ge(in_s, 48 * i + 48)
                for n in range(3):
                    did(f"sh{n}", V.tensor_tensor(z[:, n], buf[:, n, 0:N], buf[:, n, 1:N + 1], ALU.subtract), True)
                    did(f"z{n}", V.scalar_tensor_tensor(z[:, n], z[:, n], par("rwkv_mu_2", i + 3 * n), buf[:, n, 1:N + 1],
                                                        ALU.mult, ALU.add), n == 1)
                    yield
                did("kk", V.tensor_scalar(kk[:], zk, par("rwkv_k_k_2", i), None, ALU.mult))

            def body(i, following):
                def did(name, ins, wait=False):
                    ins.then_inc(*dve_s.did(name))
                    if wait:
                        dve.wait_ge(*dve_s.at(name, i))

                dve.wait_ge(*act_s.at("w", i))
                for c in range(NC2):
                    did(f"s{c}", V.tensor_tensor_scan(s[:, c * P:(c + 1) * P], co.ones[:], w[:, c * P:(c + 1) * P], 0.0,
                                                      ALU.mult, ALU.add))
                dve.wait_ge(*act_s.at("a", i))
                did("ta", V.tensor_scalar(d1[:], a[:], par("rwkv_k_a_2", i), oma[:, ds(i, 1)] if not isinstance(i, int) else oma[:, i:i + 1],
                                          ALU.mult, ALU.add), True)
                did("k2", V.tensor_tensor(zk, zk, d1[:], ALU.mult), True)
                dve.wait_ge(*act_s.at("root", i))
                did("kkn", V.tensor_tensor(kk[:], kk[:], bv[:], ALU.mult), True)
                sc = ch(s[:])
                did("d1", V.tensor_tensor(ch(d1[:]), sc, sc[:, :, HD - 1:HD].to_broadcast([P, NC2, P]), ALU.subtract), True)
                did("d2", V.tensor_tensor(w[:], d1[:], w[:], ALU.subtract))
                did("rt0", V.tensor_copy(ratio[:], ch(d1[:])[:, :, P - 1]), True)
                did("rt1", V.tensor_tensor(ratio[:, 0:NC2 - 1], ratio[:, 0:NC2 - 1], sc[:, 1:NC2, HD - 1], ALU.add))
                dve.wait_ge(out_s, 16 * i + 16)
                did("rkr", V.tensor_tensor(bo[:], zr, zk, ALU.mult), True)
                did("bonus", V.tensor_scalar(bo[:], bo[:], par("rwkv_r_k_2", i), None, ALU.mult))
                did("bv", V.scalar_tensor_tensor(bv[:], kk[:], -1.0, a[:], ALU.mult, ALU.mult), True)
                dve.wait_ge(*act_s.at("ep", i))
                did("bf", V.tensor_tensor(bf[:], bv[:], ep[:], ALU.mult))
                did("kf", V.tensor_tensor(kf[:], zk, ep[:], ALU.mult))
                dve.wait_ge(*act_s.at("ex", i))
                did("A", V.tensor_tensor(ar[:, :, 0], ch(kk[:]), ch(ex[:]), ALU.mult))
                did("R", V.tensor_tensor(ar[:, :, 1], ch(zr), ch(em[:]), ALU.mult))
                dve.wait_ge(*pe_s.at("bonus", i))
                did("bo", V.tensor_tensor(bo[:], two(2), zv, ALU.mult))
                inv.eye(dve, i)
                for e in range(2):
                    for x, n, half, mask, src in (("gT", 0, 0, mk.strict, gT), ("rb", 0, 1, mk.incl, rb),
                                                  ("ak", 1, 0, mk.strict, ak), ("rk", 1, 1, mk.incl, rk)):
                        if half == 0:
                            dve.wait_ge(*pe_s.at(f"g{'bk'[n]}{e}", i))
                            co.pr.carry(dve)
                        grams = ps[:, 4 * n:4 * n + 4].rearrange("p a b -> p (a b)").rearrange("p (c h t) -> p c h t", h=2, t=P)
                        did(f"{x}{e}", V.copy_predicated(src[:, e * NC2:(e + 1) * NC2],
                                                         mask[:].unsqueeze(1).to_broadcast([P, NC2, P]), grams[:, :, half]))
                dve.wait_ge(*dve_s.at("rk1", i))
                inv.dve(dve, i, following)
                for c in range(NC2 - 1):
                    dve.wait_ge(*pe_s.at(f"h{c}", i))
                    did(f"ht{c}", V.tensor_tensor(ht[:], ps[:, 2, 0:P], H[:, c], ALU.add), True)
                    did(f"H{c}", V.scalar_tensor_tensor(H[:, c + 1], ht[:], ratio[:, c:c + 1], mk.block[:], ALU.mult, ALU.mult), True)
                dve.wait_ge(*pe_s.at("mean", i))
                did("yc", V.tensor_tensor(d1[:], d1[:], two(0), ALU.subtract))
                dve.wait_ge(*act_s.at("yroot", i))
                did("yn", V.scalar_tensor_tensor(d1[:], d1[:], par("rwkv_gn_g_2", i), ex[:], ALU.mult, ALU.mult), True)
                did("yb", V.scalar_tensor_tensor(bo[:], d1[:], par("rwkv_gn_b_2", i), bo[:], ALU.add, ALU.add), True)
                did("yo", V.tensor_tensor(bo[:], bo[:], g[:], ALU.mult))

            each_pair(dve, first, body)


HEADS2 = 2 * PAIRS


def deltanet(co, mk):
    nc = co.nc
    N = SEQ
    ppT = co.dram["ppT"]
    par = co.par
    ps = co.psum
    ch = lambda x: x.rearrange("p (c t) -> p c t", t=P)
    two = lambda b: ps[:, b:b + 2].rearrange("p a b -> p (a b)")
    halves = [slice(0, 512), slice(512, 1024)]
    with ExitStack() as ctx:
        sb = lambda name, shape, dt=F32: ctx.enter_context(nc.sbuf_tensor("gd_" + name, shape, dt))
        gB, bB = sb("gB", [P, PAIRS, N]), sb("bB", [P, PAIRS, N])
        rowsel = sb("rowsel", [P, 2, P])
        delta_gates(co, gB, bB, rowsel)
        buf = sb("buf", [P, 3, N + 3])
        z, sg = sb("z", [P, 3, N]), sb("sg", [P, 3, N])
        gi, ga, y, o = sb("gi", [P, N]), sb("ga", [P, N]), sb("y", [P, N]), sb("o", [P, N])
        gc, eg, kd = sb("gc", [P, N]), sb("eg", [P, N]), sb("kd", [P, N])
        gct, decay = sb("gct", [P, NC2, 2]), sb("decay", [P, NC2])
        ar = sb("ar", [P, NC2, 2, P])
        At, qe, kp = sb("At", [P, N]), sb("qe", [P, N]), sb("kp", [P, 2, N])
        Dm = sb("Dm", [P, 2, N])
        gq = sb("gq", [P, 2 * NC2, 2, P])
        vt, kt = sb("vt", [P, NC2, P]), sb("kt", [P, NC2, P])
        X, XT, Y = (sb(n, [P, 2 * NC2, P]) for n in ("X", "XT", "Y"))
        H, sa = sb("H", [P, NC2, P]), sb("sa", [P, NC2, P])
        rh, ht = sb("rh", [P, P]), sb("ht", [P, P])
        rs, sq = Dm, sg[:, 0:2]
        q, k, v = z[:, 0], z[:, 1], z[:, 2]

        ipe, iact, idve = inverse_names()
        pe_s = Steps(nc, ctx, "gd_pe", ["ss", "row", "gct", "vt", "kt", "g0", "g1"] + ipe
                     + [x for c in range(NC2) for x in ([f"r{c}", f"sa{c}"] + ([f"h{c}"] if c < NC2 - 1 else []) + [f"y{c}"])]
                     + ["mean"])
        act_a = Steps(nc, ctx, "gd_act_a", ["sg", "sq"])
        act_s = Steps(nc, ctx, "gd_act", ["ln", "root", "eg", "kd", "decay", "gct", "D", "vt", "kt"] + iact + ["so"]
                      + [f"sa{c}" for c in range(NC2)] + ["y", "ysq", "yln", "yroot"])
        dve_a = Steps(nc, ctx, "gd_dve_a", [f"c{r}{n}" for n in range(3) for r in range(4)]
                      + [f"s{c}" for c in range(NC2)] + ["dkd", "silu"])
        dve_s = Steps(nc, ctx, "gd_dve", ["last", "q", "k", "bk", "v", "kdk", "At", "qe"]
                      + [f"D{e}{c}" for e in range(2) for c in range(NC2)] + ["xt_eye", "gq0", "gq1"] + idve[1:] + ["gate"]
                      + [x for c in range(NC2) for x in ([f"r{c}"] + ([f"ht{c}", f"H{c}"] if c < NC2 - 1 else []))]
                      + ["yn", "yo"])
        pool_s = Steps(nc, ctx, "gd_pool", ["kp0", "kp1", "D"])
        inv = Inverse(co, mk, gq[:, :, 0], X, XT, Y, (pe_s, act_s, dve_s))
        in_s, gate_s, out_s, zeros = (signal(nc, ctx, n) for n in ("gd_in", "gd_gate_in", "gd_out", "gd_zeros"))
        ZEROS = 3
        block = ctx.enter_context(nc.Block())

        @block.sync
        def _(sp):
            def first(i):
                src = [rows(ppT, GDN_AT + n * RW, i) for n in range(3)]
                sp.wait_ge(*dve_a.at("c32", i - 1))
                for n in range(3):
                    sp.dma_start(buf[:, n, 3:N + 3], src[n]).then_inc(in_s, 16)
                yield

            def body(i, following):
                gate = rows(ppT, GDN_AT + 3 * RW, i)
                dest = rows(co.dram["yT"], RW + 4 * HD, i)
                sp.wait_ge(*dve_s.at("gate", i - 1))
                sp.dma_start(gi[:], gate).then_inc(gate_s, 16)
                for _ in following:
                    pass
                sp.wait_ge(*dve_s.at("yo", i))
                sp.dma_start(dest, o[:]).then_inc(out_s, 16)

            each_pair(sp, first, body)
            sp.wait_ge(out_s, 16 + 16 * PAIRS)

        @block.gpsimd
        def _(pool):
            pool_s.prime(pool)
            nc.gpsimd.memset(buf[:, :, 0:3], 0.0).then_inc(zeros, 1)
            nc.gpsimd.memset(kp[:], 0.0).then_inc(zeros, 1)
            nc.gpsimd.memset(H[:, 0], 0.0).then_inc(zeros, 1)
            pool.wait_ge(zeros, ZEROS)
            with pool.Fori(0, PAIRS) as i:
                pool.wait_ge(*pool_s.at("D", i - 1))
                pool.wait_ge(*dve_s.at("k", i))
                pool.wait_ge(*pe_s.at("g1", i - 1))
                for e in range(2):
                    rows = slice(e * HD, (e + 1) * HD)
                    nc.gpsimd.tensor_tensor(kp[rows, e], k[rows], co.zero[rows].to_broadcast([HD, N]),
                                            ALU.add).then_inc(*pool_s.did(f"kp{e}"))
                pool.wait_ge(*pool_s.at("kp1", i))
                pool.wait_ge(*act_s.at("D", i))
                dmv = Dm[:].rearrange("p e (c t) -> p (e c) t", t=P)
                nc.gpsimd.tensor_tensor(dmv, dmv, mk.inclf[:].unsqueeze(1).to_broadcast([P, 2 * NC2, P]),
                                        ALU.mult).then_inc(*pool_s.did("D"))

        @block.scalar
        def _(act):
            act_a.prime(act)
            act_s.prime(act)
            act.sem_inc(out_s, 16)

            def first(i):
                for _ in range(4):
                    yield
                act.wait_ge(*dve_a.at("c32", i))
                nc.scalar.activation(sg[:], z[:], ACT.Sigmoid).then_inc(*act_a.did("sg"))
                yield
                act.wait_ge(*dve_a.at("silu", i))
                nc.scalar.activation(sq, z[:, 0:2], ACT.Square).then_inc(*act_a.did("sq"))

            def body(i, following):
                act.wait_ge(*pe_s.at("ss", i))
                nc.scalar.activation(rs[:].rearrange("p a (b t) -> p (a b) t", b=2), ps[:, 0:4], ACT.Ln,
                                     bias=co.eps[:]).then_inc(*act_s.did("ln"))
                act.wait_ge(*act_s.at("ln", i))
                nc.scalar.activation(rs[:], rs[:], ACT.Exp, scale=-0.5).then_inc(*act_s.did("root"))
                act.wait_ge(*dve_a.at("dkd", i))
                nc.scalar.activation(eg[:], gc[:], ACT.Exp).then_inc(*act_s.did("eg"))
                nc.scalar.activation(kd[:], kd[:], ACT.Exp).then_inc(*act_s.did("kd"))
                act.wait_ge(*dve_s.at("last", i))
                nc.scalar.activation(decay[:], decay[:], ACT.Exp).then_inc(*act_s.did("decay"))
                act.wait_ge(*pe_s.at("gct", i))
                nc.scalar.copy(gct[:], ch(two(4)).rearrange("p c (e k) -> p c e k", e=2)[:, :, :, 0]).then_inc(*act_s.did("gct"))
                act.wait_ge(*dve_s.at(f"D1{NC2 - 1}", i))
                nc.scalar.activation(Dm[:], Dm[:], ACT.Exp).then_inc(*act_s.did("D"))
                act.wait_ge(*pe_s.at("vt", i))
                nc.scalar.copy(vt[:], ch(two(6))).then_inc(*act_s.did("vt"))
                act.wait_ge(*pe_s.at("kt", i))
                nc.scalar.copy(kt[:], ch(two(4))).then_inc(*act_s.did("kt"))
                inv.act(act, i, following)
                act.wait_ge(gate_s, 16 * i + 16)
                act.wait_ge(*dve_s.at("yo", i - 1))
                nc.scalar.activation(ga[:], gi[:], ACT.Sigmoid).then_inc(*act_s.did("so"))
                for c in range(NC2):
                    act.wait_ge(*pe_s.at(f"sa{c}", i))
                    nc.scalar.copy(sa[:, c], ps[:, 1, 0:P]).then_inc(*act_s.did(f"sa{c}"))
                act.wait_ge(*pe_s.at(f"y{NC2 - 1}", i))
                nc.scalar.copy(y[:], two(4)).then_inc(*act_s.did("y"))
                act.wait_ge(*act_s.at("y", i))
                nc.scalar.activation(At[:], y[:], ACT.Square).then_inc(*act_s.did("ysq"))
                act.wait_ge(*pe_s.at("mean", i))
                nc.scalar.activation(At[:], two(0), ACT.Ln, bias=co.eps[:]).then_inc(*act_s.did("yln"))
                act.wait_ge(*act_s.at("yln", i))
                nc.scalar.activation(At[:], At[:], ACT.Exp, scale=-0.5).then_inc(*act_s.did("yroot"))

            each_pair(act, first, body)

        @block.tensor
        def _(pe):
            pe_s.prime(pe)
            pe.wait_ge(zeros, ZEROS)

            def wide(bank, lhsT, rhs):
                for h, cols in enumerate(halves):
                    last = nc.tensor.matmul(ps[:, bank + h], lhsT, rhs[:, cols], start=True, stop=True)
                return last

            with pe.Fori(0, PAIRS) as i:
                pe.wait_ge(*act_s.at("yln", i - 1))
                pe.wait_ge(*act_a.at("sq", i))
                wide(0, mk.block[:], sq[:, 0])
                wide(2, mk.block[:], sq[:, 1]).then_inc(*pe_s.did("ss"))
                pe.wait_ge(*act_s.at("ln", i))
                wide(0, rowsel[:, 0], gc)
                wide(2, rowsel[:, 1], gc).then_inc(*pe_s.did("row"))
                for c in range(NC2):
                    last = nc.tensor.transpose(ch(two(4))[:, c], gc[:, c * P:(c + 1) * P], co.ident[:])
                last.then_inc(*pe_s.did("gct"))
                pe.wait_ge(*dve_s.at("kdk", i))
                for c in range(NC2):
                    last = nc.tensor.transpose(ch(two(6))[:, c], v[:, c * P:(c + 1) * P], co.ident[:])
                last.then_inc(*pe_s.did("vt"))
                pe.wait_ge(*act_s.at("gct", i))
                for c in range(NC2):
                    last = nc.tensor.transpose(ch(two(4))[:, c], kd[:, c * P:(c + 1) * P], co.ident[:])
                last.then_inc(*pe_s.did("kt"))
                pe.wait_ge(*pool_s.at("kp1", i))
                for e in range(2):
                    if e == 0:
                        pe.wait_ge(*dve_s.at(f"D1{NC2 - 1}", i))
                    else:
                        pe.wait_ge(*act_s.at("kt", i))
                    for c in range(NC2):
                        last = nc.tensor.matmul(ps[:, 4 * e + c // 2, (c % 2) * 256:(c % 2) * 256 + 256],
                                                kp[:, e, c * P:(c + 1) * P],
                                                ar[:, c].rearrange("p a t -> p (a t)"), start=True, stop=True)
                    last.then_inc(*pe_s.did(f"g{e}"))
                pe.wait_ge(*dve_s.at("gq1", i))
                inv.pe(pe, i)
                for c in range(NC2):
                    if c == 0:
                        pe.wait_ge(*dve_s.at("inv_t61", i))
                    else:
                        pe.wait_ge(*dve_s.at(f"H{c - 1}", i))
                    nc.tensor.matmul(ps[:, 0, 0:P], At[:, c * P:(c + 1) * P], H[:, c], start=True, stop=True)\
                      .then_inc(*pe_s.did(f"r{c}"))
                    pe.wait_ge(*dve_s.at(f"r{c}", i))
                    for e in range(2):
                        cols = slice(e * HD, (e + 1) * HD)
                        last = nc.tensor.matmul(ps[:, 1, cols], XT[:, e * NC2 + c], rh[:, cols], start=True, stop=True)
                    last.then_inc(*pe_s.did(f"sa{c}"))
                    pe.wait_ge(*act_s.at(f"sa{c}", i))
                    if c < NC2 - 1:
                        nc.tensor.matmul(ps[:, 2, 0:P], kt[:, c], sa[:, c], start=True, stop=True).then_inc(*pe_s.did(f"h{c}"))
                    for e in range(2):
                        cols = slice(e * HD, (e + 1) * HD)
                        out = ch(two(4))[cols, c]
                        nc.tensor.matmul(out, sa[:, c, cols], gq[:, e * NC2 + c, 1], start=True, stop=False)
                        last = nc.tensor.matmul(out, H[:, c, cols], qe[:, c * P:(c + 1) * P], start=False, stop=True)
                    last.then_inc(*pe_s.did(f"y{c}"))
                pe.wait_ge(*act_s.at("ysq", i))
                wide(0, mk.half[:], At).then_inc(*pe_s.did("mean"))

        @block.vector
        def _(dve):
            dve_a.prime(dve)
            dve_s.prime(dve)
            dve.wait_ge(zeros, ZEROS)
            V = nc.vector

            def first(i):
                def did(name, ins, wait=False):
                    ins.then_inc(*dve_a.did(name))
                    if wait:
                        dve.wait_ge(*dve_a.at(name, i))

                dve.wait_ge(in_s, 48 * i + 48)
                for n in range(3):
                    tap = lambda r: par("gdn_conv_w_2", i + (9 * r + 3 * n))
                    did(f"c0{n}", V.tensor_scalar(z[:, n], buf[:, n, 0:N], tap(0), None, ALU.mult), True)
                    for r in range(1, 4):
                        did(f"c{r}{n}", V.scalar_tensor_tensor(z[:, n], buf[:, n, r:N + r], tap(r), z[:, n], ALU.mult, ALU.add),
                            r < 3)
                    yield
                for c in range(NC2):
                    decays = gB[:, ds(i, 1), c * P:(c + 1) * P].rearrange("p o t -> p (o t)") if not isinstance(i, int) \
                        else gB[:, i, c * P:(c + 1) * P]
                    did(f"s{c}", V.tensor_tensor_scan(gc[:, c * P:(c + 1) * P], co.ones[:], decays, 0.0, ALU.mult, ALU.add),
                        c == NC2 - 1)
                did("dkd", V.tensor_tensor(ch(kd[:]), ch(gc[:])[:, :, P - 1:P].to_broadcast([P, NC2, P]), ch(gc[:]), ALU.subtract))
                yield
                dve.wait_ge(*act_a.at("sg", i))
                dve.wait_ge(*dve_a.at("c32", i))
                did("silu", V.tensor_tensor(z[:], z[:], sg[:], ALU.mult))

            def body(i, following):
                def did(name, ins, wait=False):
                    ins.then_inc(*dve_s.did(name))
                    if wait:
                        dve.wait_ge(*dve_s.at(name, i))

                beta = bB[:, ds(i, 1)].rearrange("p o t -> p (o t)") if not isinstance(i, int) else bB[:, i]
                did("last", V.tensor_copy(decay[:], ch(gc[:])[:, :, P - 1]))
                dve.wait_ge(*act_s.at("root", i))
                did("q", V.scalar_tensor_tensor(ar[:, :, 1], ch(q), HD ** -0.5, ch(rs[:, 0]), ALU.mult, ALU.mult))
                did("k", V.tensor_tensor(k, k, rs[:, 1], ALU.mult), True)
                did("bk", V.scalar_tensor_tensor(ar[:, :, 0], ch(k), -1.0, ch(beta), ALU.mult, ALU.mult))
                did("v", V.tensor_tensor(v, v, beta, ALU.mult))
                dve.wait_ge(*act_s.at("kd", i))
                did("kdk", V.tensor_tensor(kd[:], kd[:], k, ALU.mult), True)
                did("At", V.tensor_tensor(ch(At[:]), ar[:, :, 0], ch(eg[:]), ALU.mult))
                did("qe", V.tensor_tensor(ch(qe[:]), ar[:, :, 1], ch(eg[:]), ALU.mult))
                dve.wait_ge(*pe_s.at("row", i))
                dve.wait_ge(*act_s.at("gct", i))
                for e in range(2):
                    for c in range(NC2):
                        did(f"D{e}{c}", V.tensor_scalar(Dm[:, e, c * P:(c + 1) * P], ch(two(2 * e))[:, c], gct[:, c, e:e + 1], 0.0,
                                                        ALU.subtract, ALU.min))
                inv.eye(dve, i)
                dve.wait_ge(*pool_s.at("D", i))
                for e in range(2):
                    dve.wait_ge(*pe_s.at(f"g{e}", i))
                    grams = ps[:, 4 * e:4 * e + 4].rearrange("p a b -> p (a b)").rearrange("p (c h t) -> p c h t", h=2, t=P)
                    did(f"gq{e}", V.tensor_tensor(gq[:, e * NC2:(e + 1) * NC2], grams,
                                                  ch(Dm[:, e]).unsqueeze(2).to_broadcast([P, NC2, 2, P]), ALU.mult))
                dve.wait_ge(*dve_s.at("gq1", i))
                inv.dve(dve, i, following)
                dve.wait_ge(*act_s.at("so", i))
                did("gate", V.tensor_tensor(ga[:], ga[:], gi[:], ALU.mult))
                dve.wait_ge(*act_s.at("vt", i))
                for c in range(NC2):
                    dve.wait_ge(*pe_s.at(f"r{c}", i))
                    did(f"r{c}", V.tensor_tensor(rh[:], ps[:, 0, 0:P], vt[:, c], ALU.add))
                    if c < NC2 - 1:
                        dve.wait_ge(*pe_s.at(f"h{c}", i))
                        did(f"ht{c}", V.scalar_tensor_tensor(ht[:], H[:, c], decay[:, c:c + 1], ps[:, 2, 0:P], ALU.mult, ALU.add), True)
                        did(f"H{c}", V.tensor_tensor(H[:, c + 1], ht[:], mk.block[:], ALU.mult), True)
                dve.wait_ge(*act_s.at("yroot", i))
                did("yn", V.scalar_tensor_tensor(y[:], y[:], par("gdn_o_norm_g_2"), At[:], ALU.mult, ALU.mult), True)
                dve.wait_ge(out_s, 16 * i + 16)
                did("yo", V.tensor_tensor(o[:], y[:], ga[:], ALU.mult))

            each_pair(dve, first, body)


def delta_gates(co, gB, bB, rowsel):
    nc = co.nc
    N = SEQ
    H6 = HEADS2
    ps = co.psum
    with ExitStack() as ctx:
        sb = lambda name, shape, dt=F32: ctx.enter_context(nc.sbuf_tensor("dg_" + name, shape, dt))
        b, a, al, e, u, t, lu = (sb(n, [H6, N]) for n in ("b", "a", "al", "e", "u", "t", "lu"))
        cols = sb("cols", [H6, 2])
        sel = sb("sel", [H6, PAIRS, 2, HD])
        sem = lambda n: signal(nc, ctx, "dg_" + n)
        loaded, sels, act_d, dve_d, pe_d = (sem(n) for n in ("loaded", "sels", "act", "dve", "pe"))
        block = ctx.enter_context(nc.Block())

        @block.sync
        def _(sp):
            at = GDN_AT + 4 * RW
            sp.dma_start(b[:], co.dram["ppT"][at:at + H6, :]).then_inc(loaded, 16)
            sp.dma_start(a[:], co.dram["ppT"][at + H6:at + 2 * H6, :]).then_inc(loaded, 16)
            sp.dma_start(cols[:, 0:1], co.dram["gdn_a_log_2"]).then_inc(loaded, 16)
            sp.dma_start(cols[:, 1:2], co.dram["gdn_dt_bias_2"]).then_inc(loaded, 16)

        @block.gpsimd
        def _(pool):
            nc.gpsimd.memset(sel[:], 0.0).then_inc(sels, 1)
            nc.gpsimd.memset(rowsel[:], 0.0).then_inc(sels, 1)
            pool.wait_ge(sels, 2)
            nc.gpsimd.affine_select(out=sel[:], in_=sel[:], compare_op=ALU.not_equal, fill=1.0, base=0,
                                    pattern=[[-2, PAIRS], [-1, 2], [0, HD]], channel_multiplier=1).then_inc(sels, 1)
            nc.gpsimd.affine_select(out=rowsel[:], in_=rowsel[:], compare_op=ALU.not_equal, fill=1.0, base=0,
                                    pattern=[[-HD, 2], [0, P]], channel_multiplier=1).then_inc(sels, 1)
            pool.wait_ge(sels, 4)

        @block.scalar
        def _(act):
            act.wait_ge(loaded, 64)
            nc.scalar.activation(b[:], b[:], ACT.Sigmoid).then_inc(act_d, 1)
            nc.scalar.activation(cols[:, 0:1], cols[:, 0:1], ACT.Exp).then_inc(act_d, 1)
            act.wait_ge(dve_d, 2)
            nc.scalar.activation(e[:], al[:], ACT.Exp, scale=-1.0).then_inc(act_d, 1)
            act.wait_ge(dve_d, 3)
            nc.scalar.activation(lu[:], u[:], ACT.Ln).then_inc(act_d, 1)
            act.wait_ge(pe_d, 1)
            nc.scalar.copy(gB[:].rearrange("p i (h t) -> p (i h) t", h=2), ps[:, 0:6]).then_inc(act_d, 1)
            act.wait_ge(pe_d, 2)
            nc.scalar.copy(bB[:].rearrange("p i (h t) -> p (i h) t", h=2), ps[:, 0:6]).then_inc(act_d, 1)

        @block.tensor
        def _(pe):
            pe.wait_ge(sels, 4)
            for n, x in enumerate((t, b)):
                if n == 0:
                    pe.wait_ge(dve_d, 9)
                else:
                    pe.wait_ge(act_d, 5)
                for i in range(PAIRS):
                    for h in range(2):
                        last = nc.tensor.matmul(ps[:, 2 * i + h], sel[:, i].rearrange("p e k -> p (e k)"),
                                                x[:, h * 512:(h + 1) * 512], start=True, stop=True)
                last.then_inc(pe_d, 1)

        @block.vector
        def _(dve):
            V = nc.vector
            n = [0]

            def did(ins):
                ins.then_inc(dve_d, 1)
                n[0] += 1
                dve.wait_ge(dve_d, n[0])

            dve.wait_ge(loaded, 64)
            did(V.tensor_scalar(a[:], a[:], cols[:, 1:2], None, ALU.add))
            did(V.scalar_tensor_tensor(al[:], a[:], -1.0, a[:], ALU.mult, ALU.max))
            dve.wait_ge(act_d, 3)
            did(V.tensor_scalar(u[:], e[:], 1.0, None, ALU.add))
            did(V.scalar_tensor_tensor(t[:], u[:], -1.0, e[:], ALU.add, ALU.subtract))
            did(V.reciprocal(al[:], u[:]))
            did(V.tensor_tensor(t[:], t[:], al[:], ALU.mult))
            dve.wait_ge(act_d, 4)
            did(V.tensor_tensor(lu[:], lu[:], t[:], ALU.subtract))
            did(V.scalar_tensor_tensor(t[:], a[:], 0.0, lu[:], ALU.max, ALU.add))
            did(V.tensor_scalar(t[:], t[:], cols[:, 0:1], -1.0, ALU.mult, ALU.mult))


HEADS_A = 4
QK = 96
ROT = 32
HALF_TURN = 3.1415925


def attention(co):
    nc = co.nc
    N = SEQ
    with ExitStack() as ctx:
        sb = lambda name, shape, dt=F32: ctx.enter_context(nc.sbuf_tensor("ml_" + name, shape, dt))
        cq, ckv = sb("cq", [P, 2, N]), sb("ckv", [P, N])
        cs = sb("cs", [P, 2, N])
        rot = sb("rot", [P, P])
        gain = sb("gain", [P, 2])
        vals = sb("vals", [P, NC2, HEADS_A * HD])
        qk = sb("qk", [P, HEADS_A, 2, N])
        latent(co, cq, ckv, cs, rot, gain, vals)
        queries_keys(co, cq, ckv, cs, rot, gain, qk)
        attend(co, qk, vals)


def queries_keys(co, cq, ckv, cs, rot, gain, qk):
    nc = co.nc
    N = SEQ
    ps = co.psum
    two = lambda b: ps[:, b:b + 2].rearrange("p a b -> p (a b)")
    four = lambda b: ps[:, b:b + 4].rearrange("p (a b) t -> p a (b t)", a=2)
    halves = [slice(0, 512), slice(512, 1024)]
    with ExitStack() as ctx:
        sb = lambda name, shape, dt=F32: ctx.enter_context(nc.sbuf_tensor("qk_" + name, shape, dt))
        wq, wk = sb("wq", [P, 2, P]), sb("wk", [P, P])
        raw = sb("raw", [P, 2, N])
        sq = sb("sq", [P, 2, N])
        rs = sb("rs", [P, 2 * NC2])
        dg = sb("dg", [P, 2 * NC2, P])
        x, t = sb("x", [P, 2, N]), sb("t", [P, 2, N])
        pe_p = Steps(nc, ctx, "qk_pe_project", ["q", "k"])
        pe_s = Steps(nc, ctx, "qk_pe", ["ss", "rs", "rot"])
        act_s = Steps(nc, ctx, "qk_act", ["q", "k", "sq", "root"])
        dve_s = Steps(nc, ctx, "qk_dve", ["ms", "recip", "dg", "q", "k", "sin", "cos", "qk"])
        w_s, rope_s, zeros = (signal(nc, ctx, "qk_" + n) for n in ("weights_in", "rope_in", "zeros"))
        ZEROS = 3
        block = ctx.enter_context(nc.Block())

        @block.sync
        def _(sp):
            at = RWKV_IN + 2 * P + P
            sp.wait_ge(zeros, ZEROS)
            sp.dma_start(raw[HD:QK, 1], co.dram["ppT"][at:at + ROT, :]).then_inc(rope_s, 16)
            with sp.Fori(0, HEADS_A) as i:
                src_q = co.dram["mla_w_uq_2"].rearrange("(k p) m -> p k m", p=P)[:, :, ds(i * QK, QK)]
                src_k = co.dram["mla_w_ukv_2"][:, ds(i * 2 * HD, HD)]
                sp.wait_ge(*pe_p.at("k", i - 1))
                sp.dma_start(wq[:, :, 0:QK], src_q).then_inc(w_s, 16)
                sp.dma_start(wk[:, 0:HD], src_k).then_inc(w_s, 16)

        @block.gpsimd
        def _(pool):
            for part in (wq, wk, raw):
                nc.gpsimd.memset(part[:], 0.0).then_inc(zeros, 1)

        @block.scalar
        def _(act):
            act_s.prime(act)
            act.wait_ge(zeros, ZEROS)
            act.wait_ge(rope_s, 16)
            with act.Fori(0, HEADS_A) as i:
                act.wait_ge(*dve_s.at("k", i - 1))
                act.wait_ge(*pe_p.at("q", i))
                nc.scalar.copy(raw[:, 0], two(0)).then_inc(*act_s.did("q"))
                act.wait_ge(*pe_p.at("k", i))
                nc.scalar.copy(raw[0:HD, 1], two(2)[0:HD]).then_inc(*act_s.did("k"))
                act.wait_ge(*act_s.at("k", i))
                nc.scalar.activation(sq[:], raw[:], ACT.Square).then_inc(*act_s.did("sq"))
                act.wait_ge(*dve_s.at("recip", i))
                nc.scalar.activation(rs[:], rs[:], ACT.Sqrt).then_inc(*act_s.did("root"))

        @block.tensor
        def _(pe):
            pe_p.prime(pe)
            pe_s.prime(pe)

            def wide(bank, lhsT, rhs, start=True, stop=True):
                for h, cols in enumerate(halves):
                    last = nc.tensor.matmul(ps[:, bank + h], lhsT, rhs[:, cols], start=start, stop=stop)
                return last

            with pe.Fori(0, HEADS_A) as i:
                pe.wait_ge(w_s, 32 * i + 32)
                pe.wait_ge(*act_s.at("k", i - 1))
                wide(0, wq[:, 0], cq[:, 0], stop=False)
                wide(0, wq[:, 1], cq[:, 1], start=False).then_inc(*pe_p.did("q"))
                wide(2, wk[:], ckv).then_inc(*pe_p.did("k"))
                pe.wait_ge(*act_s.at("sq", i))
                pe.wait_ge(*dve_s.at("sin", i - 1))
                for n in range(2):
                    for c in range(NC2):
                        at = n * NC2 + c
                        last = nc.tensor.matmul(ps[:, 4, at:at + 1], sq[:, n, c * P:(c + 1) * P], co.ones[:, 0:1], start=True, stop=True)
                last.then_inc(*pe_s.did("ss"))
                pe.wait_ge(*dve_s.at("dg", i))
                for b in range(4):
                    last = nc.tensor.matmul(ps[:, 4 + b], co.ones[:], dg[:, 4 * b:4 * b + 4].rearrange("p c t -> p (c t)"),
                                            start=True, stop=True)
                last.then_inc(*pe_s.did("rs"))
                pe.wait_ge(*dve_s.at("k", i))
                wide(4, rot[:], x[:, 0])
                wide(6, rot[:], x[:, 1]).then_inc(*pe_s.did("rot"))

        @block.vector
        def _(dve):
            dve_s.prime(dve)
            V = nc.vector
            both = lambda n: cs[:, n].unsqueeze(1).to_broadcast([P, 2, N])
            with dve.Fori(0, HEADS_A) as i:
                dve.wait_ge(*pe_s.at("ss", i))
                V.tensor_scalar(rs[:], ps[:, 4, 0:2 * NC2], 1.0 / QK, EPS, ALU.mult, ALU.add).then_inc(*dve_s.did("ms"))
                dve.wait_ge(*dve_s.at("ms", i))
                V.reciprocal(rs[:], rs[:]).then_inc(*dve_s.did("recip"))
                dve.wait_ge(*act_s.at("root", i))
                V.tensor_tensor(dg[:], co.ident[:].unsqueeze(1).to_broadcast([P, 2 * NC2, P]),
                                rs[:].unsqueeze(2).to_broadcast([P, 2 * NC2, P]), ALU.mult).then_inc(*dve_s.did("dg"))
                dve.wait_ge(*pe_s.at("rs", i))
                dve.wait_ge(*dve_s.at("qk", i - 1))
                for n, name in enumerate("qk"):
                    V.scalar_tensor_tensor(x[:, n], raw[:, n], gain[:, n:n + 1], two(4 + 2 * n), ALU.mult,
                                           ALU.mult).then_inc(*dve_s.did(name))
                dve.wait_ge(*pe_s.at("rot", i))
                V.tensor_tensor(t[:], four(4), both(1), ALU.mult).then_inc(*dve_s.did("sin"))
                V.tensor_tensor(x[:], x[:], both(0), ALU.mult).then_inc(*dve_s.did("cos"))
                dve.wait_ge(*dve_s.at("cos", i))
                V.tensor_tensor(qk[:, ds(i, 1)].rearrange("p o a t -> p (o a) t"), x[:], t[:], ALU.add).then_inc(*dve_s.did("qk"))


def attend(co, qk, vals):
    nc = co.nc
    N = SEQ
    ps = co.psum
    ch = lambda x: x.rearrange("p (c t) -> p c t", t=P)
    two = lambda b: ps[:, b:b + 2].rearrange("p a b -> p (a b)")
    SCALE = QK ** -0.5
    B = range(NC2)
    with ExitStack() as ctx:
        sb = lambda name, shape, dt=F32: ctx.enter_context(nc.sbuf_tensor("at_" + name, shape, dt))
        h_qk, vh = sb("h_qk", [P, 2, N]), sb("vh", [P, NC2, HD])
        Pm, PT = sb("Pm", [P, 2, N]), sb("PT", [P, NC2, P])
        mx, nm, sm, ri = (sb(n, [P, NC2]) for n in ("mx", "nm", "sm", "ri"))
        dg = sb("dg", [P, 2, P])
        o = sb("o", [HD, N])
        pe_s = Steps(nc, ctx, "at_pe", ["s0", "s1"] + [x for c in B for x in [f"t{c}"] + ([f"s{c + 2}"] if c + 2 < NC2 else []) + [f"o{c}"]])
        act_s = Steps(nc, ctx, "at_act", ["e0"] + [x for c in B for x in ([f"e{c + 1}"] if c + 1 < NC2 else []) + [f"t{c}"]] + ["o"])
        block_max = lambda c: [f"mask{c}", f"mx{c}", f"nm{c}"]
        dve_s = Steps(nc, ctx, "at_dve", ["h_qk", "vh"] + block_max(0)
                      + [x for c in B for x in [f"ri{c}", f"dg{c}"] + (block_max(c + 1) if c + 1 < NC2 else [])])
        out_s = signal(nc, ctx, "at_out")
        block = ctx.enter_context(nc.Block())

        @block.sync
        def _(sp):
            with sp.Fori(0, HEADS_A) as i:
                dest = co.dram["yT"][ds(RW + i * HD, HD), :]
                sp.wait_ge(*act_s.at("o", i))
                sp.dma_start(dest, o[:]).then_inc(out_s, 16)
            sp.wait_ge(out_s, 16 + 16 * HEADS_A)

        @block.scalar
        def _(act):
            act_s.prime(act)
            act.sem_inc(out_s, 16)
            with act.Fori(0, HEADS_A) as i:
                def exponential(c):
                    L = (c + 1) * P
                    act.wait_ge(*dve_s.at(f"nm{c}", i))
                    if c >= 2:
                        act.wait_ge(*pe_s.at(f"t{c - 2}", i))
                    nc.scalar.activation(Pm[:, c % 2, 0:L], two(2 * (c % 2))[:, 0:L], ACT.Exp, bias=nm[:, c:c + 1],
                                         scale=SCALE, accum_out=sm[:, c:c + 1]).then_inc(*act_s.did(f"e{c}"))

                exponential(0)
                for c in B:
                    if c + 1 < NC2:
                        exponential(c + 1)
                    act.wait_ge(*pe_s.at(f"t{c}", i))
                    nc.scalar.copy(PT[:, 0:c + 1], ch(two(4))[:, 0:c + 1]).then_inc(*act_s.did(f"t{c}"))
                act.wait_ge(out_s, 16 * i + 16)
                act.wait_ge(*pe_s.at(f"o{NC2 - 1}", i))
                nc.scalar.copy(o[:], two(6)[0:HD]).then_inc(*act_s.did("o"))

        @block.tensor
        def _(pe):
            pe_s.prime(pe)
            with pe.Fori(0, HEADS_A) as i:
                def scores(c):
                    L = (c + 1) * P
                    if c >= 2:
                        pe.wait_ge(*act_s.at(f"e{c - 2}", i))
                    for h in range(-(-L // 512)):
                        cols = slice(h * 512, min(L, (h + 1) * 512))
                        last = nc.tensor.matmul(two(2 * (c % 2))[:, cols], h_qk[:, 0, c * P:L], h_qk[:, 1, cols], start=True, stop=True)
                    last.then_inc(*pe_s.did(f"s{c}"))

                pe.wait_ge(*dve_s.at("h_qk", i))
                pe.wait_ge(*act_s.at(f"e{NC2 - 1}", i - 1))
                scores(0)
                scores(1)
                pe.wait_ge(*dve_s.at("vh", i))
                pe.wait_ge(*act_s.at("o", i - 1))
                for c in B:
                    pe.wait_ge(*dve_s.at(f"dg{c}", i))
                    if c:
                        pe.wait_ge(*act_s.at(f"t{c - 1}", i))
                    for k in range(c + 1):
                        last = nc.tensor.matmul(ch(two(4))[:, k], Pm[:, c % 2, k * P:(k + 1) * P], dg[:, c % 2], start=True, stop=True)
                    last.then_inc(*pe_s.did(f"t{c}"))
                    if c + 2 < NC2:
                        scores(c + 2)
                    pe.wait_ge(*act_s.at(f"t{c}", i))
                    for k in range(c + 1):
                        last = nc.tensor.matmul(ch(two(6))[0:HD, c], vh[:, k], PT[:, k], start=k == 0, stop=k == c)
                    last.then_inc(*pe_s.did(f"o{c}"))

        @block.vector
        def _(dve):
            dve_s.prime(dve)
            V = nc.vector
            with dve.Fori(0, HEADS_A) as i:
                def did(name, ins, wait=False):
                    ins.then_inc(*dve_s.did(name))
                    if wait:
                        dve.wait_ge(*dve_s.at(name, i))

                def maximum(c):
                    L = (c + 1) * P
                    bank = two(2 * (c % 2))
                    dve.wait_ge(*pe_s.at(f"s{c}", i))
                    did(f"mask{c}", V.memset(bank[0:HD, L - HD:L], -1e30), True)
                    did(f"mx{c}", V.tensor_reduce(mx[:, c:c + 1], bank[:, 0:L], AX_X, ALU.max), True)
                    did(f"nm{c}", V.tensor_scalar(nm[:, c:c + 1], mx[:, c:c + 1], -SCALE, None, ALU.mult))

                dve.wait_ge(*pe_s.at(f"s{NC2 - 1}", i - 1))
                did("h_qk", V.tensor_copy(h_qk[:], qk[:, ds(i, 1)].rearrange("p o a t -> p (o a) t")))
                dve.wait_ge(*pe_s.at(f"o{NC2 - 1}", i - 1))
                did("vh", V.tensor_copy(vh[:], vals[:, :, ds(i * HD, HD)]))
                maximum(0)
                for c in B:
                    dve.wait_ge(*act_s.at(f"e{c}", i))
                    did(f"ri{c}", V.reciprocal(ri[:, c:c + 1], sm[:, c:c + 1]), True)
                    if c >= 2:
                        dve.wait_ge(*pe_s.at(f"t{c - 2}", i))
                    did(f"dg{c}", V.tensor_scalar(dg[:, c % 2], co.ident[:], ri[:, c:c + 1], None, ALU.mult))
                    if c + 1 < NC2:
                        maximum(c + 1)


def latent(co, cq, ckv, cs, rot, gain, vals):
    nc = co.nc
    N = SEQ
    ps, par = co.psum, co.par
    TURN = 2 * np.pi
    C1 = 6.28125
    C2 = 507 / 2.0 ** 18
    C3 = TURN - C1 - C2
    MAGIC = 1.5 * 2.0 ** 23
    with ExitStack() as ctx:
        sb = lambda name, shape, dt=F32: ctx.enter_context(nc.sbuf_tensor("la_" + name, shape, dt))
        sq, rs = sb("sq", [P, 3, N]), sb("rs", [P, 2, N])
        wv = sb("wv", [P, HEADS_A, HD])
        pos, freq = sb("pos", [P, N], I32), sb("freq", [P, 1])
        ang, turns = sb("ang", [P, N]), sb("turns", [P, 2, N])
        sem = lambda n: signal(nc, ctx, "la_" + n)
        in_s, freq_s, pos_s, zero_s, made = (sem(n) for n in ("in", "freq_in", "pos_in", "zero", "made"))
        act_d, dve_d, pe_d = (sem(n) for n in ("act", "dve", "pe"))
        block = ctx.enter_context(nc.Block())

        @block.sync
        def _(sp):
            at = RWKV_IN
            sp.dma_start(cq[:], co.dram["ppT"][at:at + 2 * P, :].rearrange("(k p) t -> p k t", p=P)).then_inc(in_s, 16)
            sp.dma_start(ckv[:], co.dram["ppT"][at + 2 * P:at + 3 * P, :]).then_inc(in_s, 16)
            sp.dma_start(wv[:], co.dram["mla_w_ukv_2"].rearrange("p (h k) -> p h k", k=2 * HD)[:, :, HD:2 * HD]).then_inc(in_s, 16)
            sp.dma_start(pos[:], co.dram["positions"].to_broadcast([P, N])).then_inc(pos_s, 16)
            sp.wait_ge(zero_s, 2)
            sp.dma_start(freq[HD:QK], co.dram["inverse_frequency"]).then_inc(freq_s, 16)
            sp.dma_start(gain[0:QK, 0:1], co.dram["mla_q_qk_g_2"]).then_inc(freq_s, 16)
            sp.dma_start(gain[0:QK, 1:2], co.dram["mla_k_qk_g_2"]).then_inc(freq_s, 16)

        @block.gpsimd
        def _(pool):
            nc.gpsimd.memset(freq[:], 0.0).then_inc(zero_s, 1)
            nc.gpsimd.memset(gain[:], 0.0).then_inc(zero_s, 1)
            nc.gpsimd.memset(rot[:], 0.0).then_inc(made, 1)
            pool.wait_ge(made, 1)
            for at, base, fill in ((HD, -HD - ROT // 2, -1.0), (HD + ROT // 2, -HD, 1.0)):
                view = rot[:, at:at + ROT // 2]
                nc.gpsimd.affine_select(out=view, in_=view, compare_op=ALU.not_equal, fill=fill, base=base,
                                        pattern=[[-1, ROT // 2]], channel_multiplier=1).then_inc(made, 1)
            pool.wait_ge(made, 3)

        @block.scalar
        def _(act):
            act.wait_ge(in_s, 48)
            nc.scalar.activation(sq[:, 0:2], cq[:], ACT.Square).then_inc(act_d, 1)
            nc.scalar.activation(sq[:, 2], ckv[:], ACT.Square).then_inc(act_d, 1)
            act.wait_ge(dve_d, 3)
            nc.scalar.activation(rs[:], rs[:], ACT.Sqrt).then_inc(act_d, 1)
            act.wait_ge(dve_d, 16)
            nc.scalar.activation(cs[:], cs[:], ACT.Sin).then_inc(act_d, 1)
            act.wait_ge(pe_d, 2)
            nc.scalar.copy(vals[:].rearrange("p (b c) m -> p b (c m)", b=4), ps[:, 4:8]).then_inc(act_d, 1)

        @block.tensor
        def _(pe):
            pe.wait_ge(act_d, 2)
            for h in range(2):
                cols = slice(h * 512, (h + 1) * 512)
                nc.tensor.matmul(ps[:, h], co.ones[:], sq[:, 0, cols], start=True, stop=False)
                nc.tensor.matmul(ps[:, h], co.ones[:], sq[:, 1, cols], start=False, stop=True)
                last = nc.tensor.matmul(ps[:, 2 + h], co.ones[:], sq[:, 2, cols], start=True, stop=True)
            last.then_inc(pe_d, 1)
            pe.wait_ge(dve_d, 6)
            for c in range(NC2):
                last = nc.tensor.matmul(ps[:, 4 + c // 2, (c % 2) * 256:(c % 2) * 256 + 256], ckv[:, c * P:(c + 1) * P],
                                        wv[:].rearrange("p h k -> p (h k)"), start=True, stop=True)
            last.then_inc(pe_d, 1)

        @block.vector
        def _(dve):
            V = nc.vector
            n = [0]

            def did(ins):
                ins.then_inc(dve_d, 1)
                n[0] += 1
                dve.wait_ge(dve_d, n[0])

            dve.wait_ge(pe_d, 1)
            did(V.tensor_scalar(rs[:, 0].rearrange("p (b t) -> p b t", b=2), ps[:, 0:2], 0.5 / P, EPS, ALU.mult, ALU.add))
            did(V.tensor_scalar(rs[:, 1].rearrange("p (b t) -> p b t", b=2), ps[:, 2:4], 1.0 / P, EPS, ALU.mult, ALU.add))
            did(V.reciprocal(rs[:], rs[:]))
            dve.wait_ge(act_d, 3)
            for k in range(2):
                did(V.scalar_tensor_tensor(cq[:, k], cq[:, k], par("mla_q_norm_g_2", k), rs[:, 0], ALU.mult, ALU.mult))
            did(V.scalar_tensor_tensor(ckv[:], ckv[:], par("mla_kv_norm_g_2"), rs[:, 1], ALU.mult, ALU.mult))
            dve.wait_ge(pos_s, 16)
            dve.wait_ge(freq_s, 48)
            did(V.tensor_copy(ang[:], pos[:]))
            did(V.tensor_scalar(ang[:], ang[:], freq[:], None, ALU.mult))
            for x in range(2):
                did(V.tensor_scalar(turns[:, x], ang[:], 1 / TURN, (0.25, 0.0)[x], ALU.mult, ALU.add))
            did(V.tensor_scalar(turns[:], turns[:], MAGIC, MAGIC, ALU.add, ALU.subtract))
            src = ang[:].unsqueeze(1).to_broadcast([P, 2, N])
            for part in (C1, C2, C3):
                did(V.scalar_tensor_tensor(cs[:], turns[:], -part, src, ALU.mult, ALU.add))
                src = cs[:]
            did(V.tensor_scalar(cs[:, 0], cs[:, 0], np.pi / 2, None, ALU.add))
            did(V.tensor_scalar(cs[:], cs[:], HALF_TURN, -HALF_TURN, ALU.min, ALU.max))


def build(nc, dram):
    RETIRED.clear()
    with ExitStack() as ctx:
        co = Core(nc, ctx, dram)
        start_up(co)
        block_one(co, dram)
        clear_retired(nc)
        block_two(co, dram)


def block_one(co, dram):
    nc = co.nc
    W = SEQ + TAIL
    with ExitStack() as scope:
        x_hi, x_lo = (scope.enter_context(nc.sbuf_tensor(n, [P, KD, T1], F32R)) for n in ("x_hi", "x_lo"))
        seen_hi, seen_lo = x_hi[:, :, 0:W], x_lo[:, :, 0:W]
        seq_hi, seq_lo = x_hi[:, :, 0:SEQ], x_lo[:, :, 0:SEQ]
        with ExitStack() as mix:
            co.weights(mix)
            norm_split(co, "n1_", dram["h0T"], PAD, META + SEQ, "mix_norm_pre", x_hi, x_lo)
            hgrn_heads(co, x_hi, x_lo)
            a_hi, a_lo, p_hi, p_lo = (mix.enter_context(nc.sbuf_tensor(n, [P, 4, W], F32R))
                                      for n in ("a_hi", "a_lo", "p_hi", "p_lo"))
            pool_branch(co, x_hi, x_lo, p_hi, p_lo, a_hi, a_lo)
            gated_sum(co, a_hi, a_lo, p_hi, p_lo, seen_hi, seen_lo)
        with ExitStack() as out:
            y = out.enter_context(nc.sbuf_tensor("mix_y", [P, KD, W], F32))
            with ExitStack() as w:
                co.weights(w)
                square_product(co, "wo_", dram["w_out"], seen_hi, seen_lo, y, W, 3)
            residual_norm_split(co, "r1_", dram["h0T"][:, META - TAIL:], y, W, "mix_norm_post", dram["h1T"],
                                "ffn_norm_pre", seen_hi, seen_lo)
        with ExitStack() as ffn:
            acc = ffn.enter_context(nc.sbuf_tensor("ffn_acc", [P, KD, SEQ], F32))
            with ExitStack() as w:
                co.weights(w, 6)
                feed_forward(co, "f1_", seen_hi, seen_lo, dram["ffn_w_up"], dram["ffn_w_down"], acc, dram["ffn_w_gate"])
            residual_norm_split(co, "r2_", dram["h1T"][:, TAIL:], acc, SEQ, "ffn_norm_post", dram["h2T"],
                                "ln_mix_g_2", seq_hi, seq_lo)
        with ExitStack() as w:
            co.weights(w)
            input_projection(co, seq_hi, seq_lo)


def block_two(co, dram):
    nc = co.nc
    with ExitStack() as ctx:
        mk = Masks(co, ctx)
        rwkv(co, mk)
        deltanet(co, mk)
    attention(co)
    with ExitStack() as scope:
        x_hi, x_lo = (scope.enter_context(nc.sbuf_tensor(n, [P, KD, SEQ], F32R)) for n in ("y_hi", "y_lo"))
        y = scope.enter_context(nc.sbuf_tensor("sum_y", [P, KD, SEQ], F32))
        with ExitStack() as w:
            co.weights(w)
            split_from_dram(co, "ys_", dram["yT"], KD, SEQ, x_hi, x_lo)
            square_product(co, "wo2_", dram["w_out_2"], x_hi, x_lo, y, SEQ, 2)
        residual_norm_split(co, "r3_", dram["h2T"], y, SEQ, None, dram["h3T"], "ln_ffn_g_2", x_hi, x_lo)
        with ExitStack() as w:
            co.weights(w)
            feed_forward(co, "f2_", x_hi, x_lo, dram["w_ff1_2"], dram["w_ff2_2"], y)
        residual_norm(co, "r4_", dram["h3T"], y, SEQ, None, dram["outT"])


SCRATCH = [("aT", (D // 2, SEQ + TAIL)), ("gateT", (2 * D, SEQ + TAIL)), ("ppT", (P_IN, SEQ)), ("yT", (D, SEQ)), ("h1T", (D, SEQ + TAIL)), ("h2T", (D, SEQ)), ("h3T", (D, SEQ))]


def layout(x):
    out = {}
    for name in ("w_in", "w_branch_hgrn", "w_branch_pool", "w_out", "ffn_w_gate", "ffn_w_up", "ffn_w_down",
                 "w_in_2", "w_out_2", "w_ff1_2", "w_ff2_2", "rwkv_w2_2", "rwkv_a2_2", "rwkv_g2_2",
                 "mla_w_uq_2", "mla_w_ukv_2", "pool_proj"):
        out[name] = np.ascontiguousarray(x[name][0])
    out["h0T"] = np.ascontiguousarray(np.concatenate([x["meta_tokens"], x["x"][0]], axis=0).T)
    vectors = dict(x)
    vectors["gdn_o_norm_g_2"] = np.tile(x["gdn_o_norm_g_2"], (1, 2))
    out["vectors"] = np.ascontiguousarray(np.concatenate(
        [np.reshape(vectors[name], (n, P)) for name, n in PARAM_TILES], axis=0).T)
    for name in ("gdn_a_log_2", "gdn_dt_bias_2", "mla_q_qk_g_2", "mla_k_qk_g_2"):
        out[name] = np.reshape(x[name], (-1, 1))
    half = np.arange(0, ROT, 2) / ROT
    out["inverse_frequency"] = np.tile(10000.0 ** -half, 2).astype(np.float32).reshape(ROT, 1)
    out["positions"] = np.reshape(x["positions_2"], (1, SEQ))
    return out


def kernel(**inputs):
    import concourse.bacc as bacc
    from concourse.bass_utils import run_bass_kernel_spmd

    nc = bacc.Bacc("TRN2", target_bir_lowering=False, num_devices=1)
    arrays = layout({name: np.asarray(value) for name, value in inputs.items()})
    dram = {}
    for name, value in arrays.items():
        dram[name] = nc.dram_tensor(name, value.shape, mybir.dt.from_np(value.dtype), kind="ExternalInput").ap()
    for name, shape in SCRATCH:
        dram[name] = nc.dram_tensor(name, shape, F32, kind="Internal").ap()
    dram["outT"] = nc.dram_tensor("outT", (D, SEQ), F32, kind="ExternalOutput").ap()
    build(nc, dram)
    result = run_bass_kernel_spmd(nc, [arrays], core_ids=[0])
    return np.ascontiguousarray(result.results[0]["outT"].T).reshape(1, SEQ, D)
```

```python
from contextlib import ExitStack

import numpy as np
import concourse.bass as bass
from concourse import mybir

F32 = mybir.dt.float32
F32R = mybir.dt.float32r
I32 = mybir.dt.int32
ALU = mybir.AluOpType
ACT = mybir.ActivationFunctionType
AX_X = mybir.AxisListType.X
P = 128
ds = bass.ds

D = 1024
KD = D // P
SEQ = 1024
META = 16
PAD = P - META
T1 = PAD + META + SEQ
NC1 = T1 // P
TAIL = 2
EPS = 1e-6


RETIRED = []


def signal(nc, ctx, name):
    sem = nc.alloc_semaphore(name)
    ctx.callback(RETIRED.append, sem)
    return sem


def clear_retired(nc):
    nc.clear_and_free_semaphores(list(RETIRED))
    nc.all_engine_barrier()
    RETIRED.clear()


class Products:

    RAW = 2
    PRIME = 64
    UNIT = 1024

    def __init__(self, nc, ctx, slots, banks):
        self.nc, self.slots, self.banks = nc, slots, banks
        sem = lambda name: signal(nc, ctx, name)
        self.landed = [sem(f"weights_landed{r}") for r in range(self.RAW)]
        self.hi_done = sem("weights_hi_done")
        self.ready = sem("weights_ready")
        self.full = sem("psum_full")
        self.carried = sem("waits_carried")
        self.free = [sem(f"psum_free{b}") for b in range(banks)]
        self.units = 0
        self.chunks = 0
        self.ends = []
        self.uses = [0] * banks

    def carry(self, eng):
        eng.sem_inc(self.carried, 1)

    def memory(self, raw, hi, lo, zero, psum):
        self.raw, self.hi, self.lo, self.zero, self.psum = raw, hi, lo, zero, psum

    def stage(self, n, sources, chunks):
        return Stage(self, n, sources, chunks)


class Stage:

    def __init__(self, pr, n, sources, chunks, rows=P):
        self.pr, self.n, self.sources, self.body, self.rows = pr, n, sources, chunks, rows
        U, C = len(sources), len(chunks)
        assert n == 1 or (U % pr.slots == 0 and U % pr.RAW == 0 and C % pr.banks == 0)
        self.U, self.C, self.u0, self.c0 = U, C, pr.units, pr.chunks
        last = [max(c for c in range(C) if any(k[0] == j for k in chunks[c][1])) + 1 for j in range(U)]
        for i in range(n):
            pr.ends += [self.c0 + i * C + e for e in last]
        self.bank = [(self.c0 + c) % pr.banks for c in range(C)]
        self.used, uses = [], list(pr.uses)
        for b in self.bank:
            self.used.append(uses[b])
            uses[b] += 1
        per = [b - a for a, b in zip(pr.uses, uses)]
        self.per = per
        self.early = 0
        pr.uses = [a + n * k for a, k in zip(pr.uses, per)]
        pr.units += n * U
        pr.chunks += n * C

    def _slot_free(self, j):
        e = lambda u: self.pr.ends[u] if u >= 0 else 0
        at = self.u0 + j - self.pr.slots
        v = e(at)
        if self.n > 1:
            v = max(v, e(at + self.U) - self.C)
        return v

    def load(self, sp, i, j):
        pr, u = self.pr, self.u0 + j
        dst = pr.raw[0:self.rows, u % pr.RAW]
        src = self.sources[j](i)
        sp.wait_ge(pr.ready, u + 1 + i * self.U)
        if not isinstance(i, int):
            pr.carry(sp)
        if len(src.shape) == 3:
            dst = dst[:, 0:src.shape[1] * src.shape[2]].rearrange("p (a b) -> p a b", a=src.shape[1])
        else:
            dst = dst[:, 0:src.shape[1]]
        sp.dma_start(dst, src).then_inc(pr.landed[u % pr.RAW], 16)

    def split(self, pool, i, j):
        pr, u = self.pr, self.u0 + j
        r, s, rows = u % pr.RAW, u % pr.slots, self.rows
        width = int(np.prod(self.sources[j](0).shape[1:]))
        pool.wait_ge(pr.full, pr.PRIME + self._slot_free(j) + i * self.C)
        pool.wait_ge(pr.landed[r], 16 * (u // pr.RAW + 1) + i * (16 * self.U // pr.RAW))
        pr.nc.gpsimd.tensor_tensor(pr.hi[0:rows, s, 0:width], pr.raw[0:rows, r, 0:width],
                                   pr.zero[0:rows, 0:1].to_broadcast([rows, width]), ALU.add).then_inc(pr.hi_done, 1)
        pool.wait_ge(pr.hi_done, u + 1 + i * self.U)
        pr.nc.gpsimd.tensor_tensor(pr.lo[0:rows, s, 0:width], pr.raw[0:rows, r, 0:width],
                                   pr.hi[0:rows, s, 0:width].bitcast(F32), ALU.subtract).then_inc(pr.ready, 1)

    def bank_of(self, c, rows=P):
        return self.pr.psum[0:rows, self.bank[c], 0:self.body[c][0]]

    def multiply(self, pe, i, c):
        pr = self.pr
        width, terms = self.body[c]
        b = self.bank[c]
        need = max(t[0] for t in terms)
        pe.wait_ge(pr.ready, pr.RAW + self.u0 + need + 1 + i * self.U)
        pe.wait_ge(pr.free[b], 1 + self.used[c] + i * self.per[b])
        last = None
        for t, (j, pick, xh, xl) in enumerate(terms):
            s = (self.u0 + j) % pr.slots
            wh, wl = pick(pr.hi[:, s]), pick(pr.lo[:, s])
            out = pr.psum[0:wh.shape[-1], b, 0:width]
            end = t == len(terms) - 1
            pr.nc.tensor.matmul(out, wh, xh, start=t == 0, stop=False)
            pr.nc.tensor.matmul(out, wh, xl, start=False, stop=False)
            last = pr.nc.tensor.matmul(out, wl, xh, start=False, stop=end)
        last.then_inc(pr.full, 1)

    def wait_full(self, eng, i, c):
        eng.wait_ge(self.pr.full, self.pr.PRIME + self.c0 + c + 1 + i * self.C)

    def freed(self, c):
        return self.pr.free[self.bank[c]]


class Steps:

    def __init__(self, nc, ctx, name, names):
        self.sem = signal(nc, ctx, name)
        self.names, self.next = list(names), 0
        assert len(set(names)) == len(names)

    def prime(self, eng):
        eng.sem_inc(self.sem, len(self.names))

    def skip(self, eng, names):
        for name in names:
            self.did(name)
        eng.sem_inc(self.sem, len(names))

    def did(self, name):
        assert self.names[self.next] == name, (self.names[self.next], name)
        self.next = (self.next + 1) % len(self.names)
        return self.sem, 1

    def at(self, name, i=0):
        return self.sem, (i + 1) * len(self.names) + self.names.index(name) + 1


def chunks_of(start, total, parts):
    w = total // parts // 2 * 2
    out = [(start + n * w, w) for n in range(parts)]
    out[-1] = (out[-1][0], total - (parts - 1) * w)
    return out


def chunk_terms(unit, xh, xl, kd, off, width, piece=P):
    return (width, [(unit, (lambda t, k=k: t[:, k * piece:k * piece + P]),
                     xh[:, k, off:off + width], xl[:, k, off:off + width]) for k in range(kd)])


def columns(w, at):
    return w.rearrange("(k p) m -> p k m", p=P)[:, :, ds(at, P)]


class Params:

    def __init__(self):
        self.at, self.n = {}, 0

    def add(self, name, n):
        self.at[name] = (self.n, n)
        self.n += n


def param_layout():
    pl = Params()
    for name, n in PARAM_TILES:
        pl.add(name, n)
    return pl


PARAM_TILES = [
    ("mix_norm_pre", 8), ("mix_norm_post", 8), ("hgrn_lower_bounds", 4), ("hgrn_out_norm", 4),
    ("pool_scale", 4), ("ffn_norm_pre", 8), ("ffn_norm_post", 8), ("ffn_conv_w", 66), ("ffn_conv_b", 22),
    ("ln_mix_g_2", 8), ("ln_ffn_g_2", 8), ("rwkv_mu_2", 11), ("rwkv_w0_2", 3), ("rwkv_a0_2", 3),
    ("rwkv_k_k_2", 3), ("rwkv_k_a_2", 3), ("rwkv_r_k_2", 3), ("rwkv_gn_g_2", 3), ("rwkv_gn_b_2", 3),
    ("gdn_conv_w_2", 36), ("gdn_o_norm_g_2", 1), ("mla_q_norm_g_2", 2), ("mla_kv_norm_g_2", 1),
]


class Core:

    def __init__(self, nc, ctx, dram):
        self.nc, self.dram = nc, dram
        sb = lambda name, shape, dt=F32: ctx.enter_context(nc.sbuf_tensor(name, shape, dt))
        self.pl = param_layout()
        self.ident = sb("ident", [P, P])
        self.ones = sb("ones", [P, P])
        self.zero = sb("zero", [P, 1])
        self.eps = sb("eps", [P, 1])
        self.gn_eps = sb("gn_eps", [P, 1])
        self.prm = sb("prm", [P, self.pl.n])
        self.pr = Products(nc, ctx, 4, 2)
        self.psum = ctx.enter_context(nc.psum_tensor("psum", [P, 8, 512], F32))

    def weights(self, ctx, slots=4):
        sb = lambda name, shape, dt=F32: ctx.enter_context(self.nc.sbuf_tensor(f"{name}_{self.pr.units}", shape, dt))
        self.pr.slots = slots
        self.pr.memory(sb("w_raw", [P, 2, 1024]), sb("w_hi", [P, slots, 1024], F32R), sb("w_lo", [P, slots, 1024], F32R),
                       self.zero, self.psum[:, 0:2])

    def par(self, name, k=0):
        at = self.pl.at[name][0]
        if isinstance(k, int):
            return self.prm[:, at + k:at + k + 1]
        return self.prm[:, ds(k + at, 1)]


def start_up(co):
    nc, pr = co.nc, co.pr
    with ExitStack() as ctx:
        loaded = signal(nc, ctx, "vectors_loaded")
        made = signal(nc, ctx, "constants_made")
        block = ctx.enter_context(nc.Block())

        @block.sync
        def _(sp):
            sp.dma_start(co.prm[:], co.dram["vectors"]).then_inc(loaded, 16)
            sp.wait_ge(loaded, 16)

        @block.gpsimd
        def _(pool):
            pool.sem_inc(pr.ready, pr.RAW)
            nc.gpsimd.memset(co.zero[:], 0.0).then_inc(made, 1)
            nc.gpsimd.memset(co.ones[:], 1.0).then_inc(made, 1)
            nc.gpsimd.memset(co.ident[:], 0.0).then_inc(made, 1)
            nc.gpsimd.memset(co.eps[:], EPS).then_inc(made, 1)
            nc.gpsimd.memset(co.gn_eps[:], 64e-5).then_inc(made, 1)
            pool.wait_ge(made, 5)
            nc.gpsimd.affine_select(out=co.ident[:], in_=co.ident[:], compare_op=ALU.not_equal, fill=1.0,
                                    base=0, pattern=[[-1, P]], channel_multiplier=1).then_inc(made, 1)
            pool.wait_ge(made, 6)

        @block.vector
        def _(dve):
            for b in range(pr.banks):
                dve.sem_inc(pr.free[b], 1)

        @block.tensor
        def _(pe):
            pe.sem_inc(pr.full, pr.PRIME)


def norm_split(co, tag, source, pad, total, gain, u_hi, u_lo):
    nc = co.nc
    width = pad + total
    cut = chunks_of(pad, total, -(-total // 512))
    with ExitStack() as ctx:
        sb = lambda name, shape, dt=F32: ctx.enter_context(nc.sbuf_tensor(tag + name, shape, dt))
        h = sb("h", [P, KD, total])
        sq = sb("sq", [P, 2, total])
        rstd = sb("rstd", [P, total])
        u = sb("u", [P, 4, total])
        landed = [signal(nc, ctx, f"{tag}h_landed{k}") for k in range(KD)]
        by_pool = range(0, KD, 2)
        pool_s = Steps(nc, ctx, tag + "pool_steps", [f"lo{k}" for k in by_pool])
        pe_s = Steps(nc, ctx, tag + "pe_steps", [f"sum{k}" for k in range(KD)])
        act_s = Steps(nc, ctx, tag + "act_steps", [f"square{k}" for k in range(KD)]
                      + [f"ln{n}" for n in range(len(cut))] + ["root"] + [f"hi{k}" for k in range(KD)])
        dve_s = Steps(nc, ctx, tag + "dve_steps", [x for k in range(KD) for x in
                                                   ([f"u{k}"] if k % 2 or not k else [f"u{k}", f"lo{k - 1}"])] + [f"lo{KD - 1}"])
        sums = co.psum[:, 2:2 + len(cut)]
        block = ctx.enter_context(nc.Block())

        @block.sync
        def _(sp):
            for k in range(KD):
                sp.dma_start(h[:, k], source[k * P:(k + 1) * P, :]).then_inc(landed[k], 16)
            for k in range(KD):
                sp.wait_ge(landed[k], 16)

        @block.scalar
        def _(act):
            act_s.prime(act)
            for k in range(KD):
                act.wait_ge(landed[k], 16)
                if k >= 2:
                    act.wait_ge(*pe_s.at(f"sum{k - 2}"))
                nc.scalar.activation(sq[:, k % 2], h[:, k], ACT.Square).then_inc(*act_s.did(f"square{k}"))
            act.wait_ge(*pe_s.at(f"sum{KD - 1}"))
            for n, (off, w) in enumerate(cut):
                nc.scalar.activation(rstd[:, off - pad:off - pad + w], sums[:, n, 0:w], ACT.Ln, scale=1.0 / D,
                                     bias=co.eps[:]).then_inc(*act_s.did(f"ln{n}"))
            act.wait_ge(*act_s.at(f"ln{len(cut) - 1}"))
            nc.scalar.activation(rstd[:], rstd[:], ACT.Exp, scale=-0.5).then_inc(*act_s.did("root"))
            for k in range(KD):
                act.wait_ge(*dve_s.at(f"u{k}"))
                nc.scalar.copy(u_hi[:, k, pad:width], u[:, k % 4]).then_inc(*act_s.did(f"hi{k}"))

        @block.tensor
        def _(pe):
            pe_s.prime(pe)
            for k in range(KD):
                pe.wait_ge(*act_s.at(f"square{k}"))
                for n, (off, w) in enumerate(cut):
                    last = nc.tensor.matmul(sums[:, n, 0:w], co.ones[:], sq[:, k % 2, off - pad:off - pad + w],
                                            start=k == 0, stop=k == KD - 1)
                last.then_inc(*pe_s.did(f"sum{k}"))

        @block.vector
        def _(dve):
            if pad:
                nc.vector.memset(u_hi[:, :, 0:pad].bitcast(I32), 0)
                nc.vector.memset(u_lo[:, :, 0:pad].bitcast(I32), 0)
            dve_s.prime(dve)
            dve.wait_ge(*act_s.at("root"))

            def lo(k):
                dve.wait_ge(*act_s.at(f"hi{k}"))
                nc.vector.tensor_tensor(u_lo[:, k, pad:width], u[:, k % 4], u_hi[:, k, pad:width].bitcast(F32),
                                        ALU.subtract).then_inc(*dve_s.did(f"lo{k}"))

            for k in range(KD):
                if k >= 4:
                    dve.wait_ge(*(pool_s if k - 4 in by_pool else dve_s).at(f"lo{k - 4}"))
                nc.vector.scalar_tensor_tensor(u[:, k % 4], h[:, k], co.par(gain, k), rstd[:], ALU.mult,
                                               ALU.mult).then_inc(*dve_s.did(f"u{k}"))
                if k % 2 == 0 and k:
                    lo(k - 1)
            lo(KD - 1)

        @block.gpsimd
        def _(pool):
            pool_s.prime(pool)
            for k in by_pool:
                pool.wait_ge(*act_s.at(f"hi{k}"))
                nc.gpsimd.tensor_tensor(u_lo[:, k, pad:width], u[:, k % 4], u_hi[:, k, pad:width].bitcast(F32),
                                        ALU.subtract).then_inc(*pool_s.did(f"lo{k}"))


LEVELS = [64, 32, 16, 8, 4, 2, 1]


def hgrn_heads(co, u_hi, u_lo):
    nc, pr = co.nc, co.pr
    HEADS = 4
    w_in = co.dram["w_in"]
    sub = HEADS * P
    cut = chunks_of(PAD, META + SEQ, 3)
    C = slice(PAD, T1)
    tail0 = T1 - SEQ - TAIL
    tcut = chunks_of(tail0, SEQ + TAIL, 3)
    sources = [(lambda i, j=j: columns(w_in, i * P + j * sub)) for j in (1, 0, 2, 3)] + \
        [(lambda i, j=j: columns(w_in, 5 * sub + (4 * i + j) * P)) for j in range(4)]
    body = [chunk_terms(j, u_hi, u_lo, KD, off, w) for j in range(4) for off, w in cut] + \
        [chunk_terms(4 + j, u_hi, u_lo, KD, off, w) for j in range(4) for off, w in tcut]
    st = pr.stage(HEADS, sources, body)
    with ExitStack() as ctx:
        sb = lambda name, shape, dt=F32: ctx.enter_context(nc.sbuf_tensor(name, shape, dt))
        q, f, k, vT, g, b = (sb("hg_" + n, [P, T1]) for n in ("q", "f", "k", "vT", "g", "b"))
        E = sb("hg_E", [P, T1])
        ah = sb("hg_ah", [P, SEQ + TAIL])
        logits = sb("hg_logits", [P, SEQ + TAIL])
        G = sb("hg_G", [P, 2, T1])
        qE, kd = sb("hg_qE", [P, T1]), sb("hg_kd", [P, T1])
        V, kdT = sb("hg_V", [P, NC1, P]), sb("hg_kdT", [P, NC1, P])
        pT = sb("hg_pT", [P, NC1, P])
        states = sb("hg_states", [P, NC1, P])
        decay = sb("hg_decay", [P, NC1])
        lb, oml, lbt = sb("hg_lb", [P, HEADS]), sb("hg_oml", [P, HEADS]), sb("hg_lbt", [P, HEADS])
        mask = sb("hg_mask", [P, len(LEVELS), 64], I32)
        maskd = sb("hg_maskd", [P, P], I32)
        big = co.psum[:, 2:5]
        bigf = big.rearrange("p a b -> p (a b)")
        big3 = bigf[:, 0:T1].rearrange("p (c t) -> p c t", t=P)
        gram = co.psum[:, 5:7].rearrange("p a b -> p (a b)")[:, 0:NC1 * 64]
        bc = b[:].rearrange("p (c t) -> p c t", t=P)

        pool_c = signal(nc, ctx, "hg_masks")
        act_n = ["f0", "f1", "f2", "sqrt", "ln", "e_last", "e_kd", "e_q", "V", "kdT", "e1_0", "e2_0", "gate0", "gate1"] + \
            [x for l in range(1, 7) for x in (f"e1_{l}", f"e2_{l}", f"gate{l + 1}")] + \
            ["gate8", "gate9", "o", "square", "gate10", "ln_ms", "root", "gate11"]
        dve_n = ["floor", "max"] + [f"scan{c}" for c in range(NC1)] + ["d_kd", "kmul", "m_kd", "m_qE"]
        for l in range(7):
            dve_n += [f"d{l}", f"gk{l}", f"gq{l}"]
            if l == 0:
                dve_n += [f"st{c}" for c in range(NC1 - 1)]
            if l >= 1:
                dve_n += [f"p{l - 1}"]
        dve_n += ["p6", "pd", "a", "ag"]
        pe_n = ["vT", "kT", "U"] + [f"gram{l}" for l in range(7)] + ["diag", "o", "sum"]
        act_s = Steps(nc, ctx, "hg_act", act_n)
        dve_s = Steps(nc, ctx, "hg_dve", dve_n)
        pe_s = Steps(nc, ctx, "hg_pe", pe_n)
        lbs = signal(nc, ctx, "hg_bounds")
        stored = signal(nc, ctx, "hg_stored")
        gates_out = signal(nc, ctx, "hg_gates_stored")
        block = ctx.enter_context(nc.Block())

        @block.sync
        def _(sp):
            with sp.Fori(0, HEADS) as i:
                for j in range(8):
                    st.load(sp, i, j)
            sp.wait_ge(stored, 16 + 16 * HEADS)
            sp.wait_ge(gates_out, 16 + 16 * 4 * HEADS)

        @block.gpsimd
        def _(pool):
            nc.gpsimd.memset(mask[:], 1).then_inc(pool_c, 1)
            nc.gpsimd.memset(maskd[:], 0).then_inc(pool_c, 1)
            pool.wait_ge(pool_c, 2)
            n = 2
            for l, m in enumerate(LEVELS):
                view = mask[:, l].rearrange("p (b m) -> p b m", m=m)
                nb = 64 // m
                nc.gpsimd.affine_select(out=view, in_=view, compare_op=ALU.is_ge, fill=0.0, base=0,
                                        pattern=[[-2 * m, nb], [0, m]], channel_multiplier=1).then_inc(pool_c, 1)
                n += 1
                pool.wait_ge(pool_c, n)
                nc.gpsimd.affine_select(out=view, in_=view, compare_op=ALU.is_ge, fill=0.0, base=m - 1,
                                        pattern=[[2 * m, nb], [0, m]], channel_multiplier=-1).then_inc(pool_c, 1)
                n += 1
            nc.gpsimd.affine_select(out=maskd[:], in_=maskd[:], compare_op=ALU.not_equal, fill=1.0, base=0,
                                    pattern=[[-1, P]], channel_multiplier=1).then_inc(pool_c, 1)
            n += 1
            for x in (f, k, q, vT):
                nc.gpsimd.memset(x[:, 0:PAD], 0.0).then_inc(pool_c, 1)
                n += 1
            nc.gpsimd.memset(pT[:], 0.0).then_inc(pool_c, 1)
            nc.gpsimd.memset(states[:, 0], 0.0).then_inc(pool_c, 1)
            n += 2
            assert n == 2 + 14 + 1 + 4 + 2
            with pool.Fori(0, HEADS) as i:
                for j in range(8):
                    st.split(pool, i, j)

        CONSTS = 23

        @block.scalar
        def _(act):
            act_s.prime(act)
            act.wait_ge(lbs, 1)
            nc.scalar.activation(lbt[:], lbt[:], ACT.Exp).then_inc(lbs, 1)
            act.wait_ge(pool_c, CONSTS)
            act.sem_inc(gates_out, 16)

            def gate(i, n):
                j, part = divmod(n, 3)
                c = 12 + n
                W3 = (SEQ + TAIL) // 3
                if part == 0:
                    act.wait_ge(gates_out, 16 + 64 * i + 16 * j)
                st.wait_full(act, i, c)
                nc.scalar.copy(logits[:, part * W3:(part + 1) * W3], st.bank_of(c)).then_inc(*act_s.did(f"gate{n}"))
                act.wait_ge(*act_s.at(f"gate{n}", i))
                act.sem_inc(st.freed(c), 1)
                if part == 2:
                    act.dma_start(co.dram["gateT"][ds((4 * i + j) * P, P), :], logits[:]).then_inc(gates_out, 16)

            with act.Fori(0, HEADS) as i:
                for n, (off, w) in enumerate(cut):
                    st.wait_full(act, i, n)
                    nc.scalar.activation(f[:, off:off + w], st.bank_of(n), ACT.Sigmoid).then_inc(*act_s.did(f"f{n}"))
                    nc.scalar.activation(k[:, off:off + w], st.bank_of(n), ACT.Sigmoid,
                                         scale=-1.0).then_inc(st.freed(n), 1)
                for n, (off, w) in enumerate(cut):
                    st.wait_full(act, i, 3 + n)
                    nc.scalar.copy(q[:, off:off + w], st.bank_of(3 + n)).then_inc(st.freed(3 + n), 1)
                act.wait_ge(*dve_s.at("max", i))
                nc.scalar.activation(f[:, C], f[:, C], ACT.Sqrt).then_inc(*act_s.did("sqrt"))
                act.wait_ge(*act_s.at("sqrt", i))
                nc.scalar.activation(f[:, C], f[:, C], ACT.Ln).then_inc(*act_s.did("ln"))
                for n, (off, w) in enumerate(cut):
                    st.wait_full(act, i, 6 + n)
                    nc.scalar.copy(vT[:, off:off + w], st.bank_of(6 + n)).then_inc(st.freed(6 + n), 1)
                act.wait_ge(*dve_s.at("d_kd", i))
                nc.scalar.activation(decay[:], bc[:, :, P - 1], ACT.Exp, scale=2.0).then_inc(*act_s.did("e_last"))
                nc.scalar.activation(kd[:], kd[:], ACT.Exp, scale=2.0).then_inc(*act_s.did("e_kd"))
                nc.scalar.activation(qE[:], b[:], ACT.Exp, scale=2.0).then_inc(*act_s.did("e_q"))
                for n, (off, w) in enumerate(cut):
                    st.wait_full(act, i, 9 + n)
                    nc.scalar.activation(g[:, off:off + w], st.bank_of(9 + n), ACT.Sigmoid).then_inc(st.freed(9 + n), 1)
                act.wait_ge(*pe_s.at("vT", i))
                nc.scalar.copy(V[:], big3).then_inc(*act_s.did("V"))
                act.wait_ge(*pe_s.at("kT", i))
                nc.scalar.copy(kdT[:], big3).then_inc(*act_s.did("kdT"))
                for l, m in enumerate(LEVELS):
                    act.wait_ge(*dve_s.at(f"d{l}", i))
                    Ev = E[:].rearrange("p (b two m) -> p b two m", two=2, m=m)
                    nc.scalar.activation(Ev[:, :, 0], Ev[:, :, 0], ACT.Exp, scale=-2.0).then_inc(*act_s.did(f"e1_{l}"))
                    nc.scalar.activation(Ev[:, :, 1], Ev[:, :, 1], ACT.Exp, scale=2.0).then_inc(*act_s.did(f"e2_{l}"))
                    if l == 0:
                        gate(i, 0)
                    gate(i, l + 1)
                gate(i, 8)
                gate(i, 9)
                act.wait_ge(*pe_s.at("o", i))
                nc.scalar.copy(kd[:, tail0:T1], bigf[:, tail0:T1]).then_inc(*act_s.did("o"))
                act.wait_ge(*act_s.at("o", i))
                nc.scalar.activation(E[:, tail0:T1], kd[:, tail0:T1], ACT.Square).then_inc(*act_s.did("square"))
                gate(i, 10)
                act.wait_ge(*pe_s.at("sum", i))
                nc.scalar.activation(b[:, tail0:T1].rearrange("p (n t) -> p n t", n=3), big[:, :, 0:(SEQ + TAIL) // 3], ACT.Ln,
                                     scale=1.0 / P, bias=co.eps[:]).then_inc(*act_s.did("ln_ms"))
                act.wait_ge(*act_s.at("ln_ms", i))
                nc.scalar.activation(b[:, tail0:T1], b[:, tail0:T1], ACT.Exp, scale=-0.5).then_inc(*act_s.did("root"))
                gate(i, 11)
                act.wait_ge(*dve_s.at("ag", i))
                act.dma_start(co.dram["aT"][ds(i * P, P), :], ah[:]).then_inc(stored, 16)

        @block.tensor
        def _(pe):
            pe_s.prime(pe)
            pe.wait_ge(pool_c, CONSTS)
            with pe.Fori(0, HEADS) as i:
                for c in range(10):
                    st.multiply(pe, i, c)
                for b_ in range(2):
                    c = max(c for c in range(6, 9) if st.bank[c] == b_)
                    pe.wait_ge(st.freed(c), 2 + st.used[c] + i * st.per[b_])
                pe.wait_ge(*act_s.at("root", i - 1))
                for c in range(NC1):
                    last = nc.tensor.transpose(big3[:, c], vT[:, c * P:(c + 1) * P], co.ident[:])
                last.then_inc(*pe_s.did("vT"))
                for c in (10, 11):
                    st.multiply(pe, i, c)
                pe.wait_ge(*dve_s.at("m_kd", i))
                pe.wait_ge(*act_s.at("V", i))
                for c in range(NC1):
                    last = nc.tensor.transpose(big3[:, c], kd[:, c * P:(c + 1) * P], co.ident[:])
                last.then_inc(*pe_s.did("kT"))
                st.multiply(pe, i, 12)
                pe.wait_ge(*act_s.at("kdT", i))
                for c in range(NC1):
                    last = nc.tensor.matmul(big3[:, c], kdT[:, c], V[:, c], start=True, stop=True)
                last.then_inc(*pe_s.did("U"))
                st.multiply(pe, i, 13)
                for l, m in enumerate(LEVELS):
                    pe.wait_ge(*dve_s.at(f"gq{l}", i))
                    if l:
                        pe.wait_ge(*dve_s.at(f"p{l - 1}", i))
                    for c in range(NC1):
                        cols = G[:, l % 2, c * P:(c + 1) * P]
                        rhs = cols.rearrange("p (b two m) -> p b two m", two=2, m=m)[:, :, 1]
                        last = nc.tensor.matmul(gram[:, c * 64:(c + 1) * 64], cols, rhs, start=True, stop=True)
                    last.then_inc(*pe_s.did(f"gram{l}"))
                    st.multiply(pe, i, 14 + l)
                pe.wait_ge(*dve_s.at(f"st{NC1 - 2}", i))
                for c in range(NC1):
                    last = nc.tensor.matmul(big3[:, c], k[:, c * P:(c + 1) * P], q[:, c * P:(c + 1) * P],
                                            start=True, stop=True)
                last.then_inc(*pe_s.did("diag"))
                st.multiply(pe, i, 21)
                pe.wait_ge(*dve_s.at("pd", i))
                for c in range(NC1):
                    nc.tensor.matmul(big3[:, c], V[:, c], pT[:, c], start=True, stop=False)
                    last = nc.tensor.matmul(big3[:, c], states[:, c], qE[:, c * P:(c + 1) * P], start=False, stop=True)
                last.then_inc(*pe_s.did("o"))
                st.multiply(pe, i, 22)
                pe.wait_ge(*act_s.at("square", i))
                for n, (off, w) in enumerate(tcut):
                    last = nc.tensor.matmul(big[:, n, 0:w], co.ones[:], E[:, off:off + w], start=True, stop=True)
                last.then_inc(*pe_s.did("sum"))
                st.multiply(pe, i, 23)

        @block.vector
        def _(dve):
            dve_s.prime(dve)
            dve.sem_inc(stored, 16)
            raw = co.prm[:, co.pl.at["hgrn_lower_bounds"][0]:co.pl.at["hgrn_lower_bounds"][0] + HEADS]
            n = [0]

            def step(ins, add=1):
                ins.then_inc(lbs, 1)
                n[0] += 1
                dve.wait_ge(lbs, n[0] + add)
            nc.vector.tensor_tensor(lbt[:], raw, raw, ALU.subtract).then_inc(lbs, 1)
            n[0] = 1
            dve.wait_ge(lbs, 2)
            step(nc.vector.reciprocal(lb[:], lbt[:]))
            step(nc.vector.tensor_tensor(lb[:], lb[:], lbt[:], ALU.mult))
            step(nc.vector.tensor_tensor(lb[:], lb[:], lb[:], ALU.subtract))
            step(nc.vector.tensor_scalar(lb[:], lb[:], 0.0, 1.0, ALU.max, ALU.min))
            step(nc.vector.tensor_scalar(oml[:], lb[:], -1.0, 1.0, ALU.mult, ALU.add))
            dve.wait_ge(pool_c, CONSTS)
            with dve.Fori(0, HEADS) as i:
                lb_h, oml_h = lb[:, ds(i, 1)], oml[:, ds(i, 1)]
                dve.wait_ge(*act_s.at("f2", i))
                nc.vector.tensor_scalar(f[:, C], f[:, C], oml_h, lb_h, ALU.mult, ALU.add).then_inc(*dve_s.did("floor"))
                dve.wait_ge(*dve_s.at("floor", i))
                nc.vector.tensor_scalar(f[:, C], f[:, C], 1e-30, None, ALU.max).then_inc(*dve_s.did("max"))
                dve.wait_ge(*act_s.at("ln", i))
                for c in range(NC1):
                    nc.vector.tensor_tensor_scan(b[:, c * P:(c + 1) * P], co.ones[:], f[:, c * P:(c + 1) * P], 0.0,
                                                 ALU.mult, ALU.add).then_inc(*dve_s.did(f"scan{c}"))
                dve.wait_ge(*dve_s.at(f"scan{NC1 - 1}", i))
                nc.vector.tensor_tensor(kd[:].rearrange("p (c t) -> p c t", t=P),
                                        bc[:, :, P - 1:P].to_broadcast([P, NC1, P]), bc,
                                        ALU.subtract).then_inc(*dve_s.did("d_kd"))
                nc.vector.tensor_scalar(k[:, C], k[:, C], oml_h, None, ALU.mult).then_inc(*dve_s.did("kmul"))
                dve.wait_ge(*dve_s.at("kmul", i))
                dve.wait_ge(*act_s.at("e_q", i))
                nc.vector.tensor_tensor(kd[:], kd[:], k[:], ALU.mult).then_inc(*dve_s.did("m_kd"))
                nc.vector.tensor_tensor(qE[:], qE[:], q[:], ALU.mult).then_inc(*dve_s.did("m_qE"))

                def score(l):
                    m = LEVELS[l]
                    if l:
                        dve.wait_ge(*dve_s.at(f"p{l - 1}", i))
                    dve.wait_ge(*pe_s.at(f"gram{l}", i))
                    pr.carry(dve)
                    nb = 64 // m
                    out = pT[:].rearrange("p c (b two m) -> p c b two m", two=2, m=m)[:, :, :, 1]
                    src = gram.rearrange("p (c b m) -> p c b m", b=nb, m=m)
                    mk = mask[:, l].rearrange("p (b m) -> p b m", m=m).unsqueeze(1).to_broadcast([P, NC1, nb, m])
                    nc.vector.copy_predicated(out, mk, src).then_inc(*dve_s.did(f"p{l}"))

                for l, m in enumerate(LEVELS):
                    if l:
                        dve.wait_ge(*dve_s.at(f"gq{l - 1}", i))
                    bv = b[:].rearrange("p (n t) -> p n t", t=2 * m)
                    nc.vector.tensor_tensor(E[:].rearrange("p (n t) -> p n t", t=2 * m), bv,
                                            bv[:, :, m - 1:m].to_broadcast([P, T1 // (2 * m), 2 * m]),
                                            ALU.subtract).then_inc(*dve_s.did(f"d{l}"))
                    Ev, kv, qv, Gv = (x.rearrange("p (b two m) -> p b two m", two=2, m=m)
                                      for x in (E[:], k[:], q[:], G[:, l % 2]))
                    if l >= 2:
                        dve.wait_ge(*pe_s.at(f"gram{l - 2}", i))
                    dve.wait_ge(*act_s.at(f"e2_{l}", i))
                    nc.vector.tensor_tensor(Gv[:, :, 0], Ev[:, :, 0], kv[:, :, 0], ALU.mult).then_inc(*dve_s.did(f"gk{l}"))
                    nc.vector.tensor_tensor(Gv[:, :, 1], Ev[:, :, 1], qv[:, :, 1], ALU.mult).then_inc(*dve_s.did(f"gq{l}"))
                    if l == 0:
                        dve.wait_ge(*pe_s.at("U", i))
                        for c in range(NC1 - 1):
                            if c:
                                dve.wait_ge(*dve_s.at(f"st{c - 1}", i))
                            nc.vector.scalar_tensor_tensor(states[:, c + 1], states[:, c], decay[:, c:c + 1],
                                                           big3[:, c], ALU.mult, ALU.add).then_inc(*dve_s.did(f"st{c}"))
                    if l >= 1:
                        score(l - 1)
                score(6)
                dve.wait_ge(*dve_s.at("p6", i))
                dve.wait_ge(*pe_s.at("diag", i))
                pr.carry(dve)
                nc.vector.copy_predicated(pT[:], maskd[:].unsqueeze(1).to_broadcast([P, NC1, P]),
                                          big3).then_inc(*dve_s.did("pd"))
                dve.wait_ge(*act_s.at("root", i))
                nc.vector.scalar_tensor_tensor(kd[:, tail0:T1], kd[:, tail0:T1], co.par("hgrn_out_norm", i),
                                               b[:, tail0:T1], ALU.mult, ALU.mult).then_inc(*dve_s.did("a"))
                dve.wait_ge(*dve_s.at("a", i))
                dve.wait_ge(stored, 16 * i + 16)
                nc.vector.tensor_tensor(ah[:], kd[:, tail0:T1], g[:, tail0:T1], ALU.mult).then_inc(*dve_s.did("ag"))


def pool_branch(co, u_hi, u_lo, p_hi, p_lo, a_hi, a_lo):
    nc, pr = co.nc, co.pr
    W = SEQ + TAIL
    t0 = T1 - W
    cut = chunks_of(PAD, META + SEQ, 3)
    at = 4 * 512
    st = pr.stage(1, [(lambda i, j=j: columns(co.dram["w_in"], at + j * P)) for j in range(4)],
                  [chunk_terms(j, u_hi, u_lo, KD, off, w) for j in range(4) for off, w in cut])
    with ExitStack() as ctx:
        sb = lambda name, shape, dt=F32: ctx.enter_context(nc.sbuf_tensor(name, shape, dt))
        v = sb("pl_v", [P, 2, T1])
        s = sb("pl_s", [P, 2, T1])
        m = sb("pl_m", [P, W])
        y = sb("pl_y", [P, W])
        a = s[:, :, 0:W]
        a_in = [signal(nc, ctx, f"pl_a_in{r}") for r in range(2)]
        proj = sb("pl_proj", [P, 4, P])
        loaded = signal(nc, ctx, "pl_proj_loaded")
        pads = signal(nc, ctx, "pl_pads")
        act_n, dve_n = [f"ahi{k}" for k in range(4)], [f"alo{k}" for k in range(4)]
        for j in range(4):
            act_n += [f"y{j}", f"hi{j}"]
            dve_n += [f"s{j}_{r}" for r in range(j + 1)] + ([f"mean{j}"] if j < 3 else ["mean3", "mean3b"]) + \
                [f"m{j}", f"lo{j}"]
        act_s = Steps(nc, ctx, "pl_act", act_n)
        dve_s = Steps(nc, ctx, "pl_dve", dve_n)
        pe_s = Steps(nc, ctx, "pl_pe", [f"y{j}" for j in range(4)])
        out = co.psum[:, 2:5]
        block = ctx.enter_context(nc.Block())

        @block.sync
        def _(sp):
            for j in range(4):
                st.load(sp, 0, j)
            sp.dma_start(proj[:], co.dram["pool_proj"].rearrange("g c d -> c g d")).then_inc(loaded, 16)

        def load_a(pe, k):
            if k >= 2:
                pe.wait_ge(*dve_s.at(f"alo{k - 2}"))
            pe.dma_start(a[:, k % 2], co.dram["aT"][k * P:(k + 1) * P, :]).then_inc(a_in[k % 2], 16)

        @block.gpsimd
        def _(pool):
            for r in range(2):
                nc.gpsimd.memset(v[:, r, 0:PAD], 0.0).then_inc(pads, 1)
            for j in range(4):
                st.split(pool, 0, j)

        @block.scalar
        def _(act):
            act_s.prime(act)

            for k in range(4):
                load_a(act, k)
                act.wait_ge(a_in[k % 2], 16 * (k // 2 + 1))
                nc.scalar.copy(a_hi[:, k], a[:, k % 2]).then_inc(*act_s.did(f"ahi{k}"))

            def take(j):
                if j >= 2:
                    act.wait_ge(*dve_s.at(f"m{j - 2}"))
                for n, (off, w) in enumerate(cut):
                    st.wait_full(act, 0, 3 * j + n)
                    nc.scalar.copy(v[:, j % 2, off:off + w], st.bank_of(3 * j + n)).then_inc(st.freed(3 * j + n), 1)

            take(0)
            for j in range(4):
                if j < 3:
                    take(j + 1)
                act.wait_ge(*pe_s.at(f"y{j}"))
                if j:
                    act.wait_ge(*dve_s.at(f"lo{j - 1}"))
                nc.scalar.mul(y[:].rearrange("p (a b) -> p a b", a=3), out[:, :, 0:W // 3],
                              co.par("pool_scale", j)).then_inc(*act_s.did(f"y{j}"))
                act.wait_ge(*act_s.at(f"y{j}"))
                nc.scalar.copy(p_hi[:, j], y[:]).then_inc(*act_s.did(f"hi{j}"))

        def project(pe, j):
            pe.wait_ge(loaded, 16)
            pe.wait_ge(*dve_s.at(f"m{j}"))
            if j:
                pe.wait_ge(*act_s.at(f"y{j - 1}"))
            for n in range(3):
                last = nc.tensor.matmul(out[:, n, 0:W // 3], proj[:, j], m[:, n * (W // 3):(n + 1) * (W // 3)],
                                        start=True, stop=True)
            last.then_inc(*pe_s.did(f"y{j}"))

        @block.tensor
        def _(pe):
            pe_s.prime(pe)
            for j in range(4):
                for c in range(3):
                    st.multiply(pe, 0, 3 * j + c)
                if j >= 1:
                    project(pe, j - 1)
            project(pe, 3)

        @block.vector
        def _(dve):
            dve_s.prime(dve)
            for k in range(4):
                dve.wait_ge(*act_s.at(f"ahi{k}"))
                nc.vector.tensor_tensor(a_lo[:, k], a[:, k % 2], a_hi[:, k].bitcast(F32), ALU.subtract).then_inc(*dve_s.did(f"alo{k}"))
            dve.wait_ge(*dve_s.at("alo3"))
            dve.wait_ge(pads, 2)
            for j in range(4):
                st_wait_taken(dve, st, j)
                src = v[:, j % 2]
                for r in range(j + 1):
                    if r:
                        dve.wait_ge(*dve_s.at(f"s{j}_{r - 1}"))
                    step = 1 << r
                    lo = 2 * step - 1
                    nc.vector.tensor_tensor(s[:, r % 2, lo:T1], src[:, lo:T1], src[:, lo - step:T1 - step],
                                            ALU.add).then_inc(*dve_s.did(f"s{j}_{r}"))
                    src = s[:, r % 2]
                window = 2 << j
                dve.wait_ge(*dve_s.at(f"s{j}_{j}"))
                if j:
                    dve.wait_ge(*pe_s.at(f"y{j - 1}"))
                if j < 3:
                    nc.vector.tensor_scalar(m[:], src[:, t0:T1], 1.0 / window, None, ALU.mult).then_inc(*dve_s.did(f"mean{j}"))
                    dve.wait_ge(*dve_s.at(f"mean{j}"))
                else:
                    short = META - TAIL + 1
                    nc.vector.tensor_scalar(m[:, 0:1], src[:, t0:t0 + 1], 1.0 / short, None, ALU.mult).then_inc(*dve_s.did("mean3"))
                    nc.vector.tensor_scalar(m[:, 1:W], src[:, t0 + 1:T1], 1.0 / window, None, ALU.mult).then_inc(*dve_s.did("mean3b"))
                    dve.wait_ge(*dve_s.at("mean3b"))
                nc.vector.tensor_tensor(m[:], m[:], v[:, j % 2, t0:T1], ALU.subtract).then_inc(*dve_s.did(f"m{j}"))
                dve.wait_ge(*act_s.at(f"hi{j}"))
                nc.vector.tensor_tensor(p_lo[:, j], y[:], p_hi[:, j].bitcast(F32),
                                        ALU.subtract).then_inc(*dve_s.did(f"lo{j}"))


def st_wait_taken(eng, st, j):
    for c in range(3 * j, 3 * j + 3):
        eng.wait_ge(st.freed(c), 2 + st.used[c])


def gated_sum(co, a_hi, a_lo, p_hi, p_lo, z_hi, z_lo):
    nc, pr = co.nc, co.pr
    W = SEQ + TAIL
    N = W // 3
    sources = [(lambda i, w=w, h=h: columns(co.dram[w], (2 * i + h) * P)) for h in range(2) for w in ("w_branch_hgrn", "w_branch_pool")]
    body = [chunk_terms(2 * h + x, hi, lo, 4, n * N, N) for h in range(2) for x, (hi, lo) in enumerate(((a_hi, a_lo), (p_hi, p_lo)))
            for n in range(3)]
    st = pr.stage(KD // 2, sources, body)
    with ExitStack() as ctx:
        sb = lambda name, shape, dt=F32: ctx.enter_context(nc.sbuf_tensor(name, shape, dt))
        gate = [sb("gs_a", [P, W]), sb("gs_b", [P, W])]
        z = sb("gs_z", [P, 2, W])
        landed = [signal(nc, ctx, "gs_a_in"), signal(nc, ctx, "gs_b_in")]
        act_s = Steps(nc, ctx, "gs_act", ["a0", "b0", "a1", "b1", "hi0", "hi1"])
        dve_s = Steps(nc, ctx, "gs_dve", [x for h in range(2) for x in [f"za{n}{h}" for n in range(3)]
                                          + [f"zb{n}{h}" for n in range(3)] + [f"z{h}"]] + ["lo0", "lo1"])
        block = ctx.enter_context(nc.Block())

        def tile(x, k):
            return x[:, ds(k, 1), 0:W].rearrange("p o t -> p (o t)")

        def before(name, i, h):
            return dve_s.at(f"{name}0", i) if h else dve_s.at(f"{name}1", i - 1)

        @block.sync
        def _(sp):
            with sp.Fori(0, KD // 2) as i:
                for j in range(4):
                    st.load(sp, i, j)

        @block.gpsimd
        def _(pool):
            with pool.Fori(0, KD // 2) as i:
                for j in range(4):
                    st.split(pool, i, j)

        @block.scalar
        def _(act):
            act_s.prime(act)
            with act.Fori(0, KD // 2) as i:
                for h in range(2):
                    for x, name in enumerate("ab"):
                        src = co.dram["gateT"][ds((2 * i + h) * P + x * D, P), :]
                        act.wait_ge(*before(("za2", "z")[x], i, h))
                        act.dma_start(gate[x][:], src).then_inc(landed[x], 16)
                    for x, name in enumerate("ab"):
                        act.wait_ge(landed[x], 32 * i + 16 * h + 16)
                        nc.scalar.activation(gate[x][:], gate[x][:], ACT.Sigmoid).then_inc(*act_s.did(f"{name}{h}"))
                for h in range(2):
                    act.wait_ge(*dve_s.at(f"z{h}", i))
                    nc.scalar.copy(tile(z_hi, 2 * i + h), z[:, h]).then_inc(*act_s.did(f"hi{h}"))

        @block.tensor
        def _(pe):
            with pe.Fori(0, KD // 2) as i:
                for c in range(12):
                    st.multiply(pe, i, c)

        @block.vector
        def _(dve):
            dve_s.prime(dve)

            def lo(i, h):
                dve.wait_ge(*act_s.at(f"hi{h}", i))
                nc.vector.tensor_tensor(tile(z_lo, 2 * i + h), z[:, h], tile(z_hi, 2 * i + h).bitcast(F32),
                                        ALU.subtract).then_inc(*dve_s.did(f"lo{h}"))

            with dve.Fori(0, KD // 2) as i:
                for h in range(2):
                    dve.wait_ge(*dve_s.at(f"lo{h}", i - 1))
                    for x, name in enumerate("ab"):
                        dve.wait_ge(*act_s.at(f"{name}{h}", i))
                        for n in range(3):
                            cols = slice(n * N, (n + 1) * N)
                            c = 6 * h + 3 * x + n
                            st.wait_full(dve, i, c)
                            out = (z[:, h] if x == 0 else gate[1])[:, cols]
                            nc.vector.tensor_tensor(out, gate[x][:, cols], st.bank_of(c), ALU.mult)\
                              .then_inc(*dve_s.did(f"z{name}{n}{h}"))
                            dve.wait_ge(*dve_s.at(f"z{name}{n}{h}", i))
                            dve.sem_inc(st.freed(c), 1)
                    nc.vector.tensor_tensor(z[:, h], z[:, h], gate[1][:], ALU.add).then_inc(*dve_s.did(f"z{h}"))
                for h in range(2):
                    lo(i, h)


def split_from_dram(co, tag, source, tiles, width, hi, lo):
    nc = co.nc
    with ExitStack() as ctx:
        x = ctx.enter_context(nc.sbuf_tensor(tag + "x", [P, 2, width], F32))
        landed = [signal(nc, ctx, f"{tag}in{r}") for r in range(2)]
        act_s = Steps(nc, ctx, tag + "act", [f"hi{k}" for k in range(len(tiles))])
        dve_s = Steps(nc, ctx, tag + "dve", [f"lo{k}" for k in range(len(tiles))])
        block = ctx.enter_context(nc.Block())

        @block.sync
        def _(sp):
            for k, tile in enumerate(tiles):
                if k >= 2:
                    sp.wait_ge(*dve_s.at(f"lo{k - 2}"))
                sp.dma_start(x[:, k % 2], source[tile * P:(tile + 1) * P, :]).then_inc(landed[k % 2], 16)

        @block.scalar
        def _(act):
            act_s.prime(act)
            for k, tile in enumerate(tiles):
                act.wait_ge(landed[k % 2], 16 * (k // 2 + 1))
                nc.scalar.copy(hi[:, tile], x[:, k % 2]).then_inc(*act_s.did(f"hi{k}"))

        @block.vector
        def _(dve):
            dve_s.prime(dve)
            for k, tile in enumerate(tiles):
                dve.wait_ge(*act_s.at(f"hi{k}"))
                nc.vector.tensor_tensor(lo[:, tile], x[:, k % 2], hi[:, tile].bitcast(F32),
                                        ALU.subtract).then_inc(*dve_s.did(f"lo{k}"))


def square_product(co, w, x_hi, x_lo, y, width, parts):
    nc, pr = co.nc, co.pr
    N = width // parts
    st = pr.stage(1, [(lambda i, j=j: columns(w, j * P)) for j in range(KD)],
                  [chunk_terms(j, x_hi, x_lo, KD, n * N, N) for j in range(KD) for n in range(parts)])
    with ExitStack() as ctx:
        block = ctx.enter_context(nc.Block())

        @block.sync
        def _(sp):
            for j in range(KD):
                st.load(sp, 0, j)

        @block.gpsimd
        def _(pool):
            for j in range(KD):
                st.split(pool, 0, j)

        @block.tensor
        def _(pe):
            for c in range(KD * parts):
                st.multiply(pe, 0, c)

        @block.scalar
        def _(act):
            for c in range(KD * parts):
                j, n = divmod(c, parts)
                st.wait_full(act, 0, c)
                nc.scalar.copy(y[:, j, n * N:(n + 1) * N], st.bank_of(c)).then_inc(st.freed(c), 1)


def hidden_chunks(u_hi, u_lo, gated):
    tail = TAIL if gated else 0
    G = (SEQ + tail) // 3
    H = SEQ // 2
    gate = [chunk_terms(j, u_hi, u_lo, KD, n * G, G) for j in range(2) for n in range(3)] if gated else []

    def up(first):
        return [chunk_terms(first + j, u_hi, u_lo, KD, tail + n * H, H) for j in range(2) for n in range(2)]

    return gate, up


def hidden_sources(w_up, w_gate):
    pair = lambda w: [(lambda i, j=j: columns(w, (2 * i + j) * P)) for j in range(2)]
    return (pair(w_gate) if w_gate is not None else []), pair(w_up)


def feed_forward_first(co, u_hi, u_lo, w_up, w_gate=None):
    gate_src, up_src = hidden_sources(w_up, w_gate)
    gate, up = hidden_chunks(u_hi, u_lo, w_gate is not None)
    return co.pr.stage(1, gate_src + up_src, gate + up(len(gate_src)))


def feed_forward(co, tag, u_hi, u_lo, w_up, w_down, acc, first, w_gate=None, dest=None):
    nc, pr = co.nc, co.pr
    gated = w_gate is not None
    tail = TAIL if gated else 0
    W = SEQ + tail
    G = W // 3
    H = SEQ // 2
    pairs = w_up.shape[1] // (2 * P)
    gate_src, up_src = hidden_sources(w_up, w_gate)
    down_src = [(lambda i, j=j: w_down[ds((2 * i + j) * P, P), :] if not isinstance(i, int)
                 else w_down[(2 * i + j) * P:(2 * i + j + 1) * P, :]) for j in range(2)]
    with ExitStack() as ctx:
        sb = lambda name, shape, dt=F32: ctx.enter_context(nc.sbuf_tensor(tag + name, shape, dt))
        hid = sb("hid", [P, 2, SEQ])
        h_hi, h_lo = sb("h_hi", [P, 2, SEQ], F32R), sb("h_lo", [P, 2, SEQ], F32R)
        if gated:
            gt, cv = sb("gt", [P, 2, W]), sb("cv", [P, 2, SEQ])
        gate, up = hidden_chunks(u_hi, u_lo, gated)

        def down(first):
            return [(H, [(first + j, (lambda t, m=m: t[:, m * P:(m + 1) * P]), h_hi[:, j, n * H:(n + 1) * H],
                          h_lo[:, j, n * H:(n + 1) * H]) for j in range(2)]) for m in range(KD) for n in range(2)]

        ng = len(gate)
        later = lambda src: (lambda i: src(i + 1))
        gates, ups = [later(s) for s in gate_src], [later(s) for s in up_src]
        if gated:
            main = pr.stage(pairs - 1, gates + down_src + ups, gate + down(2) + up(4))
            at_down, at_up = ng, ng + 16
        else:
            main = pr.stage(pairs - 1, ups + down_src, up(0) + down(2))
            at_down, at_up = 4, 0
        last = pr.stage(1, [(lambda i, s=s: s(pairs - 1)) for s in down_src], down(0))

        act_n = [f"gelu{j}" for j in range(2)] + [f"hi{j}" for j in range(2)] if gated else \
            [f"{x}{j}" for x in ("square", "hi") for j in range(2)]
        sums, hiddens = [f"acc{n}" for n in range(16)], [f"h{j}{n}" for j in range(2) for n in range(2)]
        dve_n = ([x for j in range(2) for x in (f"c0{j}", f"c1{j}", f"c2{j}")] + sums + hiddens if gated else hiddens + sums) + \
            [f"lo{j}" for j in range(2)]
        act_s = Steps(nc, ctx, tag + "act", act_n)
        dve_s = Steps(nc, ctx, tag + "dve", dve_n)
        if dest is not None:
            stored = signal(nc, ctx, tag + "stored")
        block = ctx.enter_context(nc.Block())

        def each(eng, body):
            body(first, 0, 0, False)
            with eng.Fori(0, pairs - 1) as i:
                body(main, i, i + 1, True)

        @block.sync
        def _(sp):
            each(sp, lambda st, i, it, steady: [st.load(sp, i, j) for j in range(st.early, st.U)])
            for j in range(2):
                last.load(sp, 0, j)
            if dest is not None:
                for m in range(KD):
                    for c in (2 * m, 2 * m + 1):
                        sp.wait_ge(last.freed(c), 2 + last.used[c])
                    sp.dma_start(dest[m * P:(m + 1) * P, :], acc[:, m]).then_inc(stored, 16)
                sp.wait_ge(stored, 16 * KD)

        @block.gpsimd
        def _(pool):
            each(pool, lambda st, i, it, steady: [st.split(pool, i, j) for j in range(st.early, st.U)])
            for j in range(2):
                last.split(pool, 0, j)

        @block.tensor
        def _(pe):
            def ups(st, i, at):
                for c in range(at, at + 4):
                    st.multiply(pe, i, c)

            def body(st, i, it, steady):
                for c in range(ng):
                    st.multiply(pe, i, c)
                if not steady:
                    ups(st, i, ng)
                    return
                if not gated:
                    ups(st, i, at_up)
                pe.wait_ge(*dve_s.at("lo1", it - 1))
                for c in range(at_down, at_down + 16):
                    st.multiply(pe, i, c)
                if gated:
                    ups(st, i, at_up)

            each(pe, body)
            pe.wait_ge(*dve_s.at("lo1", pairs - 1))
            for c in range(16):
                last.multiply(pe, 0, c)

        @block.scalar
        def _(act):
            act_s.prime(act)

            def body(st, i, it, steady):
                for c in range(ng):
                    j, n = divmod(c, 3)
                    st.wait_full(act, i, c)
                    act.wait_ge(*dve_s.at(f"c2{j}", it - 1))
                    nc.scalar.copy(gt[:, j, n * G:(n + 1) * G], st.bank_of(c)).then_inc(st.freed(c), 1)
                if gated:
                    for j in range(2):
                        act.wait_ge(*dve_s.at(f"c2{j}", it))
                        nc.scalar.activation(cv[:, j], cv[:, j], ACT.Gelu_apprx_tanh).then_inc(*act_s.did(f"gelu{j}"))
                if not gated:
                    for j in range(2):
                        act.wait_ge(*dve_s.at(f"h{j}1", it))
                        nc.scalar.activation(hid[:, j], hid[:, j], ACT.Square).then_inc(*act_s.did(f"square{j}"))
                    act.wait_ge(*act_s.at("square1", it))
                    act.wait_ge(*dve_s.at("acc15", it))
                for j in range(2):
                    if gated:
                        act.wait_ge(*dve_s.at(f"h{j}1", it))
                    nc.scalar.copy(h_hi[:, j], hid[:, j]).then_inc(*act_s.did(f"hi{j}"))

            each(act, body)

        @block.vector
        def _(dve):
            dve_s.prime(dve)
            def add(st, i, it, c0):
                for c in range(16):
                    m, n = divmod(c, 2)
                    st.wait_full(dve, i, c0 + c)
                    part = acc[:, m, n * H:(n + 1) * H]
                    dve.wait_ge(*dve_s.at(f"acc{c}", it - 1))
                    nc.vector.tensor_tensor(part, part, st.bank_of(c0 + c), ALU.add).then_inc(*dve_s.did(f"acc{c}"))
                    free(st, c0 + c, f"acc{c}", it)

            def free(st, c, step, it):
                dve.wait_ge(*dve_s.at(step, it))
                dve.sem_inc(st.freed(c), 1)

            def sum_up(st, i, it, steady):
                if steady:
                    add(st, i, it, at_down)
                elif dest is not None:
                    dve.wait_ge(*dve_s.at("h11", it))
                    dve_s.skip(dve, sums)
                else:
                    for c in range(16):
                        m, n = divmod(c, 2)
                        nc.vector.memset(acc[:, m, n * H:(n + 1) * H], 0.0).then_inc(*dve_s.did(f"acc{c}"))

            def body(st, i, it, steady):
                if gated:
                    for j in range(2):
                        for b in range(2):
                            c = max(c for c in range(3 * j, 3 * j + 3) if st.bank[c] == (st.bank[0] + b) % 2)
                            dve.wait_ge(st.freed(c), 2 + st.used[c] + i * st.per[st.bank[c]])
                        dve.wait_ge(*dve_s.at(f"h{j}1", it - 1))
                        tile = 2 * it + j
                        nc.vector.tensor_scalar(cv[:, j], gt[:, j, 0:SEQ], co.par("ffn_conv_w", tile),
                                                co.par("ffn_conv_b", tile), ALU.mult, ALU.add).then_inc(*dve_s.did(f"c0{j}"))
                        for r in (1, 2):
                            dve.wait_ge(*dve_s.at(f"c{r - 1}{j}", it))
                            nc.vector.scalar_tensor_tensor(cv[:, j], gt[:, j, r:SEQ + r], co.par("ffn_conv_w", tile + 2 * pairs * r),
                                                           cv[:, j], ALU.mult, ALU.add).then_inc(*dve_s.did(f"c{r}{j}"))
                if gated:
                    sum_up(st, i, it, steady)
                at = at_up if steady else ng
                for j in range(2):
                    dve.wait_ge(*dve_s.at(f"lo{j}", it - 1))
                    if gated:
                        dve.wait_ge(*act_s.at(f"gelu{j}", it))
                    for n in range(2):
                        c = at + 2 * j + n
                        st.wait_full(dve, i, c)
                        cols = slice(n * H, (n + 1) * H)
                        if gated:
                            ins = nc.vector.tensor_tensor(hid[:, j, cols], cv[:, j, cols], st.bank_of(c), ALU.mult)
                        else:
                            ins = nc.vector.tensor_scalar(hid[:, j, cols], st.bank_of(c), 0.0, None, ALU.max)
                        ins.then_inc(*dve_s.did(f"h{j}{n}"))
                        free(st, c, f"h{j}{n}", it)
                if not gated:
                    sum_up(st, i, it, steady)
                for j in range(2):
                    dve.wait_ge(*act_s.at(f"hi{j}", it))
                    nc.vector.tensor_tensor(h_lo[:, j], hid[:, j], h_hi[:, j].bitcast(F32),
                                            ALU.subtract).then_inc(*dve_s.did(f"lo{j}"))

            each(dve, body)
            for c in range(16):
                m, n = divmod(c, 2)
                last.wait_full(dve, 0, c)
                part = acc[:, m, n * H:(n + 1) * H]
                nc.vector.tensor_tensor(part, part, last.bank_of(c), ALU.add).then_inc(last.freed(c), 1)


def residual_norm_split(co, tag, res, y, width, gain, dest, next_gain, x_hi, x_lo, following, early):
    nc = co.nc
    parts = -(-width // 512)
    N = width // parts
    norm = gain is not None
    following.early = early
    with ExitStack() as ctx:
        sb = lambda name, shape, dt=F32: ctx.enter_context(nc.sbuf_tensor(tag + name, shape, dt))
        r = sb("r", [P, 2, width])
        sq = sb("sq", [P, 2, width])
        rstd = sb("rstd", [P, 2, width])
        u = sb("u", [P, 4, width])
        landed = [signal(nc, ctx, f"{tag}in{k}") for k in range(2)]
        stored = signal(nc, ctx, f"{tag}out")
        first = [f"{x}{k}" for k in range(KD) for x in (("t", "h") if norm else ("h",))]
        pe_s = Steps(nc, ctx, tag + "pe", ([f"sum{k}" for k in range(KD)] if norm else []) + [f"next{k}" for k in range(KD)])
        act_s = Steps(nc, ctx, tag + "act", ([f"square{k}" for k in range(KD)] + ["ln", "root"] if norm else [])
                      + [f"next{k}" for k in range(KD)] + ["next_ln", "next_root"] + [f"hi{k}" for k in range(KD)])
        dve_s = Steps(nc, ctx, tag + "dve", first + [x for k in range(KD) for x in ([f"u{k}", f"lo{k - 1}"] if k % 2 == 0 and k else [f"u{k}"])]
                      + [f"lo{KD - 1}"])
        pool_s = Steps(nc, ctx, tag + "pool", [f"lo{k}" for k in range(0, KD, 2)])
        sums = [co.psum[:, 2 + 3 * n:2 + 3 * n + parts] for n in range(2)]
        by_part = lambda x: x.rearrange("p (a b) -> p a b", a=parts)
        block = ctx.enter_context(nc.Block())

        def lo_done(eng, k):
            eng.wait_ge(*(dve_s if k % 2 else pool_s).at(f"lo{k}"))

        @block.sync
        def _(sp):
            for k in range(KD):
                if k == 2:
                    for j in range(early):
                        following.load(sp, 0, j)
                if k >= 2:
                    sp.wait_ge(*dve_s.at(f"h{k - 2}"))
                sp.dma_start(r[:, k % 2], res[k * P:(k + 1) * P, :]).then_inc(landed[k % 2], 16)
            for k in range(KD if dest is not None else 0):
                sp.wait_ge(*dve_s.at(f"h{k}"))
                sp.dma_start(dest[k * P:(k + 1) * P, :], y[:, k]).then_inc(stored, 16)
            if dest is not None:
                sp.wait_ge(stored, 16 * KD)

        @block.scalar
        def _(act):
            act_s.prime(act)

            def mean_square(n, names):
                nc.scalar.activation(by_part(rstd[:, n]), sums[n][:, :, 0:N], ACT.Ln, scale=1.0 / D,
                                     bias=co.eps[:]).then_inc(*act_s.did(names[0]))
                act.wait_ge(*act_s.at(names[0]))
                nc.scalar.activation(rstd[:, n], rstd[:, n], ACT.Exp, scale=-0.5).then_inc(*act_s.did(names[1]))

            if norm:
                for k in range(KD):
                    if k >= 2:
                        act.wait_ge(*pe_s.at(f"sum{k - 2}"))
                    nc.scalar.activation(sq[:, k % 2], y[:, k], ACT.Square).then_inc(*act_s.did(f"square{k}"))
                act.wait_ge(*pe_s.at(f"sum{KD - 1}"))
                mean_square(0, ("ln", "root"))
            for k in range(KD):
                act.wait_ge(*dve_s.at(f"h{k}"))
                if k >= 2:
                    act.wait_ge(*pe_s.at(f"next{k - 2}"))
                nc.scalar.activation(sq[:, k % 2], y[:, k], ACT.Square).then_inc(*act_s.did(f"next{k}"))
            act.wait_ge(*pe_s.at(f"next{KD - 1}"))
            mean_square(1, ("next_ln", "next_root"))
            for k in range(KD):
                act.wait_ge(*dve_s.at(f"u{k}"))
                nc.scalar.copy(x_hi[:, k], u[:, k % 4]).then_inc(*act_s.did(f"hi{k}"))

        @block.tensor
        def _(pe):
            pe_s.prime(pe)
            for n, (act_name, pe_name) in enumerate((("square", "sum"), ("next", "next"))):
                if n or norm:
                    for k in range(KD):
                        pe.wait_ge(*act_s.at(f"{act_name}{k}"))
                        for part in range(parts):
                            last = nc.tensor.matmul(sums[n][:, part, 0:N], co.ones[:], sq[:, k % 2, part * N:(part + 1) * N],
                                                    start=k == 0, stop=k == KD - 1)
                        last.then_inc(*pe_s.did(f"{pe_name}{k}"))

        @block.gpsimd
        def _(pool):
            pool_s.prime(pool)
            for j in range(early):
                following.split(pool, 0, j)
            for k in range(0, KD, 2):
                pool.wait_ge(*act_s.at(f"hi{k}"))
                nc.gpsimd.tensor_tensor(x_lo[:, k], u[:, k % 4], x_hi[:, k].bitcast(F32), ALU.subtract)\
                  .then_inc(*pool_s.did(f"lo{k}"))

        @block.vector
        def _(dve):
            dve_s.prime(dve)
            V = nc.vector
            if norm:
                dve.wait_ge(*act_s.at("root"))
            for k in range(KD):
                if norm:
                    V.scalar_tensor_tensor(y[:, k], y[:, k], co.par(gain, k), rstd[:, 0], ALU.mult,
                                           ALU.mult).then_inc(*dve_s.did(f"t{k}"))
                    dve.wait_ge(*dve_s.at(f"t{k}"))
                dve.wait_ge(landed[k % 2], 16 * (k // 2 + 1))
                V.tensor_tensor(y[:, k], y[:, k], r[:, k % 2], ALU.add).then_inc(*dve_s.did(f"h{k}"))
            dve.wait_ge(*act_s.at("next_root"))

            def lo(k):
                dve.wait_ge(*act_s.at(f"hi{k}"))
                V.tensor_tensor(x_lo[:, k], u[:, k % 4], x_hi[:, k].bitcast(F32), ALU.subtract).then_inc(*dve_s.did(f"lo{k}"))

            for k in range(KD):
                if k >= 4:
                    lo_done(dve, k - 4)
                V.scalar_tensor_tensor(u[:, k % 4], y[:, k], co.par(next_gain, k), rstd[:, 1], ALU.mult,
                                       ALU.mult).then_inc(*dve_s.did(f"u{k}"))
                if k % 2 == 0 and k:
                    lo(k - 1)
            lo(KD - 1)


HD = 64
NC2 = SEQ // P
PAIRS = 3
RW = PAIRS * P
RWKV_IN = 3 * RW + 2 * P
MLA_IN = 256 + 128 + 32
GDN_AT = RWKV_IN + MLA_IN
P_IN = GDN_AT + 4 * RW + 12
DECAY = float(np.exp(-0.5))


PER = 6
FULL = P_IN // P // PER * PER


def projection_first(co, x_hi, x_lo):
    return projection_stage(co, x_hi, x_lo, 1, 0)


def projection_stage(co, x_hi, x_lo, n, at):
    H = SEQ // 2
    return co.pr.stage(n, [(lambda i, j=j: columns(co.dram["w_in_2"], (PER * i + (at + j)) * P)) for j in range(PER)],
                       [chunk_terms(j, x_hi, x_lo, KD, h * H, H) for j in range(PER) for h in range(2)])


def input_projection(co, x_hi, x_lo, first):
    nc, pr = co.nc, co.pr
    H = SEQ // 2
    w = co.dram["w_in_2"]
    n = FULL // PER - 1
    st = projection_stage(co, x_hi, x_lo, n, PER)
    rest = [(t * P, min(P, P_IN - t * P)) for t in range(FULL, -(-P_IN // P))]

    def rest_terms(j, m, h):
        return (H, [(j, (lambda t, k=k: t[:, k * m:(k + 1) * m]), x_hi[:, k, h * H:(h + 1) * H],
                     x_lo[:, k, h * H:(h + 1) * H]) for k in range(KD)])

    end = pr.stage(1, [(lambda i, at=at, m=m: w.rearrange("(k p) m -> p k m", p=P)[:, :, at:at + m]) for at, m in rest],
                   [rest_terms(j, m, h) for j, (at, m) in enumerate(rest) for h in range(2)])
    with ExitStack() as ctx:
        o = ctx.enter_context(nc.sbuf_tensor("ip_o", [P, PER, SEQ], F32))
        act_s = Steps(nc, ctx, "ip_act", [f"o{j}" for j in range(PER)])
        stored = [signal(nc, ctx, f"ip_stored{j}") for j in range(PER)]
        block = ctx.enter_context(nc.Block())

        @block.sync
        def _(sp):
            for j in range(first.early, PER):
                first.load(sp, 0, j)
            with sp.Fori(0, n) as i:
                for j in range(PER):
                    st.load(sp, i, j)
            for j in range(len(rest)):
                end.load(sp, 0, j)

        @block.gpsimd
        def _(pool):
            for j in range(first.early, PER):
                first.split(pool, 0, j)
            with pool.Fori(0, n) as i:
                for j in range(PER):
                    st.split(pool, i, j)
            for j in range(len(rest)):
                end.split(pool, 0, j)

        @block.tensor
        def _(pe):
            for c in range(2 * PER):
                first.multiply(pe, 0, c)
            with pe.Fori(0, n) as i:
                for c in range(2 * PER):
                    st.multiply(pe, i, c)
            for c in range(2 * len(rest)):
                end.multiply(pe, 0, c)

        @block.scalar
        def _(act):
            act_s.prime(act)
            for j in range(PER):
                act.sem_inc(stored[j], 16)

            def take(s, i, it, j, at, m):
                dest = co.dram["ppT"][at:at + m, :] if isinstance(at, int) else co.dram["ppT"][ds(at, m), :]
                act.wait_ge(stored[j], 16 + 16 * it)
                for h in range(2):
                    c = 2 * j + h
                    s.wait_full(act, i, c)
                    ins = nc.scalar.copy(o[0:m, j, h * H:(h + 1) * H], s.bank_of(c, m))
                    if h == 0:
                        ins.then_inc(s.freed(c), 1)
                    else:
                        ins.then_inc(*act_s.did(f"o{j}"))
                        act.wait_ge(*act_s.at(f"o{j}", it))
                        act.sem_inc(s.freed(c), 1)
                act.dma_start(dest, o[0:m, j]).then_inc(stored[j], 16)

            for j in range(PER):
                take(first, 0, 0, j, j * P, P)
            with act.Fori(0, n) as i:
                for j in range(PER):
                    take(st, i, i + 1, j, (PER * i + (PER + j)) * P, P)
            for j, (at, m) in enumerate(rest):
                take(end, 0, n + 1, j, at, m)
            for j in range(PER):
                act.wait_ge(stored[j], 16 + 16 * (n + 1) + (16 if j < len(rest) else 0))


class Masks:

    def __init__(self, co, ctx):
        nc = co.nc
        sb = lambda name, shape, dt=F32: ctx.enter_context(nc.sbuf_tensor(name, shape, dt))
        self.high = sb("mk_high", [P, len(LEVELS), 64], I32)
        self.strict = sb("mk_strict", [P, P], I32)
        self.incl = sb("mk_incl", [P, P], I32)
        self.inclf = sb("mk_inclf", [P, P])
        self.block = sb("mk_block", [P, P])
        self.half = sb("mk_half", [P, P])

    def build(self, pool, nc, made):
        n = [0]

        def did(ins):
            ins.then_inc(made, 1)
            n[0] += 1
            pool.wait_ge(made, n[0])

        for m_ in (self.high, self.strict, self.incl):
            did(nc.gpsimd.memset(m_[:], 1))
        for m_ in (self.inclf, self.block):
            did(nc.gpsimd.memset(m_[:], 1.0))

        def keep(view, base, pattern, mult):
            did(nc.gpsimd.affine_select(out=view, in_=view, compare_op=ALU.is_ge, fill=0.0, base=base,
                                        pattern=pattern, channel_multiplier=mult))

        for l, m in enumerate(LEVELS):
            nb = 64 // m
            view = self.high[:, l].rearrange("p (b m) -> p b m", m=m)
            keep(view, 0, [[-2 * m, nb], [0, m]], 1)
            keep(view, m - 1, [[2 * m, nb], [0, m]], -1)
        keep(self.strict[:], -1, [[1, P]], -1)
        keep(self.incl[:], 0, [[1, P]], -1)
        keep(self.inclf[:], 0, [[1, P]], -1)
        keep(self.block[:, 64:P], -64, [[0, 64]], 1)
        keep(self.block[:, 0:64], 63, [[0, 64]], -1)
        did(nc.gpsimd.tensor_scalar(self.half[:], self.block[:], 1.0 / HD, None, ALU.mult))


def inverse_names():
    last = len(LEVELS) - 1
    pe, act, dve = [], [], ["xt_eye"] + [f"inv_t0{e}" for e in range(2)]
    for l in range(last + 1):
        if l:
            for x in ("y", "z"):
                pe += [f"inv_{x}{l}{e}" for e in range(2)]
            act += [f"inv_y{l}{e}" for e in range(2)]
            dve += [f"inv_t{l}{e}" for e in range(2)]
        if l < last:
            pe += [f"inv_x{l}{e}" for e in range(2)]
            act += [f"inv_x{l}{e}" for e in range(2)]
    return pe, act, dve


class Inverse:

    def __init__(self, co, mk, gT, X, XT, Y, steps):
        self.co, self.mk, self.gT, self.X, self.XT, self.Y = co, mk, gT, X, XT, Y
        self.pe_s, self.act_s, self.dve_s = steps
        self.last = len(LEVELS) - 1

    def bank(self, b):
        return self.co.psum[:, b:b + 2].rearrange("p a (c t) -> p (a c) t", t=P)

    def pe(self, pe, i):
        nc, co = self.co.nc, self.co
        for l in range(self.last + 1):
            if l:
                for e in range(2):
                    pe.wait_ge(*self.act_s.at(f"inv_x{l - 1}{e}", i))
                    for c in range(NC2):
                        q = e * NC2 + c
                        last = nc.tensor.matmul(self.bank(4 * e)[:, c], self.gT[:, q], self.X[:, q], start=True, stop=True)
                    last.then_inc(*self.pe_s.did(f"inv_y{l}{e}"))
                for e in range(2):
                    pe.wait_ge(*self.act_s.at(f"inv_y{l}{e}", i))
                    for c in range(NC2):
                        q = e * NC2 + c
                        last = nc.tensor.matmul(self.bank(4 * e + 2)[:, c], self.Y[:, q], self.XT[:, q], start=True, stop=True)
                    last.then_inc(*self.pe_s.did(f"inv_z{l}{e}"))
            if l < self.last:
                for e in range(2):
                    pe.wait_ge(*self.dve_s.at(f"inv_t{l}{e}", i))
                    for c in range(NC2):
                        last = nc.tensor.transpose(self.bank(4 * e)[:, c], self.XT[:, e * NC2 + c], co.ident[:])
                    last.then_inc(*self.pe_s.did(f"inv_x{l}{e}"))

    def act(self, act, i, other):
        nc = self.co.nc
        for l in range(self.last + 1):
            for x, dst, there in (("y", self.Y, l > 0), ("x", self.X, l < self.last)):
                for e in range(2 if there else 0):
                    act.wait_ge(*self.pe_s.at(f"inv_{x}{l}{e}", i))
                    nc.scalar.copy(dst[:, e * NC2:(e + 1) * NC2], self.bank(4 * e)).then_inc(*self.act_s.did(f"inv_{x}{l}{e}"))
            next(other, None)

    def eye(self):
        nc, co = self.co.nc, self.co
        eye = co.ident[:].unsqueeze(1).to_broadcast([P, 2 * NC2, P])
        nc.vector.tensor_copy(self.XT[:], eye).then_inc(*self.dve_s.did("xt_eye"))

    def dve(self, dve, i, other):
        nc, co = self.co.nc, self.co
        for l, m in enumerate(reversed(LEVELS)):
            half = lambda x: x.rearrange("p c (b two m) -> p c b two m", two=2, m=m)[:, :, :, 1]
            mask = self.mk.high[:, self.last - l].rearrange("p (b m) -> p b m", m=m).unsqueeze(1).to_broadcast([P, NC2, 64 // m, m])
            for e in range(2):
                mine = slice(e * NC2, (e + 1) * NC2)
                if l:
                    dve.wait_ge(*self.pe_s.at(f"inv_z{l}{e}", i))
                    dve.wait_ge(*self.dve_s.at(f"inv_t{l - 1}{e}", i))
                    source = self.bank(4 * e + 2)
                else:
                    source = self.gT[:, mine]
                co.pr.carry(dve)
                nc.vector.copy_predicated(half(self.XT[:, mine]), mask, half(source)).then_inc(*self.dve_s.did(f"inv_t{l}{e}"))
            next(other, None)


def rows(x, at, i):
    return x[ds(at + i * P, P), :] if not isinstance(i, int) else x[at + i * P:at + i * P + P, :]


def each_pair(eng, first, body):
    for _ in first(0):
        pass
    with eng.Fori(0, PAIRS - 1) as i:
        body(i, first(i + 1))
    body(PAIRS - 1, iter(()))


def rwkv(co, mk):
    nc = co.nc
    N = SEQ
    ppT = co.dram["ppT"]
    with ExitStack() as ctx:
        sb = lambda name, shape, dt=F32: ctx.enter_context(nc.sbuf_tensor("rw_" + name, shape, dt))
        buf = sb("buf", [P, 3, N + 1])
        z = sb("z", [P, 3, N])
        lora, sg = sb("lora", [P, N]), sb("sg", [P, N])
        lw = sb("lw", [P, 3, P])
        oma = sb("oma", [P, PAIRS])
        w, a, g = sb("w", [P, N]), sb("a", [P, N]), sb("g", [P, N])
        s, kk, bv, bo = sb("s", [P, N]), sb("kk", [P, N]), sb("bv", [P, N]), sb("bo", [P, N])
        d1, ep, em, ex = sb("d1", [P, N]), sb("ep", [P, N]), sb("em", [P, N]), sb("ex", [P, N])
        ar = sb("ar", [P, NC2, 2, P])
        bf, kf = sb("bf", [P, N]), sb("kf", [P, N])
        bp, kp = sb("bp", [P, 2, N]), sb("kp", [P, 2, N])
        vt, bt, kt = sb("vt", [P, NC2, P]), sb("bt", [P, NC2, P]), sb("kt", [P, NC2, P])
        gT, ak, rb, rk = (sb(n, [P, 2 * NC2, P]) for n in ("gT", "ak", "rb", "rk"))
        X, XT, Y = (sb(n, [P, 2 * NC2, P]) for n in ("X", "XT", "Y"))
        low = [x[:].rearrange("p a b -> p (a b)") for x in (X, Y)]
        H = sb("H", [P, NC2, P])
        rh, sa, ht = sb("rh", [P, P]), sb("sa", [P, NC2, P]), sb("ht", [P, P])
        ratio = sb("ratio", [P, NC2])
        zr, zk, zv = z[:, 0], z[:, 1], z[:, 2]
        ch = lambda x: x.rearrange("p (c t) -> p c t", t=P)
        ps = co.psum
        two = lambda b: ps[:, b:b + 2].rearrange("p a b -> p (a b)")
        par = co.par

        ipe, iact, idve = inverse_names()
        chunkwise = [x for c in range(NC2) for x in ([f"r{c}", f"sa{c}", f"h{c}", f"y{c}"] if c < NC2 - 1 else [f"r{c}", f"sa{c}", f"y{c}"])]
        pe_s = Steps(nc, ctx, "rw_pe", ["lora", "ss", "vt", "bonus", "bt", "kt"] + [f"g{x}{e}" for e in range(2) for x in "bk"]
                     + ipe + chunkwise + ["mean", "var"])
        act_a = Steps(nc, ctx, "rw_act_a", ["sq"])
        act_s = Steps(nc, ctx, "rw_act", ["w", "a", "g", "ln", "root", "ep", "em", "ratio", "ex", "vt", "kp0", "kp1", "bt", "kt"] + iact
                      + [x for c in range(NC2) for x in (f"r{c}", f"sa{c}")] + ["y", "ysq", "yln", "yroot"])
        dve_a = Steps(nc, ctx, "rw_dve_a", [f"{x}{n}" for n in range(3) for x in ("sh", "z")] + ["kk"])
        dve_n = [f"s{c}" for c in range(NC2)] + \
            ["ta", "k2", "kkn", "d1", "d2", "rt0", "rt1", "rkr", "bonus", "bv", "bf", "kf", "A", "R", "bo"] + ["xt_eye"] + \
            [f"{x}{e}" for e in range(2) for x in ("gT", "rb", "ak", "rk")] + idve[1:] + \
            [x for c in range(NC2 - 1) for x in (f"ht{c}", f"H{c}")] + ["yc", "yn", "yb", "yo"]
        dve_s = Steps(nc, ctx, "rw_dve", dve_n)
        pool_s = Steps(nc, ctx, "rw_pool", ["bp0", "bp1"])
        inv = Inverse(co, mk, gT, X, XT, Y, (pe_s, act_s, dve_s))
        in_s = signal(nc, ctx, "rw_in")
        lw_s = signal(nc, ctx, "rw_lw")
        out_s = signal(nc, ctx, "rw_out")
        pre_in = [signal(nc, ctx, f"rw_pre_in{n}") for n in range(2)]
        pre_v = signal(nc, ctx, "rw_pre_dve")
        pre_a = signal(nc, ctx, "rw_pre_act")
        zeros = signal(nc, ctx, "rw_zeros")
        ZEROS = 11
        block = ctx.enter_context(nc.Block())

        @block.sync
        def _(sp):
            for n in range(2):
                sp.dma_start(low[n][:, 1:N + 1], ppT[3 * RW + n * P:3 * RW + (n + 1) * P, :]).then_inc(pre_in[n], 16)
            sp.wait_ge(zeros, 4)

            def first(i):
                src = [rows(ppT, n * RW, i) for n in range(3)]
                sp.wait_ge(*dve_a.at("z2", i - 1))
                for n in range(3):
                    sp.dma_start(buf[:, n, 1:N + 1], src[n]).then_inc(in_s, 16)
                yield

            def body(i, following):
                cols = ds(i * P, P) if not isinstance(i, int) else slice(i * P, (i + 1) * P)
                w2 = co.dram["rwkv_w2_2"][:, cols]
                sp.wait_ge(*pe_s.at("lora", i - 1))
                co.pr.carry(sp)
                sp.dma_start(lw[0:HD, 0], w2).then_inc(lw_s, 16)
                sp.dma_start(lw[HD:P, 1], co.dram["rwkv_a2_2"][:, cols]).then_inc(lw_s, 16)
                sp.dma_start(lw[:, 2], co.dram["rwkv_g2_2"][:, cols]).then_inc(lw_s, 16)
                for _ in following:
                    pass
                dest = rows(co.dram["yT"], 0, i)
                sp.wait_ge(*dve_s.at("yo", i))
                sp.dma_start(dest, bo[:]).then_inc(out_s, 16)

            each_pair(sp, first, body)
            sp.wait_ge(out_s, 16 + 16 * PAIRS)

        @block.gpsimd
        def _(pool):
            pool_s.prime(pool)
            for x in (low[0][:, 0:1], low[1][:, 0:1], buf[:, :, 0:1], lw[:]):
                nc.gpsimd.memset(x, 0.0).then_inc(zeros, 1)
            for x in (bp, kp, gT, ak, rb, rk):
                nc.gpsimd.memset(x[:], 0.0).then_inc(zeros, 1)
            nc.gpsimd.memset(H[:, 0], 0.0).then_inc(zeros, 1)
            pool.wait_ge(zeros, ZEROS)
            with pool.Fori(0, PAIRS) as i:
                pool.wait_ge(*dve_s.at("bf", i))
                pool.wait_ge(*pe_s.at("gb1", i - 1))
                for e in range(2):
                    rows = slice(e * HD, (e + 1) * HD)
                    nc.gpsimd.tensor_tensor(bp[rows, e], bf[rows], co.zero[rows].to_broadcast([HD, N]),
                                            ALU.add).then_inc(*pool_s.did(f"bp{e}"))

        @block.scalar
        def _(act):
            act_a.prime(act)
            act_s.prime(act)
            act.sem_inc(out_s, 16)
            act.wait_ge(pre_v, 2)
            nc.scalar.activation(lora[0:HD], lora[0:HD], ACT.Tanh).then_inc(pre_a, 1)
            act.wait_ge(pre_v, 4)
            nc.scalar.activation(sg[:], sg[:], ACT.Sigmoid).then_inc(pre_a, 1)

            def first(i):
                for _ in range(4):
                    yield
                act.wait_ge(*dve_a.at("kk", i))
                nc.scalar.activation(bf[:], kk[:], ACT.Square).then_inc(*act_a.did("sq"))

            def body(i, following):
                act.wait_ge(*pe_s.at("lora", i))
                nc.scalar.activation(w[:], two(0), ACT.Sigmoid, bias=par("rwkv_w0_2", i)).then_inc(*act_s.did("w"))
                nc.scalar.activation(a[:], two(2), ACT.Sigmoid, bias=par("rwkv_a0_2", i)).then_inc(*act_s.did("a"))
                act.wait_ge(*dve_s.at("yo", i - 1))
                nc.scalar.copy(g[:], two(4)).then_inc(*act_s.did("g"))
                act.wait_ge(*pe_s.at("ss", i))
                nc.scalar.activation(ex[:], two(0), ACT.Ln, bias=co.eps[:]).then_inc(*act_s.did("ln"))
                act.wait_ge(*act_s.at("ln", i))
                nc.scalar.activation(bv[:], ex[:], ACT.Exp, scale=-0.5).then_inc(*act_s.did("root"))
                act.wait_ge(*dve_s.at("rt1", i))
                nc.scalar.activation(ep[:], d1[:], ACT.Exp, scale=DECAY).then_inc(*act_s.did("ep"))
                nc.scalar.activation(em[:], d1[:], ACT.Exp, scale=-DECAY).then_inc(*act_s.did("em"))
                nc.scalar.activation(ratio[:], ratio[:], ACT.Exp, scale=-DECAY).then_inc(*act_s.did("ratio"))
                nc.scalar.activation(ex[:], w[:], ACT.Exp, scale=-DECAY).then_inc(*act_s.did("ex"))
                act.wait_ge(*pe_s.at("vt", i))
                nc.scalar.copy(vt[:], ch(two(0))).then_inc(*act_s.did("vt"))
                act.wait_ge(*dve_s.at("kf", i))
                for e in range(2):
                    rows = slice(e * HD, (e + 1) * HD)
                    nc.scalar.copy(kp[rows, e], kf[rows]).then_inc(*act_s.did(f"kp{e}"))
                act.wait_ge(*pe_s.at("bt", i))
                nc.scalar.copy(bt[:], ch(two(4))).then_inc(*act_s.did("bt"))
                act.wait_ge(*pe_s.at("kt", i))
                nc.scalar.copy(kt[:], ch(two(6))).then_inc(*act_s.did("kt"))
                inv.act(act, i, following)
                for c in range(NC2):
                    act.wait_ge(*pe_s.at(f"r{c}", i))
                    nc.scalar.copy(rh[:], ps[:, 0, 0:P]).then_inc(*act_s.did(f"r{c}"))
                    act.wait_ge(*pe_s.at(f"sa{c}", i))
                    nc.scalar.copy(sa[:, c], ps[:, 1, 0:P]).then_inc(*act_s.did(f"sa{c}"))
                act.wait_ge(*pe_s.at(f"y{NC2 - 1}", i))
                nc.scalar.copy(d1[:], two(4)).then_inc(*act_s.did("y"))
                act.wait_ge(*dve_s.at("yc", i))
                nc.scalar.activation(em[:], d1[:], ACT.Square).then_inc(*act_s.did("ysq"))
                act.wait_ge(*pe_s.at("var", i))
                nc.scalar.activation(ex[:], two(2), ACT.Ln, bias=co.gn_eps[:]).then_inc(*act_s.did("yln"))
                act.wait_ge(*act_s.at("yln", i))
                nc.scalar.activation(ex[:], ex[:], ACT.Exp, scale=-0.5).then_inc(*act_s.did("yroot"))

            each_pair(act, first, body)

        @block.tensor
        def _(pe):
            pe_s.prime(pe)
            pe.wait_ge(pre_a, 2)
            pe.wait_ge(pre_v, 5)
            pe.wait_ge(zeros, ZEROS)
            halves = [slice(0, 512), slice(512, 1024)]

            def wide(bank, lhsT, rhs):
                for h, cols in enumerate(halves):
                    last = nc.tensor.matmul(ps[:, bank + h], lhsT, rhs[:, cols], start=True, stop=True)
                return last

            with pe.Fori(0, PAIRS) as i:
                pe.wait_ge(lw_s, 48 * i + 48)
                pe.wait_ge(*act_s.at("y", i - 1))
                wide(4, lw[:, 2], sg)
                pe.wait_ge(*dve_s.at("yc", i - 1))
                wide(0, lw[:, 0], lora)
                pe.wait_ge(*act_s.at("yln", i - 1))
                wide(2, lw[:, 1], lora).then_inc(*pe_s.did("lora"))
                pe.wait_ge(*act_a.at("sq", i))
                pe.wait_ge(*act_s.at("w", i))
                wide(0, mk.block[:], bf).then_inc(*pe_s.did("ss"))
                pe.wait_ge(*dve_a.at("z2", i))
                pe.wait_ge(*act_s.at("ln", i))
                for c in range(NC2):
                    last = nc.tensor.transpose(ch(two(0))[:, c], zv[:, c * P:(c + 1) * P], co.ident[:])
                last.then_inc(*pe_s.did("vt"))
                pe.wait_ge(*dve_s.at("bonus", i))
                wide(2, mk.block[:], bo).then_inc(*pe_s.did("bonus"))
                pe.wait_ge(*dve_s.at("bf", i))
                pe.wait_ge(*act_s.at("g", i))
                for c in range(NC2):
                    last = nc.tensor.transpose(ch(two(4))[:, c], bf[:, c * P:(c + 1) * P], co.ident[:])
                last.then_inc(*pe_s.did("bt"))
                pe.wait_ge(*dve_s.at("kf", i))
                for c in range(NC2):
                    last = nc.tensor.transpose(ch(two(6))[:, c], kf[:, c * P:(c + 1) * P], co.ident[:])
                last.then_inc(*pe_s.did("kt"))
                pe.wait_ge(*dve_s.at("bo", i))
                pe.wait_ge(*act_s.at("vt", i))
                pe.wait_ge(*pool_s.at("bp1", i))
                for e in range(2):
                    for n, (src, x, last_read) in enumerate(((bp, "b", "rb"), (kp, "k", "rk"))):
                        if e:
                            pe.wait_ge(*dve_s.at(f"{last_read}0", i))
                        elif n:
                            pe.wait_ge(*act_s.at("kt", i))
                        for c in range(NC2):
                            last = nc.tensor.matmul(ps[:, 4 * n + c // 2, (c % 2) * 256:(c % 2) * 256 + 256],
                                                    src[:, e, c * P:(c + 1) * P],
                                                    ar[:, c].rearrange("p a t -> p (a t)"), start=True, stop=True)
                        last.then_inc(*pe_s.did(f"g{x}{e}"))
                pe.wait_ge(*dve_s.at("rk1", i))
                inv.pe(pe, i)
                for c in range(NC2):
                    if c == 0:
                        pe.wait_ge(*dve_s.at("inv_t61", i))
                    for e in range(2):
                        cols = slice(e * HD, (e + 1) * HD)
                        nc.tensor.matmul(ps[:, 0, cols], ak[:, e * NC2 + c], vt[:, c, cols], start=e == 0, stop=False)
                    if c:
                        pe.wait_ge(*dve_s.at(f"H{c - 1}", i))
                    nc.tensor.matmul(ps[:, 0, 0:P], ar[:, c, 0], H[:, c], start=False, stop=True).then_inc(*pe_s.did(f"r{c}"))
                    pe.wait_ge(*act_s.at(f"r{c}", i))
                    for e in range(2):
                        cols = slice(e * HD, (e + 1) * HD)
                        last = nc.tensor.matmul(ps[:, 1, cols], XT[:, e * NC2 + c], rh[:, cols], start=True, stop=True)
                    last.then_inc(*pe_s.did(f"sa{c}"))
                    if c < NC2 - 1:
                        nc.tensor.matmul(ps[:, 2, 0:P], kt[:, c], vt[:, c], start=True, stop=False)
                    for e in range(2):
                        cols = slice(e * HD, (e + 1) * HD)
                        out = ch(two(4))[cols, c]
                        nc.tensor.matmul(out, vt[:, c, cols], rk[:, e * NC2 + c], start=True, stop=False)
                        nc.tensor.matmul(out, H[:, c, cols], ar[:, c, 1], start=False, stop=False)
                    pe.wait_ge(*act_s.at(f"sa{c}", i))
                    if c < NC2 - 1:
                        nc.tensor.matmul(ps[:, 2, 0:P], bt[:, c], sa[:, c], start=False, stop=True)\
                          .then_inc(*pe_s.did(f"h{c}"))
                    for e in range(2):
                        cols = slice(e * HD, (e + 1) * HD)
                        out = ch(two(4))[cols, c]
                        last = nc.tensor.matmul(out, sa[:, c, cols], rb[:, e * NC2 + c], start=False, stop=True)
                    last.then_inc(*pe_s.did(f"y{c}"))
                pe.wait_ge(*act_s.at("y", i))
                wide(0, mk.half[:], d1).then_inc(*pe_s.did("mean"))
                pe.wait_ge(*act_s.at("ysq", i))
                wide(2, mk.half[:], em).then_inc(*pe_s.did("var"))

        @block.vector
        def _(dve):
            dve_a.prime(dve)
            dve_s.prime(dve)
            V = nc.vector
            dve.wait_ge(zeros, 3)
            for n, dst in ((0, lora), (1, sg)):
                dve.wait_ge(pre_in[n], 16)
                V.tensor_tensor(dst[:], low[n][:, 0:N], low[n][:, 1:N + 1], ALU.subtract).then_inc(pre_v, 1)
                dve.wait_ge(pre_v, 2 * n + 1)
                V.scalar_tensor_tensor(dst[:], dst[:], par("rwkv_mu_2", 9 + n), low[n][:, 1:N + 1], ALU.mult,
                                       ALU.add).then_inc(pre_v, 1)
            at = co.pl.at["rwkv_k_a_2"][0]
            dve.wait_ge(zeros, ZEROS)
            V.tensor_scalar(oma[:], co.prm[:, at:at + PAIRS], -1.0, 1.0, ALU.mult, ALU.add).then_inc(pre_v, 1)
            dve.wait_ge(pre_v, 5)

            def first(i):
                def did(name, ins, wait=False):
                    ins.then_inc(*dve_a.did(name))
                    if wait:
                        dve.wait_ge(*dve_a.at(name, i))

                dve.wait_ge(in_s, 48 * i + 48)
                for n in range(3):
                    did(f"sh{n}", V.tensor_tensor(z[:, n], buf[:, n, 0:N], buf[:, n, 1:N + 1], ALU.subtract), True)
                    did(f"z{n}", V.scalar_tensor_tensor(z[:, n], z[:, n], par("rwkv_mu_2", i + 3 * n), buf[:, n, 1:N + 1],
                                                        ALU.mult, ALU.add), n == 1)
                    yield
                did("kk", V.tensor_scalar(kk[:], zk, par("rwkv_k_k_2", i), None, ALU.mult))

            def body(i, following):
                def did(name, ins, wait=False):
                    ins.then_inc(*dve_s.did(name))
                    if wait:
                        dve.wait_ge(*dve_s.at(name, i))

                dve.wait_ge(*act_s.at("w", i))
                for c in range(NC2):
                    did(f"s{c}", V.tensor_tensor_scan(s[:, c * P:(c + 1) * P], co.ones[:], w[:, c * P:(c + 1) * P], 0.0,
                                                      ALU.mult, ALU.add))
                dve.wait_ge(*act_s.at("a", i))
                did("ta", V.tensor_scalar(d1[:], a[:], par("rwkv_k_a_2", i), oma[:, ds(i, 1)] if not isinstance(i, int) else oma[:, i:i + 1],
                                          ALU.mult, ALU.add), True)
                did("k2", V.tensor_tensor(zk, zk, d1[:], ALU.mult), True)
                dve.wait_ge(*act_s.at("root", i))
                did("kkn", V.tensor_tensor(kk[:], kk[:], bv[:], ALU.mult), True)
                sc = ch(s[:])
                did("d1", V.tensor_tensor(ch(d1[:]), sc, sc[:, :, HD - 1:HD].to_broadcast([P, NC2, P]), ALU.subtract), True)
                did("d2", V.tensor_tensor(w[:], d1[:], w[:], ALU.subtract))
                did("rt0", V.tensor_copy(ratio[:], ch(d1[:])[:, :, P - 1]), True)
                did("rt1", V.tensor_tensor(ratio[:, 0:NC2 - 1], ratio[:, 0:NC2 - 1], sc[:, 1:NC2, HD - 1], ALU.add))
                dve.wait_ge(out_s, 16 * i + 16)
                did("rkr", V.tensor_tensor(bo[:], zr, zk, ALU.mult), True)
                did("bonus", V.tensor_scalar(bo[:], bo[:], par("rwkv_r_k_2", i), None, ALU.mult))
                did("bv", V.scalar_tensor_tensor(bv[:], kk[:], -1.0, a[:], ALU.mult, ALU.mult), True)
                dve.wait_ge(*act_s.at("ep", i))
                did("bf", V.tensor_tensor(bf[:], bv[:], ep[:], ALU.mult))
                did("kf", V.tensor_tensor(kf[:], zk, ep[:], ALU.mult))
                dve.wait_ge(*act_s.at("ex", i))
                did("A", V.tensor_tensor(ar[:, :, 0], ch(kk[:]), ch(ex[:]), ALU.mult))
                did("R", V.tensor_tensor(ar[:, :, 1], ch(zr), ch(em[:]), ALU.mult))
                dve.wait_ge(*pe_s.at("bonus", i))
                did("bo", V.tensor_tensor(bo[:], two(2), zv, ALU.mult))
                inv.eye()
                for e in range(2):
                    for x, n, half, mask, src in (("gT", 0, 0, mk.strict, gT), ("rb", 0, 1, mk.incl, rb),
                                                  ("ak", 1, 0, mk.strict, ak), ("rk", 1, 1, mk.incl, rk)):
                        if half == 0:
                            dve.wait_ge(*pe_s.at(f"g{'bk'[n]}{e}", i))
                            co.pr.carry(dve)
                        grams = ps[:, 4 * n:4 * n + 4].rearrange("p a b -> p (a b)").rearrange("p (c h t) -> p c h t", h=2, t=P)
                        did(f"{x}{e}", V.copy_predicated(src[:, e * NC2:(e + 1) * NC2],
                                                         mask[:].unsqueeze(1).to_broadcast([P, NC2, P]), grams[:, :, half]))
                dve.wait_ge(*dve_s.at("rk1", i))
                inv.dve(dve, i, following)
                for c in range(NC2 - 1):
                    dve.wait_ge(*pe_s.at(f"h{c}", i))
                    did(f"ht{c}", V.tensor_tensor(ht[:], ps[:, 2, 0:P], H[:, c], ALU.add), True)
                    did(f"H{c}", V.scalar_tensor_tensor(H[:, c + 1], ht[:], ratio[:, c:c + 1], mk.block[:], ALU.mult, ALU.mult), True)
                dve.wait_ge(*pe_s.at("mean", i))
                did("yc", V.tensor_tensor(d1[:], d1[:], two(0), ALU.subtract))
                dve.wait_ge(*act_s.at("yroot", i))
                did("yn", V.scalar_tensor_tensor(d1[:], d1[:], par("rwkv_gn_g_2", i), ex[:], ALU.mult, ALU.mult), True)
                did("yb", V.scalar_tensor_tensor(bo[:], d1[:], par("rwkv_gn_b_2", i), bo[:], ALU.add, ALU.add), True)
                did("yo", V.tensor_tensor(bo[:], bo[:], g[:], ALU.mult))

            each_pair(dve, first, body)


HEADS2 = 2 * PAIRS


def deltanet(co, mk):
    nc = co.nc
    N = SEQ
    ppT = co.dram["ppT"]
    par = co.par
    ps = co.psum
    ch = lambda x: x.rearrange("p (c t) -> p c t", t=P)
    two = lambda b: ps[:, b:b + 2].rearrange("p a b -> p (a b)")
    halves = [slice(0, 512), slice(512, 1024)]
    with ExitStack() as ctx:
        sb = lambda name, shape, dt=F32: ctx.enter_context(nc.sbuf_tensor("gd_" + name, shape, dt))
        gB, bB = sb("gB", [P, PAIRS, N]), sb("bB", [P, PAIRS, N])
        rowsel = sb("rowsel", [P, 2, P])
        expand_gates(co, gB, bB, rowsel)
        buf = sb("buf", [P, 3, N + 3])
        z, sg = sb("z", [P, 3, N]), sb("sg", [P, 3, N])
        gi, ga, y, o = sb("gi", [P, N]), sb("ga", [P, N]), sb("y", [P, N]), sb("o", [P, N])
        gc, eg, kd = sb("gc", [P, N]), sb("eg", [P, N]), sb("kd", [P, N])
        gct, decay = sb("gct", [P, NC2, 2]), sb("decay", [P, NC2])
        ar = sb("ar", [P, NC2, 2, P])
        At, qe, kp = sb("At", [P, N]), sb("qe", [P, N]), sb("kp", [P, 2, N])
        Dm = sb("Dm", [P, 2, N])
        gq = sb("gq", [P, 2 * NC2, 2, P])
        vt, kt = sb("vt", [P, NC2, P]), sb("kt", [P, NC2, P])
        X, XT, Y = (sb(n, [P, 2 * NC2, P]) for n in ("X", "XT", "Y"))
        H, sa = sb("H", [P, NC2, P]), sb("sa", [P, NC2, P])
        rh, ht = sb("rh", [P, P]), sb("ht", [P, P])
        rs, sq = Dm, sg[:, 0:2]
        q, k, v = z[:, 0], z[:, 1], z[:, 2]

        ipe, iact, idve = inverse_names()
        pe_s = Steps(nc, ctx, "gd_pe", ["ss", "row", "gct", "vt", "kt", "g0", "g1"] + ipe
                     + [x for c in range(NC2) for x in ([f"r{c}", f"sa{c}"] + ([f"h{c}"] if c < NC2 - 1 else []) + [f"y{c}"])]
                     + ["mean"])
        act_a = Steps(nc, ctx, "gd_act_a", ["sg", "sq"])
        act_s = Steps(nc, ctx, "gd_act", ["ln", "root", "eg", "kd", "decay", "gct", "D", "vt", "kt"] + iact + ["so"]
                      + [f"sa{c}" for c in range(NC2)] + ["y", "ysq", "yln", "yroot"])
        dve_a = Steps(nc, ctx, "gd_dve_a", [f"c{r}{n}" for n in range(3) for r in range(4)]
                      + [f"s{c}" for c in range(NC2)] + ["dkd", "silu"])
        dve_s = Steps(nc, ctx, "gd_dve", ["last", "q", "k", "bk", "v", "kdk", "At", "qe"]
                      + [f"D{e}{c}" for e in range(2) for c in range(NC2)] + ["xt_eye", "gq0", "gq1"] + idve[1:] + ["gate"]
                      + [x for c in range(NC2) for x in ([f"r{c}"] + ([f"ht{c}", f"H{c}"] if c < NC2 - 1 else []))]
                      + ["yn", "yo"])
        pool_s = Steps(nc, ctx, "gd_pool", ["kp0", "kp1", "D"])
        inv = Inverse(co, mk, gq[:, :, 0], X, XT, Y, (pe_s, act_s, dve_s))
        in_s, gate_s, out_s, zeros = (signal(nc, ctx, n) for n in ("gd_in", "gd_gate_in", "gd_out", "gd_zeros"))
        ZEROS = 3
        block = ctx.enter_context(nc.Block())

        @block.sync
        def _(sp):
            def first(i):
                src = [rows(ppT, GDN_AT + n * RW, i) for n in range(3)]
                sp.wait_ge(*dve_a.at("c32", i - 1))
                for n in range(3):
                    sp.dma_start(buf[:, n, 3:N + 3], src[n]).then_inc(in_s, 16)
                yield

            def body(i, following):
                gate = rows(ppT, GDN_AT + 3 * RW, i)
                dest = rows(co.dram["yT"], RW + 4 * HD, i)
                sp.wait_ge(*dve_s.at("gate", i - 1))
                sp.dma_start(gi[:], gate).then_inc(gate_s, 16)
                for _ in following:
                    pass
                sp.wait_ge(*dve_s.at("yo", i))
                sp.dma_start(dest, o[:]).then_inc(out_s, 16)

            each_pair(sp, first, body)
            sp.wait_ge(out_s, 16 + 16 * PAIRS)

        @block.gpsimd
        def _(pool):
            pool_s.prime(pool)
            nc.gpsimd.memset(buf[:, :, 0:3], 0.0).then_inc(zeros, 1)
            nc.gpsimd.memset(kp[:], 0.0).then_inc(zeros, 1)
            nc.gpsimd.memset(H[:, 0], 0.0).then_inc(zeros, 1)
            pool.wait_ge(zeros, ZEROS)
            with pool.Fori(0, PAIRS) as i:
                pool.wait_ge(*pool_s.at("D", i - 1))
                pool.wait_ge(*dve_s.at("k", i))
                pool.wait_ge(*pe_s.at("g1", i - 1))
                for e in range(2):
                    rows = slice(e * HD, (e + 1) * HD)
                    nc.gpsimd.tensor_tensor(kp[rows, e], k[rows], co.zero[rows].to_broadcast([HD, N]),
                                            ALU.add).then_inc(*pool_s.did(f"kp{e}"))
                pool.wait_ge(*pool_s.at("kp1", i))
                pool.wait_ge(*act_s.at("D", i))
                dmv = Dm[:].rearrange("p e (c t) -> p (e c) t", t=P)
                nc.gpsimd.tensor_tensor(dmv, dmv, mk.inclf[:].unsqueeze(1).to_broadcast([P, 2 * NC2, P]),
                                        ALU.mult).then_inc(*pool_s.did("D"))

        @block.scalar
        def _(act):
            act_a.prime(act)
            act_s.prime(act)
            act.sem_inc(out_s, 16)

            def first(i):
                for _ in range(4):
                    yield
                act.wait_ge(*dve_a.at("c32", i))
                nc.scalar.activation(sg[:], z[:], ACT.Sigmoid).then_inc(*act_a.did("sg"))
                yield
                act.wait_ge(*dve_a.at("silu", i))
                nc.scalar.activation(sq, z[:, 0:2], ACT.Square).then_inc(*act_a.did("sq"))

            def body(i, following):
                act.wait_ge(*pe_s.at("ss", i))
                nc.scalar.activation(rs[:].rearrange("p a (b t) -> p (a b) t", b=2), ps[:, 0:4], ACT.Ln,
                                     bias=co.eps[:]).then_inc(*act_s.did("ln"))
                act.wait_ge(*act_s.at("ln", i))
                nc.scalar.activation(rs[:], rs[:], ACT.Exp, scale=-0.5).then_inc(*act_s.did("root"))
                act.wait_ge(*dve_a.at("dkd", i))
                nc.scalar.activation(eg[:], gc[:], ACT.Exp).then_inc(*act_s.did("eg"))
                nc.scalar.activation(kd[:], kd[:], ACT.Exp).then_inc(*act_s.did("kd"))
                act.wait_ge(*dve_s.at("last", i))
                nc.scalar.activation(decay[:], decay[:], ACT.Exp).then_inc(*act_s.did("decay"))
                act.wait_ge(*pe_s.at("gct", i))
                nc.scalar.copy(gct[:], ch(two(4)).rearrange("p c (e k) -> p c e k", e=2)[:, :, :, 0]).then_inc(*act_s.did("gct"))
                act.wait_ge(*dve_s.at(f"D1{NC2 - 1}", i))
                nc.scalar.activation(Dm[:], Dm[:], ACT.Exp).then_inc(*act_s.did("D"))
                act.wait_ge(*pe_s.at("vt", i))
                nc.scalar.copy(vt[:], ch(two(6))).then_inc(*act_s.did("vt"))
                act.wait_ge(*pe_s.at("kt", i))
                nc.scalar.copy(kt[:], ch(two(4))).then_inc(*act_s.did("kt"))
                inv.act(act, i, following)
                act.wait_ge(gate_s, 16 * i + 16)
                act.wait_ge(*dve_s.at("yo", i - 1))
                nc.scalar.activation(ga[:], gi[:], ACT.Sigmoid).then_inc(*act_s.did("so"))
                for c in range(NC2):
                    act.wait_ge(*pe_s.at(f"sa{c}", i))
                    nc.scalar.copy(sa[:, c], ps[:, 1, 0:P]).then_inc(*act_s.did(f"sa{c}"))
                act.wait_ge(*pe_s.at(f"y{NC2 - 1}", i))
                nc.scalar.copy(y[:], two(4)).then_inc(*act_s.did("y"))
                act.wait_ge(*act_s.at("y", i))
                nc.scalar.activation(At[:], y[:], ACT.Square).then_inc(*act_s.did("ysq"))
                act.wait_ge(*pe_s.at("mean", i))
                nc.scalar.activation(At[:], two(0), ACT.Ln, bias=co.eps[:]).then_inc(*act_s.did("yln"))
                act.wait_ge(*act_s.at("yln", i))
                nc.scalar.activation(At[:], At[:], ACT.Exp, scale=-0.5).then_inc(*act_s.did("yroot"))

            each_pair(act, first, body)

        @block.tensor
        def _(pe):
            pe_s.prime(pe)
            pe.wait_ge(zeros, ZEROS)

            def wide(bank, lhsT, rhs):
                for h, cols in enumerate(halves):
                    last = nc.tensor.matmul(ps[:, bank + h], lhsT, rhs[:, cols], start=True, stop=True)
                return last

            with pe.Fori(0, PAIRS) as i:
                pe.wait_ge(*act_s.at("yln", i - 1))
                pe.wait_ge(*act_a.at("sq", i))
                wide(0, mk.block[:], sq[:, 0])
                wide(2, mk.block[:], sq[:, 1]).then_inc(*pe_s.did("ss"))
                pe.wait_ge(*act_s.at("ln", i))
                wide(0, rowsel[:, 0], gc)
                wide(2, rowsel[:, 1], gc).then_inc(*pe_s.did("row"))
                for c in range(NC2):
                    last = nc.tensor.transpose(ch(two(4))[:, c], gc[:, c * P:(c + 1) * P], co.ident[:])
                last.then_inc(*pe_s.did("gct"))
                pe.wait_ge(*dve_s.at("kdk", i))
                for c in range(NC2):
                    last = nc.tensor.transpose(ch(two(6))[:, c], v[:, c * P:(c + 1) * P], co.ident[:])
                last.then_inc(*pe_s.did("vt"))
                pe.wait_ge(*act_s.at("gct", i))
                for c in range(NC2):
                    last = nc.tensor.transpose(ch(two(4))[:, c], kd[:, c * P:(c + 1) * P], co.ident[:])
                last.then_inc(*pe_s.did("kt"))
                pe.wait_ge(*pool_s.at("kp1", i))
                for e in range(2):
                    if e == 0:
                        pe.wait_ge(*dve_s.at(f"D1{NC2 - 1}", i))
                    else:
                        pe.wait_ge(*act_s.at("kt", i))
                    for c in range(NC2):
                        last = nc.tensor.matmul(ps[:, 4 * e + c // 2, (c % 2) * 256:(c % 2) * 256 + 256],
                                                kp[:, e, c * P:(c + 1) * P],
                                                ar[:, c].rearrange("p a t -> p (a t)"), start=True, stop=True)
                    last.then_inc(*pe_s.did(f"g{e}"))
                pe.wait_ge(*dve_s.at("gq1", i))
                inv.pe(pe, i)
                for c in range(NC2):
                    if c == 0:
                        pe.wait_ge(*dve_s.at("inv_t61", i))
                    else:
                        pe.wait_ge(*dve_s.at(f"H{c - 1}", i))
                    nc.tensor.matmul(ps[:, 0, 0:P], At[:, c * P:(c + 1) * P], H[:, c], start=True, stop=True)\
                      .then_inc(*pe_s.did(f"r{c}"))
                    pe.wait_ge(*dve_s.at(f"r{c}", i))
                    for e in range(2):
                        cols = slice(e * HD, (e + 1) * HD)
                        last = nc.tensor.matmul(ps[:, 1, cols], XT[:, e * NC2 + c], rh[:, cols], start=True, stop=True)
                    last.then_inc(*pe_s.did(f"sa{c}"))
                    for e in range(2):
                        cols = slice(e * HD, (e + 1) * HD)
                        nc.tensor.matmul(ch(two(4))[cols, c], H[:, c, cols], qe[:, c * P:(c + 1) * P], start=True, stop=False)
                    pe.wait_ge(*act_s.at(f"sa{c}", i))
                    if c < NC2 - 1:
                        nc.tensor.matmul(ps[:, 2, 0:P], kt[:, c], sa[:, c], start=True, stop=True).then_inc(*pe_s.did(f"h{c}"))
                    for e in range(2):
                        cols = slice(e * HD, (e + 1) * HD)
                        out = ch(two(4))[cols, c]
                        last = nc.tensor.matmul(out, sa[:, c, cols], gq[:, e * NC2 + c, 1], start=False, stop=True)
                    last.then_inc(*pe_s.did(f"y{c}"))
                pe.wait_ge(*act_s.at("ysq", i))
                wide(0, mk.half[:], At).then_inc(*pe_s.did("mean"))

        @block.vector
        def _(dve):
            dve_a.prime(dve)
            dve_s.prime(dve)
            dve.wait_ge(zeros, ZEROS)
            V = nc.vector

            def first(i):
                def did(name, ins, wait=False):
                    ins.then_inc(*dve_a.did(name))
                    if wait:
                        dve.wait_ge(*dve_a.at(name, i))

                dve.wait_ge(in_s, 48 * i + 48)
                for n in range(3):
                    tap = lambda r: par("gdn_conv_w_2", i + (9 * r + 3 * n))
                    did(f"c0{n}", V.tensor_scalar(z[:, n], buf[:, n, 0:N], tap(0), None, ALU.mult), True)
                    for r in range(1, 4):
                        did(f"c{r}{n}", V.scalar_tensor_tensor(z[:, n], buf[:, n, r:N + r], tap(r), z[:, n], ALU.mult, ALU.add),
                            r < 3)
                    yield
                for c in range(NC2):
                    decays = gB[:, ds(i, 1), c * P:(c + 1) * P].rearrange("p o t -> p (o t)") if not isinstance(i, int) \
                        else gB[:, i, c * P:(c + 1) * P]
                    did(f"s{c}", V.tensor_tensor_scan(gc[:, c * P:(c + 1) * P], co.ones[:], decays, 0.0, ALU.mult, ALU.add),
                        c == NC2 - 1)
                did("dkd", V.tensor_tensor(ch(kd[:]), ch(gc[:])[:, :, P - 1:P].to_broadcast([P, NC2, P]), ch(gc[:]), ALU.subtract))
                yield
                dve.wait_ge(*act_a.at("sg", i))
                dve.wait_ge(*dve_a.at("c32", i))
                did("silu", V.tensor_tensor(z[:], z[:], sg[:], ALU.mult))

            def body(i, following):
                def did(name, ins, wait=False):
                    ins.then_inc(*dve_s.did(name))
                    if wait:
                        dve.wait_ge(*dve_s.at(name, i))

                beta = bB[:, ds(i, 1)].rearrange("p o t -> p (o t)") if not isinstance(i, int) else bB[:, i]
                did("last", V.tensor_copy(decay[:], ch(gc[:])[:, :, P - 1]))
                dve.wait_ge(*act_s.at("root", i))
                did("q", V.scalar_tensor_tensor(ar[:, :, 1], ch(q), HD ** -0.5, ch(rs[:, 0]), ALU.mult, ALU.mult))
                did("k", V.tensor_tensor(k, k, rs[:, 1], ALU.mult), True)
                did("bk", V.scalar_tensor_tensor(ar[:, :, 0], ch(k), -1.0, ch(beta), ALU.mult, ALU.mult))
                did("v", V.tensor_tensor(v, v, beta, ALU.mult))
                dve.wait_ge(*act_s.at("kd", i))
                did("kdk", V.tensor_tensor(kd[:], kd[:], k, ALU.mult), True)
                did("At", V.tensor_tensor(ch(At[:]), ar[:, :, 0], ch(eg[:]), ALU.mult))
                did("qe", V.tensor_tensor(ch(qe[:]), ar[:, :, 1], ch(eg[:]), ALU.mult))
                dve.wait_ge(*pe_s.at("row", i))
                dve.wait_ge(*act_s.at("gct", i))
                for e in range(2):
                    for c in range(NC2):
                        did(f"D{e}{c}", V.tensor_scalar(Dm[:, e, c * P:(c + 1) * P], ch(two(2 * e))[:, c], gct[:, c, e:e + 1], 0.0,
                                                        ALU.subtract, ALU.min))
                inv.eye()
                dve.wait_ge(*pool_s.at("D", i))
                for e in range(2):
                    dve.wait_ge(*pe_s.at(f"g{e}", i))
                    grams = ps[:, 4 * e:4 * e + 4].rearrange("p a b -> p (a b)").rearrange("p (c h t) -> p c h t", h=2, t=P)
                    did(f"gq{e}", V.tensor_tensor(gq[:, e * NC2:(e + 1) * NC2], grams,
                                                  ch(Dm[:, e]).unsqueeze(2).to_broadcast([P, NC2, 2, P]), ALU.mult))
                dve.wait_ge(*dve_s.at("gq1", i))
                inv.dve(dve, i, following)
                dve.wait_ge(*act_s.at("so", i))
                did("gate", V.tensor_tensor(ga[:], ga[:], gi[:], ALU.mult))
                dve.wait_ge(*act_s.at("vt", i))
                for c in range(NC2):
                    dve.wait_ge(*pe_s.at(f"r{c}", i))
                    did(f"r{c}", V.tensor_tensor(rh[:], ps[:, 0, 0:P], vt[:, c], ALU.add))
                    if c < NC2 - 1:
                        dve.wait_ge(*pe_s.at(f"h{c}", i))
                        did(f"ht{c}", V.scalar_tensor_tensor(ht[:], H[:, c], decay[:, c:c + 1], ps[:, 2, 0:P], ALU.mult, ALU.add), True)
                        did(f"H{c}", V.tensor_tensor(H[:, c + 1], ht[:], mk.block[:], ALU.mult), True)
                dve.wait_ge(*act_s.at("yroot", i))
                did("yn", V.scalar_tensor_tensor(y[:], y[:], par("gdn_o_norm_g_2"), At[:], ALU.mult, ALU.mult), True)
                dve.wait_ge(out_s, 16 * i + 16)
                did("yo", V.tensor_tensor(o[:], y[:], ga[:], ALU.mult))

            each_pair(dve, first, body)


def masks_and_gates(co, mk):
    nc = co.nc
    N = SEQ
    H6 = HEADS2
    with ExitStack() as ctx:
        sb = lambda name, shape, dt=F32: ctx.enter_context(nc.sbuf_tensor("dg_" + name, shape, dt))
        b, a, al, e, u, t, lu = (sb(n, [H6, N]) for n in ("b", "a", "al", "e", "u", "t", "lu"))
        cols = sb("cols", [H6, 2])
        sem = lambda n: signal(nc, ctx, "dg_" + n)
        loaded, made, act_d, dve_d, stored = (sem(n) for n in ("loaded", "masks_made", "act", "dve", "stored"))
        block = ctx.enter_context(nc.Block())

        @block.sync
        def _(sp):
            at = GDN_AT + 4 * RW
            sp.dma_start(b[:], co.dram["ppT"][at:at + H6, :]).then_inc(loaded, 16)
            sp.dma_start(a[:], co.dram["ppT"][at + H6:at + 2 * H6, :]).then_inc(loaded, 16)
            sp.dma_start(cols[:, 0:1], co.dram["gdn_a_log_2"]).then_inc(loaded, 16)
            sp.dma_start(cols[:, 1:2], co.dram["gdn_dt_bias_2"]).then_inc(loaded, 16)
            sp.wait_ge(act_d, 1)
            sp.dma_start(co.dram["deltaT"][1], b[:]).then_inc(stored, 16)
            sp.wait_ge(dve_d, 9)
            sp.dma_start(co.dram["deltaT"][0], t[:]).then_inc(stored, 16)
            sp.wait_ge(stored, 32)

        @block.gpsimd
        def _(pool):
            mk.build(pool, nc, made)

        @block.scalar
        def _(act):
            act.wait_ge(loaded, 64)
            nc.scalar.activation(b[:], b[:], ACT.Sigmoid).then_inc(act_d, 1)
            nc.scalar.activation(cols[:, 0:1], cols[:, 0:1], ACT.Exp).then_inc(act_d, 1)
            act.wait_ge(dve_d, 2)
            nc.scalar.activation(e[:], al[:], ACT.Exp, scale=-1.0).then_inc(act_d, 1)
            act.wait_ge(dve_d, 3)
            nc.scalar.activation(lu[:], u[:], ACT.Ln).then_inc(act_d, 1)

        @block.vector
        def _(dve):
            V = nc.vector
            n = [0]

            def did(ins):
                ins.then_inc(dve_d, 1)
                n[0] += 1
                dve.wait_ge(dve_d, n[0])

            dve.wait_ge(loaded, 64)
            did(V.tensor_scalar(a[:], a[:], cols[:, 1:2], None, ALU.add))
            did(V.scalar_tensor_tensor(al[:], a[:], -1.0, a[:], ALU.mult, ALU.max))
            dve.wait_ge(act_d, 3)
            did(V.tensor_scalar(u[:], e[:], 1.0, None, ALU.add))
            did(V.scalar_tensor_tensor(t[:], u[:], -1.0, e[:], ALU.add, ALU.subtract))
            did(V.reciprocal(al[:], u[:]))
            did(V.tensor_tensor(t[:], t[:], al[:], ALU.mult))
            dve.wait_ge(act_d, 4)
            did(V.tensor_tensor(lu[:], lu[:], t[:], ALU.subtract))
            did(V.scalar_tensor_tensor(t[:], a[:], 0.0, lu[:], ALU.max, ALU.add))
            did(V.tensor_scalar(t[:], t[:], cols[:, 0:1], -1.0, ALU.mult, ALU.mult))


def expand_gates(co, gB, bB, rowsel):
    nc = co.nc
    ps = co.psum
    with ExitStack() as ctx:
        rows = ctx.enter_context(nc.sbuf_tensor("dg_rows", [HEADS2, 2, SEQ], F32))
        sel = ctx.enter_context(nc.sbuf_tensor("dg_sel", [HEADS2, PAIRS, 2, HD], F32))
        loaded, sels, act_d, pe_d = (signal(nc, ctx, "dx_" + n) for n in ("loaded", "selectors", "act", "pe"))
        block = ctx.enter_context(nc.Block())

        @block.sync
        def _(sp):
            sp.dma_start(rows[:], co.dram["deltaT"].rearrange("a h t -> h a t")).then_inc(loaded, 16)

        @block.gpsimd
        def _(pool):
            nc.gpsimd.memset(sel[:], 0.0).then_inc(sels, 1)
            nc.gpsimd.memset(rowsel[:], 0.0).then_inc(sels, 1)
            pool.wait_ge(sels, 2)
            nc.gpsimd.affine_select(out=sel[:], in_=sel[:], compare_op=ALU.not_equal, fill=1.0, base=0,
                                    pattern=[[-2, PAIRS], [-1, 2], [0, HD]], channel_multiplier=1).then_inc(sels, 1)
            nc.gpsimd.affine_select(out=rowsel[:], in_=rowsel[:], compare_op=ALU.not_equal, fill=1.0, base=0,
                                    pattern=[[-HD, 2], [0, P]], channel_multiplier=1).then_inc(sels, 1)
            pool.wait_ge(sels, 4)

        @block.tensor
        def _(pe):
            pe.wait_ge(sels, 4)
            pe.wait_ge(loaded, 16)
            for n in range(2):
                if n:
                    pe.wait_ge(act_d, 1)
                for i in range(PAIRS):
                    for h in range(2):
                        last = nc.tensor.matmul(ps[:, 2 * i + h], sel[:, i].rearrange("p e k -> p (e k)"),
                                                rows[:, n, h * 512:(h + 1) * 512], start=True, stop=True)
                last.then_inc(pe_d, 1)

        @block.scalar
        def _(act):
            for n, dst in enumerate((gB, bB)):
                act.wait_ge(pe_d, n + 1)
                nc.scalar.copy(dst[:].rearrange("p i (h t) -> p (i h) t", h=2), ps[:, 0:6]).then_inc(act_d, 1)


HEADS_A = 4
QK = 96
ROT = 32
HALF_TURN = 3.1415925


OTHERS = [0, 1, 2, 5, 6, 7]


def attention(co, y_hi, y_lo):
    nc = co.nc
    N = SEQ
    with ExitStack() as ctx:
        sb = lambda name, shape, dt=F32: ctx.enter_context(nc.sbuf_tensor("ml_" + name, shape, dt))
        cq, ckv = sb("cq", [P, 2, N]), sb("ckv", [P, N])
        cs = sb("cs", [P, 2, N])
        rot = sb("rot", [P, P])
        gain = sb("gain", [P, 2])
        vals = sb("vals", [P, NC2, HEADS_A * HD])
        qk = sb("qk", [P, HEADS_A, 2, N])
        latent(co, cq, ckv, cs, rot, gain, vals)
        queries_keys(co, cq, ckv, cs, rot, gain, qk)
        attend(co, qk, vals, y_hi, y_lo)


def queries_keys(co, cq, ckv, cs, rot, gain, qk):
    nc = co.nc
    N = SEQ
    ps = co.psum
    two = lambda b: ps[:, b:b + 2].rearrange("p a b -> p (a b)")
    four = lambda b: ps[:, b:b + 4].rearrange("p (a b) t -> p a (b t)", a=2)
    halves = [slice(0, 512), slice(512, 1024)]
    with ExitStack() as ctx:
        sb = lambda name, shape, dt=F32: ctx.enter_context(nc.sbuf_tensor("qk_" + name, shape, dt))
        wq, wk = sb("wq", [P, 2, P]), sb("wk", [P, P])
        raw = sb("raw", [P, 2, N])
        sq = sb("sq", [P, 2, N])
        rs = sb("rs", [P, 2 * NC2])
        dg = sb("dg", [P, 2 * NC2, P])
        x, t = sb("x", [P, 2, N]), sb("t", [P, 2, N])
        pe_p = Steps(nc, ctx, "qk_pe_project", ["q", "k"])
        pe_s = Steps(nc, ctx, "qk_pe", ["ss", "rs", "rot"])
        act_s = Steps(nc, ctx, "qk_act", ["q", "k", "sq", "root"])
        dve_s = Steps(nc, ctx, "qk_dve", ["ms", "recip", "dg", "q", "k", "sin", "cos", "qk"])
        w_s, rope_s, zeros = (signal(nc, ctx, "qk_" + n) for n in ("weights_in", "rope_in", "zeros"))
        ZEROS = 3
        block = ctx.enter_context(nc.Block())

        @block.sync
        def _(sp):
            at = RWKV_IN + 2 * P + P
            sp.wait_ge(zeros, ZEROS)
            sp.dma_start(raw[HD:QK, 1], co.dram["ppT"][at:at + ROT, :]).then_inc(rope_s, 16)
            with sp.Fori(0, HEADS_A) as i:
                src_q = co.dram["mla_w_uq_2"].rearrange("(k p) m -> p k m", p=P)[:, :, ds(i * QK, QK)]
                src_k = co.dram["mla_w_ukv_2"][:, ds(i * 2 * HD, HD)]
                sp.wait_ge(*pe_p.at("k", i - 1))
                sp.dma_start(wq[:, :, 0:QK], src_q).then_inc(w_s, 16)
                sp.dma_start(wk[:, 0:HD], src_k).then_inc(w_s, 16)

        @block.gpsimd
        def _(pool):
            for part in (wq, wk, raw):
                nc.gpsimd.memset(part[:], 0.0).then_inc(zeros, 1)

        @block.scalar
        def _(act):
            act_s.prime(act)
            act.wait_ge(zeros, ZEROS)
            act.wait_ge(rope_s, 16)
            with act.Fori(0, HEADS_A) as i:
                act.wait_ge(*dve_s.at("k", i - 1))
                act.wait_ge(*pe_p.at("q", i))
                nc.scalar.copy(raw[:, 0], two(0)).then_inc(*act_s.did("q"))
                act.wait_ge(*pe_p.at("k", i))
                nc.scalar.copy(raw[0:HD, 1], two(2)[0:HD]).then_inc(*act_s.did("k"))
                act.wait_ge(*act_s.at("k", i))
                nc.scalar.activation(sq[:], raw[:], ACT.Square).then_inc(*act_s.did("sq"))
                act.wait_ge(*dve_s.at("recip", i))
                nc.scalar.activation(rs[:], rs[:], ACT.Sqrt).then_inc(*act_s.did("root"))

        @block.tensor
        def _(pe):
            pe_p.prime(pe)
            pe_s.prime(pe)

            def wide(bank, lhsT, rhs, start=True, stop=True):
                for h, cols in enumerate(halves):
                    last = nc.tensor.matmul(ps[:, bank + h], lhsT, rhs[:, cols], start=start, stop=stop)
                return last

            with pe.Fori(0, HEADS_A) as i:
                pe.wait_ge(w_s, 32 * i + 32)
                pe.wait_ge(*act_s.at("k", i - 1))
                wide(0, wq[:, 0], cq[:, 0], stop=False)
                wide(0, wq[:, 1], cq[:, 1], start=False).then_inc(*pe_p.did("q"))
                wide(2, wk[:], ckv).then_inc(*pe_p.did("k"))
                pe.wait_ge(*act_s.at("sq", i))
                pe.wait_ge(*dve_s.at("sin", i - 1))
                for n in range(2):
                    for c in range(NC2):
                        at = n * NC2 + c
                        last = nc.tensor.matmul(ps[:, 4, at:at + 1], sq[:, n, c * P:(c + 1) * P], co.ones[:, 0:1], start=True, stop=True)
                last.then_inc(*pe_s.did("ss"))
                pe.wait_ge(*dve_s.at("dg", i))
                for b in range(4):
                    last = nc.tensor.matmul(ps[:, 4 + b], co.ones[:], dg[:, 4 * b:4 * b + 4].rearrange("p c t -> p (c t)"),
                                            start=True, stop=True)
                last.then_inc(*pe_s.did("rs"))
                pe.wait_ge(*dve_s.at("k", i))
                wide(4, rot[:], x[:, 0])
                wide(6, rot[:], x[:, 1]).then_inc(*pe_s.did("rot"))

        @block.vector
        def _(dve):
            dve_s.prime(dve)
            V = nc.vector
            both = lambda n: cs[:, n].unsqueeze(1).to_broadcast([P, 2, N])
            with dve.Fori(0, HEADS_A) as i:
                dve.wait_ge(*pe_s.at("ss", i))
                V.tensor_scalar(rs[:], ps[:, 4, 0:2 * NC2], 1.0 / QK, EPS, ALU.mult, ALU.add).then_inc(*dve_s.did("ms"))
                dve.wait_ge(*dve_s.at("ms", i))
                V.reciprocal(rs[:], rs[:]).then_inc(*dve_s.did("recip"))
                dve.wait_ge(*act_s.at("root", i))
                V.tensor_tensor(dg[:], co.ident[:].unsqueeze(1).to_broadcast([P, 2 * NC2, P]),
                                rs[:].unsqueeze(2).to_broadcast([P, 2 * NC2, P]), ALU.mult).then_inc(*dve_s.did("dg"))
                dve.wait_ge(*pe_s.at("rs", i))
                dve.wait_ge(*dve_s.at("qk", i - 1))
                for n, name in enumerate("qk"):
                    V.scalar_tensor_tensor(x[:, n], raw[:, n], gain[:, n:n + 1], two(4 + 2 * n), ALU.mult,
                                           ALU.mult).then_inc(*dve_s.did(name))
                dve.wait_ge(*pe_s.at("rot", i))
                V.tensor_tensor(t[:], four(4), both(1), ALU.mult).then_inc(*dve_s.did("sin"))
                V.tensor_tensor(x[:], x[:], both(0), ALU.mult).then_inc(*dve_s.did("cos"))
                dve.wait_ge(*dve_s.at("cos", i))
                V.tensor_tensor(qk[:, ds(i, 1)].rearrange("p o a t -> p (o a) t"), x[:], t[:], ALU.add).then_inc(*dve_s.did("qk"))


def attend(co, qk, vals, y_hi, y_lo):
    nc = co.nc
    N = SEQ
    ps = co.psum
    ch = lambda x: x.rearrange("p (c t) -> p c t", t=P)
    two = lambda b: ps[:, b:b + 2].rearrange("p a b -> p (a b)")
    SCALE = QK ** -0.5
    B = range(NC2)
    with ExitStack() as ctx:
        sb = lambda name, shape, dt=F32: ctx.enter_context(nc.sbuf_tensor("at_" + name, shape, dt))
        h_qk, vh = sb("h_qk", [P, 2, N]), sb("vh", [P, NC2, HD])
        Pm, PT = sb("Pm", [P, 2, N]), sb("PT", [P, NC2, P])
        mx, nm, sm, ri = (sb(n, [P, NC2]) for n in ("mx", "nm", "sm", "ri"))
        dg = sb("dg", [P, 2, P])
        o = sb("o", [HD, N])
        pe_s = Steps(nc, ctx, "at_pe", ["s0", "s1"] + [x for c in B for x in [f"t{c}"] + ([f"s{c + 2}"] if c + 2 < NC2 else []) + [f"o{c}"]])
        act_s = Steps(nc, ctx, "at_act", ["e0"] + [x for c in B for x in ([f"e{c + 1}"] if c + 1 < NC2 else []) + [f"t{c}"]] + ["o"])
        block_max = lambda c: [f"mask{c}", f"mx{c}", f"nm{c}"]
        dve_s = Steps(nc, ctx, "at_dve", ["h_qk", "vh"] + block_max(0)
                      + [x for c in B for x in [f"ri{c}", f"dg{c}"] + (block_max(c + 1) if c + 1 < NC2 else [])])
        out_s = signal(nc, ctx, "at_out")
        other = sb("other", [P, 2, N])
        other_in = [signal(nc, ctx, f"at_other_in{r}") for r in range(2)]
        pool_s = Steps(nc, ctx, "at_pool", [f"{x}{n}" for n in range(len(OTHERS)) for x in ("hi", "lo")])
        block = ctx.enter_context(nc.Block())

        @block.gpsimd
        def _(pool):
            pool_s.prime(pool)
            for n, k in enumerate(OTHERS):
                pool.wait_ge(other_in[n % 2], 16 * (n // 2 + 1))
                nc.gpsimd.tensor_tensor(y_hi[:, k], other[:, n % 2], co.zero[:].to_broadcast([P, N]), ALU.add)\
                  .then_inc(*pool_s.did(f"hi{n}"))
                pool.wait_ge(*pool_s.at(f"hi{n}"))
                nc.gpsimd.tensor_tensor(y_lo[:, k], other[:, n % 2], y_hi[:, k].bitcast(F32), ALU.subtract)\
                  .then_inc(*pool_s.did(f"lo{n}"))

        @block.sync
        def _(sp):
            for n, k in enumerate(OTHERS):
                if n >= 2:
                    sp.wait_ge(*pool_s.at(f"lo{n - 2}"))
                sp.dma_start(other[:, n % 2], co.dram["yT"][k * P:(k + 1) * P, :]).then_inc(other_in[n % 2], 16)
            with sp.Fori(0, HEADS_A) as i:
                dest = co.dram["yT"][ds(RW + i * HD, HD), :]
                sp.wait_ge(*act_s.at("o", i))
                sp.dma_start(dest, o[:]).then_inc(out_s, 16)
            sp.wait_ge(out_s, 16 + 16 * HEADS_A)

        @block.scalar
        def _(act):
            act_s.prime(act)
            act.sem_inc(out_s, 16)
            with act.Fori(0, HEADS_A) as i:
                def exponential(c):
                    L = (c + 1) * P
                    act.wait_ge(*dve_s.at(f"nm{c}", i))
                    if c >= 2:
                        act.wait_ge(*pe_s.at(f"t{c - 2}", i))
                    nc.scalar.activation(Pm[:, c % 2, 0:L], two(2 * (c % 2))[:, 0:L], ACT.Exp, bias=nm[:, c:c + 1],
                                         scale=SCALE, accum_out=sm[:, c:c + 1]).then_inc(*act_s.did(f"e{c}"))

                exponential(0)
                for c in B:
                    if c + 1 < NC2:
                        exponential(c + 1)
                    act.wait_ge(*pe_s.at(f"t{c}", i))
                    nc.scalar.copy(PT[:, 0:c + 1], ch(two(4))[:, 0:c + 1]).then_inc(*act_s.did(f"t{c}"))
                act.wait_ge(out_s, 16 * i + 16)
                act.wait_ge(*pe_s.at(f"o{NC2 - 1}", i))
                nc.scalar.copy(o[:], two(6)[0:HD]).then_inc(*act_s.did("o"))

        @block.tensor
        def _(pe):
            pe_s.prime(pe)
            with pe.Fori(0, HEADS_A) as i:
                def scores(c):
                    L = (c + 1) * P
                    if c >= 2:
                        pe.wait_ge(*act_s.at(f"e{c - 2}", i))
                    for h in range(-(-L // 512)):
                        cols = slice(h * 512, min(L, (h + 1) * 512))
                        last = nc.tensor.matmul(two(2 * (c % 2))[:, cols], h_qk[:, 0, c * P:L], h_qk[:, 1, cols], start=True, stop=True)
                    last.then_inc(*pe_s.did(f"s{c}"))

                pe.wait_ge(*dve_s.at("h_qk", i))
                pe.wait_ge(*act_s.at(f"e{NC2 - 1}", i - 1))
                scores(0)
                scores(1)
                pe.wait_ge(*dve_s.at("vh", i))
                pe.wait_ge(*act_s.at("o", i - 1))
                for c in B:
                    pe.wait_ge(*dve_s.at(f"dg{c}", i))
                    if c:
                        pe.wait_ge(*act_s.at(f"t{c - 1}", i))
                    for k in range(c + 1):
                        last = nc.tensor.matmul(ch(two(4))[:, k], Pm[:, c % 2, k * P:(k + 1) * P], dg[:, c % 2], start=True, stop=True)
                    last.then_inc(*pe_s.did(f"t{c}"))
                    if c + 2 < NC2:
                        scores(c + 2)
                    pe.wait_ge(*act_s.at(f"t{c}", i))
                    for k in range(c + 1):
                        last = nc.tensor.matmul(ch(two(6))[0:HD, c], vh[:, k], PT[:, k], start=k == 0, stop=k == c)
                    last.then_inc(*pe_s.did(f"o{c}"))

        @block.vector
        def _(dve):
            dve_s.prime(dve)
            V = nc.vector
            with dve.Fori(0, HEADS_A) as i:
                def did(name, ins, wait=False):
                    ins.then_inc(*dve_s.did(name))
                    if wait:
                        dve.wait_ge(*dve_s.at(name, i))

                def maximum(c):
                    L = (c + 1) * P
                    bank = two(2 * (c % 2))
                    dve.wait_ge(*pe_s.at(f"s{c}", i))
                    did(f"mask{c}", V.memset(bank[0:HD, L - HD:L], -1e30), True)
                    did(f"mx{c}", V.tensor_reduce(mx[:, c:c + 1], bank[:, 0:L], AX_X, ALU.max), True)
                    did(f"nm{c}", V.tensor_scalar(nm[:, c:c + 1], mx[:, c:c + 1], -SCALE, None, ALU.mult))

                dve.wait_ge(*pe_s.at(f"s{NC2 - 1}", i - 1))
                did("h_qk", V.tensor_copy(h_qk[:], qk[:, ds(i, 1)].rearrange("p o a t -> p (o a) t")))
                dve.wait_ge(*pe_s.at(f"o{NC2 - 1}", i - 1))
                did("vh", V.tensor_copy(vh[:], vals[:, :, ds(i * HD, HD)]))
                maximum(0)
                for c in B:
                    dve.wait_ge(*act_s.at(f"e{c}", i))
                    did(f"ri{c}", V.reciprocal(ri[:, c:c + 1], sm[:, c:c + 1]), True)
                    if c >= 2:
                        dve.wait_ge(*pe_s.at(f"t{c - 2}", i))
                    did(f"dg{c}", V.tensor_scalar(dg[:, c % 2], co.ident[:], ri[:, c:c + 1], None, ALU.mult))
                    if c + 1 < NC2:
                        maximum(c + 1)


def latent(co, cq, ckv, cs, rot, gain, vals):
    nc = co.nc
    N = SEQ
    ps, par = co.psum, co.par
    TURN = 2 * np.pi
    C1 = 6.28125
    C2 = 507 / 2.0 ** 18
    C3 = TURN - C1 - C2
    MAGIC = 1.5 * 2.0 ** 23
    with ExitStack() as ctx:
        sb = lambda name, shape, dt=F32: ctx.enter_context(nc.sbuf_tensor("la_" + name, shape, dt))
        sq, rs = sb("sq", [P, 3, N]), sb("rs", [P, 2, N])
        wv = sb("wv", [P, HEADS_A, HD])
        pos, freq = sb("pos", [P, N], I32), sb("freq", [P, 1])
        ang, turns = sb("ang", [P, N]), sb("turns", [P, 2, N])
        sem = lambda n: signal(nc, ctx, "la_" + n)
        in_s, freq_s, pos_s, zero_s, made = (sem(n) for n in ("in", "freq_in", "pos_in", "zero", "made"))
        act_d, dve_d, pe_d = (sem(n) for n in ("act", "dve", "pe"))
        block = ctx.enter_context(nc.Block())

        @block.sync
        def _(sp):
            at = RWKV_IN
            sp.dma_start(cq[:], co.dram["ppT"][at:at + 2 * P, :].rearrange("(k p) t -> p k t", p=P)).then_inc(in_s, 16)
            sp.dma_start(ckv[:], co.dram["ppT"][at + 2 * P:at + 3 * P, :]).then_inc(in_s, 16)
            sp.dma_start(wv[:], co.dram["mla_w_ukv_2"].rearrange("p (h k) -> p h k", k=2 * HD)[:, :, HD:2 * HD]).then_inc(in_s, 16)
            sp.dma_start(pos[:], co.dram["positions"].to_broadcast([P, N])).then_inc(pos_s, 16)
            sp.wait_ge(zero_s, 2)
            sp.dma_start(freq[HD:QK], co.dram["inverse_frequency"]).then_inc(freq_s, 16)
            sp.dma_start(gain[0:QK, 0:1], co.dram["mla_q_qk_g_2"]).then_inc(freq_s, 16)
            sp.dma_start(gain[0:QK, 1:2], co.dram["mla_k_qk_g_2"]).then_inc(freq_s, 16)

        @block.gpsimd
        def _(pool):
            nc.gpsimd.memset(freq[:], 0.0).then_inc(zero_s, 1)
            nc.gpsimd.memset(gain[:], 0.0).then_inc(zero_s, 1)
            nc.gpsimd.memset(rot[:], 0.0).then_inc(made, 1)
            pool.wait_ge(made, 1)
            for at, base, fill in ((HD, -HD - ROT // 2, -1.0), (HD + ROT // 2, -HD, 1.0)):
                view = rot[:, at:at + ROT // 2]
                nc.gpsimd.affine_select(out=view, in_=view, compare_op=ALU.not_equal, fill=fill, base=base,
                                        pattern=[[-1, ROT // 2]], channel_multiplier=1).then_inc(made, 1)
            pool.wait_ge(made, 3)

        @block.scalar
        def _(act):
            act.wait_ge(in_s, 48)
            nc.scalar.activation(sq[:, 0:2], cq[:], ACT.Square).then_inc(act_d, 1)
            nc.scalar.activation(sq[:, 2], ckv[:], ACT.Square).then_inc(act_d, 1)
            act.wait_ge(pe_d, 1)
            rs2 = rs[:].rearrange("p a (b t) -> p a b t", b=2)
            nc.scalar.activation(rs2[:, 0], ps[:, 0:2], ACT.Ln, scale=0.5 / P, bias=co.eps[:]).then_inc(act_d, 1)
            nc.scalar.activation(rs2[:, 1], ps[:, 2:4], ACT.Ln, scale=1.0 / P, bias=co.eps[:]).then_inc(act_d, 1)
            act.wait_ge(act_d, 4)
            nc.scalar.activation(rs[:], rs[:], ACT.Exp, scale=-0.5).then_inc(act_d, 1)
            act.wait_ge(dve_d, 10)
            nc.scalar.activation(cs[:], cs[:], ACT.Sin).then_inc(act_d, 1)
            act.wait_ge(pe_d, 2)
            nc.scalar.copy(vals[:].rearrange("p (b c) m -> p b (c m)", b=4), ps[:, 4:8]).then_inc(act_d, 1)

        @block.tensor
        def _(pe):
            pe.wait_ge(act_d, 2)
            for h in range(2):
                cols = slice(h * 512, (h + 1) * 512)
                nc.tensor.matmul(ps[:, h], co.ones[:], sq[:, 0, cols], start=True, stop=False)
                nc.tensor.matmul(ps[:, h], co.ones[:], sq[:, 1, cols], start=False, stop=True)
                last = nc.tensor.matmul(ps[:, 2 + h], co.ones[:], sq[:, 2, cols], start=True, stop=True)
            last.then_inc(pe_d, 1)
            pe.wait_ge(dve_d, 13)
            for c in range(NC2):
                last = nc.tensor.matmul(ps[:, 4 + c // 2, (c % 2) * 256:(c % 2) * 256 + 256], ckv[:, c * P:(c + 1) * P],
                                        wv[:].rearrange("p h k -> p (h k)"), start=True, stop=True)
            last.then_inc(pe_d, 1)

        @block.vector
        def _(dve):
            V = nc.vector
            n = [0]

            def did(ins):
                ins.then_inc(dve_d, 1)
                n[0] += 1
                dve.wait_ge(dve_d, n[0])

            dve.wait_ge(pos_s, 16)
            dve.wait_ge(freq_s, 48)
            did(V.tensor_copy(ang[:], pos[:]))
            did(V.tensor_scalar(ang[:], ang[:], freq[:], None, ALU.mult))
            for x in range(2):
                did(V.tensor_scalar(turns[:, x], ang[:], 1 / TURN, (0.25, 0.0)[x], ALU.mult, ALU.add))
            did(V.tensor_scalar(turns[:], turns[:], MAGIC, MAGIC, ALU.add, ALU.subtract))
            src = ang[:].unsqueeze(1).to_broadcast([P, 2, N])
            for part in (C1, C2, C3):
                did(V.scalar_tensor_tensor(cs[:], turns[:], -part, src, ALU.mult, ALU.add))
                src = cs[:]
            did(V.tensor_scalar(cs[:, 0], cs[:, 0], np.pi / 2, None, ALU.add))
            did(V.tensor_scalar(cs[:], cs[:], HALF_TURN, -HALF_TURN, ALU.min, ALU.max))
            dve.wait_ge(act_d, 5)
            for k in range(2):
                did(V.scalar_tensor_tensor(cq[:, k], cq[:, k], par("mla_q_norm_g_2", k), rs[:, 0], ALU.mult, ALU.mult))
            did(V.scalar_tensor_tensor(ckv[:], ckv[:], par("mla_kv_norm_g_2"), rs[:, 1], ALU.mult, ALU.mult))


def build(nc, dram):
    RETIRED.clear()
    with ExitStack() as ctx:
        co = Core(nc, ctx, dram)
        start_up(co)
        block_one(co, dram)
        clear_retired(nc)
        block_two(co, dram)


def block_one(co, dram):
    nc = co.nc
    W = SEQ + TAIL
    with ExitStack() as scope:
        x_hi, x_lo = (scope.enter_context(nc.sbuf_tensor(n, [P, KD, T1], F32R)) for n in ("x_hi", "x_lo"))
        seen_hi, seen_lo = x_hi[:, :, 0:W], x_lo[:, :, 0:W]
        seq_hi, seq_lo = x_hi[:, :, 0:SEQ], x_lo[:, :, 0:SEQ]
        with ExitStack() as mix:
            co.weights(mix)
            norm_split(co, "n1_", dram["h0T"], PAD, META + SEQ, "mix_norm_pre", x_hi, x_lo)
            hgrn_heads(co, x_hi, x_lo)
            a_hi, a_lo, p_hi, p_lo = (mix.enter_context(nc.sbuf_tensor(n, [P, 4, W], F32R))
                                      for n in ("a_hi", "a_lo", "p_hi", "p_lo"))
            pool_branch(co, x_hi, x_lo, p_hi, p_lo, a_hi, a_lo)
            gated_sum(co, a_hi, a_lo, p_hi, p_lo, seen_hi, seen_lo)
        co.weights(scope, 6)
        with ExitStack() as out:
            y = out.enter_context(nc.sbuf_tensor("mix_y", [P, KD, W], F32))
            square_product(co, dram["w_out"], seen_hi, seen_lo, y, W, 3)
            first = feed_forward_first(co, seen_hi, seen_lo, dram["ffn_w_up"], dram["ffn_w_gate"])
            residual_norm_split(co, "r1_", dram["h0T"][:, META - TAIL:], y, W, "mix_norm_post", dram["h1T"],
                                "ffn_norm_pre", seen_hi, seen_lo, first, 4)
        with ExitStack() as ffn:
            acc = ffn.enter_context(nc.sbuf_tensor("ffn_acc", [P, KD, SEQ], F32))
            feed_forward(co, "f1_", seen_hi, seen_lo, dram["ffn_w_up"], dram["ffn_w_down"], acc, first, dram["ffn_w_gate"])
            first = projection_first(co, seq_hi, seq_lo)
            residual_norm_split(co, "r2_", dram["h1T"][:, TAIL:], acc, SEQ, "ffn_norm_post", dram["h2T"],
                                "ln_mix_g_2", seq_hi, seq_lo, first, 4)
        input_projection(co, seq_hi, seq_lo, first)


def block_two(co, dram):
    nc = co.nc
    with ExitStack() as ctx:
        mk = Masks(co, ctx)
        masks_and_gates(co, mk)
        rwkv(co, mk)
        deltanet(co, mk)
    with ExitStack() as scope:
        x_hi, x_lo = (scope.enter_context(nc.sbuf_tensor(n, [P, KD, SEQ], F32R)) for n in ("y_hi", "y_lo"))
        attention(co, x_hi, x_lo)
        y = scope.enter_context(nc.sbuf_tensor("sum_y", [P, KD, SEQ], F32))
        co.weights(scope)
        split_from_dram(co, "ys_", dram["yT"], [k for k in range(KD) if k not in OTHERS], SEQ, x_hi, x_lo)
        square_product(co, dram["w_out_2"], x_hi, x_lo, y, SEQ, 2)
        first = feed_forward_first(co, x_hi, x_lo, dram["w_ff1_2"])
        residual_norm_split(co, "r3_", dram["h2T"], y, SEQ, None, None, "ln_ffn_g_2", x_hi, x_lo, first, 2)
        feed_forward(co, "f2_", x_hi, x_lo, dram["w_ff1_2"], dram["w_ff2_2"], y, first, dest=dram["outT"])


SCRATCH = [("aT", (D // 2, SEQ + TAIL)), ("gateT", (2 * D, SEQ + TAIL)), ("ppT", (P_IN, SEQ)), ("yT", (D, SEQ)), ("h1T", (D, SEQ + TAIL)), ("h2T", (D, SEQ)), ("deltaT", (2, HEADS2, SEQ))]


def layout(x):
    out = {}
    for name in ("w_in", "w_branch_hgrn", "w_branch_pool", "w_out", "ffn_w_gate", "ffn_w_up", "ffn_w_down",
                 "w_in_2", "w_out_2", "w_ff1_2", "w_ff2_2", "rwkv_w2_2", "rwkv_a2_2", "rwkv_g2_2",
                 "mla_w_uq_2", "mla_w_ukv_2", "pool_proj"):
        out[name] = np.ascontiguousarray(x[name][0])
    out["h0T"] = np.ascontiguousarray(np.concatenate([x["meta_tokens"], x["x"][0]], axis=0).T)
    vectors = dict(x)
    vectors["gdn_o_norm_g_2"] = np.tile(x["gdn_o_norm_g_2"], (1, 2))
    out["vectors"] = np.ascontiguousarray(np.concatenate(
        [np.reshape(vectors[name], (n, P)) for name, n in PARAM_TILES], axis=0).T)
    for name in ("gdn_a_log_2", "gdn_dt_bias_2", "mla_q_qk_g_2", "mla_k_qk_g_2"):
        out[name] = np.reshape(x[name], (-1, 1))
    half = np.arange(0, ROT, 2) / ROT
    out["inverse_frequency"] = np.tile(10000.0 ** -half, 2).astype(np.float32).reshape(ROT, 1)
    out["positions"] = np.reshape(x["positions_2"], (1, SEQ))
    return out


def kernel(**inputs):
    import concourse.bacc as bacc
    from concourse.bass_utils import run_bass_kernel_spmd

    nc = bacc.Bacc("TRN2", target_bir_lowering=False, num_devices=1)
    arrays = layout({name: np.asarray(value) for name, value in inputs.items()})
    dram = {}
    for name, value in arrays.items():
        dram[name] = nc.dram_tensor(name, value.shape, mybir.dt.from_np(value.dtype), kind="ExternalInput").ap()
    for name, shape in SCRATCH:
        dram[name] = nc.dram_tensor(name, shape, F32, kind="Internal").ap()
    dram["outT"] = nc.dram_tensor("outT", (D, SEQ), F32, kind="ExternalOutput").ap()
    build(nc, dram)
    result = run_bass_kernel_spmd(nc, [arrays], core_ids=[0])
    return np.ascontiguousarray(result.results[0]["outT"].T).reshape(1, SEQ, D)
```
